# Optimizing a Trainium2 kernel written in Bass

```python
import math
import jax, jax.numpy as jnp
from jax import lax
import numpy as np
import jax
import jax.numpy as jnp

D_MODEL = 1024
BATCH = 1
SEQ = 512
DEPTH = 1

HEAD_DIM = 64
ATT_WIDTH = D_MODEL // 2
RWKV_WIDTH = D_MODEL - ATT_WIDTH
ATT_HEADS = ATT_WIDTH // HEAD_DIM
RWKV_HEADS = RWKV_WIDTH // HEAD_DIM
MIX_WIDTH = ATT_WIDTH + RWKV_WIDTH
DILATED_PATTERNS = ((128, 1), (512, 4), (2048, 16))
DECAY_LORA = 64
AAA_LORA = 64
GATE_LORA = 128
SHIFT_WIDTH = 3 * RWKV_WIDTH + DECAY_LORA + AAA_LORA + GATE_LORA
IN_WIDTH = 3 * ATT_WIDTH + SHIFT_WIDTH
PEER_N_KEYS = 128
PEER_N_EXPERTS = PEER_N_KEYS * PEER_N_KEYS
PEER_HEADS = 8
PEER_KEY_DIM = 256
PEER_TOPK = 16
PEER_TOKEN_BLOCK = 128
NORM_EPS = 1e-6
LNX_EPS = 64e-5
MASK_VALUE = -1e30


def rms_norm(x, g, eps=NORM_EPS):
    x32 = x.astype(jnp.float32)
    y = x32 * lax.rsqrt(jnp.mean(x32 * x32, axis=-1, keepdims=True) + eps)
    return y * g.astype(jnp.float32)

def alibi_slopes(n_heads):
    return jnp.exp2(-8.0 * (jnp.arange(n_heads, dtype=jnp.float32) + 1.0) / n_heads)

def dilated_window_attention(q, k, v, slopes, window, dilation):
    B, S, H, E = q.shape
    d = dilation
    n = window // (2 * d)
    L = S // d
    nb = -(-L // n)
    Lp = nb * n
    qs = jnp.pad(q.reshape(B, L, d, H, E), ((0, 0), (0, Lp - L), (0, 0), (0, 0), (0, 0)))
    qs = qs.reshape(B, nb, n, d, H, E)

    def neighbourhood(t):
        tp = jnp.pad(t.reshape(B, L, d, H, E), ((0, 0), (n, Lp - L + n), (0, 0), (0, 0), (0, 0)))
        tp = tp.reshape(B, nb + 2, n, d, H, E)
        return jnp.concatenate([tp[:, :-2], tp[:, 1:-1], tp[:, 2:]], axis=2)

    kb = neighbourhood(k)
    vb = neighbourhood(v)
    qi = jnp.arange(nb)[:, None] * n + jnp.arange(n)[None, :]
    kj = (jnp.arange(nb)[:, None] - 1) * n + jnp.arange(3 * n)[None, :]
    off = kj[:, None, :] - qi[:, :, None]
    valid = (jnp.abs(off) <= n) & (kj[:, None, :] >= 0) & (kj[:, None, :] < L)
    dist = (d * jnp.abs(off)).astype(jnp.float32)

    s = jnp.einsum('bnqrhe,bnkrhe->bhrnqk', qs, kb) * (E ** -0.5)
    s = s - slopes[None, :, None, None, None, None] * dist[None, None, None]
    s = jnp.where(valid[None, None, None], s, MASK_VALUE)
    m = jnp.max(s, axis=-1, keepdims=True)
    p = jnp.exp(s - m)
    den = jnp.sum(p, axis=-1)
    lse = m[..., 0] + jnp.log(den)
    out = jnp.einsum('bhrnqk,bnkrhe->bnqrhe', p, vb)
    out = out / jnp.transpose(den, (0, 3, 4, 2, 1))[..., None]
    out = out.reshape(B, Lp, d, H, E)[:, :L].reshape(B, S, H, E)
    lse = jnp.transpose(lse, (0, 3, 4, 2, 1)).reshape(B, Lp, d, H)[:, :L].reshape(B, S, H)
    return out, lse

def dilated_mixture_attention(q, k, v):
    slopes = alibi_slopes(q.shape[2])
    outs, lses = [], []
    for window, dilation in DILATED_PATTERNS:
        o, l = dilated_window_attention(q, k, v, slopes, window, dilation)
        outs.append(o)
        lses.append(l)
    wts = jax.nn.softmax(jnp.stack(lses, axis=0), axis=0)
    return jnp.einsum('pbsh,pbshe->bshe', wts, jnp.stack(outs, axis=0))

def token_shift(z, mu_prev, mu_next):
    z_prev = jnp.pad(z, ((0, 0), (1, 0), (0, 0)))[:, :-1]
    z_next = jnp.pad(z, ((0, 0), (0, 1), (0, 0)))[:, 1:]
    return z + mu_prev * (z_prev - z) + mu_next * (z_next - z)

def wkv7_scan(r, w, k, v, kk, a, reverse):
    B, S, H, N = r.shape
    xs = tuple(jnp.moveaxis(t, 1, 0) for t in (r, w, k, v, kk, a))
    state0 = jnp.zeros((B, H, N, N), jnp.float32)

    def step(state, inp):
        r_t, w_t, k_t, v_t, kk_t, a_t = inp
        sa = jnp.einsum('bhvk,bhk->bhv', state, -kk_t)
        state = (state * w_t[:, :, None, :]
                 + sa[..., :, None] * (kk_t * a_t)[..., None, :]
                 + v_t[..., :, None] * k_t[..., None, :])
        y = jnp.einsum('bhvk,bhk->bhv', state, r_t)
        return state, y

    _, ys = lax.scan(step, state0, xs, reverse=reverse)
    return jnp.moveaxis(ys, 0, 1)

def rwkv7_bidirectional(r, k, v, xw, xa, xg, w_decay0, w_decay_up, a_gate0, a_gate_up,
                        g_up, k_k, k_a, r_k, lnx_g, lnx_b):
    B, S, _ = r.shape

    def hs(t):
        return t.reshape(B, S, RWKV_HEADS, HEAD_DIM)

    g = jax.nn.sigmoid(xg) @ g_up
    kk = hs(k * k_k)
    kk = kk * lax.rsqrt(jnp.maximum(jnp.sum(kk * kk, axis=-1, keepdims=True), 1e-12))
    ys, a_dirs = [], []
    for direction in range(2):
        w = -jax.nn.softplus(-(w_decay0[direction] + jnp.tanh(xw) @ w_decay_up[direction])) - 0.5
        decay = jnp.exp(-jnp.exp(w))
        a = jax.nn.sigmoid(a_gate0[direction] + xa @ a_gate_up[direction])
        k_dir = k * (1.0 + (a - 1.0) * k_a)
        ys.append(wkv7_scan(hs(r), hs(decay), hs(k_dir), hs(v), kk, hs(a), reverse=(direction == 1)))
        a_dirs.append(a)
    y = ys[0] + ys[1]
    mean = jnp.mean(y, axis=-1, keepdims=True)
    var = jnp.mean(jnp.square(y - mean), axis=-1, keepdims=True)
    yn = ((y - mean) * lax.rsqrt(var + LNX_EPS)).reshape(B, S, RWKV_WIDTH) * lnx_g + lnx_b
    k_bonus = hs(k * (1.0 + (0.5 * (a_dirs[0] + a_dirs[1]) - 1.0) * k_a))
    bonus = jnp.sum(hs(r) * k_bonus * r_k, axis=-1, keepdims=True) * hs(v)
    return (yn + bonus.reshape(B, S, RWKV_WIDTH)) * g

def peer_ffn(h, w_query, sub_keys1, sub_keys2, expert_u, expert_v):
    B, S, D = h.shape
    T = B * S
    half = PEER_KEY_DIM // 2
    x = h.reshape(T, D)
    q = (x @ w_query).astype(jnp.float32).reshape(T, PEER_HEADS, PEER_KEY_DIM)
    s1 = jnp.einsum('thd,nd->thn', q[..., :half], sub_keys1.astype(jnp.float32))
    s2 = jnp.einsum('thd,nd->thn', q[..., half:], sub_keys2.astype(jnp.float32))
    v1, i1 = lax.top_k(s1, PEER_TOPK)
    v2, i2 = lax.top_k(s2, PEER_TOPK)
    cand = (v1[..., :, None] + v2[..., None, :]).reshape(T, PEER_HEADS, PEER_TOPK * PEER_TOPK)
    top_s, top_p = lax.top_k(cand, PEER_TOPK)
    e_idx = (jnp.take_along_axis(i1, top_p // PEER_TOPK, axis=-1) * PEER_N_KEYS
             + jnp.take_along_axis(i2, top_p % PEER_TOPK, axis=-1))
    gate = jax.nn.softmax(top_s, axis=-1)
    HK = PEER_HEADS * PEER_TOPK
    nblk = T // PEER_TOKEN_BLOCK
    xb = x.reshape(nblk, PEER_TOKEN_BLOCK, D)
    ib = e_idx.reshape(nblk, PEER_TOKEN_BLOCK, HK)
    gb = gate.reshape(nblk, PEER_TOKEN_BLOCK, HK)

    def block(args):
        xc, ic, gc = args
        u = jnp.take(expert_u, ic, axis=0)
        act = jax.nn.gelu(jnp.einsum('cd,ced->ce', xc, u).astype(jnp.float32), approximate=False)
        vv = jnp.take(expert_v, ic, axis=0)
        return jnp.einsum('ce,ced->cd', (gc * act).astype(vv.dtype), vv)

    y = lax.map(block, (xb, ib, gb))
    return y.reshape(B, S, D)

def first_inputs(seed: int = 0) -> dict:
    key = jax.random.key(seed)
    ks = jax.random.split(key, 32)
    f32 = jnp.float32
    nrm = lambda k, shape, s: jax.random.normal(k, shape, f32) * s
    RW = RWKV_WIDTH
    return {
        "x": nrm(ks[0], (BATCH, SEQ, D_MODEL), 1.0),
        "c": nrm(ks[1], (BATCH, D_MODEL), 1.0),
        "ada_w": nrm(ks[2], (DEPTH, D_MODEL, 6 * D_MODEL), 0.5 * D_MODEL ** -0.5),
        "ada_b": nrm(ks[3], (DEPTH, 6 * D_MODEL), 0.1),
        "norm1_g": 1.0 + nrm(ks[4], (DEPTH, D_MODEL), 0.05),
        "w_in": nrm(ks[5], (DEPTH, D_MODEL, IN_WIDTH), D_MODEL ** -0.5),
        "mu_prev": jax.random.uniform(ks[6], (DEPTH, SHIFT_WIDTH), f32, 0.0, 0.5),
        "mu_next": jax.random.uniform(ks[7], (DEPTH, SHIFT_WIDTH), f32, 0.0, 0.5),
        "q_norm_g": 1.0 + nrm(ks[8], (DEPTH, HEAD_DIM), 0.05),
        "k_norm_g": 1.0 + nrm(ks[9], (DEPTH, HEAD_DIM), 0.05),
        "w_decay0": jax.random.uniform(ks[10], (DEPTH, 2, RW), f32, -5.0, -1.0),
        "w_decay_up": nrm(ks[11], (DEPTH, 2, DECAY_LORA, RW), 0.5 * DECAY_LORA ** -0.5),
        "a_gate0": nrm(ks[12], (DEPTH, 2, RW), 0.5),
        "a_gate_up": nrm(ks[13], (DEPTH, 2, AAA_LORA, RW), AAA_LORA ** -0.5),
        "g_up": nrm(ks[14], (DEPTH, GATE_LORA, RW), GATE_LORA ** -0.5),
        "k_k": 0.85 + nrm(ks[15], (DEPTH, RW), 0.05),
        "k_a": 1.0 + nrm(ks[16], (DEPTH, RW), 0.05),
        "r_k": nrm(ks[17], (DEPTH, RWKV_HEADS, HEAD_DIM), 0.1),
        "lnx_g": 1.0 + nrm(ks[18], (DEPTH, RW), 0.05),
        "lnx_b": nrm(ks[19], (DEPTH, RW), 0.01),
        "w_out": nrm(ks[20], (DEPTH, MIX_WIDTH, D_MODEL), MIX_WIDTH ** -0.5),
        "norm2_g": 1.0 + nrm(ks[21], (DEPTH, D_MODEL), 0.05),
        "peer_w_query": nrm(ks[22], (DEPTH, D_MODEL, PEER_HEADS * PEER_KEY_DIM), D_MODEL ** -0.5),
        "peer_sub_keys1": nrm(ks[23], (DEPTH, PEER_N_KEYS, PEER_KEY_DIM // 2), (PEER_KEY_DIM // 2) ** -0.5),
        "peer_sub_keys2": nrm(ks[24], (DEPTH, PEER_N_KEYS, PEER_KEY_DIM // 2), (PEER_KEY_DIM // 2) ** -0.5),
        "peer_u": nrm(ks[25], (DEPTH, PEER_N_EXPERTS, D_MODEL), D_MODEL ** -0.5),
        "peer_v": nrm(ks[26], (DEPTH, PEER_N_EXPERTS, D_MODEL), (PEER_HEADS * PEER_TOPK) ** -0.5),
    }

def first_block(x, c, ada_w, ada_b, norm1_g, w_in, mu_prev, mu_next, q_norm_g, k_norm_g,
              w_decay0, w_decay_up, a_gate0, a_gate_up, g_up, k_k, k_a, r_k, lnx_g, lnx_b,
              w_out, norm2_g, peer_w_query, peer_sub_keys1, peer_sub_keys2, peer_u, peer_v):
    in_dtype = x.dtype
    B, S, _ = x.shape
    A = ATT_WIDTH
    RW = RWKV_WIDTH
    for l in range(DEPTH):
        mod = (jax.nn.silu(c.astype(jnp.float32)) @ ada_w[l].astype(jnp.float32)
               + ada_b[l].astype(jnp.float32))[:, None, :]
        shift1, scale1, gate1, shift2, scale2, gate2 = jnp.split(mod, 6, axis=-1)

        h = rms_norm(x, norm1_g[l]) * (1.0 + scale1) + shift1
        z = (h.astype(in_dtype) @ w_in[l]).astype(jnp.float32)
        qa = rms_norm(z[..., :A].reshape(B, S, ATT_HEADS, HEAD_DIM), q_norm_g[l])
        ka = rms_norm(z[..., A:2 * A].reshape(B, S, ATT_HEADS, HEAD_DIM), k_norm_g[l])
        va = z[..., 2 * A:3 * A].reshape(B, S, ATT_HEADS, HEAD_DIM)
        att = dilated_mixture_attention(qa, ka, va).reshape(B, S, A)

        zr = token_shift(z[..., 3 * A:], mu_prev[l].astype(jnp.float32), mu_next[l].astype(jnp.float32))
        o1, o2, o3 = RW, 2 * RW, 3 * RW
        o4, o5 = o3 + DECAY_LORA, o3 + DECAY_LORA + AAA_LORA
        rw = rwkv7_bidirectional(
            zr[..., :o1], zr[..., o1:o2], zr[..., o2:o3],
            zr[..., o3:o4], zr[..., o4:o5], zr[..., o5:],
            w_decay0[l].astype(jnp.float32), w_decay_up[l].astype(jnp.float32),
            a_gate0[l].astype(jnp.float32), a_gate_up[l].astype(jnp.float32),
            g_up[l].astype(jnp.float32), k_k[l].astype(jnp.float32), k_a[l].astype(jnp.float32),
            r_k[l].astype(jnp.float32), lnx_g[l].astype(jnp.float32), lnx_b[l].astype(jnp.float32))
        mixed = jnp.concatenate([att, rw], axis=-1).astype(in_dtype) @ w_out[l]
        x = (x.astype(jnp.float32) + gate1 * mixed.astype(jnp.float32)).astype(in_dtype)

        h2 = (rms_norm(x, norm2_g[l]) * (1.0 + scale2) + shift2).astype(in_dtype)
        ff = peer_ffn(h2, peer_w_query[l], peer_sub_keys1[l], peer_sub_keys2[l], peer_u[l], peer_v[l])
        x = (x.astype(jnp.float32) + gate2 * ff.astype(jnp.float32)).astype(in_dtype)
    return x


RET_W = 3 * D_MODEL // 8
RET_HEADS = RET_W // HEAD_DIM
HGRN_W = 3 * D_MODEL // 8
HGRN_HEADS = HGRN_W // HEAD_DIM
HGRN_DK = HEAD_DIM
GLA_W = D_MODEL // 4
GLA_HEADS = GLA_W // HEAD_DIM
GLA_DK = HEAD_DIM // 2
GLA_QK = GLA_HEADS * GLA_DK
GLA_GATE_RANK = 16
GLA_TAU = 16.0
D_MIX = RET_W + HGRN_W + GLA_W
CHUNK = 64
ROPE_BASE = 10000.0
EPS = 1e-6
F_MIN = 1e-30
N_GROUPS = 4
EXPERTS_PER_GROUP = 8
N_EXPERTS = N_GROUPS * EXPERTS_PER_GROUP
TOP_K_INNER = 2
D_EXPERT = D_MODEL // 4
N_MOD = 6
IN_PROJ_SIZES = (RET_W,) * 4 + (HGRN_W,) * 4 + (GLA_QK, GLA_QK, GLA_W, GLA_W, GLA_GATE_RANK)
IN_PROJ_DIM = sum(IN_PROJ_SIZES)


def rmsnorm(x, gain):
    xf = x.astype(jnp.float32)
    y = xf * lax.rsqrt(jnp.mean(xf * xf, axis=-1, keepdims=True) + EPS)
    return y.astype(x.dtype) * gain

def split_heads(t, n_heads):
    b, s, w = t.shape
    return t.reshape(b, s, n_heads, w // n_heads).transpose(0, 2, 1, 3).astype(jnp.float32)

def head_rmsnorm(o, gain):
    b, h, s, d = o.shape
    o = o.transpose(0, 2, 1, 3)
    o = o * lax.rsqrt(jnp.mean(o * o, axis=-1, keepdims=True) + EPS)
    return o.reshape(b, s, h * d) * gain.astype(jnp.float32)

def rope_tables(positions, dim):
    inv_freq = ROPE_BASE ** (-jnp.arange(0, dim, 2, dtype=jnp.float32) / dim)
    ang = positions.astype(jnp.float32)[..., None] * inv_freq
    return jnp.cos(ang)[:, None], jnp.sin(ang)[:, None]

def apply_rope(t, cos, sin):
    t1, t2 = jnp.split(t, 2, axis=-1)
    return jnp.concatenate([t1 * cos - t2 * sin, t1 * sin + t2 * cos], axis=-1)

def retention_chunkwise(q, k, v):
    b, h, s, dk = q.shape
    dv = v.shape[-1]
    n = s // CHUNK
    log_gamma = jnp.log1p(-jnp.exp2(-5.0 - jnp.arange(h, dtype=jnp.float32)))
    idx = jnp.arange(CHUNK, dtype=jnp.float32)
    rel = idx[:, None] - idx[None, :]
    decay = jnp.where(rel >= 0, jnp.exp(log_gamma[:, None, None] * jnp.maximum(rel, 0.0)), 0.0)
    zeta = jnp.exp(log_gamma[:, None] * (CHUNK - 1 - idx))
    xi = jnp.exp(log_gamma[:, None] * (idx + 1.0))
    chunk_decay = jnp.exp(log_gamma * CHUNK)[:, None, None]
    qc = q.reshape(b, h, n, CHUNK, dk)
    kc = k.reshape(b, h, n, CHUNK, dk)
    vc = v.reshape(b, h, n, CHUNK, dv)
    scores = jnp.einsum('bhnid,bhnjd->bhnij', qc, kc) * decay[:, None]
    o_intra = jnp.einsum('bhnij,bhnje->bhnie', scores, vc)
    u = jnp.einsum('bhnjd,hj,bhnje->nbhde', kc, zeta, vc)

    def step(r, u_i):
        return r * chunk_decay + u_i, r

    _, r_prev = lax.scan(step, jnp.zeros((b, h, dk, dv), jnp.float32), u)
    o_inter = jnp.einsum('bhnid,nbhde,hi->bhnie', qc, r_prev, xi)
    return (o_intra + o_inter).reshape(b, h, s, dv)

def gated_linear_recurrence_chunkwise(q, k, v, log_a):
    b, h, s, dk = q.shape
    dv = v.shape[-1]
    n = s // CHUNK
    mask = jnp.tril(jnp.ones((CHUNK, CHUNK), dtype=bool))[:, :, None]

    def to_chunks(t):
        return jnp.moveaxis(t.reshape(b, h, n, CHUNK, t.shape[-1]), 2, 0)

    def step(state, inp):
        qc, kc, vc, lac = inp
        cum = jnp.cumsum(lac, axis=-2)
        o_inter = jnp.einsum('bhcd,bhde->bhce', qc * jnp.exp(cum), state)
        diff = cum[:, :, :, None, :] - cum[:, :, None, :, :]
        dec = jnp.where(mask, jnp.exp(jnp.where(mask, diff, 0.0)), 0.0)
        scores = jnp.einsum('bhtd,bhsd,bhtsd->bhts', qc, kc, dec)
        o = o_inter + jnp.einsum('bhts,bhse->bhte', scores, vc)
        cum_last = cum[:, :, -1:, :]
        new_state = (jnp.exp(cum_last[:, :, 0, :])[..., None] * state
                     + jnp.einsum('bhsd,bhse->bhde', kc * jnp.exp(cum_last - cum), vc))
        return new_state, o

    s0 = jnp.zeros((b, h, dk, dv), jnp.float32)
    _, o = lax.scan(step, s0, (to_chunks(q), to_chunks(k), to_chunks(v), to_chunks(log_a)))
    return jnp.moveaxis(o, 0, 2).reshape(b, h, s, dv)

def hybrid_mixer(h, cos, sin, w_in, ret_norm, hgrn_norm, hgrn_lb, gla_wa2, gla_ba, gla_norm, w_out):
    proj = h @ w_in
    splits = np.cumsum(IN_PROJ_SIZES)[:-1].tolist()
    (rq, rk, rv, rg, hq, hf, hi, hg, gq, gk, gv, gg, ga) = jnp.split(proj, splits, axis=-1)

    q = apply_rope(split_heads(rq, RET_HEADS), cos, sin)
    k = apply_rope(split_heads(rk, RET_HEADS), cos, sin) * HEAD_DIM ** -0.5
    o_ret = retention_chunkwise(q, k, split_heads(rv, RET_HEADS))
    o_ret = head_rmsnorm(o_ret, ret_norm) * jax.nn.silu(rg.astype(jnp.float32))

    lb = hgrn_lb.astype(jnp.float32).reshape(HGRN_HEADS, 1, HGRN_DK)
    z = split_heads(hf, HGRN_HEADS)
    f = lb + (1.0 - lb) * jax.nn.sigmoid(z)
    log_f = jnp.log(jnp.maximum(f, F_MIN))
    k = (1.0 - lb) * jax.nn.sigmoid(-z)
    q = jax.nn.silu(split_heads(hq, HGRN_HEADS)) * HGRN_DK ** -0.5
    o_hgrn = gated_linear_recurrence_chunkwise(q, k, split_heads(hi, HGRN_HEADS), log_f)
    o_hgrn = head_rmsnorm(o_hgrn, hgrn_norm) * jax.nn.silu(hg.astype(jnp.float32))

    log_a = jax.nn.log_sigmoid((ga @ gla_wa2 + gla_ba).astype(jnp.float32)) / GLA_TAU
    q = split_heads(gq, GLA_HEADS) * GLA_DK ** -0.5
    o_gla = gated_linear_recurrence_chunkwise(q, split_heads(gk, GLA_HEADS), split_heads(gv, GLA_HEADS),
                                              split_heads(log_a, GLA_HEADS))
    o_gla = head_rmsnorm(o_gla, gla_norm) * jax.nn.silu(gg.astype(jnp.float32))

    merged = jnp.concatenate([o_ret, o_hgrn, o_gla], axis=-1).astype(h.dtype)
    return merged @ w_out

def hierarchical_moe(h, w_rg, b_rg, w_re, b_re, w_gate, w_up, w_down):
    b, s, d = h.shape
    tok = h.reshape(b * s, d)
    g_logits = (tok @ w_rg + b_rg).astype(jnp.float32)
    g_idx = jnp.argmax(g_logits, axis=-1)
    g_w = jnp.max(jax.nn.softmax(g_logits, axis=-1), axis=-1, keepdims=True)
    e_logits = (tok @ w_re + b_re).astype(jnp.float32).reshape(-1, N_GROUPS, EXPERTS_PER_GROUP)
    e_in_group = jnp.einsum('nge,ng->ne', e_logits, jax.nn.one_hot(g_idx, N_GROUPS, dtype=jnp.float32))
    top_val, top_idx = lax.top_k(e_in_group, TOP_K_INNER)
    top_w = jax.nn.softmax(top_val, axis=-1) * g_w
    expert_ids = g_idx[:, None] * EXPERTS_PER_GROUP + top_idx
    combine = jnp.einsum('nk,nke->ne', top_w,
                         jax.nn.one_hot(expert_ids, N_EXPERTS, dtype=jnp.float32)).astype(h.dtype)
    out = jnp.zeros_like(tok)
    for e in range(N_EXPERTS):
        hid = jax.nn.silu(tok @ w_gate[e]) * (tok @ w_up[e])
        out = out + combine[:, e:e + 1] * (hid @ w_down[e])
    return out.reshape(b, s, d)

def second_inputs(seed: int = 0) -> dict:
    key = jax.random.key(seed)
    ks = jax.random.split(key, 24)
    f32 = jnp.float32

    def nrm(k, shape, scale):
        return jax.random.normal(k, shape, f32) * scale

    x = nrm(ks[0], (BATCH, SEQ, D_MODEL), 1.0)
    c = nrm(ks[1], (BATCH, D_MODEL), 1.0)
    positions = (jax.random.randint(ks[2], (BATCH, 1), 0, 1024)
                 + jnp.arange(SEQ, dtype=jnp.int32)[None, :]).astype(jnp.int32)
    w_ada = nrm(ks[3], (DEPTH, D_MODEL, N_MOD * D_MODEL), 0.5 * D_MODEL ** -0.5)
    b_ada = nrm(ks[4], (DEPTH, N_MOD * D_MODEL), 0.02)
    norm_mix = 1.0 + nrm(ks[5], (DEPTH, D_MODEL), 0.02)
    norm_ffn = 1.0 + nrm(ks[6], (DEPTH, D_MODEL), 0.02)
    w_in = nrm(ks[7], (DEPTH, D_MODEL, IN_PROJ_DIM), D_MODEL ** -0.5)
    ret_norm = 1.0 + nrm(ks[8], (DEPTH, RET_W), 0.02)
    hgrn_norm = 1.0 + nrm(ks[9], (DEPTH, HGRN_W), 0.02)
    hgrn_lb_logits = nrm(ks[10], (DEPTH, HGRN_HEADS * HGRN_DK), 1.0)
    gla_wa2 = nrm(ks[11], (DEPTH, GLA_GATE_RANK, GLA_QK), GLA_GATE_RANK ** -0.5)
    gla_ba = nrm(ks[12], (DEPTH, GLA_QK), 0.1)
    gla_norm = 1.0 + nrm(ks[13], (DEPTH, GLA_W), 0.02)
    w_out = nrm(ks[14], (DEPTH, D_MIX, D_MODEL), D_MIX ** -0.5)
    router_group_w = nrm(ks[15], (DEPTH, D_MODEL, N_GROUPS), D_MODEL ** -0.5)
    router_group_b = nrm(ks[16], (DEPTH, N_GROUPS), 0.01)
    router_expert_w = nrm(ks[17], (DEPTH, D_MODEL, N_EXPERTS), D_MODEL ** -0.5)
    router_expert_b = nrm(ks[18], (DEPTH, N_EXPERTS), 0.01)
    expert_w_gate = nrm(ks[19], (DEPTH, N_EXPERTS, D_MODEL, D_EXPERT), D_MODEL ** -0.5)
    expert_w_up = nrm(ks[20], (DEPTH, N_EXPERTS, D_MODEL, D_EXPERT), D_MODEL ** -0.5)
    expert_w_down = nrm(ks[21], (DEPTH, N_EXPERTS, D_EXPERT, D_MODEL), D_EXPERT ** -0.5)
    norm_final = 1.0 + nrm(ks[22], (D_MODEL,), 0.02)
    return {"x": x, "c": c, "positions": positions, "w_ada": w_ada, "b_ada": b_ada,
            "norm_mix": norm_mix, "norm_ffn": norm_ffn, "w_in": w_in, "ret_norm": ret_norm,
            "hgrn_norm": hgrn_norm, "hgrn_lb_logits": hgrn_lb_logits, "gla_wa2": gla_wa2,
            "gla_ba": gla_ba, "gla_norm": gla_norm, "w_out": w_out,
            "router_group_w": router_group_w, "router_group_b": router_group_b,
            "router_expert_w": router_expert_w, "router_expert_b": router_expert_b,
            "expert_w_gate": expert_w_gate, "expert_w_up": expert_w_up,
            "expert_w_down": expert_w_down, "norm_final": norm_final}

def second_block(x, c, positions, w_ada, b_ada, norm_mix, norm_ffn, w_in, ret_norm, hgrn_norm,
              hgrn_lb_logits, gla_wa2, gla_ba, gla_norm, w_out, router_group_w, router_group_b,
              router_expert_w, router_expert_b, expert_w_gate, expert_w_up, expert_w_down,
              norm_final):
    cos, sin = rope_tables(positions, HEAD_DIM)
    lb_w = jax.nn.softmax(hgrn_lb_logits.astype(jnp.float32), axis=0)
    lower_bounds = jnp.cumsum(lb_w, axis=0) - lb_w[0]
    c_act = jax.nn.silu(c)
    for layer in range(DEPTH):
        mod = c_act @ w_ada[layer] + b_ada[layer]
        shift_m, scale_m, gate_m, shift_f, scale_f, gate_f = [m[:, None, :] for m in jnp.split(mod, N_MOD, axis=-1)]
        h = rmsnorm(x, norm_mix[layer]) * (1.0 + scale_m) + shift_m
        x = x + gate_m * hybrid_mixer(h, cos, sin, w_in[layer], ret_norm[layer], hgrn_norm[layer],
                                      lower_bounds[layer], gla_wa2[layer], gla_ba[layer],
                                      gla_norm[layer], w_out[layer])
        h = rmsnorm(x, norm_ffn[layer]) * (1.0 + scale_f) + shift_f
        x = x + gate_f * hierarchical_moe(h, router_group_w[layer], router_group_b[layer],
                                          router_expert_w[layer], router_expert_b[layer],
                                          expert_w_gate[layer], expert_w_up[layer], expert_w_down[layer])
    return rmsnorm(x, norm_final)


def setup_inputs(seed=0):
    out = dict(first_inputs(seed))
    for name, value in second_inputs(seed + 1).items():
        if name != "x":
            out[name + "_2"] = value
    return out


def reference(
    x, c, ada_w, ada_b, norm1_g, w_in, mu_prev, mu_next, q_norm_g, k_norm_g, w_decay0,
    w_decay_up, a_gate0, a_gate_up, g_up, k_k, k_a, r_k, lnx_g, lnx_b, w_out, norm2_g,
    peer_w_query, peer_sub_keys1, peer_sub_keys2, peer_u, peer_v, c_2, positions_2, w_ada_2,
    b_ada_2, norm_mix_2, norm_ffn_2, w_in_2, ret_norm_2, hgrn_norm_2, hgrn_lb_logits_2,
    gla_wa2_2, gla_ba_2, gla_norm_2, w_out_2, router_group_w_2, router_group_b_2,
    router_expert_w_2, router_expert_b_2, expert_w_gate_2, expert_w_up_2, expert_w_down_2,
    norm_final_2,
):
    x = first_block(
        x, c, ada_w, ada_b, norm1_g, w_in, mu_prev, mu_next, q_norm_g, k_norm_g, w_decay0,
        w_decay_up, a_gate0, a_gate_up, g_up, k_k, k_a, r_k, lnx_g, lnx_b, w_out, norm2_g,
        peer_w_query, peer_sub_keys1, peer_sub_keys2, peer_u, peer_v,
    )
    return second_block(
        x, c_2, positions_2, w_ada_2, b_ada_2, norm_mix_2, norm_ffn_2, w_in_2, ret_norm_2,
        hgrn_norm_2, hgrn_lb_logits_2, gla_wa2_2, gla_ba_2, gla_norm_2, w_out_2,
        router_group_w_2, router_group_b_2, router_expert_w_2, router_expert_b_2,
        expert_w_gate_2, expert_w_up_2, expert_w_down_2, norm_final_2,
    )


_drawn_inputs = setup_inputs


def setup_inputs(seed=0):
    import zlib

    import numpy as np

    out = dict(_drawn_inputs(seed))
    spreads = {}
    factors = {'norm1_g': 4.017,
     'q_norm_g': 8.0,
     'k_norm_g': 8.0,
     'w_decay_up': 6.894,
     'k_k': 3.93,
     'k_a': 3.237,
     'lnx_g': 8.0,
     'lnx_b': 8.0,
     'norm2_g': 8.0,
     'peer_w_query': 3.061,
     'peer_sub_keys1': 3.006,
     'peer_sub_keys2': 3.229,
     'peer_u': 3.38,
     'peer_v': 3.004,
     'norm_mix_2': 5.812,
     'norm_ffn_2': 6.405,
     'ret_norm_2': 8.0,
     'hgrn_norm_2': 8.0,
     'gla_ba_2': 8.0,
     'gla_norm_2': 8.0,
     'router_group_b_2': 8.0,
     'router_expert_b_2': 34.868,
     'norm_final_2': 8.861}
    for name, (base, spread) in spreads.items():
        noise = np.random.default_rng([zlib.crc32(name.encode()), seed]).standard_normal(out[name].shape)
        drawn = base * np.exp(spread * noise) if base else spread * noise
        out[name] = jnp.asarray(drawn.astype(out[name].dtype))
    for name, factor in factors.items():
        out[name] = (out[name] * factor).astype(out[name].dtype)
    return out
```

```python
from contextlib import ExitStack
import math

import numpy as np

import concourse.bass as bass
from concourse import mybir

ALU = mybir.AluOpType
ACT = mybir.ActivationFunctionType
AX = mybir.AxisListType
F32 = mybir.dt.float32
I32 = mybir.dt.int32
U32 = mybir.dt.uint32

P = 128
S = 512
TT = S // P
D = 1024
KD = D // P
HD = 64
NEG_LOG_DECAY = math.exp(-0.5)
N_KEYS, PEER_HEADS, TOPK = 128, 8, 16
HK = PEER_HEADS * TOPK
N_EXPERTS, N_GROUPS, PER_GROUP, D_EXPERT = 32, 4, 8, 256

VEC_COLS = [("c", 8), ("c_2", 8), ("ada_b", 48), ("b_ada_2", 48), ("norm1_g", 8), ("norm2_g", 8),
            ("norm_mix_2", 8), ("norm_ffn_2", 8), ("norm_final_2", 8), ("mu_prev", 14), ("mu_next", 14),
            ("q_norm_g", 1), ("k_norm_g", 1), ("w_decay0", 8), ("a_gate0", 8), ("k_k", 4), ("k_a", 4),
            ("r_k", 4), ("lnx_g", 4), ("lnx_b", 4), ("ret_norm_2", 3), ("hgrn_norm_2", 3),
            ("hgrn_lb_logits_2", 3), ("gla_ba_2", 1), ("gla_norm_2", 2)]
VEC_AT, _n = {}, 0
for _name, _k in VEC_COLS:
    VEC_AT[_name] = (_n, _k)
    _n += _k
NVEC = _n

RET_HEADS = 6
LEVELS = [1, 2, 4, 8, 16, 32, 64]


def constant_tables():
    r = np.arange(P)[:, None]
    c = np.arange(P)[None, :]
    eye = (r == c).astype(np.float32)
    out = {"ident": eye, "ones": np.ones((P, P), np.float32),
           "headones": (r // HD == c // HD).astype(np.float32)}
    t = np.arange(S)[None, :]
    half = {m: ((r // (2 * m) == c // (2 * m)) & (r % (2 * m) < m) & (c % (2 * m) >= m)) for m in LEVELS}
    out["rw_fwd"] = np.stack([r < c, half[1].T, half[1] | (r == c)]
                             + [half[m].T | (r == c) for m in LEVELS[1:]] + [r <= c], 1).astype(np.float32)
    out["rw_rev"] = np.stack([r > c, half[1], half[1].T | (r == c)]
                             + [half[m] | (r == c) for m in LEVELS[1:]] + [r >= c], 1).astype(np.float32)
    out["halves"] = np.stack([half[m] for m in LEVELS], 1).astype(np.uint32)
    tq = np.arange(S)[:, None]
    dist = np.abs(tq - t)
    count = sum(((dist % d == 0) & (dist <= w // 2)).astype(np.float32) for w, d in ((128, 1), (512, 4), (2048, 16)))
    masked = np.where(count > 0, dist, 1e30).astype(np.float32)
    out["dist"] = np.ascontiguousarray(masked.reshape(TT, P, S).transpose(1, 0, 2))
    out["count"] = np.ascontiguousarray(count.reshape(TT, P, S).transpose(1, 0, 2)).astype(np.float32)
    out["slopes"] = np.broadcast_to(-np.exp2(-np.arange(1, 9, dtype=np.float32)), (P, 8)).copy()
    restart = np.ones((P, S), np.float32)
    restart[:, ::P] = 0.0
    out["restart"] = restart
    gamma = 1.0 - np.exp2(-5.0 - np.arange(RET_HEADS))
    rel = (t - np.arange(P)[:, None]).astype(np.float64)
    out["ret_decay"] = np.stack([np.where(rel >= 0, g ** np.maximum(rel, 0), 0.0) * HD ** -0.5 for g in gamma],
                                1).astype(np.float32)
    rot = np.zeros((P, P), np.float32)
    for h in range(P // HD):
        for i in range(HD // 2):
            rot[h * HD + HD // 2 + i, h * HD + i] = -1.0
            rot[h * HD + i, h * HD + HD // 2 + i] = 1.0
    out["rot"] = rot
    inv = np.float32(10000.0) ** (-np.arange(0, HD, 2, dtype=np.float32) / np.float32(HD))
    out["inv_freq"] = np.tile(inv.astype(np.float32), P // (HD // 2))[:, None].copy()
    out["iota16"] = np.broadcast_to(np.arange(16, dtype=np.float32), (P, 16)).copy()
    out["expert_rows"] = (np.arange(N_EXPERTS)[:, None, None] == np.arange(N_EXPERTS)[None, :, None]
                          ).astype(np.float32) * np.ones((1, 1, P), np.float32)
    return out


class Core:

    def __init__(self, nc, dram, ctx):
        self.nc, self.dram, self.ctx = nc, dram, ctx
        self.names = {}
        self.bank = [ctx.enter_context(nc.psum_tensor(f"bank{i}", [P, S], F32)) for i in range(8)]

    def sb(self, name, shape, dt=F32, ctx=None):
        n = self.names[name] = self.names.get(name, 0) + 1
        name = name if n == 1 else f"{name}_{n}"
        return (ctx or self.ctx).enter_context(self.nc.sbuf_tensor(name, shape, dt))

    def sems(self, ctx, *names):
        found = [ctx.enter_context(self.nc.semaphore(n)) for n in names]
        self.clear(found)
        return found if len(found) > 1 else found[0]

    def clear(self, sems):
        with self.nc.Block() as block:
            @block.sync
            def _(sp):
                for s in sems:
                    sp.sem_clear(s)

    def col(self, name, i=0, n=1):
        at = VEC_AT[name][0]
        return self.vec[:, at + i:at + i + n] if isinstance(i, int) else self.vec[:, bass.ds(i + at, n)]


class Steps:

    def __init__(self, eng, sem):
        self.eng, self.sem, self.n = eng, sem, 0

    def __call__(self, ins):
        self.n += 1
        ins.then_inc(self.sem, 1)
        return ins

    def done(self):
        self.eng.wait_ge(self.sem, self.n)

    def then(self, ins):
        self(ins)
        self.done()


RING = 3


class WeightRing:

    def __init__(self, core, items):
        self.core, self.items, self.issued = core, items, 0
        self.slots = core.sb("weight_slots", [P, RING, KD * S])
        self.loaded = [core.ctx.enter_context(core.nc.semaphore(f"weight_loaded{i}")) for i in range(RING)]
        self.used = core.ctx.enter_context(core.nc.semaphore("weight_used"))

    def view(self, i):
        n = self.items[i].shape[1]
        return self.slots[:, i % RING, 0:KD * n].rearrange("p (k n) -> p k n", k=KD)

    def load(self, sp, upto):
        while self.issued < min(upto, len(self.items)):
            i = self.issued
            if i >= RING:
                sp.wait_ge(self.used, i - RING + 1)
            sp.dma_start(self.view(i), self.items[i].rearrange("(k p) n -> p k n", p=P)).then_inc(self.loaded[i % RING], 16)
            self.issued += 1

    def arrived(self, pe, i):
        pe.wait_ge(self.loaded[i % RING], 16 * (i // RING + 1))


def repeat(ap, n):
    return ap.unsqueeze(2).to_broadcast([ap.shape[0], ap.shape[1], n])


def tiled(ap, n):
    return ap.unsqueeze(1).to_broadcast([ap.shape[0], n, ap.shape[1]])


def stage_load(core):
    nc = core.nc
    core.x = core.sb("x", [P, KD, S])
    core.vec = core.sb("vec", [P, NVEC])
    core.ident = core.sb("ident", [P, P])
    core.ones = core.sb("ones", [P, P])
    core.headones = core.sb("headones", [P, P])
    core.cond = core.sb("cond", [P, 2 * KD])
    core.mod = core.sb("mod", [P, 12 * KD])
    core.gain = core.sb("gain", [P, 4 * KD])
    with ExitStack() as st:
        in_loaded = core.sems(st, "in_loaded")
        with nc.Block() as block:
            @block.sync
            def _(sp):
                sp.dma_start(core.vec[:, :], core.dram["vec"]).then_inc(in_loaded, 16)
                core.ring.load(sp, RING)

            @block.scalar
            def _(act):
                act.dma_start(core.x[:, :, :], core.dram["xT"].rearrange("(k p) t -> p k t", p=P)).then_inc(in_loaded, 16)
                act.dma_start(core.ident[:, :], core.dram["ident"]).then_inc(in_loaded, 16)
                act.dma_start(core.ones[:, :], core.dram["ones"]).then_inc(in_loaded, 16)
                act.dma_start(core.headones[:, :], core.dram["headones"]).then_inc(in_loaded, 16)
                act.wait_ge(in_loaded, 80)
                act.activation(core.cond[:, :], core.vec[:, 0:2 * KD], ACT.Silu)


def stage_modulation(core, b, first):
    nc, ring = core.nc, core.ring
    n_items = 12
    with ExitStack() as st:
        mod_added = core.sems(st, "mod_added")
        out = core.bank[0]
        mod = core.mod[:, 48 * b:48 * b + 48]
        with nc.Block() as block:
            @block.sync
            def _(sp):
                ring.load(sp, first + n_items + RING)

            @block.tensor
            def _(pe):
                for i in range(n_items):
                    ring.arrived(pe, first + i)
                    w = ring.view(first + i)
                    for f in range(4):
                        for k in range(KD):
                            mm = pe.matmul(out[:, 4 * i + f:4 * i + f + 1], w[:, k, f * P:f * P + P],
                                           core.cond[:, b * KD + k:b * KD + k + 1], start=k == 0, stop=k == KD - 1)
                    mm.then_inc(ring.used, 1)

            @block.vector
            def _(dve):
                dve.wait_ge(ring.used, first + n_items)
                dve.tensor_tensor(mod, out[:, 0:48], core.col("ada_b" if b == 0 else "b_ada_2", 0, 48),
                                  ALU.add).then_inc(mod_added, 1)
                dve.wait_ge(mod_added, 1)
                g = ("norm1_g", "norm2_g") if b == 0 else ("norm_mix_2", "norm_ffn_2")
                for j in range(2):
                    dve.scalar_tensor_tensor(out=core.gain[:, (2 * b + j) * KD:(2 * b + j + 1) * KD],
                                             in0=mod[:, 8 + 24 * j:16 + 24 * j], scalar=1.0, in1=core.col(g[j], 0, 8),
                                             op0=ALU.add, op1=ALU.mult)


def stage_norm(core, out, gain, shift):
    nc, x, total = core.nc, core.x, core.bank[0]
    with ExitStack() as st:
        rms = core.sb("rms", [P, S], ctx=st)
        squared, summed, rooted, scaled, shifted = core.sems(
            st, "squared", "summed", "rooted", "scaled", "shifted")
        with nc.Block() as block:
            @block.scalar
            def _(act):
                for k in range(KD):
                    act.activation(out[:, k, :], x[:, k, :], ACT.Square).then_inc(squared, 1)
                act.wait_ge(summed, 1)
                act.activation(rms[:, :], total[:, :], ACT.Sqrt, scale=1.0 / D, bias=1e-6).then_inc(rooted, 1)
                if shift is not None:
                    for k in range(KD):
                        act.wait_ge(scaled, k + 2)
                        act.activation(out[:, k, :], out[:, k, :], ACT.Identity, bias=shift[:, k:k + 1]).then_inc(shifted, 1)

            @block.tensor
            def _(pe):
                for k in range(KD):
                    pe.wait_ge(squared, k + 1)
                    mm = pe.matmul(total[:, :], core.ones[:, :], out[:, k, :], start=k == 0, stop=k == KD - 1)
                mm.then_inc(summed, 1)

            @block.vector
            def _(dve):
                dve.wait_ge(rooted, 1)
                dve.reciprocal(rms[:, :], rms[:, :]).then_inc(scaled, 1)
                dve.wait_ge(scaled, 1)
                for k in range(KD):
                    dve.scalar_tensor_tensor(out=out[:, k, :], in0=x[:, k, :], scalar=gain[:, k:k + 1], in1=rms[:, :],
                                             op0=ALU.mult, op1=ALU.mult).then_inc(scaled, 1)


def stage_project(core, first, plan, rhs, only_dve=False):
    nc, ring = core.nc, core.ring
    units = []
    for i, (kind, evac) in enumerate(plan):
        n = ring.items[first + i].shape[1]
        if kind == "T":
            for f in range(-(-n // P)):
                units.append((i, "T", f, min(P, n - f * P), S, evac[f]))
        else:
            for t in range(TT):
                units.append((i, "N", t, P, n, evac))
    NB = 6
    with ExitStack() as st:
        bank_full, act_emptied, dve_emptied = core.sems(st, "bank_full", "act_emptied", "dve_emptied")

        def evacuate(eng, parity, emptied):
            for u, (_, kind, f, rows, width, evac) in enumerate(units):
                if only_dve and parity or not only_dve and u % 2 == parity:
                    eng.wait_ge(bank_full, u + 1)
                    evac(eng, core.bank[u % NB][0:rows, 0:width], f).then_inc(emptied, 1)

        with nc.Block() as block:
            @block.sync
            def _(sp):
                ring.load(sp, first + len(plan) + RING)

            @block.tensor
            def _(pe):
                for u, (i, kind, f, rows, width, _) in enumerate(units):
                    ring.arrived(pe, first + i)
                    if u >= NB:
                        if only_dve:
                            pe.wait_ge(dve_emptied, u - NB + 1)
                        else:
                            pe.wait_ge(act_emptied if u % 2 == 0 else dve_emptied, (u - NB) // 2 + 1)
                    w = ring.view(first + i)
                    for k in range(KD):
                        if kind == "T":
                            a, b = w[:, k, f * P:f * P + rows], rhs[:, k, :]
                        else:
                            a, b = rhs[:, k, f * P:f * P + P], w[:, k, :]
                        mm = pe.matmul(core.bank[u % NB][0:rows, 0:width], a, b, start=k == 0, stop=k == KD - 1)
                    mm.then_inc(bank_full, 1)
                    if u + 1 == len(units) or units[u + 1][0] != i:
                        pe.wait_ge(bank_full, u + 1)
                        pe.sem_inc(ring.used, 1)

            @block.scalar
            def _(act):
                evacuate(act, 0, act_emptied)

            @block.vector
            def _(dve):
                evacuate(dve, 1, dve_emptied)


def copy_to(dest):
    def evac(eng, psum, f):
        d = dest(f)
        if eng.engine == mybir.EngineType.Activation:
            return eng.activation(d, psum, ACT.Copy)
        return eng.tensor_copy(d, psum)
    return evac


def stage_attention(core, qk, v, att):
    nc = core.nc
    with ExitStack() as st:
        dist = core.sb("dist", [P, TT, S], ctx=st)
        count = core.sb("count", [P, TT, S], ctx=st)
        slopes = core.sb("slopes", [P, 8], ctx=st)
        gains = core.sb("qk_gains", [P, 2], ctx=st)
        sq = core.sb("qk_sq", [P, 2, S], ctx=st)
        qn = core.sb("qk_n", [P, 2, S], ctx=st)
        vs = core.sb("v_pair", [P, TT, P], ctx=st)
        score = core.sb("score", [P, 2, S], ctx=st)
        prob = core.sb("prob", [P, 2, S], ctx=st)
        diag = core.sb("diag", [P, 2, P], ctx=st)
        slope = core.sb("slope", [P, 2], ctx=st)
        top = core.sb("top", [P, 8], ctx=st)
        den = core.sb("den", [P, 8], ctx=st)
        probT = core.sb("probT", [P, 2, TT, S], ctx=st)
        tables = core.sems(st, "att_tables")
        names = ("squared", "summed", "rooted", "inverted", "normed", "v_staged", "scored", "biased", "topped",
                 "raised", "counted", "inverse", "scaled", "turned", "copied", "mixed", "stored")
        sems = core.sems(st, *names)
        (squared, summed, rooted, inverted, normed, v_staged, scored, biased, topped, raised, counted, inverse,
         scaled, turned, copied, mixed, stored) = sems
        with nc.Block() as block:
            @block.sync
            def _(sp):
                sp.dma_start(dist[:, :, :], core.dram["dist"]).then_inc(tables, 16)
                sp.dma_start(count[:, :, :], core.dram["count"]).then_inc(tables, 16)
                sp.dma_start(slopes[:, :], core.dram["slopes"]).then_inc(tables, 16)
                sp.wait_ge(tables, 48)

            @block.vector
            def _(dve):
                dve.tensor_scalar(gains[:, 0:1], core.col("q_norm_g"), HD ** -0.5, None, ALU.mult)
                dve.tensor_copy(gains[:, 1:2], core.col("k_norm_g"))
        UNITS = [(h, i) for h in range(2) for i in range(TT)]
        with nc.Fori(0, 4) as pair:
            core.clear(sems)
            with nc.Block() as block:
                @block.gpsimd
                def _(pool):
                    pool.tensor_copy(vs[:, :, :], v[:, :, bass.ds(pair * P, P)]).then_inc(v_staged, 1)

                def copy_turned(act, u):
                    h, i = UNITS[u]
                    act.wait_ge(turned, u + 1)
                    act.activation(probT[:, h, :, i * P:i * P + P],
                                   core.bank[2 + u % 2][:, :].rearrange("p (j t) -> p j t", j=TT), ACT.Copy).then_inc(copied, 1)

                @block.scalar
                def _(act):
                    for j in range(2):
                        act.activation(sq[:, j, :], qk[:, bass.ds(4 * j + pair, 1), :], ACT.Square).then_inc(squared, 1)
                    for j in range(2):
                        act.wait_ge(summed, j + 1)
                        act.activation(sq[:, j, :], core.bank[j][:, :], ACT.Sqrt, scale=1.0 / HD, bias=1e-6).then_inc(rooted, 1)
                    for u, (h, i) in enumerate(UNITS):
                        act.wait_ge(topped, u + 1)
                        act.activation(score[:, u % 2, :], score[:, u % 2, :], ACT.Exp, bias=top[:, u:u + 1]).then_inc(raised, 1)
                        if u >= 1:
                            copy_turned(act, u - 1)
                    copy_turned(act, 7)
                    for h in range(2):
                        act.wait_ge(mixed, h + 1)
                        r = slice(HD * h, HD * h + HD)
                        act.activation(att[r, bass.ds(pair, 1), :], core.bank[4 + h][r, :], ACT.Copy).then_inc(stored, 1)

                @block.tensor
                def _(pe):
                    for j in range(2):
                        pe.wait_ge(squared, j + 1)
                        pe.matmul(core.bank[j][:, :], core.headones[:, :], sq[:, j, :], start=True, stop=True).then_inc(summed, 1)

                    def turn(u):
                        pe.wait_ge(scaled, u + 1)
                        if u >= 2:
                            pe.wait_ge(copied, u - 1)
                        for j in range(TT):
                            mm = pe.matmul(core.bank[2 + u % 2][:, j * P:j * P + P], prob[:, u % 2, j * P:j * P + P],
                                           diag[:, u % 2, :], start=True, stop=True)
                        mm.then_inc(turned, 1)

                    def mix(h):
                        pe.wait_ge(copied, 4 * h + 4)
                        pe.wait_ge(v_staged, 1)
                        r = slice(HD * h, HD * h + HD)
                        for j in range(TT):
                            mm = pe.matmul(core.bank[4 + h][r, :], vs[:, j, r], probT[:, h, j, :],
                                           start=j == 0, stop=j == TT - 1)
                        mm.then_inc(mixed, 1)

                    pe.wait_ge(normed, 2)
                    for u, (h, i) in enumerate(UNITS):
                        if u >= 2:
                            pe.wait_ge(biased, u - 1)
                        r = slice(HD * h, HD * h + HD)
                        pe.matmul(core.bank[u % 2][:, :], qn[r, 0, i * P:i * P + P], qn[r, 1, :],
                                  start=True, stop=True).then_inc(scored, 1)
                        if u >= 1:
                            turn(u - 1)
                        if u == 5:
                            mix(0)
                    turn(7)
                    mix(1)

                @block.vector
                def _(dve):
                    dve.tensor_copy(slope[:, :], slopes[:, bass.ds(pair * 2, 2)]).then_inc(inverted, 1)
                    for j in range(2):
                        dve.wait_ge(rooted, j + 1)
                        dve.reciprocal(sq[:, j, :], sq[:, j, :]).then_inc(inverted, 1)
                        dve.wait_ge(inverted, j + 2)
                        dve.scalar_tensor_tensor(out=qn[:, j, :], in0=qk[:, bass.ds(4 * j + pair, 1), :].rearrange("p a t -> p (a t)"),
                                                 scalar=gains[:, j:j + 1], in1=sq[:, j, :],
                                                 op0=ALU.mult, op1=ALU.mult).then_inc(normed, 1)

                    def bias_and_top(u):
                        h, i = UNITS[u]
                        dve.wait_ge(scored, u + 1)
                        if u >= 2:
                            dve.wait_ge(counted, u - 1)
                        dve.scalar_tensor_tensor(out=score[:, u % 2, :], in0=dist[:, i, :], scalar=slope[:, h:h + 1],
                                                 in1=core.bank[u % 2][:, :], op0=ALU.mult, op1=ALU.add).then_inc(biased, 1)
                        dve.wait_ge(biased, u + 1)
                        dve.tensor_reduce(top[:, u:u + 1], score[:, u % 2, :], AX.X, ALU.max, negate=True).then_inc(topped, 1)

                    def weigh(u):
                        h, i = UNITS[u]
                        dve.wait_ge(raised, u + 1)
                        if u >= 2:
                            dve.wait_ge(turned, u - 1)
                        dve.scalar_tensor_tensor(out=prob[:, u % 2, :], in0=score[:, u % 2, :], scalar=1.0, in1=count[:, i, :],
                                                 op0=ALU.mult, op1=ALU.mult, accum_out=den[:, u:u + 1]).then_inc(counted, 1)
                        dve.wait_ge(counted, u + 1)
                        dve.reciprocal(den[:, u:u + 1], den[:, u:u + 1]).then_inc(inverse, 1)
                        dve.wait_ge(inverse, u + 1)
                        dve.tensor_scalar(diag[:, u % 2, :], core.ident[:, :], den[:, u:u + 1], None, ALU.mult).then_inc(scaled, 1)

                    for u in range(8):
                        bias_and_top(u)
                        if u >= 1:
                            weigh(u - 1)
                    weigh(7)


def inputs_to_dram(inputs):
    a = {k: np.asarray(v) for k, v in inputs.items()}
    cols = []
    for name, n in VEC_COLS:
        flat = a[name].reshape(-1)
        if name in ("q_norm_g", "k_norm_g"):
            flat = np.tile(flat, 2)
        cols.append(flat.reshape(n, P).T)
    rows = lambda name: a[name][0]
    dram = {"vec": np.concatenate(cols, 1), "xT": a["x"][0].T, "positions": a["positions_2"]}
    for name, src in (("ada_w", "ada_w"), ("ada_w2", "w_ada_2"), ("w_in", "w_in"), ("w_in2", "w_in_2"), ("w_out", "w_out"),
                      ("w_out2", "w_out_2"), ("w_query", "peer_w_query"), ("g_up", "g_up"), ("wa2", "gla_wa2_2"),
                      ("gate_w", "expert_w_gate_2"), ("up_w", "expert_w_up_2"), ("down_w", "expert_w_down_2")):
        dram[name] = rows(src)
    dram["decay_up"] = np.concatenate(list(rows("w_decay_up")), 1)
    dram["a_up"] = np.concatenate(list(rows("a_gate_up")), 1)
    dram["keys"] = np.concatenate([rows("peer_sub_keys1").T, rows("peer_sub_keys2").T], 1)
    dram["uv"] = np.concatenate([rows("peer_u"), rows("peer_v")], 1)
    dram["router_w"] = np.concatenate([rows("router_group_w_2"), rows("router_expert_w_2")], 1)
    dram["router_b"] = np.concatenate([rows("router_group_b_2"), rows("router_expert_b_2")])[None]
    dram.update(constant_tables())
    return {k: np.ascontiguousarray(v) for k, v in dram.items()}


def build(nc, dram, out):
    with ExitStack() as ctx:
        core = Core(nc, dram, ctx)
        cuts = lambda w, widths: [w[:, sum(widths[:i]):sum(widths[:i + 1])] for i in range(len(widths))]
        IN1 = [512, 512, 512, 512, 512, 512, 256]
        IN2 = [384] * 8 + [256, 256, 272]
        core.ring = WeightRing(core, cuts(dram["ada_w"], [512] * 12) + cuts(dram["ada_w2"], [512] * 12)
                               + cuts(dram["w_in"], IN1) + cuts(dram["w_out"], [512] * 2)
                               + cuts(dram["w_query"], [512] * 4) + cuts(dram["w_in2"], IN2)
                               + cuts(dram["w_out2"], [512] * 2))
        stage_load(core)
        stage_modulation(core, 0, 0)
        stage_modulation(core, 1, 12)
        first_block(core, 24)
        second_block(core, 24 + 13, core.mixed)
        stage_output(core, core.mixed, out)
        ring = core.ring
        with nc.Block() as block:
            @block.sync
            def _(sp):
                for i in range(max(0, ring.issued - RING), ring.issued):
                    ring.arrived(sp, i)


def first_block(core, first):
    nc = core.nc
    mixed = core.mixed = core.sb("mixed", [P, KD, S])
    with ExitStack() as st:
        zr = core.sb("zr", [P, 14, S], ctx=st)
        with ExitStack() as s2:
            qk = core.sb("qk", [P, KD, S], ctx=s2)
            v = core.sb("v", [P, TT, S], ctx=s2)
            h = mixed
            stage_norm(core, h, core.gain[:, 0:8], core.mod[:, 0:8])
            stage_project(core, first, [("T", [copy_to(lambda f: qk[:, f, :])] * 4), ("T", [copy_to(lambda f: qk[:, 4 + f, :])] * 4),
                                        ("N", copy_to(lambda t: v[:, t, :]))], h)
            stage_shifted(core, first + 3, h, zr)
            stage_attention(core, qk, v, mixed)
        stage_rwkv(core, zr, mixed)
    stage_residual(core, first + 7, mixed, core.mod[:, 16:24])
    stage_peer(core, first + 9, mixed)


def stage_shifted(core, first, h, zr):
    nc, ring = core.nc, core.ring
    N = 14
    with ExitStack() as st:
        stay = core.sb("stay", [P, N], ctx=st)
        stay_ready, bank_full, stayed, left, emptied = core.sems(st, "stay_ready", "bank_full", "stayed", "left", "emptied")
        with nc.Block() as block:
            @block.sync
            def _(sp):
                ring.load(sp, first + 4 + RING)

            @block.tensor
            def _(pe):
                for u in range(N):
                    ring.arrived(pe, first + u // 4)
                    if u >= 6:
                        pe.wait_ge(emptied, u - 5)
                    w = ring.view(first + u // 4)
                    for k in range(KD):
                        mm = pe.matmul(core.bank[u % 6][:, :], w[:, k, (u % 4) * P:(u % 4) * P + P], h[:, k, :],
                                       start=k == 0, stop=k == KD - 1)
                    mm.then_inc(bank_full, 1)
                    if u % 4 == 3 or u == N - 1:
                        pe.wait_ge(bank_full, u + 1)
                        pe.sem_inc(ring.used, 1)

            @block.scalar
            def _(act):
                act.wait_ge(stay_ready, 2)
                for u in range(N):
                    act.wait_ge(bank_full, u + 1)
                    act.activation(zr[:, u, :], core.bank[u % 6][:, :], ACT.Copy, scale=stay[:, u:u + 1]).then_inc(stayed, 1)

            @block.vector
            def _(dve):
                dve.tensor_tensor(stay[:, :], core.col("mu_prev", 0, N), core.col("mu_next", 0, N), ALU.add).then_inc(stay_ready, 1)
                dve.wait_ge(stay_ready, 1)
                dve.tensor_scalar(stay[:, :], stay[:, :], -1.0, 1.0, ALU.mult, ALU.add).then_inc(stay_ready, 1)
                for u in range(N):
                    ps = core.bank[u % 6]
                    dve.wait_ge(stayed, u + 1)
                    dve.scalar_tensor_tensor(out=zr[:, u, 1:S], in0=ps[:, 0:S - 1], scalar=core.col("mu_prev", u),
                                             in1=zr[:, u, 1:S], op0=ALU.mult, op1=ALU.add).then_inc(left, 1)
                    dve.wait_ge(left, u + 1)
                    dve.scalar_tensor_tensor(out=zr[:, u, 0:S - 1], in0=ps[:, 1:S], scalar=core.col("mu_next", u),
                                             in1=zr[:, u, 0:S - 1], op0=ALU.mult, op1=ALU.add).then_inc(emptied, 1)


def stage_rwkv(core, zr, mixed):
    nc = core.nc
    R, K, V = 0, 4, 8
    with ExitStack() as st:
        sig = core.sb("decay_sig", [P, 8, S], ctx=st)
        a = core.sb("a", [P, 8, S], ctx=st)
        kk = core.sb("kk", [P, 4, S], ctx=st)
        sel = core.sb("rwkv_cols", [P, 4, 6], ctx=st)
        restart = core.sb("restart", [P, S], ctx=st)
        stage_rwkv_inputs(core, zr, sig, a, kk, sel, restart)
        for rev in range(2):
            stage_rwkv_scan(core, zr, sig, a, kk, sel, restart, mixed, rev)
        stage_rwkv_output(core, zr, a, sel, mixed)


def stage_rwkv_inputs(core, zr, sig, a, kk, sel, restart):
    nc = core.nc
    with ExitStack() as st:
        lora = core.sb("lora", [P, 2 * S], ctx=st)
        low = core.sb("low", [HD, S], ctx=st)
        sq = core.sb("kk_sq", [P, 2, S], ctx=st)
        loaded, squashed, bank_full, emptied, made, squared, kk_full, clamped, rooted, inverted = core.sems(
            st, "lora_loaded", "squashed", "bank_full", "emptied", "kk_made", "squared", "kk_full", "clamped", "rooted", "inverted")
        UNITS = [(d, f, which) for d in range(2) for f in range(4) for which in range(2)]
        with nc.Block() as block:
            @block.sync
            def _(sp):
                sp.dma_start(lora[0:HD, :], core.dram["decay_up"]).then_inc(loaded, 16)
                sp.dma_start(lora[HD:P, :], core.dram["a_up"]).then_inc(loaded, 16)
                sp.dma_start(restart[:, :], core.dram["restart"]).then_inc(loaded, 16)
                sp.wait_ge(loaded, 48)

            @block.scalar
            def _(act):
                act.activation(low[:, :], zr[0:HD, 12, :], ACT.Tanh).then_inc(squashed, 1)
                for u, (d, f, which) in enumerate(UNITS):
                    act.wait_ge(bank_full, u + 1)
                    dest, bias = (sig, "w_decay0") if which == 0 else (a, "a_gate0")
                    act.activation(dest[:, 4 * d + f, :], core.bank[u % 6][:, :], ACT.Sigmoid,
                                   bias=core.col(bias, 4 * d + f)).then_inc(emptied, 1)
                for f in range(4):
                    act.wait_ge(made, f + 1)
                    if f >= 2:
                        act.wait_ge(inverted, 2 * f - 2)
                    act.activation(sq[:, f % 2, :], kk[:, f, :], ACT.Square).then_inc(squared, 1)
                    act.wait_ge(clamped, f + 1)
                    act.activation(sq[:, f % 2, :], sq[:, f % 2, :], ACT.Sqrt).then_inc(rooted, 1)

            @block.tensor
            def _(pe):
                pe.wait_ge(loaded, 48)
                pe.wait_ge(squashed, 1)
                for u, (d, f, which) in enumerate(UNITS):
                    if u >= 6:
                        pe.wait_ge(emptied, u - 5)
                    w = lora[HD * which:HD * which + HD, d * S + f * P:d * S + f * P + P]
                    rhs = low[:, :] if which == 0 else zr[HD:P, 12, :]
                    pe.matmul(core.bank[u % 6][:, :], w, rhs, start=True, stop=True).then_inc(bank_full, 1)
                for f in range(4):
                    pe.wait_ge(squared, f + 1)
                    pe.matmul(core.bank[6 + f % 2][:, :], core.headones[:, :], sq[:, f % 2, :], start=True, stop=True).then_inc(kk_full, 1)

            @block.vector
            def _(dve):
                for f in range(4):
                    dve.tensor_scalar(kk[:, f, :], zr[:, 4 + f, :], core.col("k_k", f), None, ALU.mult).then_inc(made, 1)
                for i, name in ((0, "k_a"), (3, "r_k"), (4, "lnx_g"), (5, "lnx_b")):
                    dve.tensor_copy(sel[:, :, i], core.col(name, 0, 4))
                dve.tensor_scalar(sel[:, :, 1], core.col("k_a", 0, 4), -1.0, 1.0, ALU.mult, ALU.add)
                dve.tensor_scalar(sel[:, :, 2], core.col("k_a", 0, 4), 0.5, None, ALU.mult)
                for f in range(4):
                    dve.wait_ge(kk_full, f + 1)
                    dve.tensor_scalar(sq[:, f % 2, :], core.bank[6 + f % 2][:, :], 1e-12, None, ALU.max).then_inc(clamped, 1)
                    dve.wait_ge(rooted, f + 1)
                    dve.reciprocal(sq[:, f % 2, :], sq[:, f % 2, :]).then_inc(inverted, 1)
                    dve.wait_ge(inverted, 2 * f + 1)
                    dve.tensor_tensor(kk[:, f, :], kk[:, f, :], sq[:, f % 2, :], ALU.mult).then_inc(inverted, 1)


def stage_rwkv_scan(core, zr, sig, a, kk, sel, restart, mixed, rev):
    nc, bank = core.nc, core.bank
    R, K, V = 0, 4, 8
    NL = len(LEVELS) - 1
    order = list(range(TT))[::-1] if rev else list(range(TT))
    Q = 3 if rev else 0
    with ExitStack() as st:
        masks = core.sb("rwkv_masks", [P, 10, P], ctx=st)
        work = core.sb("rwkv_work", [P, 23, S], ctx=st)
        xs = core.sb("rwkv_x", [P, 2, TT, HD], ctx=st)
        u_sb = core.sb("rwkv_u", [P, 2, HD], ctx=st)
        state = core.sb("rwkv_state", [P, 2, HD], ctx=st)
        held = core.sb("rwkv_held", [P, HD], ctx=st)
        total = core.sb("rwkv_total", [P, TT], ctx=st)
        step = core.sb("rwkv_step", [P, TT], ctx=st)
        cols = core.sb("rwkv_col", [P, 6], ctx=st)
        slot = lambda i: work[:, i, :]
        e1, e2, p_at, p_inv, p_prev, alpha, beta, kappa, rho = [slot(i) for i in range(9)]
        alphaN, betaN, kappaN, vN = [work[:, 9 + i, :].rearrange("p (i d) -> p i d", i=TT) for i in range(4)]
        vT, ahat = slot(13), slot(14)
        tri = [slot(15), slot(16)]
        inv = [slot(17), slot(18)]
        invT = [slot(19), slot(20)]
        off = [slot(21), slot(22)]
        m_rb = [slot(0), slot(1)]
        m_rk = [slot(2), slot(4)]
        mask = lambda i: tiled(masks[:, i, :], TT)
        four = lambda ap: ap.rearrange("p (i t) -> p i t", i=TT)
        t_of = lambda ap, i: ap[:, i * P:i * P + P]
        names = ("rwkv_tables", "summed", "raised", "v_staged", "ops_dve", "ops_pool", "turned", "turn_copied", "cols_staged",
                 "filled0", "filled1", "evac0", "evac1", "copied0", "copied1", "unit0", "unit1", "state0", "state1", "y_stored")
        sems = core.sems(st, *names)
        (tables, summed, raised, v_staged, ops_dve, ops_pool, turned, turn_copied, cols_staged,
         f0, f1, d0, d1, a0, a1, u0, u1, s0, s1, y_stored) = sems
        filled, evac, copied, unit, stated = [f0, f1], [d0, d1], [a0, a1], [u0, u1], [s0, s1]
        Z_FULL = [7 + 3 * l for l in range(NL)]
        W_LAST = Z_FULL[-1] + 1
        A_FULL = W_LAST + 1
        U_FULL = [A_FULL + 1 + 3 * n for n in range(TT)]
        Z_EVAC = [7 + l for l in range(NL)]
        U_EVAC = [7 + NL + n for n in range(TT)]
        W_COPY = [3 + 2 * l for l in range(NL - 1)] + [2 * NL]
        A_COPY = 2 * NL + 1
        with nc.Block() as block:
            @block.sync
            def _(sp):
                sp.dma_start(masks[:, :, :], core.dram["rw_rev" if rev else "rw_fwd"]).then_inc(tables, 16)
                sp.wait_ge(tables, 16)
        with nc.Fori(0, 4) as f:
            core.clear(sems)
            row = lambda t, first: t[:, bass.ds(f + first, 1), :].rearrange("p a t -> p (a t)")
            with nc.Block() as block:
                @block.vector
                def _(dve):
                    dve.tensor_copy(cols[:, :], row(sel, 0)).then_inc(cols_staged, 1)
                    dve.tensor_tensor_scan(e1, restart[:, :], row(sig, 4 * rev), 0.0, ALU.mult, ALU.add).then_inc(summed, 1)
                    dve.wait_ge(summed, 1)
                    dve.tensor_copy(total[:, :], e1[:, P - 1:S:P]).then_inc(summed, 1)
                    dve.wait_ge(summed, 2)
                    dve.scalar_tensor_tensor(out=four(e1), in0=repeat(total[:, :], P), scalar=-0.5, in1=four(e1),
                                             op0=ALU.mult, op1=ALU.add).then_inc(summed, 1)
                    dve.wait_ge(summed, 3)
                    dve.tensor_tensor(e2, e1, row(sig, 4 * rev), ALU.subtract).then_inc(summed, 1)
                    dve.tensor_tensor(step[:, 0:TT - 1], total[:, 0:TT - 1], total[:, 1:TT], ALU.add).then_inc(summed, 1)
                    dve.wait_ge(cols_staged, 1)
                    dve.tensor_scalar(kappa, row(a, 4 * rev), cols[:, 0:1], cols[:, 1:2], ALU.mult, ALU.add).then_inc(summed, 1)
                    dve.wait_ge(summed, 6)
                    dve.tensor_tensor(kappa, kappa, row(zr, K), ALU.mult).then_inc(summed, 1)
                    dve.wait_ge(raised, 2)
                    dve.scalar_tensor_tensor(out=alpha, in0=row(kk, 0), scalar=-1.0, in1=p_prev, op0=ALU.mult, op1=ALU.mult).then_inc(ops_dve, 1)
                    dve.wait_ge(ops_pool, 1)
                    dve.wait_ge(raised, 3)
                    dve.tensor_tensor(beta, beta, p_inv, ALU.mult).then_inc(ops_dve, 1)
                    dve.wait_ge(summed, 7)
                    dve.tensor_tensor(kappa, kappa, p_inv, ALU.mult).then_inc(ops_dve, 1)
                    for h in range(2):
                        dve.wait_ge(filled[h], 1)
                        dve.tensor_tensor(four(tri[h]), four(bank[4 * h][:, :]), mask(0), ALU.mult).then_inc(evac[h], 1)
                        dve.wait_ge(filled[h], 2)
                        dve.tensor_tensor(four(inv[h]), four(bank[4 * h + 1][:, :]), mask(1), ALU.mult).then_inc(evac[h], 1)
                        dve.wait_ge(filled[h], 3)
                        dve.tensor_tensor(four(off[h]), four(bank[4 * h + 2][:, :]), mask(0), ALU.mult).then_inc(evac[h], 1)
                        dve.wait_ge(filled[h], 4)
                        dve.wait_ge(ops_pool, 2)
                        dve.tensor_tensor(four(m_rb[h]), four(bank[4 * h + 3][:, :]), mask(9), ALU.mult).then_inc(evac[h], 1)
                    for h in range(2):
                        dve.wait_ge(filled[h], 5)
                        dve.tensor_tensor(four(m_rk[h]), four(bank[4 * h][:, :]), mask(9), ALU.mult).then_inc(evac[h], 1)
                        dve.wait_ge(unit[h], 1)
                        dve.tensor_tensor(four(invT[h]), four(tri[h]), mask(2), ALU.mult).then_inc(evac[h], 1)
                    for l in range(NL):
                        for h in range(2):
                            dve.wait_ge(filled[h], Z_FULL[l])
                            dve.tensor_tensor(four(off[h]), four(bank[4 * h + 2][:, :]), mask(3 + l), ALU.mult).then_inc(evac[h], 1)
                    held_n = 0
                    for n, i in enumerate(order):
                        for h in range(2):
                            dve.wait_ge(filled[h], U_FULL[n])
                            if n >= 1:
                                dve.wait_ge(filled[h], U_FULL[n - 1] + 2)
                            dve.tensor_copy(u_sb[:, h, :], bank[4 * h + 2][:, 0:HD]).then_inc(evac[h], 1)
                        if n == TT - 1:
                            break
                        for h in range(2):
                            r = slice(HD * h, HD * h + HD)
                            b = min(i, order[n + 1])
                            fac = step[r, b:b + 1]
                            if n == 0:
                                dve.wait_ge(raised, 4)
                                dve.wait_ge(filled[h], U_FULL[n] + 1)
                                dve.tensor_scalar(state[r, 0, :], bank[4 * h + 3][r, 0:HD], fac, None, ALU.mult).then_inc(stated[h], 1)
                                continue
                            dve.wait_ge(stated[h], 2 * n - 1)
                            dve.tensor_scalar(held[r, :], state[r, (n - 1) % 2, :], fac, None, ALU.mult).then_inc(stated[h], 1)
                            dve.wait_ge(stated[h], 2 * n)
                            dve.wait_ge(filled[h], U_FULL[n] + 1)
                            dve.scalar_tensor_tensor(out=state[r, n % 2, :], in0=bank[4 * h + 3][r, 0:HD], scalar=fac, in1=held[r, :],
                                                     op0=ALU.mult, op1=ALU.add).then_inc(stated[h], 1)
                    if rev:
                        for h in range(2):
                            r = slice(HD * h, HD * h + HD)
                            dve.wait_ge(filled[h], U_FULL[-1] + 1)
                            y = mixed[r, bass.ds(f + 4, 1), :].rearrange("p a t -> p (a t)")
                            dve.tensor_tensor(y, bank[4 * h][r, :], y, ALU.add).then_inc(y_stored, 1)

                @block.gpsimd
                def _(pool):
                    pool.tensor_copy(vT, row(zr, V)).then_inc(v_staged, 1)
                    pool.tensor_tensor(beta, row(a, 4 * rev), row(kk, 0), ALU.mult).then_inc(ops_pool, 1)
                    pool.wait_ge(raised, 1)
                    pool.tensor_tensor(rho, row(zr, R), p_at, ALU.mult).then_inc(ops_pool, 1)
                    for h in range(2):
                        pool.wait_ge(evac[h], 1)
                        pool.tensor_tensor(four(tri[h]), four(tri[h]), tiled(core.ident[:, :], TT), ALU.add).then_inc(unit[h], 1)
                        pool.wait_ge(evac[h], 2)
                        pool.tensor_tensor(four(inv[h]), four(inv[h]), tiled(core.ident[:, :], TT), ALU.add).then_inc(unit[h], 1)

                @block.scalar
                def _(act):
                    lam = NEG_LOG_DECAY
                    act.wait_ge(summed, 4)
                    at, prev, sign = (e2, e1, lam) if rev else (e1, e2, -lam)
                    act.activation(p_at, at, ACT.Exp, scale=sign).then_inc(raised, 1)
                    act.activation(p_prev, prev, ACT.Exp, scale=sign).then_inc(raised, 1)
                    act.activation(p_inv, at, ACT.Exp, scale=-sign).then_inc(raised, 1)
                    act.wait_ge(summed, 5)
                    act.activation(step[:, 0:TT - 1], step[:, 0:TT - 1], ACT.Exp, scale=-0.5 * lam).then_inc(raised, 1)
                    for j in range(4):
                        act.wait_ge(turned, j + 1)
                        act.activation(slot(9 + j), bank[(2, 3, 6, 7)[j]][:, :], ACT.Copy).then_inc(turn_copied, 1)
                    for h in range(2):
                        act.wait_ge(filled[h], 6)
                        act.activation(xs[:, h, :, :].rearrange("p i d -> p (i d)"), bank[4 * h + 1][:, 0:TT * HD], ACT.Copy).then_inc(copied[h], 1)
                    for l in range(NL):
                        for h in range(2):
                            if l < NL - 1:
                                act.wait_ge(filled[h], Z_FULL[l] + 2)
                                act.activation(inv[h], bank[4 * h + 3][:, :], ACT.Copy).then_inc(copied[h], 1)
                            else:
                                act.wait_ge(filled[h], W_LAST)
                            act.activation(invT[h], bank[4 * h][:, :], ACT.Copy).then_inc(copied[h], 1)
                    for h in range(2):
                        r = slice(HD * h, HD * h + HD)
                        act.wait_ge(filled[h], A_FULL)
                        act.activation(ahat[r, :], bank[4 * h + 1][r, :], ACT.Copy).then_inc(copied[h], 1)
                    if not rev:
                        for h in range(2):
                            r = slice(HD * h, HD * h + HD)
                            act.wait_ge(filled[h], U_FULL[-1] + 1)
                            act.activation(mixed[r, bass.ds(f + 4, 1), :].rearrange("p a t -> p (a t)"), bank[4 * h][r, :],
                                           ACT.Copy).then_inc(y_stored, 1)

                @block.tensor
                def _(pe):
                    for j, src in enumerate((alpha, beta, kappa, vT)):
                        if j < 3:
                            pe.wait_ge(ops_dve, j + 1)
                        else:
                            pe.wait_ge(v_staged, 1)
                        for i in range(TT):
                            mm = pe.transpose(bank[(2, 3, 6, 7)[j]][:, i * P:i * P + P], t_of(src, i), core.ident[:, :])
                        mm.then_inc(turned, 1)

                    def triangle(h, b, lhs, rhs):
                        r = slice(HD * h, HD * h + HD)
                        for i in range(TT):
                            mm = pe.matmul(bank[4 * h + b][:, i * P:i * P + P], lhs[r, i * P:i * P + P], rhs[r, i * P:i * P + P],
                                           start=True, stop=True)
                        mm.then_inc(filled[h], 1)

                    def product(h, b, lhs, rhs):
                        for i in range(TT):
                            mm = pe.matmul(bank[4 * h + b][:, i * P:i * P + P], t_of(lhs, i), t_of(rhs, i), start=True, stop=True)
                        mm.then_inc(filled[h], 1)

                    for h in range(2):
                        triangle(h, 0, beta, alpha)
                        triangle(h, 1, alpha, beta)
                    pe.wait_ge(ops_pool, 2)
                    for h in range(2):
                        pe.wait_ge(turn_copied, 2 * h + 2)
                        triangle(h, 2, kappa, alpha)
                        triangle(h, 3, beta, rho)
                    for h in range(2):
                        pe.wait_ge(evac[h], 1)
                        triangle(h, 0, kappa, rho)
                    for h in range(2):
                        r = slice(HD * h, HD * h + HD)
                        pe.wait_ge(evac[h], 3)
                        pe.wait_ge(turn_copied, 4)
                        for i in range(TT):
                            mm = pe.matmul(bank[4 * h + 1][:, i * HD:i * HD + HD], t_of(off[h], i), vN[:, i, r], start=True, stop=True)
                        mm.then_inc(filled[h], 1)
                    for l in range(NL):
                        for h in range(2):
                            if l == 0:
                                pe.wait_ge(unit[h], 2)
                            else:
                                pe.wait_ge(copied[h], W_COPY[l - 1])
                            product(h, 2, tri[h], inv[h])
                        for h in range(2):
                            pe.wait_ge(evac[h], Z_EVAC[l])
                            if l < NL - 1:
                                product(h, 3, invT[h], off[h])
                            product(h, 0, off[h], invT[h])
                    for h in range(2):
                        r = slice(HD * h, HD * h + HD)
                        pe.wait_ge(copied[h], W_COPY[-1])
                        for i in range(TT):
                            mm = pe.matmul(bank[4 * h + 1][r, i * P:i * P + P], alphaN[:, i, r], t_of(invT[h], i), start=True, stop=True)
                        mm.then_inc(filled[h], 1)
                    for n, i in enumerate(order):
                        for h in range(2):
                            r = slice(HD * h, HD * h + HD)
                            u_ps = bank[4 * h + 2][:, 0:HD]
                            mm = pe.matmul(u_ps, t_of(invT[h], i), xs[:, h, i, :], start=True, stop=n == 0)
                            if n >= 1:
                                pe.wait_ge(copied[h], A_COPY)
                                pe.wait_ge(stated[h], 2 * n - 1)
                                mm = pe.matmul(u_ps, ahat[r, i * P:i * P + P], state[r, (n - 1) % 2, :], start=False, stop=True)
                            mm.then_inc(filled[h], 1)
                        for h in range(2):
                            r = slice(HD * h, HD * h + HD)
                            pe.wait_ge(evac[h], U_EVAC[n])
                            if n < TT - 1:
                                s_ps = bank[4 * h + 3][r, 0:HD]
                                pe.matmul(s_ps, betaN[:, i, r], u_sb[:, h, :], start=True, stop=False)
                                pe.matmul(s_ps, kappaN[:, i, r], vN[:, i, r], start=False, stop=True).then_inc(filled[h], 1)
                            y_ps = bank[4 * h][r, i * P:i * P + P]
                            pe.matmul(y_ps, u_sb[:, h, :], t_of(m_rb[h], i), start=True, stop=False)
                            mm = pe.matmul(y_ps, vN[:, i, r], t_of(m_rk[h], i), start=False, stop=n == 0)
                            if n >= 1:
                                mm = pe.matmul(y_ps, state[r, (n - 1) % 2, :], rho[r, i * P:i * P + P], start=False, stop=True)
                            mm.then_inc(filled[h], 1)


def stage_rwkv_output(core, zr, a, sel, mixed):
    nc, bank = core.nc, core.bank
    with ExitStack() as st:
        gate_in = core.sb("gate_in", [P, S], ctx=st)
        g_up = core.sb("g_up", [P, S], ctx=st)
        g_w = core.sb("g_w", [P, P], ctx=st)
        yc = core.sb("yc", [P, S], ctx=st)
        sq = core.sb("y_sq", [P, S], ctx=st)
        bonus = core.sb("bonus", [P, S], ctx=st)
        cols = core.sb("out_cols", [P, 6], ctx=st)
        sems = core.sems(st, "g_loaded", "cols_staged", "gate_staged", "y_summed", "centred", "squared", "sq_summed", "rooted",
                         "inverted", "normed", "rates", "weighed", "b_summed", "bonused", "added", "gated", "stored")
        (g_loaded, cols_staged, gate_staged, y_summed, centred, squared, sq_summed, rooted, inverted, normed, rates, weighed,
         b_summed, bonused, added, gated, stored) = sems
        with nc.Block() as block:
            @block.sync
            def _(sp):
                sp.dma_start(g_up[:, :], core.dram["g_up"]).then_inc(g_loaded, 16)
                sp.wait_ge(g_loaded, 16)

            @block.scalar
            def _(act):
                act.activation(gate_in[:, :], zr[:, 13, :], ACT.Sigmoid)
        with nc.Fori(0, 4) as f:
            core.clear(sems)
            row = lambda t, first: t[:, bass.ds(f + first, 1), :].rearrange("p a t -> p (a t)")
            with nc.Block() as block:
                @block.tensor
                def _(pe):
                    pe.matmul(bank[0][:, :], core.headones[:, :], row(mixed, 4), start=True, stop=True).then_inc(y_summed, 1)
                    pe.wait_ge(gate_staged, 1)
                    pe.matmul(bank[3][:, :], g_w[:, :], gate_in[:, :], start=True, stop=True).then_inc(gated, 1)
                    pe.wait_ge(squared, 1)
                    pe.matmul(bank[1][:, :], core.headones[:, :], sq[:, :], start=True, stop=True).then_inc(sq_summed, 1)
                    pe.wait_ge(weighed, 4)
                    pe.matmul(bank[2][:, :], core.headones[:, :], bonus[:, :], start=True, stop=True).then_inc(b_summed, 1)

                @block.gpsimd
                def _(pool):
                    pool.tensor_tensor(bonus[:, :], row(a, 0), row(a, 4), ALU.add).then_inc(rates, 1)
                    pool.tensor_copy(g_w[:, :], g_up[:, bass.ds(f * P, P)]).then_inc(gate_staged, 1)

                @block.scalar
                def _(act):
                    act.wait_ge(centred, 1)
                    act.activation(sq[:, :], yc[:, :], ACT.Square).then_inc(squared, 1)
                    act.wait_ge(sq_summed, 1)
                    act.activation(sq[:, :], bank[1][:, :], ACT.Sqrt, scale=1.0 / HD, bias=64e-5).then_inc(rooted, 1)

                @block.vector
                def _(dve):
                    dve.tensor_copy(cols[:, :], row(sel, 0)).then_inc(cols_staged, 1)
                    dve.wait_ge(y_summed, 1)
                    dve.scalar_tensor_tensor(out=yc[:, :], in0=bank[0][:, :], scalar=-1.0 / HD, in1=row(mixed, 4),
                                             op0=ALU.mult, op1=ALU.add).then_inc(centred, 1)
                    dve.wait_ge(cols_staged, 1)
                    dve.wait_ge(rates, 1)
                    dve.tensor_scalar(bonus[:, :], bonus[:, :], cols[:, 2:3], cols[:, 1:2], ALU.mult, ALU.add).then_inc(weighed, 1)
                    dve.wait_ge(weighed, 1)
                    dve.tensor_tensor(bonus[:, :], bonus[:, :], row(zr, 4), ALU.mult).then_inc(weighed, 1)
                    dve.wait_ge(weighed, 2)
                    dve.scalar_tensor_tensor(out=bonus[:, :], in0=bonus[:, :], scalar=cols[:, 3:4], in1=row(zr, 0),
                                             op0=ALU.mult, op1=ALU.mult).then_inc(weighed, 1)
                    dve.wait_ge(rooted, 1)
                    dve.wait_ge(weighed, 3)
                    dve.reciprocal(sq[:, :], sq[:, :]).then_inc(weighed, 1)
                    dve.wait_ge(weighed, 4)
                    dve.scalar_tensor_tensor(out=yc[:, :], in0=yc[:, :], scalar=cols[:, 4:5], in1=sq[:, :],
                                             op0=ALU.mult, op1=ALU.mult).then_inc(normed, 1)
                    dve.wait_ge(b_summed, 1)
                    dve.tensor_tensor(bonus[:, :], bank[2][:, :], row(zr, 8), ALU.mult).then_inc(bonused, 1)
                    dve.wait_ge(normed, 1)
                    dve.wait_ge(bonused, 1)
                    dve.scalar_tensor_tensor(out=yc[:, :], in0=yc[:, :], scalar=cols[:, 5:6], in1=bonus[:, :],
                                             op0=ALU.add, op1=ALU.add).then_inc(added, 1)
                    dve.wait_ge(added, 1)
                    dve.wait_ge(gated, 1)
                    dve.tensor_tensor(row(mixed, 4), bank[3][:, :], yc[:, :], ALU.mult).then_inc(stored, 1)


def stage_residual(core, first, src, gate):
    x = core.x

    def evac(half):
        def f(eng, psum, t):
            k = 4 * half + t
            return eng.scalar_tensor_tensor(out=x[:, k, :], in0=psum, scalar=gate[:, k:k + 1], in1=x[:, k, :],
                                            op0=ALU.mult, op1=ALU.add)
        return f
    stage_project(core, first, [("T", [evac(0)] * 4), ("T", [evac(1)] * 4)], src, only_dve=True)


def stage_peer(core, first, mixed):
    nc = core.nc
    h2 = mixed
    with ExitStack() as st:
        idx = core.sb("expert_idx", [P, TT, HK], U32, ctx=st)
        gates = core.sb("expert_gate", [P, TT, HK], ctx=st)
        hN = core.sb("h_rows", [P, TT, D], ctx=st)
        stage_norm(core, h2, core.gain[:, 8:16], core.mod[:, 24:32])
        with ExitStack() as s2:
            q = core.sb("peer_q", [P, 2 * PEER_HEADS, S], ctx=s2)
            sc = core.sb("peer_scores", [P, TT, 2 * PEER_HEADS, N_KEYS], ctx=s2)
            stage_project(core, first, [("T", [copy_to(lambda f, i=i: q[:, 4 * i + f, :])] * 4) for i in range(4)], h2)
            stage_peer_scores(core, q, h2, sc, hN)
            stage_peer_topk(core, sc, q, idx, gates)
        stage_peer_experts(core, idx, gates, hN)


def stage_peer_scores(core, q, h2, sc, hN):
    nc, bank = core.nc, core.bank
    with ExitStack() as st:
        keys = core.sb("peer_keys", [P, 2 * N_KEYS], ctx=st)
        keys_loaded, bank_full, act_emptied, dve_emptied = core.sems(st, "keys_loaded", "bank_full", "act_emptied", "dve_emptied")
        units = [("turn", i, g, 0) for i in range(TT) for g in range(2)]
        units += [("score", i, g, half) for i in range(TT) for half in range(2) for g in range(2)]

        def dest(unit):
            kind, i, g, half = unit
            if kind == "turn":
                return hN[:, i, g * S:g * S + S]
            at = half * PEER_HEADS + 4 * g
            return sc[:, i, at:at + 4, :].rearrange("p r n -> p (r n)")

        with nc.Block() as block:
            @block.sync
            def _(sp):
                sp.dma_start(keys[:, :], core.dram["keys"]).then_inc(keys_loaded, 16)
                sp.wait_ge(keys_loaded, 16)

            @block.tensor
            def _(pe):
                for u, (kind, i, g, half) in enumerate(units):
                    if u >= 6:
                        pe.wait_ge(dve_emptied if u % 2 else act_emptied, (u - 6) // 2 + 1)
                    if kind == "score":
                        pe.wait_ge(keys_loaded, 16)
                    for j in range(4):
                        out = bank[u % 6][:, j * P:j * P + P]
                        if kind == "turn":
                            mm = pe.transpose(out, h2[:, 4 * g + j, i * P:i * P + P], core.ident[:, :])
                        else:
                            mm = pe.matmul(out, q[:, 2 * (4 * g + j) + half, i * P:i * P + P],
                                           keys[:, half * N_KEYS:half * N_KEYS + N_KEYS], start=True, stop=True)
                    mm.then_inc(bank_full, 1)

            @block.scalar
            def _(act):
                for u in range(0, len(units), 2):
                    act.wait_ge(bank_full, u + 1)
                    act.activation(dest(units[u]), bank[u % 6][:, :], ACT.Copy).then_inc(act_emptied, 1)

            @block.vector
            def _(dve):
                for u in range(1, len(units), 2):
                    dve.wait_ge(bank_full, u + 1)
                    dve.tensor_copy(dest(units[u]), bank[u % 6][:, :]).then_inc(dve_emptied, 1)


def stage_peer_topk(core, sc, scratch, idx, gates):
    nc = core.nc
    ROWS = 2 * PEER_HEADS
    LOWEST = -3.0e38
    with ExitStack() as st:
        row = core.sb("topk_row", [P, ROWS, N_KEYS], ctx=st)
        scr = lambda i, n: scratch[:, 4 * i:4 * i + 4, :].rearrange("p a t -> p (a t)").rearrange("p (r n) -> p r n", n=n)
        rest, cand = scr(0, N_KEYS), scr(1, TOPK * TOPK)
        cand_rest, pick = scr(2, TOPK * TOPK), scr(3, TOPK)
        val = core.sb("topk_val", [P, ROWS, TOPK], ctx=st)
        at = core.sb("topk_at", [P, ROWS, TOPK], U32, ctx=st)
        atf = core.sb("topk_atf", [P, ROWS, TOPK], ctx=st)
        best = core.sb("best", [P, PEER_HEADS, TOPK], ctx=st)
        pos = core.sb("pos", [P, PEER_HEADS, TOPK], U32, ctx=st)
        part = core.sb("pos_part", [P, 2, HK], U32, ctx=st)
        partf = core.sb("pos_partf", [P, 2, HK], ctx=st)
        key = core.sb("key", [P, 2, HK], ctx=st)
        den = core.sb("topk_den", [P, PEER_HEADS], ctx=st)
        iota = core.sb("iota16", [P, TOPK], ctx=st)
        sems = core.sems(st, "iota_loaded", "row_staged", "topk_step", "shifted", "raised")
        iota_loaded, row_staged, topk_step, shifted, raised = sems
        with nc.Block() as block:
            @block.sync
            def _(sp):
                sp.dma_start(iota[:, :], core.dram["iota16"]).then_inc(iota_loaded, 16)
                sp.wait_ge(iota_loaded, 16)
        heads = lambda ap: ap.rearrange("p (h k) -> p h k", h=PEER_HEADS)
        with nc.Fori(0, TT) as i:
            core.clear(sems)
            with nc.Block() as block:
                @block.gpsimd
                def _(pool):
                    pool.tensor_copy(row[:, :, :].rearrange("p r n -> p (r n)"),
                                     sc[:, bass.ds(i, 1), :, :].rearrange("p a r n -> p (a r n)")).then_inc(row_staged, 1)

                @block.scalar
                def _(act):
                    act.wait_ge(shifted, 1)
                    act.activation(best[:, :, :], best[:, :, :], ACT.Exp).then_inc(raised, 1)

                @block.vector
                def _(dve):
                    step = Steps(dve, topk_step)

                    def top16(n, v, where, values, others):
                        for r in range(n):
                            step(dve.max(v[:, r, 0:8], values[:, r, :]))
                        step.done()
                        for r in range(n):
                            step(dve.max_index(where[:, r, 0:8], v[:, r, 0:8], values[:, r, :]))
                            step(dve.match_replace(others[:, r, :], v[:, r, 0:8], values[:, r, :], LOWEST))
                        step.done()
                        for r in range(n):
                            step(dve.max(v[:, r, 8:16], others[:, r, :]))
                        step.done()
                        for r in range(n):
                            step(dve.max_index(where[:, r, 8:16], v[:, r, 8:16], others[:, r, :]))
                        step.done()

                    dve.wait_ge(row_staged, 1)
                    top16(ROWS, val, at, row, rest)
                    step(dve.tensor_copy(atf[:, :, :], at[:, :, :]))
                    four = [P, PEER_HEADS, TOPK, TOPK]
                    step.then(dve.tensor_tensor(cand[:, :, :].rearrange("p h (a b) -> p h a b", a=TOPK),
                                                val[:, 0:PEER_HEADS, :].unsqueeze(3).to_broadcast(four),
                                                val[:, PEER_HEADS:ROWS, :].unsqueeze(2).to_broadcast(four), ALU.add))
                    top16(PEER_HEADS, best, pos, cand, cand_rest)
                    flat = pos[:, :, :].rearrange("p h k -> p (h k)")
                    step(dve.tensor_scalar(part[:, 0, :], flat, 4, None, ALU.logical_shift_right))
                    step(dve.tensor_scalar(part[:, 1, :], flat, TOPK - 1, None, ALU.bitwise_and))
                    step(dve.tensor_copy(den[:, :], best[:, :, 0]))
                    step.done()
                    dve.tensor_tensor(best[:, :, :], best[:, :, :], repeat(den[:, :], TOPK), ALU.subtract).then_inc(shifted, 1)
                    step.then(dve.tensor_copy(partf[:, :, :], part[:, :, :]))
                    for half in range(2):
                        step.then(dve.tensor_tensor(pick[:, :, :], repeat(partf[:, half, :], TOPK), tiled(iota[:, :], HK), ALU.is_equal))
                        keys = atf[:, half * PEER_HEADS:(half + 1) * PEER_HEADS, :]
                        p4 = pick[:, :, :].rearrange("p (h k) a -> p h k a", h=PEER_HEADS)
                        step.then(dve.tensor_tensor(p4, p4, keys.unsqueeze(2).to_broadcast(four), ALU.mult))
                        step.then(dve.tensor_reduce(key[:, half, :], pick[:, :, :], AX.X, ALU.add))
                    step.then(dve.scalar_tensor_tensor(out=key[:, 0, :], in0=key[:, 0, :], scalar=float(N_KEYS), in1=key[:, 1, :],
                                                       op0=ALU.mult, op1=ALU.add))
                    step(dve.tensor_copy(idx[:, bass.ds(i, 1), :].rearrange("p a k -> p (a k)"), key[:, 0, :]))
                    dve.wait_ge(raised, 1)
                    step.then(dve.tensor_reduce(den[:, :], best[:, :, :], AX.X, ALU.add))
                    step.then(dve.reciprocal(den[:, :], den[:, :]))
                    step(dve.tensor_tensor(gates[:, bass.ds(i, 1), :].rearrange("p a (h k) -> p (a h) k", h=PEER_HEADS),
                                           best[:, :, :], repeat(den[:, :], TOPK), ALU.mult))
                    step.done()


def stage_peer_experts(core, idx, gates, hN):
    nc, bank, x = core.nc, core.bank, core.x
    SLOTS, PAIR = 8, 2
    TURNS = HK // SLOTS
    gate2 = core.mod[:, 40:48]
    with ExitStack() as st:
        rows = core.sb("expert_rows", [P, SLOTS, 2 * D], ctx=st)
        place = core.sb("expert_place", [P, SLOTS], U32, ctx=st)
        dot = core.sb("expert_dot", [P, SLOTS], ctx=st)
        act_out = core.sb("expert_act", [P, SLOTS], ctx=st)
        diag = core.sb("expert_diag", [P, SLOTS, P], ctx=st)
        zeros = core.sb("zeros", [P, P], ctx=st)
        y = core.sb("expert_y", [P, D], ctx=st)
        names = ["slot_free", "pool_gate", "placed", "dotted", "gelued", "weighted", "zeroed", "y_full", "y_copied", "y_turned", "x_added"]
        slot_free, pool_gate, placed, dotted, gelued, weighted, zeroed, y_full, y_copied, y_turned, x_added = core.sems(st, *names)
        arrived = [core.ctx.enter_context(nc.semaphore(f"rows_arrived{j}")) for j in range(SLOTS)]
        core.clear(arrived)
        with nc.Block() as block:
            @block.gpsimd
            def _(pool):
                for t in range(TT):
                    with pool.Fori(0, TURNS) as i:
                        for j in range(SLOTS):
                            n = i * SLOTS + (t * HK + j)
                            pool.wait_ge(slot_free, n + 1)
                            pool.sem_inc(pool_gate, 1)
                            pool.tensor_copy(place[:, j:j + 1], idx[:, t, bass.ds(i * SLOTS + j, 1)]).then_inc(placed, 1)
                            pool.wait_ge(placed, n + 1)
                            pool.sem_inc(pool_gate, 1)
                            pool.indirect_dma_start(rows[:, j, :], None, core.dram["uv"],
                                                    bass.IndirectOffsetOnAxis(place[:, j:j + 1], 0)).then_inc(arrived[j], 16)

            @block.vector
            def _(dve):
                dve.memset(zeros[:, :], 0.0).then_inc(zeroed, 1)
                for t in range(TT):
                    with dve.Fori(0, TURNS) as i:
                        for g in range(SLOTS // PAIR):
                            for j in range(g * PAIR, g * PAIR + PAIR):
                                dve.wait_ge(arrived[j], i * 16 + (t * TURNS + 1) * 16)
                                u = rows[:, j, 0:D]
                                dve.scalar_tensor_tensor(out=u, in0=u, scalar=1.0, in1=hN[:, t, :], op0=ALU.mult, op1=ALU.mult,
                                                         accum_out=dot[:, j:j + 1]).then_inc(dotted, 1)
                            dve.wait_ge(gelued, i * (SLOTS // PAIR) + (t * TURNS * (SLOTS // PAIR) + g + 1))
                            for j in range(g * PAIR, g * PAIR + PAIR):
                                dve.tensor_scalar(diag[:, j, :], core.ident[:, :], act_out[:, j:j + 1],
                                                  gates[:, t, bass.ds(i * SLOTS + j, 1)], ALU.mult, ALU.mult).then_inc(weighted, 1)
                    for k in range(KD):
                        if k % 4 == 0:
                            dve.wait_ge(y_turned, 2 * t + k // 4 + 1)
                        xk = x[:, k, t * P:t * P + P]
                        dve.scalar_tensor_tensor(out=xk, in0=bank[4 + k // 4][:, (k % 4) * P:(k % 4) * P + P],
                                                 scalar=gate2[:, k:k + 1], in1=xk, op0=ALU.mult, op1=ALU.add).then_inc(x_added, 1)

            @block.scalar
            def _(act):
                for t in range(TT):
                    with act.Fori(0, TURNS) as i:
                        for g in range(SLOTS // PAIR):
                            act.wait_ge(dotted, i * SLOTS + (t * HK + (g + 1) * PAIR))
                            act.activation(act_out[:, g * PAIR:(g + 1) * PAIR], dot[:, g * PAIR:(g + 1) * PAIR], ACT.Gelu).then_inc(gelued, 1)
                    act.wait_ge(y_full, t + 1)
                    if t >= 1:
                        act.wait_ge(y_turned, 2 * t)
                    for half in range(2):
                        act.activation(y[:, half * S:half * S + S], bank[2 * (t % 2) + half][:, :], ACT.Copy).then_inc(y_copied, 1)

            @block.tensor
            def _(pe):
                pe.sem_inc(slot_free, SLOTS)
                pe.wait_ge(zeroed, 1)
                for t in range(TT):
                    yb = [bank[2 * (t % 2) + half] for half in range(2)]
                    if t >= 2:
                        pe.wait_ge(y_copied, 2 * t - 2)
                    for half in range(2):
                        pe.matmul(yb[half][:, :], zeros[:, :], hN[:, t, 0:S], start=True, stop=False)
                    with pe.Fori(0, TURNS) as i:
                        for j in range(SLOTS):
                            pe.wait_ge(weighted, i * SLOTS + (t * HK + j + 1))
                            for half in range(2):
                                mm = pe.matmul(yb[half][:, :], diag[:, j, :], rows[:, j, D + half * S:D + half * S + S],
                                               start=False, stop=False, skip_group_check=True)
                            mm.then_inc(slot_free, 1)
                    for half in range(2):
                        mm = pe.matmul(yb[half][:, :], zeros[:, :], hN[:, t, 0:S], start=False, stop=True)
                    mm.then_inc(y_full, 1)
                    pe.wait_ge(y_copied, 2 * t + 2)
                    for half in range(2):
                        if t >= 1:
                            pe.wait_ge(x_added, KD * (t - 1) + 4 * half + 4)
                        for k in range(4):
                            mm = pe.transpose(bank[4 + half][:, k * P:k * P + P], y[:, (4 * half + k) * P:(4 * half + k + 1) * P], core.ident[:, :])
                        mm.then_inc(y_turned, 1)


def second_block(core, first, mixed):
    nc = core.nc
    with ExitStack() as st:
        zg = core.sb("zg", [P, 14, S], ctx=st)
        v = core.sb("v2", [P, TT, D], ctx=st)
        with ExitStack() as s2:
            zt = core.sb("zt", [P, 9, S], ctx=s2)
            stage_norm(core, mixed, core.gain[:, 16:24], core.mod[:, 48:56])
            into = lambda z, at, n: ("T", [copy_to(lambda f: z[:, at + f, :])] * n)
            rows = lambda at, n: ("N", copy_to(lambda t: v[:, t, at:at + n]))
            plan = [into(zt, 0, 3), into(zt, 3, 3), rows(0, 384), into(zt, 6, 3), into(zg, 0, 3), into(zg, 3, 3), rows(384, 384),
                    into(zg, 6, 3), into(zg, 9, 2), rows(768, 256),
                    ("T", [copy_to(lambda f: zg[:, 11 + f, :])] * 2 + [copy_to(lambda f: zg[0:16, 13, :])])]
            stage_project(core, first, plan, mixed)
            stage_retention(core, zt, v, mixed)
        logs = core.sb("log_decay", [P, 4, S], ctx=st)
        keys = core.sb("hgrn_keys", [P, 3, S], ctx=st)
        stage_recurrence_inputs(core, zg, logs, keys)
        stage_recurrence(core, 3, 2, lambda i: (zg[:, bass.ds(i, 1), :], keys[:, bass.ds(i, 1), :], logs[:, bass.ds(i, 1), :]),
                         lambda i: v[:, :, bass.ds(i * P + 384, P)], lambda i, n: zg[:, bass.ds(i + 6, 1), :], "hgrn_norm_2", mixed, 3, zg[:, 3:6, :])
        stage_recurrence(core, 1, 4, lambda i: (zg[:, 9:10, :], zg[:, 10:11, :], logs[:, 3:4, :]),
                         lambda i: v[:, :, 768:1024], lambda i, n: zg[:, 11 + n:12 + n, :], "gla_norm_2", mixed, 6, zg[:, 3:6, :])
    stage_residual(core, first + 11, mixed, core.mod[:, 64:72])
    stage_norm(core, mixed, core.gain[:, 24:32], core.mod[:, 72:80])
    stage_moe(core, mixed)


def flat(ap):
    return ap.rearrange("p a t -> p (a t)")


class HeadTail:
    NAMES = ("o_full", "o_copied", "o_squared", "o_summed", "o_rooted", "o_inverted", "o_scaled", "gate_raised", "o_stored")

    def __init__(self, core, st, scratch=None):
        self.core = core
        if scratch is None:
            scratch = core.sb("head_scratch", [P, 3, S], ctx=st)
        self.o, self.sq, self.gate = [scratch[:, i, :] for i in range(3)]
        self.gain = core.sb("head_gain", [P, 1], ctx=st)
        self.sems = core.sems(st, *self.NAMES)

    def on_scalar(self, act, n, halves, gate, gain):
        (o_full, o_copied, o_squared, o_summed, o_rooted, o_inverted, o_scaled, gate_raised, o_stored) = self.sems
        if n >= 1:
            act.wait_ge(o_stored, n)
        act.activation(self.gain[:, :], gain, ACT.Copy).then_inc(gate_raised, 1)
        act.activation(self.gate[:, :], flat(gate), ACT.Silu).then_inc(gate_raised, 1)
        for h in range(2):
            act.wait_ge(o_full, 2 * n + h + 1)
            r = slice(HD * h, HD * h + HD)
            act.activation(self.o[r, :], halves[h][r, :], ACT.Copy).then_inc(o_copied, 1)
        act.wait_ge(o_copied, 2 * n + 2)
        act.activation(self.sq[:, :], self.o[:, :], ACT.Square).then_inc(o_squared, 1)
        act.wait_ge(o_summed, n + 1)
        act.activation(self.sq[:, :], self.core.bank[0][:, :], ACT.Sqrt, scale=1.0 / HD, bias=1e-6).then_inc(o_rooted, 1)

    def on_tensor(self, pe, n, bank_free):
        (o_full, o_copied, o_squared, o_summed, o_rooted, o_inverted, o_scaled, gate_raised, o_stored) = self.sems
        pe.wait_ge(o_squared, n + 1)
        bank_free()
        pe.matmul(self.core.bank[0][:, :], self.core.headones[:, :], self.sq[:, :], start=True, stop=True).then_inc(o_summed, 1)

    def on_vector(self, dve, n, dest):
        (o_full, o_copied, o_squared, o_summed, o_rooted, o_inverted, o_scaled, gate_raised, o_stored) = self.sems
        dve.wait_ge(o_rooted, n + 1)
        dve.reciprocal(self.sq[:, :], self.sq[:, :]).then_inc(o_inverted, 1)
        dve.wait_ge(gate_raised, 2 * n + 2)
        dve.wait_ge(o_inverted, n + 1)
        dve.scalar_tensor_tensor(out=self.o[:, :], in0=self.o[:, :], scalar=self.gain[:, 0:1], in1=self.sq[:, :],
                                 op0=ALU.mult, op1=ALU.mult).then_inc(o_scaled, 1)
        dve.wait_ge(o_scaled, n + 1)
        dve.tensor_tensor(flat(dest), self.o[:, :], self.gate[:, :], ALU.mult).then_inc(o_stored, 1)


def stage_retention(core, zt, v, mixed):
    nc, bank = core.nc, core.bank
    with ExitStack() as st:
        decay = core.sb("ret_decay", [P, RET_HEADS, S], ctx=st)
        rot = core.sb("rot", [P, P], ctx=st)
        cos = core.sb("cos", [P, S], ctx=st)
        sin = core.sb("sin", [P, S], ctx=st)
        qr = core.sb("qk_rot", [P, 2, S], ctx=st)
        part = core.sb("rot_part", [P, 2, S], ctx=st)
        vs = core.sb("v_pair2", [P, TT, P], ctx=st)
        score = core.sb("ret_score", [P, 2, TT, S], ctx=st)
        stage_rotary(core, cos, sin, decay, rot)
        tail = HeadTail(core, st)
        sems = core.sems(st, "turned", "cos_done", "sin_done", "rotated", "v_staged", "scored", "decayed")
        turned, cos_done, sin_done, rotated, v_staged, scored, decayed = sems
        o_full = tail.sems[0]
        UNITS = [(h, j) for h in range(2) for j in range(TT)]
        with nc.Fori(0, 3) as i:
            core.clear(sems + tail.sems)
            with nc.Block() as block:
                @block.gpsimd
                def _(pool):
                    for w in range(2):
                        pool.tensor_tensor(qr[:, w, :], flat(zt[:, bass.ds(i + 3 * w, 1), :]), cos[:, :], ALU.mult).then_inc(cos_done, 1)
                    pool.tensor_copy(vs[:, :, :], v[:, :, bass.ds(i * P, P)]).then_inc(v_staged, 1)

                @block.scalar
                def _(act):
                    tail.on_scalar(act, 0, bank[4:6], zt[:, bass.ds(i + 6, 1), :], core.col("ret_norm_2", i))

                @block.tensor
                def _(pe):
                    for w in range(2):
                        pe.matmul(bank[w][:, :], rot[:, :], flat(zt[:, bass.ds(i + 3 * w, 1), :]), start=True, stop=True).then_inc(turned, 1)
                    pe.wait_ge(rotated, 2)

                    def mix(h):
                        pe.wait_ge(decayed, 4 * h + 4)
                        pe.wait_ge(v_staged, 1)
                        r = slice(HD * h, HD * h + HD)
                        for j in range(TT):
                            mm = pe.matmul(bank[4 + h][r, j * P:S], vs[:, j, r], score[:, h, j, 0:S - j * P], start=j == 0, stop=j == TT - 1)
                        mm.then_inc(o_full, 1)

                    for u, (h, j) in enumerate(UNITS):
                        if u >= 2:
                            pe.wait_ge(decayed, u - 1)
                        r = slice(HD * h, HD * h + HD)
                        pe.matmul(bank[2 + u % 2][:, 0:S - j * P], qr[r, 1, j * P:j * P + P], qr[r, 0, j * P:S],
                                  start=True, stop=True).then_inc(scored, 1)
                        if u == 5:
                            mix(0)
                    mix(1)
                    tail.on_tensor(pe, 0, lambda: pe.wait_ge(sin_done, 1))

                @block.vector
                def _(dve):
                    for w in range(2):
                        dve.wait_ge(turned, w + 1)
                        dve.tensor_tensor(part[:, w, :], bank[w][:, :], sin[:, :], ALU.mult).then_inc(sin_done, 1)
                        dve.wait_ge(cos_done, w + 1)
                        dve.wait_ge(sin_done, w + 1)
                        dve.tensor_tensor(qr[:, w, :], qr[:, w, :], part[:, w, :], ALU.add).then_inc(rotated, 1)
                    for u, (h, j) in enumerate(UNITS):
                        dve.wait_ge(scored, u + 1)
                        dve.tensor_tensor(score[:, h, j, 0:S - j * P], bank[2 + u % 2][:, 0:S - j * P],
                                          flat(decay[:, bass.ds(i * 2 + h, 1), 0:S - j * P]), ALU.mult).then_inc(decayed, 1)
                    tail.on_vector(dve, 0, mixed[:, bass.ds(i, 1), :])


def stage_rotary(core, cos, sin, decay, rot):
    nc = core.nc
    TURN = 2.0 * math.pi
    C1 = 6.28125
    C2 = 0.0019350051879882812
    C3 = TURN - C1 - C2
    MAGIC = 12582912.0
    with ExitStack() as st:
        pos = core.sb("pos", [P, S], I32, ctx=st)
        turns = core.sb("turns", [P, S], ctx=st)
        freq = core.sb("inv_freq", [P, 1], ctx=st)
        loaded, step_sem, reduced, done = core.sems(st, "rot_loaded", "rot_step", "reduced", "rot_done")
        with nc.Block() as block:
            @block.sync
            def _(sp):
                sp.dma_start(pos[:, :], core.dram["positions"].rearrange("a t -> (a t)").partition_broadcast(P)).then_inc(loaded, 16)
                sp.dma_start(freq[:, :], core.dram["inv_freq"]).then_inc(loaded, 16)
                sp.dma_start(decay[:, :, :], core.dram["ret_decay"]).then_inc(loaded, 16)
                sp.dma_start(rot[:, :], core.dram["rot"]).then_inc(loaded, 16)
                sp.wait_ge(loaded, 64)

            @block.vector
            def _(dve):
                step = Steps(dve, step_sem)
                ang = sin[:, :]
                dve.wait_ge(loaded, 64)
                step.then(dve.tensor_copy(cos[:, :], pos[:, :]))
                step.then(dve.tensor_scalar(ang, cos[:, :], freq[:, 0:1], None, ALU.mult))
                step.then(dve.tensor_scalar(turns[:, :], ang, 1.0 / TURN, MAGIC, ALU.mult, ALU.add))
                step.then(dve.tensor_scalar(turns[:, :], turns[:, :], MAGIC, None, ALU.subtract))
                for c in (C1, C2, C3):
                    step.then(dve.scalar_tensor_tensor(out=ang, in0=turns[:, :], scalar=-c, in1=ang, op0=ALU.mult, op1=ALU.add))
                step.then(dve.tensor_scalar(ang, ang, math.pi, -math.pi, ALU.min, ALU.max))
                step.then(dve.scalar_tensor_tensor(out=cos[:, :], in0=ang, scalar=-1.0, in1=ang, op0=ALU.mult, op1=ALU.max))
                dve.tensor_scalar(cos[:, :], cos[:, :], -1.0, 0.5 * math.pi, ALU.mult, ALU.add).then_inc(reduced, 1)

            @block.scalar
            def _(act):
                act.wait_ge(reduced, 1)
                act.activation(cos[:, :], cos[:, :], ACT.Sin).then_inc(done, 1)
                act.activation(sin[:, :], sin[:, :], ACT.Sin).then_inc(done, 1)


def stage_recurrence_inputs(core, zg, logs, keys):
    nc, bank = core.nc, core.bank
    HUGE = 2.0 ** 60
    with ExitStack() as st:
        lb = core.sb("lower_bound", [P, 3, 3], ctx=st)
        low = core.sb("log_low", [P, 3, S], ctx=st)
        u = core.sb("gla_u", [P, 3, S], ctx=st)
        wa2 = core.sb("wa2", [16, P], ctx=st)
        (loaded, step_sem, lb_shift, lb_raised, sig_done, split, logged, u_full, u_biased, u_abs, u_logged, q_raised) = core.sems(
            st, "wa2_loaded", "step", "lb_shifted", "lb_raised", "sig_done", "split", "logged", "u_full", "u_biased", "u_abs",
            "u_logged", "q_raised")
        logits = core.col("hgrn_lb_logits_2", 0, 3)
        with nc.Block() as block:
            @block.sync
            def _(sp):
                sp.dma_start(wa2[:, :], core.dram["wa2"]).then_inc(loaded, 16)
                sp.wait_ge(loaded, 16)

            @block.tensor
            def _(pe):
                pe.wait_ge(loaded, 16)
                pe.matmul(bank[0][:, :], wa2[:, :], zg[0:16, 13, :], start=True, stop=True).then_inc(u_full, 1)

            @block.scalar
            def _(act):
                act.activation(logs[:, 0:3, :], zg[:, 3:6, :], ACT.Sigmoid).then_inc(sig_done, 1)
                act.activation(keys[:, :, :], zg[:, 3:6, :], ACT.Sigmoid, scale=-1.0).then_inc(sig_done, 1)
                act.activation(zg[:, 0:3, :], zg[:, 0:3, :], ACT.Silu).then_inc(q_raised, 1)
                act.wait_ge(u_full, 1)
                act.activation(u[:, 0, :], bank[0][:, :], ACT.Identity, bias=core.col("gla_ba_2")).then_inc(u_biased, 1)
                act.wait_ge(lb_shift, 1)
                act.activation(lb[:, 2, :], lb[:, 2, :], ACT.Exp).then_inc(lb_raised, 1)
                act.wait_ge(u_abs, 1)
                act.activation(u[:, 1, :], u[:, 1, :], ACT.Exp, scale=-1.0).then_inc(u_logged, 1)
                act.wait_ge(u_logged, 1)
                act.activation(u[:, 1, :], u[:, 1, :], ACT.Ln, bias=1.0).then_inc(u_logged, 1)
                act.wait_ge(split, 1)
                act.activation(logs[:, 0:3, :], logs[:, 0:3, :], ACT.Ln).then_inc(logged, 1)
                act.activation(low[:, :, :], low[:, :, :], ACT.Ln).then_inc(logged, 1)

            @block.vector
            def _(dve):
                step = Steps(dve, step_sem)
                dve.tensor_tensor(lb[:, 2, :], logits, logits, ALU.subtract).then_inc(lb_shift, 1)
                dve.wait_ge(lb_raised, 1)
                step.then(dve.reciprocal(lb[:, 0, :], lb[:, 2, :]))
                step.then(dve.tensor_tensor(lb[:, 2, :], lb[:, 2, :], lb[:, 0, :], ALU.mult))
                step.then(dve.tensor_tensor(lb[:, 0, :], lb[:, 2, :], lb[:, 2, :], ALU.subtract))
                step.then(dve.tensor_scalar(lb[:, 1, :], lb[:, 0, :], -1.0, 1.0, ALU.mult, ALU.add))
                dve.wait_ge(u_biased, 1)
                dve.scalar_tensor_tensor(out=u[:, 1, :], in0=u[:, 0, :], scalar=-1.0, in1=u[:, 0, :], op0=ALU.mult, op1=ALU.max).then_inc(u_abs, 1)
                step(dve.tensor_scalar(u[:, 2, :], u[:, 0, :], 0.0, None, ALU.min))
                dve.wait_ge(sig_done, 2)
                for f in range(3):
                    step(dve.tensor_scalar(logs[:, f, :], logs[:, f, :], lb[:, 1, f:f + 1], lb[:, 0, f:f + 1], ALU.mult, ALU.add))
                    step(dve.tensor_scalar(keys[:, f, :], keys[:, f, :], lb[:, 1, f:f + 1], None, ALU.mult))
                step.done()
                step.then(dve.tensor_scalar(low[:, :, :], logs[:, 0:3, :], 1e-30, HUGE, ALU.max, ALU.mult))
                step(dve.tensor_scalar(low[:, :, :], low[:, :, :], 1.0, None, ALU.min))
                step(dve.tensor_scalar(logs[:, 0:3, :], logs[:, 0:3, :], 1.0 / HUGE, None, ALU.max))
                step.done()
                dve.sem_inc(split, 1)
                dve.wait_ge(q_raised, 1)
                step(dve.tensor_scalar(zg[:, 0:3, :], zg[:, 0:3, :], HD ** -0.5, None, ALU.mult))
                step(dve.tensor_scalar(zg[:, 9, :], zg[:, 9, :], 32 ** -0.5, None, ALU.mult))
                dve.wait_ge(u_logged, 2)
                step.then(dve.tensor_tensor(u[:, 2, :], u[:, 2, :], u[:, 1, :], ALU.subtract))
                step(dve.tensor_scalar(logs[:, 3, :], u[:, 2, :], 1.0 / 16.0, None, ALU.mult))
                dve.wait_ge(logged, 2)
                step(dve.tensor_tensor(logs[:, 0:3, :], logs[:, 0:3, :], low[:, :, :], ALU.add))
                step.done()


def stage_recurrence(core, turns, heads, source, values, gate, gain, mixed, base, scratch):
    nc, bank = core.nc, core.bank
    dk = P // heads
    NT = heads // 2
    NLV = len(LEVELS)
    with ExitStack() as st:
        halves = core.sb("halves", [P, NLV, P], U32, ctx=st)
        restart = core.sb("restart", [P, S], ctx=st)
        qs = core.sb("rec_q", [P, S], ctx=st)
        ks = core.sb("rec_k", [P, S], ctx=st)
        cum = core.sb("rec_cum", [P, S], ctx=st)
        q_end = core.sb("rec_q_end", [P, S], ctx=st)
        k_end = core.sb("rec_k_end", [P, S], ctx=st)
        total = core.sb("rec_total", [P, TT], ctx=st)
        far = core.sb("rec_far", [P, 2, P], ctx=st)
        dec = core.sb("rec_dec", [P, 2, S], ctx=st)
        qm = core.sb("rec_qm", [P, 2, S], ctx=st)
        km = core.sb("rec_km", [P, 2, S], ctx=st)
        vs = core.sb("rec_v", [P, TT, heads * HD], ctx=st)
        score = core.sb("rec_score", [P, heads, TT, S], ctx=st)
        tail = HeadTail(core, st, scratch)
        names = ("rec_tables", "staged", "q_staged", "k_staged", "summed", "total_ready", "ended", "raised", "far_ready", "halved", "dec_raised",
                 "q_ready", "k_ready", "scored", "merged", "far_scored", "far_copied")
        sems = core.sems(st, *names)
        (tables, staged, q_staged, k_staged, summed, total_ready, ended, raised, far_ready, halved, dec_raised, q_ready, k_ready, scored,
         merged, far_scored, far_copied) = sems
        o_full = tail.sems[0]
        with nc.Block() as block:
            @block.sync
            def _(sp):
                sp.dma_start(halves[:, :, :], core.dram["halves"]).then_inc(tables, 16)
                sp.dma_start(restart[:, :], core.dram["restart"]).then_inc(tables, 16)
                sp.wait_ge(tables, 32)
        tl = lambda ap, i: ap[:, i * P:i * P + P]

        def turn(i):
            q_in, k_in, log_in = [flat(s) for s in source(i)]
            with nc.Block() as block:
                @block.gpsimd
                def _(pool):
                    pool.tensor_copy(qs[:, :], q_in).then_inc(q_staged, 1)
                    pool.tensor_copy(ks[:, :], k_in).then_inc(k_staged, 1)
                    pool.tensor_copy(vs[:, :, :], values(i)).then_inc(staged, 1)
                    pool.wait_ge(k_staged, 1)
                    for l in range(NLV):
                        pool.wait_ge(dec_raised, l + 1)
                        if l >= 2:
                            pool.wait_ge(scored, heads * l)
                        pool.tensor_tensor(km[:, l % 2, :], ks[:, :], dec[:, l % 2, :], ALU.mult).then_inc(k_ready, 1)

                @block.scalar
                def _(act):
                    act.wait_ge(summed, 1)
                    act.activation(q_end[:, :], cum[:, :], ACT.Exp).then_inc(raised, 1)
                    act.wait_ge(ended, 1)
                    act.activation(k_end[:, :], k_end[:, :], ACT.Exp).then_inc(raised, 1)
                    act.wait_ge(total_ready, 1)
                    act.wait_ge(ended, 1)
                    act.activation(total[:, :], total[:, :], ACT.Exp).then_inc(raised, 1)
                    for l in range(NLV):
                        act.wait_ge(halved, 2 * l + 2)
                        act.activation(dec[:, l % 2, :], dec[:, l % 2, :], ACT.Exp).then_inc(dec_raised, 1)
                    for h in range(heads):
                        act.wait_ge(far_scored, 2 * h + 1)
                        act.activation(score[:, h, 0:3, P:2 * P], bank[4][:, 0:3 * P].rearrange("p (j t) -> p j t", t=P), ACT.Copy).then_inc(far_copied, 1)
                        act.wait_ge(far_scored, 2 * h + 2)
                        act.activation(score[:, h, 0:2, 2 * P:3 * P], bank[5][:, 0:2 * P].rearrange("p (j t) -> p j t", t=P), ACT.Copy).then_inc(far_copied, 1)
                        act.activation(score[:, h, 0, 3 * P:4 * P], bank[5][:, 2 * P:3 * P], ACT.Copy).then_inc(far_copied, 1)
                    for n in range(NT):
                        tail.on_scalar(act, n, bank[6:8], gate(i, n), core.col(gain, i + n))

                @block.tensor
                def _(pe):
                    unit = 0
                    for l in range(NLV + 1):
                        if l == 0:
                            pe.wait_ge(q_staged, 1)
                            pe.wait_ge(k_staged, 1)
                            a, b = ks, qs
                        else:
                            pe.wait_ge(q_ready, l)
                            pe.wait_ge(k_ready, l)
                            a, b = km[:, (l - 1) % 2, :], qm[:, (l - 1) % 2, :]
                        for h in range(heads):
                            if unit >= 4:
                                pe.wait_ge(merged, unit - 3)
                            r = slice(dk * h, dk * h + dk)
                            for t in range(TT):
                                mm = pe.matmul(bank[unit % 4][:, t * P:t * P + P], a[r, t * P:t * P + P], b[r, t * P:t * P + P], start=True, stop=True)
                            mm.then_inc(scored, 1)
                            unit += 1
                    pe.wait_ge(far_ready, 4)
                    for h in range(heads):
                        r = slice(dk * h, dk * h + dk)
                        if h >= 1:
                            pe.wait_ge(far_copied, 3 * h - 2)
                        for j in range(3):
                            mm = pe.matmul(bank[4][:, j * P:j * P + P], k_end[r, j * P:j * P + P], q_end[r, (j + 1) * P:(j + 2) * P], start=True, stop=True)
                        mm.then_inc(far_scored, 1)
                        if h >= 1:
                            pe.wait_ge(far_copied, 3 * h)
                        k0, k1, q2, q3 = far[r, 0, :], k_end[r, P:2 * P], q_end[r, 2 * P:3 * P], far[r, 1, :]
                        for j, (a, b) in enumerate(((k0, q2), (k1, q3), (k0, q3))):
                            mm = pe.matmul(bank[5][:, j * P:j * P + P], a, b, start=True, stop=True)
                        mm.then_inc(far_scored, 1)
                    pe.wait_ge(staged, 1)
                    for n in range(NT):
                        for hh in range(2):
                            h = 2 * n + hh
                            pe.wait_ge(far_copied, 3 * h + 3)
                            pe.wait_ge(merged, heads * NLV + h + 1)
                            if n >= 1:
                                pe.wait_ge(tail.sems[1], 2 * (n - 1) + hh + 1)
                            r = slice(HD * hh, HD * hh + HD)
                            for j in range(TT):
                                mm = pe.matmul(bank[6 + hh][r, j * P:S], vs[:, j, h * HD:h * HD + HD], score[:, h, j, 0:S - j * P], start=j == 0, stop=j == TT - 1)
                            mm.then_inc(o_full, 1)
                        tail.on_tensor(pe, n, lambda: pe.wait_ge(merged, heads * (NLV + 1)))

                @block.vector
                def _(dve):
                    dve.tensor_tensor_scan(cum[:, :], restart[:, :], log_in, 0.0, ALU.mult, ALU.add).then_inc(summed, 1)
                    dve.wait_ge(summed, 1)
                    dve.tensor_copy(total[:, :], cum[:, P - 1:S:P]).then_inc(total_ready, 1)
                    dve.wait_ge(total_ready, 1)
                    c3 = cum[:, :].rearrange("p (i t) -> p i t", t=P)
                    dve.tensor_tensor(k_end[:, :].rearrange("p (i t) -> p i t", t=P), repeat(total[:, :], P), c3, ALU.subtract).then_inc(ended, 1)

                    def halve(l):
                        m = LEVELS[l]
                        if l >= 2:
                            dve.wait_ge(k_ready, l - 1)
                            dve.wait_ge(q_ready, l - 1)
                        cm = cum[:, :].rearrange("p (b w) -> p b w", w=2 * m)
                        dm = dec[:, l % 2, :].rearrange("p (b w) -> p b w", w=2 * m)
                        mid = cm[:, :, m - 1:m].to_broadcast([P, S // (2 * m), m])
                        dve.tensor_tensor(dm[:, :, 0:m], mid, cm[:, :, 0:m], ALU.subtract).then_inc(halved, 1)
                        dve.tensor_tensor(dm[:, :, m:2 * m], cm[:, :, m:2 * m], mid, ALU.subtract).then_inc(halved, 1)

                    def query(l):
                        dve.wait_ge(dec_raised, l + 1)
                        if l >= 2:
                            dve.wait_ge(scored, heads * l)
                        dve.tensor_tensor(qm[:, l % 2, :], qs[:, :], dec[:, l % 2, :], ALU.mult).then_inc(q_ready, 1)

                    def merge(l):
                        for h in range(heads):
                            u = heads * l + h
                            dve.wait_ge(scored, u + 1)
                            src = bank[u % 4][:, :].rearrange("p (i t) -> p i t", t=P)
                            if l == 0:
                                dve.tensor_tensor(score[:, h, :, 0:P], src, tiled(core.ident[:, :], TT), ALU.mult).then_inc(merged, 1)
                            else:
                                dve.wait_ge(merged, heads * (l - 1) + h + 1)
                                dve.copy_predicated(score[:, h, :, 0:P], tiled(halves[:, l - 1, :], TT), src).then_inc(merged, 1)

                    halve(0)
                    halve(1)
                    dve.wait_ge(q_staged, 1)
                    merge(0)
                    for l in range(NLV):
                        query(l)
                        if l + 2 < NLV:
                            halve(l + 2)
                        merge(l + 1)
                    dve.wait_ge(raised, 3)
                    dve.tensor_tensor(q_end[:, :], q_end[:, :], qs[:, :], ALU.mult).then_inc(far_ready, 1)
                    dve.wait_ge(k_staged, 1)
                    dve.tensor_tensor(k_end[:, :], k_end[:, :], ks[:, :], ALU.mult).then_inc(far_ready, 1)
                    dve.wait_ge(far_ready, 2)
                    dve.tensor_scalar(far[:, 0, :], k_end[:, 0:P], total[:, 1:2], None, ALU.mult).then_inc(far_ready, 1)
                    dve.tensor_scalar(far[:, 1, :], q_end[:, 3 * P:S], total[:, 2:3], None, ALU.mult).then_inc(far_ready, 1)
                    for n in range(NT):
                        dest = mixed[:, bass.ds(i + base, 1), :] if turns > 1 else mixed[:, base + n:base + n + 1, :]
                        tail.on_vector(dve, n, dest)

        if turns > 1:
            with nc.Fori(0, turns) as i:
                core.clear(sems + tail.sems)
                turn(i)
        else:
            turn(0)


def stage_route(core, h, combT):
    nc, bank = core.nc, core.bank
    NR = N_GROUPS + N_EXPERTS
    with ExitStack() as st:
        w = core.sb("router_w", [P, KD, NR], ctx=st)
        b = core.sb("router_b", [P, NR], ctx=st)
        iota = core.sb("iota8", [P, TOPK], ctx=st)
        lg = core.sb("logits", [P, TT, NR], ctx=st)
        top = core.sb("group_top", [P, TT], ctx=st)
        hot = core.sb("group_hot", [P, TT, N_GROUPS], ctx=st)
        free = core.sb("group_free", [P, TT], ctx=st)
        ex = core.sb("group_exp", [P, TT, N_GROUPS], ctx=st)
        gw = core.sb("group_w", [P, TT], ctx=st)
        within = core.sb("within", [P, TT, N_GROUPS, PER_GROUP], ctx=st)
        el = core.sb("expert_logit", [P, TT, PER_GROUP], ctx=st)
        best = core.sb("expert_best", [P, TT, 8], ctx=st)
        at = core.sb("expert_at", [P, TT, 8], U32, ctx=st)
        atf = core.sb("expert_atf", [P, TT, 8], ctx=st)
        wt = core.sb("expert_wt", [P, 2, TT], ctx=st)
        pick = core.sb("expert_pick", [P, 2, TT, PER_GROUP], ctx=st)
        comb = core.sb("comb", [P, TT, N_EXPERTS], ctx=st)
        loaded, scored, step_sem, g_shifted, g_raised, e_shifted, e_raised, combined, turned, copied = core.sems(
            st, "router_loaded", "scored", "step", "g_shifted", "g_raised", "e_shifted", "e_raised", "combined", "turned", "copied")
        with nc.Block() as block:
            @block.sync
            def _(sp):
                sp.dma_start(w[:, :, :], core.dram["router_w"].rearrange("(k p) n -> p k n", p=P)).then_inc(loaded, 16)
                sp.dma_start(b[:, :], core.dram["router_b"].rearrange("a n -> (a n)").partition_broadcast(P)).then_inc(loaded, 16)
                sp.dma_start(iota[:, :], core.dram["iota16"]).then_inc(loaded, 16)
                sp.wait_ge(loaded, 48)

            @block.tensor
            def _(pe):
                pe.wait_ge(loaded, 48)
                for i in range(TT):
                    for k in range(KD):
                        mm = pe.matmul(bank[0][:, i * NR:i * NR + NR], h[:, k, i * P:i * P + P], w[:, k, :], start=k == 0, stop=k == KD - 1)
                mm.then_inc(scored, 1)
                pe.wait_ge(combined, 1)
                for i in range(TT):
                    mm = pe.transpose(bank[1][0:N_EXPERTS, i * P:i * P + P], comb[:, i, :], core.ident[:, :])
                mm.then_inc(turned, 1)

            @block.scalar
            def _(act):
                act.wait_ge(g_shifted, 1)
                act.activation(ex[:, :, :], ex[:, :, :], ACT.Exp).then_inc(g_raised, 1)
                act.wait_ge(e_shifted, 1)
                act.activation(wt[:, 1, :], wt[:, 1, :], ACT.Exp).then_inc(e_raised, 1)
                act.wait_ge(turned, 1)
                act.activation(combT, bank[1][0:N_EXPERTS, :], ACT.Copy).then_inc(copied, 1)

            @block.vector
            def _(dve):
                step = Steps(dve, step_sem)
                dve.wait_ge(scored, 1)
                dve.wait_ge(loaded, 48)
                step.then(dve.tensor_tensor(lg[:, :, :], bank[0][:, 0:TT * NR].rearrange("p (i n) -> p i n", n=NR), tiled(b[:, :], TT), ALU.add))
                gl = lg[:, :, 0:N_GROUPS]
                step.then(dve.tensor_reduce(top[:, :], gl, AX.X, ALU.max))
                dve.tensor_tensor(ex[:, :, :], gl, repeat(top[:, :], N_GROUPS), ALU.subtract).then_inc(g_shifted, 1)
                step.then(dve.tensor_tensor(hot[:, :, :], gl, repeat(top[:, :], N_GROUPS), ALU.is_equal))
                step.then(dve.tensor_scalar(free[:, :], hot[:, :, 0], -1.0, 1.0, ALU.mult, ALU.add))
                for g in range(1, N_GROUPS):
                    step.then(dve.tensor_tensor(hot[:, :, g], hot[:, :, g], free[:, :], ALU.mult))
                    step.then(dve.tensor_tensor(free[:, :], free[:, :], hot[:, :, g], ALU.subtract))
                el4 = lg[:, :, N_GROUPS:NR].rearrange("p i (g e) -> p i g e", g=N_GROUPS)
                hot4 = hot[:, :, :].unsqueeze(3).to_broadcast([P, TT, N_GROUPS, PER_GROUP])
                step.then(dve.tensor_tensor(within[:, :, :, :], el4, hot4, ALU.mult))
                step.then(dve.tensor_reduce(el[:, :, :], within[:, :, :, :].rearrange("p i g e -> p i e g"), AX.X, ALU.add))
                for i in range(TT):
                    step(dve.max(best[:, i, :], el[:, i, :]))
                step.done()
                for i in range(TT):
                    step(dve.max_index(at[:, i, :], best[:, i, :], el[:, i, :]))
                dve.tensor_tensor(wt[:, 1, :], best[:, :, 1], best[:, :, 0], ALU.subtract).then_inc(e_shifted, 1)
                step.done()
                step(dve.tensor_copy(atf[:, :, :], at[:, :, :]))
                dve.wait_ge(g_raised, 1)
                step.then(dve.tensor_reduce(gw[:, :], ex[:, :, :], AX.X, ALU.add))
                dve.wait_ge(e_raised, 1)
                step.then(dve.tensor_scalar(wt[:, 0, :], wt[:, 1, :], 1.0, None, ALU.add))
                step.then(dve.tensor_tensor(gw[:, :], gw[:, :], wt[:, 0, :], ALU.mult))
                step.then(dve.reciprocal(wt[:, 0, :], gw[:, :]))
                step.then(dve.tensor_tensor(wt[:, 1, :], wt[:, 1, :], wt[:, 0, :], ALU.mult))
                for j in range(2):
                    step.then(dve.tensor_tensor(pick[:, j, :, :], repeat(atf[:, :, j], PER_GROUP), tiled(iota[:, 0:PER_GROUP], TT), ALU.is_equal))
                    step.then(dve.tensor_tensor(pick[:, j, :, :], pick[:, j, :, :], repeat(wt[:, j, :], PER_GROUP), ALU.mult))
                step.then(dve.tensor_tensor(pick[:, 0, :, :], pick[:, 0, :, :], pick[:, 1, :, :], ALU.add))
                dve.tensor_tensor(comb[:, :, :].rearrange("p i (g e) -> p i g e", g=N_GROUPS), hot4,
                                  pick[:, 0, :, :].unsqueeze(2).to_broadcast([P, TT, N_GROUPS, PER_GROUP]), ALU.mult).then_inc(combined, 1)


def stage_moe(core, h):
    nc, bank, x = core.nc, core.bank, core.x
    NF = D_EXPERT // P
    with ExitStack() as st:
        combT = core.sb("combT", [N_EXPERTS, S], ctx=st)
        rowsel = core.sb("row_select", [N_EXPERTS, N_EXPERTS, P], ctx=st)
        stage_route(core, h, combT[:, :])
        gate_w = core.sb("gate_w", [P, 2, KD, D_EXPERT], ctx=st)
        up_w = core.sb("up_w", [P, 2, KD, D_EXPERT], ctx=st)
        down_w = core.sb("down_w", [P, 2, NF, D], ctx=st)
        rs = core.sb("row_now", [N_EXPERTS, 2, P], ctx=st)
        hid = core.sb("hidden", [P, 2, NF, S], ctx=st)
        y = core.sb("moe_y", [P, KD, S], ctx=st)
        names = ("rows_loaded", "gate_loaded0", "gate_loaded1", "up_loaded0", "up_loaded1", "down_loaded0", "down_loaded1", "row_staged", "comb_full",
                 "gate_full", "up_full", "silu_done", "weighed", "y_full", "y_added")
        sems = core.sems(st, *names)
        (rows_loaded, gl0, gl1, ul0, ul1, dl0, dl1, row_staged, comb_full, gate_full, up_full, silu_done, weighed, y_full, y_added) = sems
        g_loaded, u_loaded, d_loaded = [gl0, gl1], [ul0, ul1], [dl0, dl1]
        with nc.Block() as block:
            @block.sync
            def _(sp):
                sp.dma_start(rowsel[:, :, :], core.dram["expert_rows"]).then_inc(rows_loaded, 16)
                sp.wait_ge(rows_loaded, 16)

            @block.vector
            def _(dve):
                dve.memset(y[:, :, :], 0.0)
        with nc.Fori(0, N_EXPERTS // 2) as i:
            core.clear(sems)
            with nc.Block() as block:
                @block.sync
                def _(sp):
                    for w in range(2):
                        e = bass.ds(i * 2 + w, 1)
                        src = lambda name: core.dram[name][e, :, :].rearrange("a (k p) n -> p (a k) n", p=P)
                        sp.dma_start(gate_w[:, w, :, :], src("gate_w")).then_inc(g_loaded[w], 16)
                        sp.dma_start(up_w[:, w, :, :], src("up_w")).then_inc(u_loaded[w], 16)
                        sp.dma_start(down_w[:, w, :, :], src("down_w")).then_inc(d_loaded[w], 16)

                @block.gpsimd
                def _(pool):
                    pool.tensor_copy(rs[:, :, :], rowsel[:, bass.ds(i * 2, 2), :]).then_inc(row_staged, 1)

                @block.tensor
                def _(pe):
                    for w in range(2):
                        if w == 0:
                            pe.wait_ge(row_staged, 1)
                        else:
                            pe.wait_ge(weighed, 2 * NF)
                        pe.matmul(bank[0][:, :], rs[:, w, :], combT[:, :], start=True, stop=True).then_inc(comb_full, 1)
                        for name, wt, first, full, loaded in (("gate", gate_w, 1, gate_full, g_loaded), ("up", up_w, 3, up_full, u_loaded)):
                            pe.wait_ge(loaded[w], 16)
                            for f in range(NF):
                                for k in range(KD):
                                    mm = pe.matmul(bank[first + f][:, :], wt[:, w, k, f * P:f * P + P], h[:, k, :], start=k == 0, stop=k == KD - 1)
                                mm.then_inc(full, 1)
                    pe.wait_ge(weighed, 4 * NF)
                    for w in range(2):
                        pe.wait_ge(d_loaded[w], 16)
                    for d in range(KD):
                        if d >= 3:
                            pe.wait_ge(y_added, d - 2)
                        for n, (w, f) in enumerate([(w, f) for w in range(2) for f in range(NF)]):
                            mm = pe.matmul(bank[5 + d % 3][:, :], down_w[:, w, f, d * P:d * P + P], hid[:, w, f, :], start=n == 0, stop=n == 3)
                        mm.then_inc(y_full, 1)

                @block.scalar
                def _(act):
                    for w in range(2):
                        for f in range(NF):
                            act.wait_ge(gate_full, NF * w + f + 1)
                            act.activation(hid[:, w, f, :], bank[1 + f][:, :], ACT.Silu).then_inc(silu_done, 1)

                @block.vector
                def _(dve):
                    n = 0
                    for w in range(2):
                        for f in range(NF):
                            dve.wait_ge(silu_done, NF * w + f + 1)
                            dve.wait_ge(up_full, NF * w + f + 1)
                            dve.tensor_tensor(hid[:, w, f, :], hid[:, w, f, :], bank[3 + f][:, :], ALU.mult).then_inc(weighed, 1)
                            n += 1
                            dve.wait_ge(weighed, n)
                            dve.wait_ge(comb_full, w + 1)
                            dve.tensor_tensor(hid[:, w, f, :], hid[:, w, f, :], bank[0][:, :], ALU.mult).then_inc(weighed, 1)
                            n += 1
                    for d in range(KD):
                        dve.wait_ge(y_full, d + 1)
                        dve.tensor_tensor(y[:, d, :], y[:, d, :], bank[5 + d % 3][:, :], ALU.add).then_inc(y_added, 1)
        with nc.Block() as block:
            @block.vector
            def _(dve):
                for k in range(KD):
                    dve.scalar_tensor_tensor(out=x[:, k, :], in0=y[:, k, :], scalar=core.mod[:, 88 + k:89 + k], in1=x[:, k, :],
                                             op0=ALU.mult, op1=ALU.add)


def stage_output(core, buf, out):
    nc = core.nc
    stage_norm(core, buf, core.col("norm_final_2", 0, 8), None)
    stored = core.sems(core.ctx, "stored")
    with nc.Block() as block:
        @block.sync
        def _(sp):
            sp.dma_start(out.rearrange("(k p) t -> p k t", p=P), buf[:, :, :]).then_inc(stored, 16)
            sp.wait_ge(stored, 16)


def kernel(**inputs):
    import concourse.bacc as bacc
    from concourse.bass_utils import run_bass_kernel_spmd

    arrays = {f"in_{k}": a for k, a in inputs_to_dram(inputs).items()}
    nc = bacc.Bacc("TRN2", target_bir_lowering=False, num_devices=1)
    dram = {k[3:]: nc.dram_tensor(k, a.shape, mybir.dt.from_np(a.dtype), kind="ExternalInput").ap() for k, a in arrays.items()}
    out = nc.dram_tensor("outT", (D, S), F32, kind="ExternalOutput").ap()
    build(nc, dram, out)
    result = run_bass_kernel_spmd(nc, [arrays], core_ids=[0])
    return np.ascontiguousarray(result.results[0]["outT"].T)[None]
```

```python
from contextlib import ExitStack
import math

import numpy as np

import concourse.bass as bass
from concourse import mybir

ALU = mybir.AluOpType
ACT = mybir.ActivationFunctionType
AX = mybir.AxisListType
F32 = mybir.dt.float32
I32 = mybir.dt.int32
U32 = mybir.dt.uint32

P = 128
S = 512
TT = S // P
D = 1024
KD = D // P
HD = 64
NEG_LOG_DECAY = math.exp(-0.5)
N_KEYS, PEER_HEADS, TOPK = 128, 8, 16
HK = PEER_HEADS * TOPK
N_EXPERTS, N_GROUPS, PER_GROUP, D_EXPERT = 32, 4, 8, 256
MOE_T = 96
MOE_EXTRA = 2 * S // MOE_T
MOE_TILES = N_EXPERTS + MOE_EXTRA
MOE_RING = 3

VEC_COLS = [("c", 8), ("c_2", 8), ("ada_b", 48), ("b_ada_2", 48), ("norm1_g", 8), ("norm2_g", 8),
            ("norm_mix_2", 8), ("norm_ffn_2", 8), ("norm_final_2", 8), ("mu_prev", 14), ("mu_next", 14),
            ("q_norm_g", 1), ("k_norm_g", 1), ("w_decay0", 8), ("a_gate0", 8), ("k_k", 4), ("k_a", 4),
            ("r_k", 4), ("lnx_g", 4), ("lnx_b", 4), ("ret_norm_2", 3), ("hgrn_norm_2", 3),
            ("hgrn_lb_logits_2", 3), ("gla_ba_2", 1), ("gla_norm_2", 2)]
VEC_AT, _n = {}, 0
for _name, _k in VEC_COLS:
    VEC_AT[_name] = (_n, _k)
    _n += _k
NVEC = _n

RET_HEADS = 6
LEVELS = [1, 2, 4, 8, 16, 32, 64]


def constant_tables():
    r = np.arange(P)[:, None]
    c = np.arange(P)[None, :]
    eye = (r == c).astype(np.float32)
    out = {"ident": eye, "ones": np.ones((P, P), np.float32),
           "headones": (r // HD == c // HD).astype(np.float32)}
    t = np.arange(S)[None, :]
    half = {m: ((r // (2 * m) == c // (2 * m)) & (r % (2 * m) < m) & (c % (2 * m) >= m)) for m in LEVELS}
    out["rw_fwd"] = np.stack([r < c, half[1].T, half[1] | (r == c)]
                             + [half[m].T | (r == c) for m in LEVELS[1:]] + [r <= c], 1).astype(np.float32)
    out["rw_rev"] = np.stack([r > c, half[1], half[1].T | (r == c)]
                             + [half[m] | (r == c) for m in LEVELS[1:]] + [r >= c], 1).astype(np.float32)
    out["halves"] = np.stack([half[m] for m in LEVELS], 1).astype(np.uint32)
    tq = np.arange(S)[:, None]
    dist = np.abs(tq - t)
    count = sum(((dist % d == 0) & (dist <= w // 2)).astype(np.float32) for w, d in ((128, 1), (512, 4), (2048, 16)))
    masked = np.where(count > 0, dist, 1e30).astype(np.float32)
    out["dist"] = np.ascontiguousarray(masked.reshape(TT, P, S).transpose(1, 0, 2))
    out["count"] = np.ascontiguousarray(count.reshape(TT, P, S).transpose(1, 0, 2)).astype(np.float32)
    out["slopes"] = np.broadcast_to(-np.exp2(-np.arange(1, 9, dtype=np.float32)), (P, 8)).copy()
    restart = np.ones((P, S), np.float32)
    restart[:, ::P] = 0.0
    out["restart"] = restart
    gamma = 1.0 - np.exp2(-5.0 - np.arange(RET_HEADS))
    rel = (t - np.arange(P)[:, None]).astype(np.float64)
    out["ret_decay"] = np.stack([np.where(rel >= 0, g ** np.maximum(rel, 0), 0.0) * HD ** -0.5 for g in gamma],
                                1).astype(np.float32)
    rot = np.zeros((P, P), np.float32)
    for h in range(P // HD):
        for i in range(HD // 2):
            rot[h * HD + HD // 2 + i, h * HD + i] = -1.0
            rot[h * HD + i, h * HD + HD // 2 + i] = 1.0
    out["rot"] = rot
    inv = np.float32(10000.0) ** (-np.arange(0, HD, 2, dtype=np.float32) / np.float32(HD))
    out["inv_freq"] = np.tile(inv.astype(np.float32), P // (HD // 2))[:, None].copy()
    out["iota16"] = np.broadcast_to(np.arange(16, dtype=np.float32), (P, 16)).copy()
    out["earlier"] = (r < c).astype(np.float32)
    n = np.concatenate([np.arange(N_EXPERTS), np.arange(MOE_EXTRA)])
    own = np.arange(N_EXPERTS)[None, :] * P + np.arange(P)[:, None]
    out["dispatch"] = np.concatenate([np.broadcast_to(n, (P, len(n))), own, np.broadcast_to(r, (P, MOE_EXTRA))],
                                     1).astype(np.float32)
    return out


class Core:

    def __init__(self, nc, dram, ctx):
        self.nc, self.dram, self.ctx = nc, dram, ctx
        self.names = {}
        self.bank = [ctx.enter_context(nc.psum_tensor(f"bank{i}", [P, S], F32)) for i in range(8)]

    def sb(self, name, shape, dt=F32, ctx=None):
        n = self.names[name] = self.names.get(name, 0) + 1
        name = name if n == 1 else f"{name}_{n}"
        return (ctx or self.ctx).enter_context(self.nc.sbuf_tensor(name, shape, dt))

    def sems(self, ctx, *names):
        found = [ctx.enter_context(self.nc.semaphore(n)) for n in names]
        self.clear(found)
        return found if len(found) > 1 else found[0]

    def clear(self, sems):
        with self.nc.Block() as block:
            @block.sync
            def _(sp):
                for s in sems:
                    sp.sem_clear(s)

    def col(self, name, i=0, n=1):
        at = VEC_AT[name][0]
        return self.vec[:, at + i:at + i + n] if isinstance(i, int) else self.vec[:, bass.ds(i + at, n)]


class Steps:

    def __init__(self, eng, sem):
        self.eng, self.sem, self.n = eng, sem, 0

    def __call__(self, ins):
        self.n += 1
        ins.then_inc(self.sem, 1)
        return ins

    def done(self):
        self.eng.wait_ge(self.sem, self.n)

    def then(self, ins):
        self(ins)
        self.done()


RING = 3


class WeightRing:

    def __init__(self, core, items):
        self.core, self.items, self.issued = core, items, 0
        self.slots = core.sb("weight_slots", [P, RING, KD * S])
        self.loaded = [core.ctx.enter_context(core.nc.semaphore(f"weight_loaded{i}")) for i in range(RING)]
        self.used = core.ctx.enter_context(core.nc.semaphore("weight_used"))

    def view(self, i):
        n = self.items[i].shape[1]
        return self.slots[:, i % RING, 0:KD * n].rearrange("p (k n) -> p k n", k=KD)

    def load(self, sp, upto):
        while self.issued < min(upto, len(self.items)):
            i = self.issued
            if i >= RING:
                sp.wait_ge(self.used, i - RING + 1)
            sp.dma_start(self.view(i), self.items[i].rearrange("(k p) n -> p k n", p=P)).then_inc(self.loaded[i % RING], 16)
            self.issued += 1

    def arrived(self, pe, i):
        pe.wait_ge(self.loaded[i % RING], 16 * (i // RING + 1))


def repeat(ap, n):
    return ap.unsqueeze(2).to_broadcast([ap.shape[0], ap.shape[1], n])


def tiled(ap, n):
    return ap.unsqueeze(1).to_broadcast([ap.shape[0], n, ap.shape[1]])


def stage_load(core):
    nc = core.nc
    core.x = core.sb("x", [P, KD, S])
    core.vec = core.sb("vec", [P, NVEC])
    core.ident = core.sb("ident", [P, P])
    core.ones = core.sb("ones", [P, P])
    core.headones = core.sb("headones", [P, P])
    core.cond = core.sb("cond", [P, 2 * KD])
    core.mod = core.sb("mod", [P, 12 * KD])
    core.gain = core.sb("gain", [P, 4 * KD])
    n_rows = -(-(MOE_TILES + MOE_RING) * MOE_T // P) * P
    core.dispatched = nc.dram_tensor("dispatched", (n_rows, D), F32, kind="Internal").ap()
    core.answered = nc.dram_tensor("answered", (MOE_TILES * MOE_T, D), F32, kind="Internal").ap()
    with ExitStack() as st:
        in_loaded = core.sems(st, "in_loaded")
        with nc.Block() as block:
            @block.sync
            def _(sp):
                sp.dma_start(core.vec[:, :], core.dram["vec"]).then_inc(in_loaded, 16)
                core.ring.load(sp, RING)

            @block.scalar
            def _(act):
                act.dma_start(core.x[:, :, :], core.dram["xT"].rearrange("(k p) t -> p k t", p=P)).then_inc(in_loaded, 16)
                act.dma_start(core.ident[:, :], core.dram["ident"]).then_inc(in_loaded, 16)
                act.dma_start(core.ones[:, :], core.dram["ones"]).then_inc(in_loaded, 16)
                act.dma_start(core.headones[:, :], core.dram["headones"]).then_inc(in_loaded, 16)
                act.wait_ge(in_loaded, 80)
                act.activation(core.cond[:, :], core.vec[:, 0:2 * KD], ACT.Silu)


def stage_modulation(core, b, first):
    nc, ring = core.nc, core.ring
    n_items = 12
    with ExitStack() as st:
        acc = core.sb("mod_acc", [P, 2, 2, S], ctx=st)
        weighed, summed, mod_added = core.sems(st, "weighed", "summed", "mod_added")
        out = core.bank[0]
        mod = core.mod[:, 48 * b:48 * b + 48]
        with nc.Block() as block:
            @block.sync
            def _(sp):
                ring.load(sp, first + n_items + RING)

            @block.tensor
            def _(pe):
                for i in range(n_items):
                    pe.wait_ge(ring.used, first + i + 1)
                    for f in range(4):
                        for odd in range(2):
                            mm = pe.matmul(out[:, 4 * i + f:4 * i + f + 1], acc[:, i % 2, odd, f * P:f * P + P],
                                           core.ones[:, 0:1], start=odd == 0, stop=odd == 1)
                    mm.then_inc(summed, 1)

            @block.vector
            def _(dve):
                for i in range(n_items):
                    ring.arrived(dve, first + i)
                    w = ring.view(first + i)
                    if i >= 2:
                        dve.wait_ge(summed, i - 1)
                    for k in range(KD):
                        a, c = acc[:, i % 2, k % 2, :], core.cond[:, b * KD + k:b * KD + k + 1]
                        if k < 2:
                            dve.tensor_scalar(a, w[:, k, :], c, None, ALU.mult).then_inc(weighed, 1)
                        else:
                            dve.wait_ge(weighed, KD * i + k - 1)
                            dve.scalar_tensor_tensor(out=a, in0=w[:, k, :], scalar=c, in1=a, op0=ALU.mult, op1=ALU.add).then_inc(weighed, 1)
                    dve.wait_ge(weighed, KD * (i + 1))
                    dve.sem_inc(ring.used, 1)
                dve.wait_ge(summed, n_items)
                dve.tensor_tensor(mod, out[:, 0:48], core.col("ada_b" if b == 0 else "b_ada_2", 0, 48),
                                  ALU.add).then_inc(mod_added, 1)
                dve.wait_ge(mod_added, 1)
                g = ("norm1_g", "norm2_g") if b == 0 else ("norm_mix_2", "norm_ffn_2")
                for j in range(2):
                    dve.scalar_tensor_tensor(out=core.gain[:, (2 * b + j) * KD:(2 * b + j + 1) * KD],
                                             in0=mod[:, 8 + 24 * j:16 + 24 * j], scalar=1.0, in1=core.col(g[j], 0, 8),
                                             op0=ALU.add, op1=ALU.mult)


def stage_norm(core, out, gain, shift):
    nc, x, total = core.nc, core.x, core.bank[0]
    with ExitStack() as st:
        rms = core.sb("rms", [P, S], ctx=st)
        squared, summed, rooted, scaled, shifted = core.sems(
            st, "squared", "summed", "rooted", "scaled", "shifted")
        with nc.Block() as block:
            @block.scalar
            def _(act):
                for k in range(KD):
                    act.activation(out[:, k, :], x[:, k, :], ACT.Square).then_inc(squared, 1)
                act.wait_ge(summed, 1)
                act.activation(rms[:, :], total[:, :], ACT.Sqrt, scale=1.0 / D, bias=1e-6).then_inc(rooted, 1)
                if shift is not None:
                    for k in range(KD):
                        act.wait_ge(scaled, k + 2)
                        act.activation(out[:, k, :], out[:, k, :], ACT.Identity, bias=shift[:, k:k + 1]).then_inc(shifted, 1)

            @block.tensor
            def _(pe):
                for k in range(KD):
                    pe.wait_ge(squared, k + 1)
                    mm = pe.matmul(total[:, :], core.ones[:, :], out[:, k, :], start=k == 0, stop=k == KD - 1)
                mm.then_inc(summed, 1)

            @block.vector
            def _(dve):
                dve.wait_ge(rooted, 1)
                dve.reciprocal(rms[:, :], rms[:, :]).then_inc(scaled, 1)
                dve.wait_ge(scaled, 1)
                for k in range(KD):
                    dve.scalar_tensor_tensor(out=out[:, k, :], in0=x[:, k, :], scalar=gain[:, k:k + 1], in1=rms[:, :],
                                             op0=ALU.mult, op1=ALU.mult).then_inc(scaled, 1)


def stage_project(core, first, plan, rhs, only_dve=False):
    nc, ring = core.nc, core.ring
    units = []
    for i, (kind, evac) in enumerate(plan):
        n = ring.items[first + i].shape[1]
        if kind == "T":
            for f in range(-(-n // P)):
                units.append((i, "T", f, min(P, n - f * P), S, evac[f]))
        else:
            for t in range(TT):
                units.append((i, "N", t, P, n, evac))
    NB = 6
    with ExitStack() as st:
        bank_full, act_emptied, dve_emptied = core.sems(st, "bank_full", "act_emptied", "dve_emptied")

        def evacuate(eng, parity, emptied):
            for u, (_, kind, f, rows, width, evac) in enumerate(units):
                if only_dve and parity or not only_dve and u % 2 == parity:
                    eng.wait_ge(bank_full, u + 1)
                    evac(eng, core.bank[u % NB][0:rows, 0:width], f).then_inc(emptied, 1)

        with nc.Block() as block:
            @block.sync
            def _(sp):
                ring.load(sp, first + len(plan) + RING)

            @block.tensor
            def _(pe):
                for u, (i, kind, f, rows, width, _) in enumerate(units):
                    ring.arrived(pe, first + i)
                    if u >= NB:
                        if only_dve:
                            pe.wait_ge(dve_emptied, u - NB + 1)
                        else:
                            pe.wait_ge(act_emptied if u % 2 == 0 else dve_emptied, (u - NB) // 2 + 1)
                    w = ring.view(first + i)
                    for k in range(KD):
                        if kind == "T":
                            a, b = w[:, k, f * P:f * P + rows], rhs[:, k, :]
                        else:
                            a, b = rhs[:, k, f * P:f * P + P], w[:, k, :]
                        mm = pe.matmul(core.bank[u % NB][0:rows, 0:width], a, b, start=k == 0, stop=k == KD - 1)
                    mm.then_inc(bank_full, 1)
                    if u + 1 == len(units) or units[u + 1][0] != i:
                        pe.wait_ge(bank_full, u + 1)
                        pe.sem_inc(ring.used, 1)

            @block.scalar
            def _(act):
                evacuate(act, 0, act_emptied)

            @block.vector
            def _(dve):
                evacuate(dve, 1, dve_emptied)


def copy_to(dest):
    def evac(eng, psum, f):
        d = dest(f)
        if eng.engine == mybir.EngineType.Activation:
            return eng.activation(d, psum, ACT.Copy)
        return eng.tensor_copy(d, psum)
    return evac


def stage_attention(core, qk, v, att):
    nc = core.nc
    with ExitStack() as st:
        dist = core.sb("dist", [P, TT, S], ctx=st)
        count = core.sb("count", [P, TT, S], ctx=st)
        slopes = core.sb("slopes", [P, 8], ctx=st)
        qn = core.sb("qk_n", [P, 2, S], ctx=st)
        vs = core.sb("v_pair", [P, TT, P], ctx=st)
        score = core.sb("score", [P, 4, S], ctx=st)
        prob = core.sb("prob", [P, 2, S], ctx=st)
        diag = core.sb("diag", [P, 2, P], ctx=st)
        slope = core.sb("slope", [P, 2], ctx=st)
        top = core.sb("top", [P, 8], ctx=st)
        den = core.sb("den", [P, 8], ctx=st)
        probT = core.sb("probT", [P, 2, TT, S], ctx=st)
        tables, slots_filled = core.sems(st, "att_tables", "slots_filled")
        names = ("qk_staged", "v_staged", "slope_staged", "scored", "biased", "topped",
                 "raised", "counted", "inverse", "scaled", "turned", "copied", "mixed", "stored")
        sems = core.sems(st, *names)
        (qk_staged, v_staged, slope_staged, scored, biased, topped, raised, counted, inverse,
         scaled, turned, copied, mixed, stored) = sems
        with nc.Block() as block:
            @block.sync
            def _(sp):
                sp.dma_start(dist[:, :, :], core.dram["dist"]).then_inc(tables, 16)
                sp.dma_start(count[:, :, :], core.dram["count"]).then_inc(tables, 16)
                sp.dma_start(slopes[:, :], core.dram["slopes"]).then_inc(tables, 16)
                rows = core.dispatched.rearrange("(n p) d -> p n d", p=P)
                for n in range(0, rows.shape[1], KD // 2):
                    m = min(KD // 2, rows.shape[1] - n)
                    sp.dma_start(rows[:, n:n + m, :], core.x[:, 0:2 * m, :].rearrange("p k t -> p (k t)").rearrange("p (n d) -> p n d", d=D)).then_inc(slots_filled, 16)
                sp.wait_ge(tables, 48)
        n_fills = -(-(core.dispatched.shape[0] // P) // (KD // 2))
        UNITS = [(h, i) for h in range(2) for i in range(TT)]
        with nc.Fori(0, 4) as pair:
            core.clear(sems)
            with nc.Block() as block:
                @block.gpsimd
                def _(pool):
                    for j in range(2):
                        pool.tensor_copy(qn[:, j, :], flat(qk[:, bass.ds(pair + 4 * j, 1), :])).then_inc(qk_staged, 1)
                    pool.tensor_copy(vs[:, :, :], v[:, :, bass.ds(pair * P, P)]).then_inc(v_staged, 1)

                @block.scalar
                def _(act):
                    def copy_turned(u):
                        h, i = UNITS[u]
                        act.wait_ge(turned, u + 1)
                        act.activation(probT[:, h, :, i * P:i * P + P],
                                       core.bank[4 + u % 2][:, :].rearrange("p (j t) -> p j t", j=TT), ACT.Copy).then_inc(copied, 1)

                    for u, (h, i) in enumerate(UNITS):
                        act.wait_ge(topped, u + 1)
                        act.activation(score[:, u % 4, :], score[:, u % 4, :], ACT.Exp, bias=top[:, u:u + 1]).then_inc(raised, 1)
                        if u >= 2:
                            copy_turned(u - 2)
                    copy_turned(6)
                    copy_turned(7)
                    for h in range(2):
                        act.wait_ge(mixed, h + 1)
                        r = slice(HD * h, HD * h + HD)
                        act.activation(att[r, bass.ds(pair, 1), :], core.bank[6 + h][r, :], ACT.Copy).then_inc(stored, 1)

                @block.tensor
                def _(pe):
                    def scores(u):
                        h, i = UNITS[u]
                        if u >= 4:
                            pe.wait_ge(biased, u - 3)
                        r = slice(HD * h, HD * h + HD)
                        pe.matmul(core.bank[u % 4][:, :], qn[r, 0, i * P:i * P + P], qn[r, 1, :],
                                  start=True, stop=True).then_inc(scored, 1)

                    def turn(u):
                        pe.wait_ge(scaled, u + 1)
                        if u >= 2:
                            pe.wait_ge(copied, u - 1)
                        for j in range(TT):
                            mm = pe.matmul(core.bank[4 + u % 2][:, j * P:j * P + P], prob[:, u % 2, j * P:j * P + P],
                                           diag[:, u % 2, :], start=True, stop=True)
                        mm.then_inc(turned, 1)

                    def mix(h):
                        pe.wait_ge(copied, 4 * h + 4)
                        pe.wait_ge(v_staged, 1)
                        r = slice(HD * h, HD * h + HD)
                        for j in range(TT):
                            mm = pe.matmul(core.bank[6 + h][r, :], vs[:, j, r], probT[:, h, j, :],
                                           start=j == 0, stop=j == TT - 1)
                        mm.then_inc(mixed, 1)

                    pe.wait_ge(qk_staged, 2)
                    for u in range(3):
                        scores(u)
                    for u in range(8):
                        if u + 3 < 8:
                            scores(u + 3)
                        turn(u)
                        if u == 5:
                            mix(0)
                    mix(1)

                @block.vector
                def _(dve):
                    dve.tensor_copy(slope[:, :], slopes[:, bass.ds(pair * 2, 2)]).then_inc(slope_staged, 1)
                    dve.wait_ge(slope_staged, 1)

                    def bias_and_top(u):
                        h, i = UNITS[u]
                        dve.wait_ge(scored, u + 1)
                        if u >= 4:
                            dve.wait_ge(counted, u - 3)
                        dve.scalar_tensor_tensor(out=score[:, u % 4, :], in0=dist[:, i, :], scalar=slope[:, h:h + 1],
                                                 in1=core.bank[u % 4][:, :], op0=ALU.mult, op1=ALU.add).then_inc(biased, 1)
                        dve.wait_ge(biased, u + 1)
                        dve.tensor_reduce(top[:, u:u + 1], score[:, u % 4, :], AX.X, ALU.max, negate=True).then_inc(topped, 1)

                    def weigh(u):
                        h, i = UNITS[u]
                        dve.wait_ge(raised, u + 1)
                        if u >= 2:
                            dve.wait_ge(turned, u - 1)
                        dve.scalar_tensor_tensor(out=prob[:, u % 2, :], in0=score[:, u % 4, :], scalar=1.0, in1=count[:, i, :],
                                                 op0=ALU.mult, op1=ALU.mult, accum_out=den[:, u:u + 1]).then_inc(counted, 1)
                        dve.wait_ge(counted, u + 1)
                        dve.reciprocal(den[:, u:u + 1], den[:, u:u + 1]).then_inc(inverse, 1)
                        dve.wait_ge(inverse, u + 1)
                        dve.tensor_scalar(diag[:, u % 2, :], core.ident[:, :], den[:, u:u + 1], None, ALU.mult).then_inc(scaled, 1)

                    bias_and_top(0)
                    bias_and_top(1)
                    for u in range(8):
                        if u + 2 < 8:
                            bias_and_top(u + 2)
                        weigh(u)
        with nc.Block() as block:
            @block.sync
            def _(sp):
                sp.wait_ge(slots_filled, 16 * n_fills)


def inputs_to_dram(inputs):
    a = {k: np.asarray(v) for k, v in inputs.items()}
    cols = []
    for name, n in VEC_COLS:
        flat = a[name].reshape(-1)
        if name in ("q_norm_g", "k_norm_g"):
            flat = np.tile(flat, 2)
        cols.append(flat.reshape(n, P).T)
    rows = lambda name: a[name][0]
    dram = {"vec": np.concatenate(cols, 1), "xT": a["x"][0].T, "positions": a["positions_2"]}
    for name, src in (("ada_w", "ada_w"), ("ada_w2", "w_ada_2"), ("w_in", "w_in"), ("w_in2", "w_in_2"), ("w_out", "w_out"),
                      ("w_out2", "w_out_2"), ("w_query", "peer_w_query"), ("g_up", "g_up"), ("wa2", "gla_wa2_2")):
        dram[name] = rows(src)
    dram["experts"] = np.concatenate(
        [rows(n).reshape(N_EXPERTS, -1, P, w).transpose(0, 2, 1, 3).reshape(N_EXPERTS * P, -1)
         for n, w in (("expert_w_gate_2", D_EXPERT), ("expert_w_up_2", D_EXPERT), ("expert_w_down_2", D))], 1)
    dram["decay_up"] = np.concatenate(list(rows("w_decay_up")), 1)
    dram["a_up"] = np.concatenate(list(rows("a_gate_up")), 1)
    dram["keys"] = np.concatenate([rows("peer_sub_keys1").T, rows("peer_sub_keys2").T], 1)
    dram["uv"] = np.concatenate([rows("peer_u"), rows("peer_v")], 1)
    dram["router_w"] = np.concatenate([rows("router_group_w_2"), rows("router_expert_w_2")], 1)
    dram["router_b"] = np.concatenate([rows("router_group_b_2"), rows("router_expert_b_2")])[None]
    dram.update(constant_tables())
    return {k: np.ascontiguousarray(v) for k, v in dram.items()}


def build(nc, dram, out):
    with ExitStack() as ctx:
        core = Core(nc, dram, ctx)
        cuts = lambda w, widths: [w[:, sum(widths[:i]):sum(widths[:i + 1])] for i in range(len(widths))]
        IN1 = [512, 512, 512, 512, 512, 512, 256]
        IN2 = [384] * 8 + [256, 256, 272]
        core.ring = WeightRing(core, cuts(dram["ada_w"], [512] * 12) + cuts(dram["ada_w2"], [512] * 12)
                               + cuts(dram["w_in"], IN1) + cuts(dram["w_out"], [512] * 2)
                               + cuts(dram["w_query"], [512] * 4) + cuts(dram["w_in2"], IN2)
                               + cuts(dram["w_out2"], [512] * 2))
        stage_load(core)
        stage_modulation(core, 0, 0)
        stage_modulation(core, 1, 12)
        first_block(core, 24)
        second_block(core, 24 + 13, core.mixed)
        stage_output(core, core.mixed, out)
        ring = core.ring
        with nc.Block() as block:
            @block.sync
            def _(sp):
                for i in range(max(0, ring.issued - RING), ring.issued):
                    ring.arrived(sp, i)


def first_block(core, first):
    nc = core.nc
    mixed = core.mixed = core.sb("mixed", [P, KD, S])
    with ExitStack() as st:
        zr = core.sb("zr", [P, 14, S], ctx=st)
        with ExitStack() as s2:
            qk = core.sb("qk", [P, KD, S], ctx=s2)
            v = core.sb("v", [P, TT, S], ctx=s2)
            h = mixed
            stage_norm(core, h, core.gain[:, 0:8], core.mod[:, 0:8])
            stage_project(core, first, [("T", [copy_to(lambda f: qk[:, f, :])] * 4), ("T", [copy_to(lambda f: qk[:, 4 + f, :])] * 4),
                                        ("N", copy_to(lambda t: v[:, t, :]))], h)
            stage_shifted(core, first + 3, h, zr, qk)
            stage_attention(core, qk, v, mixed)
        stage_rwkv(core, zr, mixed)
    stage_residual(core, first + 7, mixed, core.mod[:, 16:24])
    stage_peer(core, first + 9, mixed)


def stage_shifted(core, first, h, zr, qk):
    nc, ring = core.nc, core.ring
    N = 14
    with ExitStack() as st:
        stay = core.sb("stay", [P, N], ctx=st)
        gains = core.sb("qk_gains", [P, 2], ctx=st)
        sq = core.sb("qk_sq", [P, 2, S], ctx=st)
        stay_ready, gains_ready, bank_full, stayed, left, emptied = core.sems(
            st, "stay_ready", "gains_ready", "bank_full", "stayed", "left", "emptied")
        squared, summed, rooted, inverted, normed = core.sems(st, "squared", "summed", "rooted", "inverted", "normed")
        NQ = 8
        with nc.Block() as block:
            @block.sync
            def _(sp):
                ring.load(sp, first + 4 + RING)

            @block.tensor
            def _(pe):
                for u in range(N):
                    ring.arrived(pe, first + u // 4)
                    if u >= 6:
                        pe.wait_ge(emptied, u - 5)
                    w = ring.view(first + u // 4)
                    for k in range(KD):
                        mm = pe.matmul(core.bank[u % 6][:, :], w[:, k, (u % 4) * P:(u % 4) * P + P], h[:, k, :],
                                       start=k == 0, stop=k == KD - 1)
                    mm.then_inc(bank_full, 1)
                    if u % 4 == 3 or u == N - 1:
                        pe.wait_ge(bank_full, u + 1)
                        pe.sem_inc(ring.used, 1)
                    if u < NQ:
                        pe.wait_ge(squared, u + 1)
                        if u >= 2:
                            pe.wait_ge(rooted, u - 1)
                        pe.matmul(core.bank[6 + u % 2][:, :], core.headones[:, :], sq[:, u % 2, :], start=True, stop=True).then_inc(summed, 1)

            @block.scalar
            def _(act):
                def square(j):
                    if j >= 2:
                        act.wait_ge(normed, j - 1)
                    act.activation(sq[:, j % 2, :], qk[:, j, :], ACT.Square).then_inc(squared, 1)

                def root(j):
                    act.wait_ge(summed, j + 1)
                    act.activation(sq[:, j % 2, :], core.bank[6 + j % 2][:, :], ACT.Sqrt, scale=1.0 / HD, bias=1e-6).then_inc(rooted, 1)

                act.wait_ge(stay_ready, 2)
                square(0)
                square(1)
                for u in range(N):
                    if 1 <= u <= NQ:
                        root(u - 1)
                    if 2 <= u + 1 < NQ:
                        square(u + 1)
                    act.wait_ge(bank_full, u + 1)
                    act.activation(zr[:, u, :], core.bank[u % 6][:, :], ACT.Copy, scale=stay[:, u:u + 1]).then_inc(stayed, 1)

            @block.vector
            def _(dve):
                dve.tensor_tensor(stay[:, :], core.col("mu_prev", 0, N), core.col("mu_next", 0, N), ALU.add).then_inc(stay_ready, 1)
                dve.wait_ge(stay_ready, 1)
                dve.tensor_scalar(stay[:, :], stay[:, :], -1.0, 1.0, ALU.mult, ALU.add).then_inc(stay_ready, 1)
                dve.tensor_scalar(gains[:, 0:1], core.col("q_norm_g"), HD ** -0.5, None, ALU.mult).then_inc(gains_ready, 1)
                dve.tensor_copy(gains[:, 1:2], core.col("k_norm_g")).then_inc(gains_ready, 1)
                dve.wait_ge(gains_ready, 2)

                def normalise(j):
                    dve.wait_ge(rooted, j + 1)
                    dve.reciprocal(sq[:, j % 2, :], sq[:, j % 2, :]).then_inc(inverted, 1)
                    dve.wait_ge(inverted, j + 1)
                    dve.scalar_tensor_tensor(out=qk[:, j, :], in0=qk[:, j, :], scalar=gains[:, j // 4:j // 4 + 1], in1=sq[:, j % 2, :],
                                             op0=ALU.mult, op1=ALU.mult).then_inc(normed, 1)

                for u in range(N):
                    if 1 <= u <= NQ:
                        normalise(u - 1)
                    ps = core.bank[u % 6]
                    dve.wait_ge(stayed, u + 1)
                    dve.scalar_tensor_tensor(out=zr[:, u, 1:S], in0=ps[:, 0:S - 1], scalar=core.col("mu_prev", u),
                                             in1=zr[:, u, 1:S], op0=ALU.mult, op1=ALU.add).then_inc(left, 1)
                    dve.wait_ge(left, u + 1)
                    dve.scalar_tensor_tensor(out=zr[:, u, 0:S - 1], in0=ps[:, 1:S], scalar=core.col("mu_next", u),
                                             in1=zr[:, u, 0:S - 1], op0=ALU.mult, op1=ALU.add).then_inc(emptied, 1)


def stage_rwkv(core, zr, mixed):
    nc = core.nc
    R, K, V = 0, 4, 8
    with ExitStack() as st:
        sig = core.sb("decay_sig", [P, 8, S], ctx=st)
        a = core.sb("a", [P, 8, S], ctx=st)
        kk = core.sb("kk", [P, 4, S], ctx=st)
        sel = core.sb("rwkv_cols", [P, 4, 6], ctx=st)
        restart = core.sb("restart", [P, S], ctx=st)
        stage_rwkv_inputs(core, zr, sig, a, kk, sel, restart)
        for rev in range(2):
            stage_rwkv_scan(core, zr, sig, a, kk, sel, restart, mixed, rev)
        stage_rwkv_output(core, zr, a, sel, mixed)


def stage_rwkv_inputs(core, zr, sig, a, kk, sel, restart):
    nc = core.nc
    with ExitStack() as st:
        lora = core.sb("lora", [P, 2 * S], ctx=st)
        low = core.sb("low", [HD, S], ctx=st)
        sq = core.sb("kk_sq", [P, 2, S], ctx=st)
        loaded, squashed, bank_full, emptied, made, squared, kk_full, clamped, rooted, inverted = core.sems(
            st, "lora_loaded", "squashed", "bank_full", "emptied", "kk_made", "squared", "kk_full", "clamped", "rooted", "inverted")
        UNITS = [(d, f, which) for d in range(2) for f in range(4) for which in range(2)]
        with nc.Block() as block:
            @block.sync
            def _(sp):
                sp.dma_start(lora[0:HD, :], core.dram["decay_up"]).then_inc(loaded, 16)
                sp.dma_start(lora[HD:P, :], core.dram["a_up"]).then_inc(loaded, 16)
                sp.dma_start(restart[:, :], core.dram["restart"]).then_inc(loaded, 16)
                sp.wait_ge(loaded, 48)

            @block.scalar
            def _(act):
                act.activation(low[:, :], zr[0:HD, 12, :], ACT.Tanh).then_inc(squashed, 1)
                for u, (d, f, which) in enumerate(UNITS):
                    act.wait_ge(bank_full, u + 1)
                    dest, bias = (sig, "w_decay0") if which == 0 else (a, "a_gate0")
                    act.activation(dest[:, 4 * d + f, :], core.bank[u % 6][:, :], ACT.Sigmoid,
                                   bias=core.col(bias, 4 * d + f)).then_inc(emptied, 1)
                for f in range(4):
                    act.wait_ge(made, f + 1)
                    if f >= 2:
                        act.wait_ge(inverted, 2 * f - 2)
                    act.activation(sq[:, f % 2, :], kk[:, f, :], ACT.Square).then_inc(squared, 1)
                    act.wait_ge(clamped, f + 1)
                    act.activation(sq[:, f % 2, :], sq[:, f % 2, :], ACT.Sqrt).then_inc(rooted, 1)

            @block.tensor
            def _(pe):
                pe.wait_ge(loaded, 48)
                pe.wait_ge(squashed, 1)
                for u, (d, f, which) in enumerate(UNITS):
                    if u >= 6:
                        pe.wait_ge(emptied, u - 5)
                    w = lora[HD * which:HD * which + HD, d * S + f * P:d * S + f * P + P]
                    rhs = low[:, :] if which == 0 else zr[HD:P, 12, :]
                    pe.matmul(core.bank[u % 6][:, :], w, rhs, start=True, stop=True).then_inc(bank_full, 1)
                for f in range(4):
                    pe.wait_ge(squared, f + 1)
                    pe.matmul(core.bank[6 + f % 2][:, :], core.headones[:, :], sq[:, f % 2, :], start=True, stop=True).then_inc(kk_full, 1)

            @block.vector
            def _(dve):
                for f in range(4):
                    dve.tensor_scalar(kk[:, f, :], zr[:, 4 + f, :], core.col("k_k", f), None, ALU.mult).then_inc(made, 1)
                for i, name in ((0, "k_a"), (3, "r_k"), (4, "lnx_g"), (5, "lnx_b")):
                    dve.tensor_copy(sel[:, :, i], core.col(name, 0, 4))
                dve.tensor_scalar(sel[:, :, 1], core.col("k_a", 0, 4), -1.0, 1.0, ALU.mult, ALU.add)
                dve.tensor_scalar(sel[:, :, 2], core.col("k_a", 0, 4), 0.5, None, ALU.mult)
                for f in range(4):
                    dve.wait_ge(kk_full, f + 1)
                    dve.tensor_scalar(sq[:, f % 2, :], core.bank[6 + f % 2][:, :], 1e-12, None, ALU.max).then_inc(clamped, 1)
                    dve.wait_ge(rooted, f + 1)
                    dve.reciprocal(sq[:, f % 2, :], sq[:, f % 2, :]).then_inc(inverted, 1)
                    dve.wait_ge(inverted, 2 * f + 1)
                    dve.tensor_tensor(kk[:, f, :], kk[:, f, :], sq[:, f % 2, :], ALU.mult).then_inc(inverted, 1)


def stage_rwkv_scan(core, zr, sig, a, kk, sel, restart, mixed, rev):
    nc, bank = core.nc, core.bank
    R, K, V = 0, 4, 8
    NL = len(LEVELS) - 1
    order = list(range(TT))[::-1] if rev else list(range(TT))
    Q = 3 if rev else 0
    with ExitStack() as st:
        masks = core.sb("rwkv_masks", [P, 10, P], ctx=st)
        work = core.sb("rwkv_work", [P, 23, S], ctx=st)
        xs = core.sb("rwkv_x", [P, 2, TT, HD], ctx=st)
        u_sb = core.sb("rwkv_u", [P, 2, HD], ctx=st)
        state = core.sb("rwkv_state", [P, 2, HD], ctx=st)
        held = core.sb("rwkv_held", [P, HD], ctx=st)
        total = core.sb("rwkv_total", [P, TT], ctx=st)
        step = core.sb("rwkv_step", [P, TT], ctx=st)
        cols = core.sb("rwkv_col", [P, 6], ctx=st)
        slot = lambda i: work[:, i, :]
        e1, e2, p_at, p_inv, p_prev, alpha, beta, kappa, rho = [slot(i) for i in range(9)]
        alphaN, betaN, kappaN, vN = [work[:, 9 + i, :].rearrange("p (i d) -> p i d", i=TT) for i in range(4)]
        vT, ahat = slot(13), slot(14)
        tri = [slot(15), slot(16)]
        inv = [slot(17), slot(18)]
        invT = [slot(19), slot(20)]
        off = [slot(21), slot(22)]
        m_rb = [slot(0), slot(1)]
        m_rk = [slot(2), slot(4)]
        mask = lambda i: tiled(masks[:, i, :], TT)
        four = lambda ap: ap.rearrange("p (i t) -> p i t", i=TT)
        t_of = lambda ap, i: ap[:, i * P:i * P + P]
        names = ("rwkv_tables", "summed", "raised", "v_staged", "ops_dve", "ops_pool", "turned", "turn_copied", "cols_staged",
                 "filled0", "filled1", "evac0", "evac1", "copied0", "copied1", "unit0", "unit1", "state0", "state1", "y_stored")
        sems = core.sems(st, *names)
        (tables, summed, raised, v_staged, ops_dve, ops_pool, turned, turn_copied, cols_staged,
         f0, f1, d0, d1, a0, a1, u0, u1, s0, s1, y_stored) = sems
        filled, evac, copied, unit, stated = [f0, f1], [d0, d1], [a0, a1], [u0, u1], [s0, s1]
        Z_FULL = [7 + 3 * l for l in range(NL)]
        W_LAST = Z_FULL[-1] + 1
        A_FULL = W_LAST + 1
        U_FULL = [A_FULL + 1 + 3 * n for n in range(TT)]
        Z_EVAC = [7 + l for l in range(NL)]
        U_EVAC = [7 + NL + n for n in range(TT)]
        W_COPY = [3 + 2 * l for l in range(NL - 1)] + [2 * NL]
        A_COPY = 2 * NL + 1
        with nc.Block() as block:
            @block.sync
            def _(sp):
                sp.dma_start(masks[:, :, :], core.dram["rw_rev" if rev else "rw_fwd"]).then_inc(tables, 16)
                sp.wait_ge(tables, 16)
        with nc.Fori(0, 4) as f:
            core.clear(sems)
            row = lambda t, first: t[:, bass.ds(f + first, 1), :].rearrange("p a t -> p (a t)")
            with nc.Block() as block:
                @block.vector
                def _(dve):
                    dve.tensor_copy(cols[:, :], row(sel, 0)).then_inc(cols_staged, 1)
                    dve.tensor_tensor_scan(e1, restart[:, :], row(sig, 4 * rev), 0.0, ALU.mult, ALU.add).then_inc(summed, 1)
                    dve.wait_ge(summed, 1)
                    dve.tensor_copy(total[:, :], e1[:, P - 1:S:P]).then_inc(summed, 1)
                    dve.wait_ge(summed, 2)
                    dve.scalar_tensor_tensor(out=four(e1), in0=repeat(total[:, :], P), scalar=-0.5, in1=four(e1),
                                             op0=ALU.mult, op1=ALU.add).then_inc(summed, 1)
                    dve.wait_ge(summed, 3)
                    dve.tensor_tensor(e2, e1, row(sig, 4 * rev), ALU.subtract).then_inc(summed, 1)
                    dve.tensor_tensor(step[:, 0:TT - 1], total[:, 0:TT - 1], total[:, 1:TT], ALU.add).then_inc(summed, 1)
                    dve.wait_ge(cols_staged, 1)
                    dve.tensor_scalar(kappa, row(a, 4 * rev), cols[:, 0:1], cols[:, 1:2], ALU.mult, ALU.add).then_inc(summed, 1)
                    dve.wait_ge(summed, 6)
                    dve.tensor_tensor(kappa, kappa, row(zr, K), ALU.mult).then_inc(summed, 1)
                    dve.wait_ge(raised, 2)
                    dve.scalar_tensor_tensor(out=alpha, in0=row(kk, 0), scalar=-1.0, in1=p_prev, op0=ALU.mult, op1=ALU.mult).then_inc(ops_dve, 1)
                    dve.wait_ge(ops_pool, 1)
                    dve.wait_ge(raised, 3)
                    dve.tensor_tensor(beta, beta, p_inv, ALU.mult).then_inc(ops_dve, 1)
                    dve.wait_ge(summed, 7)
                    dve.tensor_tensor(kappa, kappa, p_inv, ALU.mult).then_inc(ops_dve, 1)
                    for h in range(2):
                        dve.wait_ge(filled[h], 1)
                        dve.tensor_tensor(four(tri[h]), four(bank[4 * h][:, :]), mask(0), ALU.mult).then_inc(evac[h], 1)
                        dve.wait_ge(filled[h], 2)
                        dve.tensor_tensor(four(inv[h]), four(bank[4 * h + 1][:, :]), mask(1), ALU.mult).then_inc(evac[h], 1)
                        dve.wait_ge(filled[h], 3)
                        dve.tensor_tensor(four(off[h]), four(bank[4 * h + 2][:, :]), mask(0), ALU.mult).then_inc(evac[h], 1)
                        dve.wait_ge(filled[h], 4)
                        dve.wait_ge(ops_pool, 2)
                        dve.tensor_tensor(four(m_rb[h]), four(bank[4 * h + 3][:, :]), mask(9), ALU.mult).then_inc(evac[h], 1)
                    for h in range(2):
                        dve.wait_ge(filled[h], 5)
                        dve.tensor_tensor(four(m_rk[h]), four(bank[4 * h][:, :]), mask(9), ALU.mult).then_inc(evac[h], 1)
                        dve.wait_ge(unit[h], 1)
                        dve.tensor_tensor(four(invT[h]), four(tri[h]), mask(2), ALU.mult).then_inc(evac[h], 1)
                    for l in range(NL):
                        for h in range(2):
                            dve.wait_ge(filled[h], Z_FULL[l])
                            dve.tensor_tensor(four(off[h]), four(bank[4 * h + 2][:, :]), mask(3 + l), ALU.mult).then_inc(evac[h], 1)
                    held_n = 0
                    for n, i in enumerate(order):
                        for h in range(2):
                            dve.wait_ge(filled[h], U_FULL[n])
                            if n >= 1:
                                dve.wait_ge(filled[h], U_FULL[n - 1] + 2)
                            dve.tensor_copy(u_sb[:, h, :], bank[4 * h + 2][:, 0:HD]).then_inc(evac[h], 1)
                        if n == TT - 1:
                            break
                        for h in range(2):
                            r = slice(HD * h, HD * h + HD)
                            b = min(i, order[n + 1])
                            fac = step[r, b:b + 1]
                            if n == 0:
                                dve.wait_ge(raised, 4)
                                dve.wait_ge(filled[h], U_FULL[n] + 1)
                                dve.tensor_scalar(state[r, 0, :], bank[4 * h + 3][r, 0:HD], fac, None, ALU.mult).then_inc(stated[h], 1)
                                continue
                            dve.wait_ge(stated[h], 2 * n - 1)
                            dve.tensor_scalar(held[r, :], state[r, (n - 1) % 2, :], fac, None, ALU.mult).then_inc(stated[h], 1)
                            dve.wait_ge(stated[h], 2 * n)
                            dve.wait_ge(filled[h], U_FULL[n] + 1)
                            dve.scalar_tensor_tensor(out=state[r, n % 2, :], in0=bank[4 * h + 3][r, 0:HD], scalar=fac, in1=held[r, :],
                                                     op0=ALU.mult, op1=ALU.add).then_inc(stated[h], 1)
                    if rev:
                        for h in range(2):
                            r = slice(HD * h, HD * h + HD)
                            dve.wait_ge(filled[h], U_FULL[-1] + 1)
                            y = mixed[r, bass.ds(f + 4, 1), :].rearrange("p a t -> p (a t)")
                            dve.tensor_tensor(y, bank[4 * h][r, :], y, ALU.add).then_inc(y_stored, 1)

                @block.gpsimd
                def _(pool):
                    pool.tensor_copy(vT, row(zr, V)).then_inc(v_staged, 1)
                    pool.tensor_tensor(beta, row(a, 4 * rev), row(kk, 0), ALU.mult).then_inc(ops_pool, 1)
                    pool.wait_ge(raised, 1)
                    pool.tensor_tensor(rho, row(zr, R), p_at, ALU.mult).then_inc(ops_pool, 1)
                    for h in range(2):
                        pool.wait_ge(evac[h], 1)
                        pool.tensor_tensor(four(tri[h]), four(tri[h]), tiled(core.ident[:, :], TT), ALU.add).then_inc(unit[h], 1)
                        pool.wait_ge(evac[h], 2)
                        pool.tensor_tensor(four(inv[h]), four(inv[h]), tiled(core.ident[:, :], TT), ALU.add).then_inc(unit[h], 1)

                @block.scalar
                def _(act):
                    lam = NEG_LOG_DECAY
                    act.wait_ge(summed, 4)
                    at, prev, sign = (e2, e1, lam) if rev else (e1, e2, -lam)
                    act.activation(p_at, at, ACT.Exp, scale=sign).then_inc(raised, 1)
                    act.activation(p_prev, prev, ACT.Exp, scale=sign).then_inc(raised, 1)
                    act.activation(p_inv, at, ACT.Exp, scale=-sign).then_inc(raised, 1)
                    act.wait_ge(summed, 5)
                    act.activation(step[:, 0:TT - 1], step[:, 0:TT - 1], ACT.Exp, scale=-0.5 * lam).then_inc(raised, 1)
                    for j in range(4):
                        act.wait_ge(turned, j + 1)
                        act.activation(slot(9 + j), bank[(2, 3, 6, 7)[j]][:, :], ACT.Copy).then_inc(turn_copied, 1)
                    for h in range(2):
                        act.wait_ge(filled[h], 6)
                        act.activation(xs[:, h, :, :].rearrange("p i d -> p (i d)"), bank[4 * h + 1][:, 0:TT * HD], ACT.Copy).then_inc(copied[h], 1)
                    for l in range(NL):
                        for h in range(2):
                            if l < NL - 1:
                                act.wait_ge(filled[h], Z_FULL[l] + 2)
                                act.activation(inv[h], bank[4 * h + 3][:, :], ACT.Copy).then_inc(copied[h], 1)
                            else:
                                act.wait_ge(filled[h], W_LAST)
                            act.activation(invT[h], bank[4 * h][:, :], ACT.Copy).then_inc(copied[h], 1)
                    for h in range(2):
                        r = slice(HD * h, HD * h + HD)
                        act.wait_ge(filled[h], A_FULL)
                        act.activation(ahat[r, :], bank[4 * h + 1][r, :], ACT.Copy).then_inc(copied[h], 1)
                    if not rev:
                        for h in range(2):
                            r = slice(HD * h, HD * h + HD)
                            act.wait_ge(filled[h], U_FULL[-1] + 1)
                            act.activation(mixed[r, bass.ds(f + 4, 1), :].rearrange("p a t -> p (a t)"), bank[4 * h][r, :],
                                           ACT.Copy).then_inc(y_stored, 1)

                @block.tensor
                def _(pe):
                    for j, src in enumerate((alpha, beta, kappa, vT)):
                        if j < 3:
                            pe.wait_ge(ops_dve, j + 1)
                        else:
                            pe.wait_ge(v_staged, 1)
                        for i in range(TT):
                            mm = pe.transpose(bank[(2, 3, 6, 7)[j]][:, i * P:i * P + P], t_of(src, i), core.ident[:, :])
                        mm.then_inc(turned, 1)

                    def triangle(h, b, lhs, rhs):
                        r = slice(HD * h, HD * h + HD)
                        for i in range(TT):
                            mm = pe.matmul(bank[4 * h + b][:, i * P:i * P + P], lhs[r, i * P:i * P + P], rhs[r, i * P:i * P + P],
                                           start=True, stop=True)
                        mm.then_inc(filled[h], 1)

                    def product(h, b, lhs, rhs):
                        for i in range(TT):
                            mm = pe.matmul(bank[4 * h + b][:, i * P:i * P + P], t_of(lhs, i), t_of(rhs, i), start=True, stop=True)
                        mm.then_inc(filled[h], 1)

                    for h in range(2):
                        triangle(h, 0, beta, alpha)
                        triangle(h, 1, alpha, beta)
                    pe.wait_ge(ops_pool, 2)
                    for h in range(2):
                        pe.wait_ge(turn_copied, 2 * h + 2)
                        triangle(h, 2, kappa, alpha)
                        triangle(h, 3, beta, rho)
                    for h in range(2):
                        pe.wait_ge(evac[h], 1)
                        triangle(h, 0, kappa, rho)
                    for h in range(2):
                        r = slice(HD * h, HD * h + HD)
                        pe.wait_ge(evac[h], 3)
                        pe.wait_ge(turn_copied, 4)
                        for i in range(TT):
                            mm = pe.matmul(bank[4 * h + 1][:, i * HD:i * HD + HD], t_of(off[h], i), vN[:, i, r], start=True, stop=True)
                        mm.then_inc(filled[h], 1)
                    for l in range(NL):
                        for h in range(2):
                            if l == 0:
                                pe.wait_ge(unit[h], 2)
                            else:
                                pe.wait_ge(copied[h], W_COPY[l - 1])
                            product(h, 2, tri[h], inv[h])
                        for h in range(2):
                            pe.wait_ge(evac[h], Z_EVAC[l])
                            if l < NL - 1:
                                product(h, 3, invT[h], off[h])
                            product(h, 0, off[h], invT[h])
                    for h in range(2):
                        r = slice(HD * h, HD * h + HD)
                        pe.wait_ge(copied[h], W_COPY[-1])
                        for i in range(TT):
                            mm = pe.matmul(bank[4 * h + 1][r, i * P:i * P + P], alphaN[:, i, r], t_of(invT[h], i), start=True, stop=True)
                        mm.then_inc(filled[h], 1)
                    for n, i in enumerate(order):
                        for h in range(2):
                            r = slice(HD * h, HD * h + HD)
                            u_ps = bank[4 * h + 2][:, 0:HD]
                            mm = pe.matmul(u_ps, t_of(invT[h], i), xs[:, h, i, :], start=True, stop=n == 0)
                            if n >= 1:
                                pe.wait_ge(copied[h], A_COPY)
                                pe.wait_ge(stated[h], 2 * n - 1)
                                mm = pe.matmul(u_ps, ahat[r, i * P:i * P + P], state[r, (n - 1) % 2, :], start=False, stop=True)
                            mm.then_inc(filled[h], 1)
                        for h in range(2):
                            r = slice(HD * h, HD * h + HD)
                            pe.wait_ge(evac[h], U_EVAC[n])
                            if n < TT - 1:
                                s_ps = bank[4 * h + 3][r, 0:HD]
                                pe.matmul(s_ps, betaN[:, i, r], u_sb[:, h, :], start=True, stop=False)
                                pe.matmul(s_ps, kappaN[:, i, r], vN[:, i, r], start=False, stop=True).then_inc(filled[h], 1)
                            y_ps = bank[4 * h][r, i * P:i * P + P]
                            pe.matmul(y_ps, u_sb[:, h, :], t_of(m_rb[h], i), start=True, stop=False)
                            mm = pe.matmul(y_ps, vN[:, i, r], t_of(m_rk[h], i), start=False, stop=n == 0)
                            if n >= 1:
                                mm = pe.matmul(y_ps, state[r, (n - 1) % 2, :], rho[r, i * P:i * P + P], start=False, stop=True)
                            mm.then_inc(filled[h], 1)


def stage_rwkv_output(core, zr, a, sel, mixed):
    nc, bank = core.nc, core.bank
    with ExitStack() as st:
        gate_in = core.sb("gate_in", [P, S], ctx=st)
        g_up = core.sb("g_up", [P, S], ctx=st)
        g_w = core.sb("g_w", [P, P], ctx=st)
        yc = core.sb("yc", [P, S], ctx=st)
        sq = core.sb("y_sq", [P, S], ctx=st)
        bonus = core.sb("bonus", [P, S], ctx=st)
        cols = core.sb("out_cols", [P, 6], ctx=st)
        sems = core.sems(st, "g_loaded", "cols_staged", "gate_staged", "y_summed", "centred", "squared", "sq_summed", "rooted",
                         "inverted", "normed", "rates", "weighed", "b_summed", "bonused", "added", "gated", "stored")
        (g_loaded, cols_staged, gate_staged, y_summed, centred, squared, sq_summed, rooted, inverted, normed, rates, weighed,
         b_summed, bonused, added, gated, stored) = sems
        with nc.Block() as block:
            @block.sync
            def _(sp):
                sp.dma_start(g_up[:, :], core.dram["g_up"]).then_inc(g_loaded, 16)
                sp.wait_ge(g_loaded, 16)

            @block.scalar
            def _(act):
                act.activation(gate_in[:, :], zr[:, 13, :], ACT.Sigmoid)
        with nc.Fori(0, 4) as f:
            core.clear(sems)
            row = lambda t, first: t[:, bass.ds(f + first, 1), :].rearrange("p a t -> p (a t)")
            with nc.Block() as block:
                @block.tensor
                def _(pe):
                    pe.matmul(bank[0][:, :], core.headones[:, :], row(mixed, 4), start=True, stop=True).then_inc(y_summed, 1)
                    pe.wait_ge(gate_staged, 1)
                    pe.matmul(bank[3][:, :], g_w[:, :], gate_in[:, :], start=True, stop=True).then_inc(gated, 1)
                    pe.wait_ge(squared, 1)
                    pe.matmul(bank[1][:, :], core.headones[:, :], sq[:, :], start=True, stop=True).then_inc(sq_summed, 1)
                    pe.wait_ge(weighed, 4)
                    pe.matmul(bank[2][:, :], core.headones[:, :], bonus[:, :], start=True, stop=True).then_inc(b_summed, 1)

                @block.gpsimd
                def _(pool):
                    pool.tensor_tensor(bonus[:, :], row(a, 0), row(a, 4), ALU.add).then_inc(rates, 1)
                    pool.tensor_copy(g_w[:, :], g_up[:, bass.ds(f * P, P)]).then_inc(gate_staged, 1)

                @block.scalar
                def _(act):
                    act.wait_ge(centred, 1)
                    act.activation(sq[:, :], yc[:, :], ACT.Square).then_inc(squared, 1)
                    act.wait_ge(sq_summed, 1)
                    act.activation(sq[:, :], bank[1][:, :], ACT.Sqrt, scale=1.0 / HD, bias=64e-5).then_inc(rooted, 1)

                @block.vector
                def _(dve):
                    dve.tensor_copy(cols[:, :], row(sel, 0)).then_inc(cols_staged, 1)
                    dve.wait_ge(y_summed, 1)
                    dve.scalar_tensor_tensor(out=yc[:, :], in0=bank[0][:, :], scalar=-1.0 / HD, in1=row(mixed, 4),
                                             op0=ALU.mult, op1=ALU.add).then_inc(centred, 1)
                    dve.wait_ge(cols_staged, 1)
                    dve.wait_ge(rates, 1)
                    dve.tensor_scalar(bonus[:, :], bonus[:, :], cols[:, 2:3], cols[:, 1:2], ALU.mult, ALU.add).then_inc(weighed, 1)
                    dve.wait_ge(weighed, 1)
                    dve.tensor_tensor(bonus[:, :], bonus[:, :], row(zr, 4), ALU.mult).then_inc(weighed, 1)
                    dve.wait_ge(weighed, 2)
                    dve.scalar_tensor_tensor(out=bonus[:, :], in0=bonus[:, :], scalar=cols[:, 3:4], in1=row(zr, 0),
                                             op0=ALU.mult, op1=ALU.mult).then_inc(weighed, 1)
                    dve.wait_ge(rooted, 1)
                    dve.wait_ge(weighed, 3)
                    dve.reciprocal(sq[:, :], sq[:, :]).then_inc(weighed, 1)
                    dve.wait_ge(weighed, 4)
                    dve.scalar_tensor_tensor(out=yc[:, :], in0=yc[:, :], scalar=cols[:, 4:5], in1=sq[:, :],
                                             op0=ALU.mult, op1=ALU.mult).then_inc(normed, 1)
                    dve.wait_ge(b_summed, 1)
                    dve.tensor_tensor(bonus[:, :], bank[2][:, :], row(zr, 8), ALU.mult).then_inc(bonused, 1)
                    dve.wait_ge(normed, 1)
                    dve.wait_ge(bonused, 1)
                    dve.scalar_tensor_tensor(out=yc[:, :], in0=yc[:, :], scalar=cols[:, 5:6], in1=bonus[:, :],
                                             op0=ALU.add, op1=ALU.add).then_inc(added, 1)
                    dve.wait_ge(added, 1)
                    dve.wait_ge(gated, 1)
                    dve.tensor_tensor(row(mixed, 4), bank[3][:, :], yc[:, :], ALU.mult).then_inc(stored, 1)


def stage_residual(core, first, src, gate):
    x = core.x

    def evac(half):
        def f(eng, psum, t):
            k = 4 * half + t
            return eng.scalar_tensor_tensor(out=x[:, k, :], in0=psum, scalar=gate[:, k:k + 1], in1=x[:, k, :],
                                            op0=ALU.mult, op1=ALU.add)
        return f
    stage_project(core, first, [("T", [evac(0)] * 4), ("T", [evac(1)] * 4)], src, only_dve=True)


def stage_peer(core, first, mixed):
    nc = core.nc
    h2 = mixed
    with ExitStack() as st:
        idx = core.sb("expert_idx", [P, TT, HK], U32, ctx=st)
        gates = core.sb("expert_gate", [P, TT, HK], ctx=st)
        hN = core.sb("h_rows", [P, TT, D], ctx=st)
        sc = core.sb("peer_scores", [P, TT, 2 * PEER_HEADS, N_KEYS], ctx=st)
        stage_norm(core, h2, core.gain[:, 8:16], core.mod[:, 24:32])
        with ExitStack() as s2:
            q = core.sb("peer_q", [P, 2 * PEER_HEADS, S], ctx=s2)
            stage_project(core, first, [("T", [copy_to(lambda f, i=i: q[:, 4 * i + f, :])] * 4) for i in range(4)], h2)
            stage_peer_scores(core, q, h2, sc, hN)
        stage_peer_experts(core, sc, idx, gates, hN, mixed)


def stage_peer_scores(core, q, h2, sc, hN):
    nc, bank = core.nc, core.bank
    with ExitStack() as st:
        keys = core.sb("peer_keys", [P, 2 * N_KEYS], ctx=st)
        keys_loaded, bank_full, act_emptied, dve_emptied = core.sems(st, "keys_loaded", "bank_full", "act_emptied", "dve_emptied")
        units = [("turn", i, g, 0) for i in range(TT) for g in range(2)]
        units += [("score", i, g, half) for i in range(TT) for half in range(2) for g in range(2)]

        def dest(unit):
            kind, i, g, half = unit
            if kind == "turn":
                return hN[:, i, g * S:g * S + S]
            at = half * PEER_HEADS + 4 * g
            return sc[:, i, at:at + 4, :].rearrange("p r n -> p (r n)")

        with nc.Block() as block:
            @block.sync
            def _(sp):
                sp.dma_start(keys[:, :], core.dram["keys"]).then_inc(keys_loaded, 16)
                sp.wait_ge(keys_loaded, 16)

            @block.tensor
            def _(pe):
                for u, (kind, i, g, half) in enumerate(units):
                    if u >= 6:
                        pe.wait_ge(dve_emptied if u % 2 else act_emptied, (u - 6) // 2 + 1)
                    if kind == "score":
                        pe.wait_ge(keys_loaded, 16)
                    for j in range(4):
                        out = bank[u % 6][:, j * P:j * P + P]
                        if kind == "turn":
                            mm = pe.transpose(out, h2[:, 4 * g + j, i * P:i * P + P], core.ident[:, :])
                        else:
                            mm = pe.matmul(out, q[:, 2 * (4 * g + j) + half, i * P:i * P + P],
                                           keys[:, half * N_KEYS:half * N_KEYS + N_KEYS], start=True, stop=True)
                    mm.then_inc(bank_full, 1)

            @block.scalar
            def _(act):
                for u in range(0, len(units), 2):
                    act.wait_ge(bank_full, u + 1)
                    act.activation(dest(units[u]), bank[u % 6][:, :], ACT.Copy).then_inc(act_emptied, 1)

            @block.vector
            def _(dve):
                for u in range(1, len(units), 2):
                    dve.wait_ge(bank_full, u + 1)
                    dve.tensor_copy(dest(units[u]), bank[u % 6][:, :]).then_inc(dve_emptied, 1)


class TopKeys:
    LOWEST = -3.0e38
    OPS = 27

    def __init__(self, core, st, sc, idx, gates, scratch, iota):
        self.sc, self.idx, self.gates, self.iota = sc, idx, gates, iota
        self.step, self.gate = core.sems(st, "topk_step", "topk_gate")
        self.row = scratch[:, 0, 0:2 * N_KEYS].rearrange("p (a n) -> p a n", a=2)
        self.rest = scratch[:, 0, 2 * N_KEYS:4 * N_KEYS].rearrange("p (a n) -> p a n", a=2)
        self.cand, self.cand_rest = scratch[:, 1, 0:TOPK * TOPK], scratch[:, 1, TOPK * TOPK:2 * TOPK * TOPK]
        self.pick = scratch[:, 2, :].rearrange("p (k a) -> p k a", a=TOPK)
        small = lambda i: scratch[:, 3, 2 * TOPK * i:2 * TOPK * (i + 1)].rearrange("p (a k) -> p a k", a=2)
        self.val, self.atf, self.partf, self.key = [small(i) for i in range(4)]
        self.best, self.expert = scratch[:, 3, 8 * TOPK:9 * TOPK], scratch[:, 3, 9 * TOPK:10 * TOPK]
        self.at = core.sb("topk_at", [P, 2, TOPK], U32, ctx=st)
        self.pos = core.sb("topk_pos", [P, TOPK], U32, ctx=st)
        self.part = core.sb("topk_part", [P, 2, TOPK], U32, ctx=st)

    def head(self, dve, t, h):
        n = 0
        heads = lambda ap: ap.rearrange("p (h k) -> p h k", k=TOPK)[:, bass.ds(h, 1), :].rearrange("p h k -> p (h k)")

        def do(ins):
            nonlocal n
            n += 1
            ins.then_inc(self.step, 1)

        def settled():
            dve.wait_ge(self.step, h * self.OPS + (t * PEER_HEADS * self.OPS + n))

        def gated():
            settled()
            dve.sem_inc(self.gate, 1)

        def top16(v, where, values, others):
            rows = range(len(v))
            for r in rows:
                do(dve.max(v[r][:, 0:8], values[r]))
            gated()
            for r in rows:
                do(dve.match_replace(others[r], v[r][:, 0:8], values[r], self.LOWEST))
            for r in rows:
                do(dve.max_index(where[r][:, 0:8], v[r][:, 0:8], values[r]))
            gated()
            for r in rows:
                do(dve.max(v[r][:, 8:16], others[r]))
            gated()
            for r in rows:
                do(dve.max_index(where[r][:, 8:16], v[r][:, 8:16], others[r]))

        sc = self.sc[:, t, :, :].rearrange("p (a h) n -> p a h n", a=2)[:, :, bass.ds(h, 1), :]
        do(dve.tensor_copy(self.row, sc.rearrange("p a h n -> p a (h n)")))
        gated()
        two = lambda ap: [ap[:, 0, :], ap[:, 1, :]]
        top16(two(self.val), two(self.at), two(self.row), two(self.rest))
        square = [P, TOPK, TOPK]
        settled()
        do(dve.tensor_tensor(self.cand.rearrange("p (a b) -> p a b", a=TOPK), self.val[:, 0, :].unsqueeze(2).to_broadcast(square),
                             self.val[:, 1, :].unsqueeze(1).to_broadcast(square), ALU.add))
        settled()
        do(dve.tensor_copy(self.atf, self.at[:, :, :]))
        gated()
        top16([self.best], [self.pos[:, :]], [self.cand], [self.cand_rest])
        settled()
        do(dve.tensor_scalar(self.part[:, 0, :], self.pos[:, :], 4, None, ALU.logical_shift_right))
        do(dve.tensor_scalar(self.part[:, 1, :], self.pos[:, :], TOPK - 1, None, ALU.bitwise_and))
        do(dve.tensor_scalar(heads(self.gates[:, t, :]), self.best, self.best[:, 0:1], None, ALU.subtract))
        settled()
        do(dve.tensor_copy(self.partf, self.part[:, :, :]))
        settled()
        flat_part = self.partf.rearrange("p a k -> p (a k)")
        do(dve.tensor_tensor(self.pick, repeat(flat_part, TOPK), tiled(self.iota[:, :], 2 * TOPK), ALU.is_equal))
        settled()
        p4 = self.pick.rearrange("p (a k) b -> p a k b", a=2)
        do(dve.tensor_tensor(p4, p4, self.atf.unsqueeze(2).to_broadcast([P, 2, TOPK, TOPK]), ALU.mult))
        settled()
        do(dve.tensor_reduce(self.key.rearrange("p a k -> p (a k)"), self.pick, AX.X, ALU.add))
        settled()
        do(dve.scalar_tensor_tensor(out=self.expert, in0=self.key[:, 0, :], scalar=float(N_KEYS), in1=self.key[:, 1, :],
                                    op0=ALU.mult, op1=ALU.add))
        settled()
        do(dve.tensor_copy(heads(self.idx[:, t, :]), self.expert))
        settled()
        dve.sem_inc(self.gate, 1)
        assert n == self.OPS, n


def stage_peer_experts(core, sc, idx, gates, hN, scratch):
    nc, bank, x = core.nc, core.bank, core.x
    SLOTS, PAIR = 8, 2
    TURNS = HK // SLOTS
    gate2 = core.mod[:, 40:48]
    with ExitStack() as st:
        rows = core.sb("expert_rows", [P, SLOTS, 2 * D], ctx=st)
        place = core.sb("expert_place", [P, SLOTS], U32, ctx=st)
        dot = core.sb("expert_dot", [P, SLOTS], ctx=st)
        act_out = core.sb("expert_act", [P, SLOTS], ctx=st)
        y = scratch[:, 0:2, :].rearrange("p a t -> p (a t)")
        diag = scratch[:, 2:4, :].rearrange("p a t -> p (a t)").rearrange("p (s t) -> p s t", s=SLOTS)
        zeros = scratch[:, 7, S - P:S]
        iota = core.sb("iota16", [P, TOPK], ctx=st)
        den = core.sb("gate_den", [P, PEER_HEADS], ctx=st)
        topk = TopKeys(core, st, sc, idx, gates, scratch[:, 4:8, :], iota)
        names = ["slot_free", "pool_gate", "placed", "dotted", "gelued", "weighted", "zeroed", "y_full", "y_copied", "y_turned", "x_added",
                 "iota_loaded", "ranked", "raised", "normed"]
        (slot_free, pool_gate, placed, dotted, gelued, weighted, zeroed, y_full, y_copied, y_turned, x_added,
         iota_loaded, ranked, raised, normed) = core.sems(st, *names)
        RANKING = PEER_HEADS
        arrived = [core.ctx.enter_context(nc.semaphore(f"rows_arrived{j}")) for j in range(SLOTS)]
        core.clear(arrived)
        with nc.Block() as block:
            @block.sync
            def _(sp):
                sp.dma_start(iota[:, :], core.dram["iota16"]).then_inc(iota_loaded, 16)
                sp.wait_ge(iota_loaded, 16)

            @block.gpsimd
            def _(pool):
                for t in range(TT):
                    pool.wait_ge(ranked, t + 1)
                    with pool.Fori(0, TURNS) as i:
                        for j in range(SLOTS):
                            n = i * SLOTS + (t * HK + j)
                            pool.wait_ge(slot_free, n + 1)
                            pool.sem_inc(pool_gate, 1)
                            pool.tensor_copy(place[:, j:j + 1], idx[:, t, bass.ds(i * SLOTS + j, 1)]).then_inc(placed, 1)
                            pool.wait_ge(placed, n + 1)
                            pool.sem_inc(pool_gate, 1)
                            pool.indirect_dma_start(rows[:, j, :], None, core.dram["uv"],
                                                    bass.IndirectOffsetOnAxis(place[:, j:j + 1], 0)).then_inc(arrived[j], 16)

            @block.vector
            def _(dve):
                def turn(t, i):
                    for g in range(SLOTS // PAIR):
                        for j in range(g * PAIR, g * PAIR + PAIR):
                            dve.wait_ge(arrived[j], i * 16 + (t * TURNS + 1) * 16)
                            u = rows[:, j, 0:D]
                            dve.scalar_tensor_tensor(out=u, in0=u, scalar=1.0, in1=hN[:, t, :], op0=ALU.mult, op1=ALU.mult,
                                                     accum_out=dot[:, j:j + 1]).then_inc(dotted, 1)
                        dve.wait_ge(gelued, i * (SLOTS // PAIR) + (t * TURNS * (SLOTS // PAIR) + g + 1))
                        for j in range(g * PAIR, g * PAIR + PAIR):
                            dve.tensor_scalar(diag[:, j, :], core.ident[:, :], act_out[:, j:j + 1],
                                              gates[:, t, bass.ds(i * SLOTS + j, 1)], ALU.mult, ALU.mult).then_inc(weighted, 1)

                def chosen(t):
                    dve.wait_ge(topk.step, (t + 1) * PEER_HEADS * topk.OPS)
                    dve.sem_inc(ranked, 1)

                dve.memset(zeros, 0.0).then_inc(zeroed, 1)
                dve.wait_ge(iota_loaded, 16)
                with dve.Fori(0, PEER_HEADS) as h:
                    topk.head(dve, 0, h)
                chosen(0)
                for t in range(TT):
                    g = gates[:, t, :].rearrange("p (h k) -> p h k", h=PEER_HEADS)
                    dve.wait_ge(raised, t + 1)
                    dve.tensor_reduce(den[:, :], g, AX.X, ALU.add).then_inc(normed, 1)
                    dve.wait_ge(normed, 3 * t + 1)
                    dve.reciprocal(den[:, :], den[:, :]).then_inc(normed, 1)
                    dve.wait_ge(normed, 3 * t + 2)
                    dve.tensor_tensor(g, g, repeat(den[:, :], TOPK), ALU.mult).then_inc(normed, 1)
                    dve.wait_ge(normed, 3 * t + 3)
                    with dve.Fori(0, RANKING) as i:
                        turn(t, i)
                        if t + 1 < TT:
                            topk.head(dve, t + 1, i)
                    if t + 1 < TT:
                        chosen(t + 1)
                    with dve.Fori(RANKING, TURNS) as i:
                        turn(t, i)
                    for k in range(KD):
                        if k % 4 == 0:
                            dve.wait_ge(y_turned, 2 * t + k // 4 + 1)
                        xk = x[:, k, t * P:t * P + P]
                        dve.scalar_tensor_tensor(out=xk, in0=bank[4 + k // 4][:, (k % 4) * P:(k % 4) * P + P],
                                                 scalar=gate2[:, k:k + 1], in1=xk, op0=ALU.mult, op1=ALU.add).then_inc(x_added, 1)

            @block.scalar
            def _(act):
                def turn(t, i):
                    for g in range(SLOTS // PAIR):
                        act.wait_ge(dotted, i * SLOTS + (t * HK + (g + 1) * PAIR))
                        act.activation(act_out[:, g * PAIR:(g + 1) * PAIR], dot[:, g * PAIR:(g + 1) * PAIR], ACT.Gelu).then_inc(gelued, 1)

                def raise_gates(t):
                    act.wait_ge(ranked, t + 1)
                    act.activation(gates[:, t, :], gates[:, t, :], ACT.Exp).then_inc(raised, 1)

                raise_gates(0)
                for t in range(TT):
                    with act.Fori(0, RANKING) as i:
                        turn(t, i)
                    if t + 1 < TT:
                        raise_gates(t + 1)
                    with act.Fori(RANKING, TURNS) as i:
                        turn(t, i)
                    act.wait_ge(y_full, t + 1)
                    if t >= 1:
                        act.wait_ge(y_turned, 2 * t)
                    for half in range(2):
                        act.activation(y[:, half * S:half * S + S], bank[2 * (t % 2) + half][:, :], ACT.Copy).then_inc(y_copied, 1)

            @block.tensor
            def _(pe):
                pe.sem_inc(slot_free, SLOTS)
                pe.wait_ge(zeroed, 1)
                for t in range(TT):
                    yb = [bank[2 * (t % 2) + half] for half in range(2)]
                    if t >= 2:
                        pe.wait_ge(y_copied, 2 * t - 2)
                    for half in range(2):
                        pe.matmul(yb[half][:, :], zeros, hN[:, t, 0:S], start=True, stop=False)
                    with pe.Fori(0, TURNS) as i:
                        for j in range(SLOTS):
                            pe.wait_ge(weighted, i * SLOTS + (t * HK + j + 1))
                            for half in range(2):
                                mm = pe.matmul(yb[half][:, :], diag[:, j, :], rows[:, j, D + half * S:D + half * S + S],
                                               start=False, stop=False, skip_group_check=True)
                            mm.then_inc(slot_free, 1)
                    for half in range(2):
                        mm = pe.matmul(yb[half][:, :], zeros, hN[:, t, 0:S], start=False, stop=True)
                    mm.then_inc(y_full, 1)
                    pe.wait_ge(y_copied, 2 * t + 2)
                    for half in range(2):
                        if t >= 1:
                            pe.wait_ge(x_added, KD * (t - 1) + 4 * half + 4)
                        for k in range(4):
                            mm = pe.transpose(bank[4 + half][:, k * P:k * P + P], y[:, (4 * half + k) * P:(4 * half + k + 1) * P], core.ident[:, :])
                        mm.then_inc(y_turned, 1)


def second_block(core, first, mixed):
    nc = core.nc
    with ExitStack() as st:
        zg = core.sb("zg", [P, 14, S], ctx=st)
        v = core.sb("v2", [P, TT, D], ctx=st)
        with ExitStack() as s2:
            zt = core.sb("zt", [P, 9, S], ctx=s2)
            stage_norm(core, mixed, core.gain[:, 16:24], core.mod[:, 48:56])
            into = lambda z, at, n: ("T", [copy_to(lambda f: z[:, at + f, :])] * n)
            rows = lambda at, n: ("N", copy_to(lambda t: v[:, t, at:at + n]))
            plan = [into(zt, 0, 3), into(zt, 3, 3), rows(0, 384), into(zt, 6, 3), into(zg, 0, 3), into(zg, 3, 3), rows(384, 384),
                    into(zg, 6, 3), into(zg, 9, 2), rows(768, 256),
                    ("T", [copy_to(lambda f: zg[:, 11 + f, :])] * 2 + [copy_to(lambda f: zg[0:16, 13, :])])]
            stage_project(core, first, plan, mixed)
            stage_retention(core, zt, v, mixed)
        logs = core.sb("log_decay", [P, 4, S], ctx=st)
        keys = core.sb("hgrn_keys", [P, 3, S], ctx=st)
        stage_recurrence_inputs(core, zg, logs, keys)
        stage_recurrence(core, 3, 2, lambda i: (zg[:, bass.ds(i, 1), :], keys[:, bass.ds(i, 1), :], logs[:, bass.ds(i, 1), :]),
                         lambda i: v[:, :, bass.ds(i * P + 384, P)], lambda i, n: zg[:, bass.ds(i + 6, 1), :], "hgrn_norm_2", mixed, 3, zg[:, 3:6, :])
        stage_recurrence(core, 1, 4, lambda i: (zg[:, 9:10, :], zg[:, 10:11, :], logs[:, 3:4, :]),
                         lambda i: v[:, :, 768:1024], lambda i, n: zg[:, 11 + n:12 + n, :], "gla_norm_2", mixed, 6, zg[:, 3:6, :])
    stage_residual(core, first + 11, mixed, core.mod[:, 64:72])
    stage_norm(core, mixed, core.gain[:, 24:32], core.mod[:, 72:80])
    stage_moe(core, mixed)


def flat(ap):
    return ap.rearrange("p a t -> p (a t)")


class HeadTail:
    NAMES = ("o_full", "o_copied", "o_squared", "o_summed", "o_rooted", "o_inverted", "o_scaled", "gate_raised", "o_stored")

    def __init__(self, core, st, scratch=None):
        self.core = core
        if scratch is None:
            scratch = core.sb("head_scratch", [P, 3, S], ctx=st)
        self.o, self.sq, self.gate = [scratch[:, i, :] for i in range(3)]
        self.gain = core.sb("head_gain", [P, 1], ctx=st)
        self.sems = core.sems(st, *self.NAMES)

    def on_scalar(self, act, n, halves, gate, gain):
        (o_full, o_copied, o_squared, o_summed, o_rooted, o_inverted, o_scaled, gate_raised, o_stored) = self.sems
        if n >= 1:
            act.wait_ge(o_stored, n)
        act.activation(self.gain[:, :], gain, ACT.Copy).then_inc(gate_raised, 1)
        act.activation(self.gate[:, :], flat(gate), ACT.Silu).then_inc(gate_raised, 1)
        for h in range(2):
            act.wait_ge(o_full, 2 * n + h + 1)
            r = slice(HD * h, HD * h + HD)
            act.activation(self.o[r, :], halves[h][r, :], ACT.Copy).then_inc(o_copied, 1)
        act.wait_ge(o_copied, 2 * n + 2)
        act.activation(self.sq[:, :], self.o[:, :], ACT.Square).then_inc(o_squared, 1)
        act.wait_ge(o_summed, n + 1)
        act.activation(self.sq[:, :], self.core.bank[0][:, :], ACT.Sqrt, scale=1.0 / HD, bias=1e-6).then_inc(o_rooted, 1)

    def on_tensor(self, pe, n, bank_free):
        (o_full, o_copied, o_squared, o_summed, o_rooted, o_inverted, o_scaled, gate_raised, o_stored) = self.sems
        pe.wait_ge(o_squared, n + 1)
        bank_free()
        pe.matmul(self.core.bank[0][:, :], self.core.headones[:, :], self.sq[:, :], start=True, stop=True).then_inc(o_summed, 1)

    def on_vector(self, dve, n, dest):
        (o_full, o_copied, o_squared, o_summed, o_rooted, o_inverted, o_scaled, gate_raised, o_stored) = self.sems
        dve.wait_ge(o_rooted, n + 1)
        dve.reciprocal(self.sq[:, :], self.sq[:, :]).then_inc(o_inverted, 1)
        dve.wait_ge(gate_raised, 2 * n + 2)
        dve.wait_ge(o_inverted, n + 1)
        dve.scalar_tensor_tensor(out=self.o[:, :], in0=self.o[:, :], scalar=self.gain[:, 0:1], in1=self.sq[:, :],
                                 op0=ALU.mult, op1=ALU.mult).then_inc(o_scaled, 1)
        dve.wait_ge(o_scaled, n + 1)
        dve.tensor_tensor(flat(dest), self.o[:, :], self.gate[:, :], ALU.mult).then_inc(o_stored, 1)


def stage_retention(core, zt, v, mixed):
    nc, bank = core.nc, core.bank
    with ExitStack() as st:
        decay = core.sb("ret_decay", [P, RET_HEADS, S], ctx=st)
        rot = core.sb("rot", [P, P], ctx=st)
        cos = core.sb("cos", [P, S], ctx=st)
        sin = core.sb("sin", [P, S], ctx=st)
        qr = core.sb("qk_rot", [P, 2, S], ctx=st)
        part = core.sb("rot_part", [P, 2, S], ctx=st)
        vs = core.sb("v_pair2", [P, TT, P], ctx=st)
        score = core.sb("ret_score", [P, 2, TT, S], ctx=st)
        stage_rotary(core, cos, sin, decay, rot)
        tail = HeadTail(core, st)
        sems = core.sems(st, "turned", "cos_done", "sin_done", "rotated", "v_staged", "scored", "decayed")
        turned, cos_done, sin_done, rotated, v_staged, scored, decayed = sems
        o_full = tail.sems[0]
        UNITS = [(h, j) for h in range(2) for j in range(TT)]
        with nc.Fori(0, 3) as i:
            core.clear(sems + tail.sems)
            with nc.Block() as block:
                @block.gpsimd
                def _(pool):
                    for w in range(2):
                        pool.tensor_tensor(qr[:, w, :], flat(zt[:, bass.ds(i + 3 * w, 1), :]), cos[:, :], ALU.mult).then_inc(cos_done, 1)
                    pool.tensor_copy(vs[:, :, :], v[:, :, bass.ds(i * P, P)]).then_inc(v_staged, 1)

                @block.scalar
                def _(act):
                    tail.on_scalar(act, 0, bank[4:6], zt[:, bass.ds(i + 6, 1), :], core.col("ret_norm_2", i))

                @block.tensor
                def _(pe):
                    for w in range(2):
                        pe.matmul(bank[w][:, :], rot[:, :], flat(zt[:, bass.ds(i + 3 * w, 1), :]), start=True, stop=True).then_inc(turned, 1)
                    pe.wait_ge(rotated, 2)

                    def mix(h):
                        pe.wait_ge(decayed, 4 * h + 4)
                        pe.wait_ge(v_staged, 1)
                        r = slice(HD * h, HD * h + HD)
                        for j in range(TT):
                            mm = pe.matmul(bank[4 + h][r, j * P:S], vs[:, j, r], score[:, h, j, 0:S - j * P], start=j == 0, stop=j == TT - 1)
                        mm.then_inc(o_full, 1)

                    for u, (h, j) in enumerate(UNITS):
                        if u >= 2:
                            pe.wait_ge(decayed, u - 1)
                        r = slice(HD * h, HD * h + HD)
                        pe.matmul(bank[2 + u % 2][:, 0:S - j * P], qr[r, 1, j * P:j * P + P], qr[r, 0, j * P:S],
                                  start=True, stop=True).then_inc(scored, 1)
                        if u == 5:
                            mix(0)
                    mix(1)
                    tail.on_tensor(pe, 0, lambda: pe.wait_ge(sin_done, 1))

                @block.vector
                def _(dve):
                    for w in range(2):
                        dve.wait_ge(turned, w + 1)
                        dve.tensor_tensor(part[:, w, :], bank[w][:, :], sin[:, :], ALU.mult).then_inc(sin_done, 1)
                        dve.wait_ge(cos_done, w + 1)
                        dve.wait_ge(sin_done, w + 1)
                        dve.tensor_tensor(qr[:, w, :], qr[:, w, :], part[:, w, :], ALU.add).then_inc(rotated, 1)
                    for u, (h, j) in enumerate(UNITS):
                        dve.wait_ge(scored, u + 1)
                        dve.tensor_tensor(score[:, h, j, 0:S - j * P], bank[2 + u % 2][:, 0:S - j * P],
                                          flat(decay[:, bass.ds(i * 2 + h, 1), 0:S - j * P]), ALU.mult).then_inc(decayed, 1)
                    tail.on_vector(dve, 0, mixed[:, bass.ds(i, 1), :])


def stage_rotary(core, cos, sin, decay, rot):
    nc = core.nc
    TURN = 2.0 * math.pi
    C1 = 6.28125
    C2 = 0.0019350051879882812
    C3 = TURN - C1 - C2
    MAGIC = 12582912.0
    with ExitStack() as st:
        pos = core.sb("pos", [P, S], I32, ctx=st)
        turns = core.sb("turns", [P, S], ctx=st)
        freq = core.sb("inv_freq", [P, 1], ctx=st)
        loaded, step_sem, reduced, done = core.sems(st, "rot_loaded", "rot_step", "reduced", "rot_done")
        with nc.Block() as block:
            @block.sync
            def _(sp):
                sp.dma_start(pos[:, :], core.dram["positions"].rearrange("a t -> (a t)").partition_broadcast(P)).then_inc(loaded, 16)
                sp.dma_start(freq[:, :], core.dram["inv_freq"]).then_inc(loaded, 16)
                sp.dma_start(decay[:, :, :], core.dram["ret_decay"]).then_inc(loaded, 16)
                sp.dma_start(rot[:, :], core.dram["rot"]).then_inc(loaded, 16)
                sp.wait_ge(loaded, 64)

            @block.vector
            def _(dve):
                step = Steps(dve, step_sem)
                ang = sin[:, :]
                dve.wait_ge(loaded, 64)
                step.then(dve.tensor_copy(cos[:, :], pos[:, :]))
                step.then(dve.tensor_scalar(ang, cos[:, :], freq[:, 0:1], None, ALU.mult))
                step.then(dve.tensor_scalar(turns[:, :], ang, 1.0 / TURN, MAGIC, ALU.mult, ALU.add))
                step.then(dve.tensor_scalar(turns[:, :], turns[:, :], MAGIC, None, ALU.subtract))
                for c in (C1, C2, C3):
                    step.then(dve.scalar_tensor_tensor(out=ang, in0=turns[:, :], scalar=-c, in1=ang, op0=ALU.mult, op1=ALU.add))
                step.then(dve.tensor_scalar(ang, ang, math.pi, -math.pi, ALU.min, ALU.max))
                step.then(dve.scalar_tensor_tensor(out=cos[:, :], in0=ang, scalar=-1.0, in1=ang, op0=ALU.mult, op1=ALU.max))
                dve.tensor_scalar(cos[:, :], cos[:, :], -1.0, 0.5 * math.pi, ALU.mult, ALU.add).then_inc(reduced, 1)

            @block.scalar
            def _(act):
                act.wait_ge(reduced, 1)
                act.activation(cos[:, :], cos[:, :], ACT.Sin).then_inc(done, 1)
                act.activation(sin[:, :], sin[:, :], ACT.Sin).then_inc(done, 1)


def stage_recurrence_inputs(core, zg, logs, keys):
    nc, bank = core.nc, core.bank
    HUGE = 2.0 ** 60
    with ExitStack() as st:
        lb = core.sb("lower_bound", [P, 3, 3], ctx=st)
        low = core.sb("log_low", [P, 3, S], ctx=st)
        u = core.sb("gla_u", [P, 3, S], ctx=st)
        wa2 = core.sb("wa2", [16, P], ctx=st)
        (loaded, step_sem, lb_shift, lb_raised, sig_done, split, logged, u_full, u_biased, u_abs, u_logged, q_raised) = core.sems(
            st, "wa2_loaded", "step", "lb_shifted", "lb_raised", "sig_done", "split", "logged", "u_full", "u_biased", "u_abs",
            "u_logged", "q_raised")
        logits = core.col("hgrn_lb_logits_2", 0, 3)
        with nc.Block() as block:
            @block.sync
            def _(sp):
                sp.dma_start(wa2[:, :], core.dram["wa2"]).then_inc(loaded, 16)
                sp.wait_ge(loaded, 16)

            @block.tensor
            def _(pe):
                pe.wait_ge(loaded, 16)
                pe.matmul(bank[0][:, :], wa2[:, :], zg[0:16, 13, :], start=True, stop=True).then_inc(u_full, 1)

            @block.scalar
            def _(act):
                act.activation(logs[:, 0:3, :], zg[:, 3:6, :], ACT.Sigmoid).then_inc(sig_done, 1)
                act.activation(keys[:, :, :], zg[:, 3:6, :], ACT.Sigmoid, scale=-1.0).then_inc(sig_done, 1)
                act.activation(zg[:, 0:3, :], zg[:, 0:3, :], ACT.Silu).then_inc(q_raised, 1)
                act.wait_ge(u_full, 1)
                act.activation(u[:, 0, :], bank[0][:, :], ACT.Identity, bias=core.col("gla_ba_2")).then_inc(u_biased, 1)
                act.wait_ge(lb_shift, 1)
                act.activation(lb[:, 2, :], lb[:, 2, :], ACT.Exp).then_inc(lb_raised, 1)
                act.wait_ge(u_abs, 1)
                act.activation(u[:, 1, :], u[:, 1, :], ACT.Exp, scale=-1.0).then_inc(u_logged, 1)
                act.wait_ge(u_logged, 1)
                act.activation(u[:, 1, :], u[:, 1, :], ACT.Ln, bias=1.0).then_inc(u_logged, 1)
                act.wait_ge(split, 1)
                act.activation(logs[:, 0:3, :], logs[:, 0:3, :], ACT.Ln).then_inc(logged, 1)
                act.activation(low[:, :, :], low[:, :, :], ACT.Ln).then_inc(logged, 1)

            @block.vector
            def _(dve):
                step = Steps(dve, step_sem)
                dve.tensor_tensor(lb[:, 2, :], logits, logits, ALU.subtract).then_inc(lb_shift, 1)
                dve.wait_ge(lb_raised, 1)
                step.then(dve.reciprocal(lb[:, 0, :], lb[:, 2, :]))
                step.then(dve.tensor_tensor(lb[:, 2, :], lb[:, 2, :], lb[:, 0, :], ALU.mult))
                step.then(dve.tensor_tensor(lb[:, 0, :], lb[:, 2, :], lb[:, 2, :], ALU.subtract))
                step.then(dve.tensor_scalar(lb[:, 1, :], lb[:, 0, :], -1.0, 1.0, ALU.mult, ALU.add))
                dve.wait_ge(u_biased, 1)
                dve.scalar_tensor_tensor(out=u[:, 1, :], in0=u[:, 0, :], scalar=-1.0, in1=u[:, 0, :], op0=ALU.mult, op1=ALU.max).then_inc(u_abs, 1)
                step(dve.tensor_scalar(u[:, 2, :], u[:, 0, :], 0.0, None, ALU.min))
                dve.wait_ge(sig_done, 2)
                for f in range(3):
                    step(dve.tensor_scalar(logs[:, f, :], logs[:, f, :], lb[:, 1, f:f + 1], lb[:, 0, f:f + 1], ALU.mult, ALU.add))
                    step(dve.tensor_scalar(keys[:, f, :], keys[:, f, :], lb[:, 1, f:f + 1], None, ALU.mult))
                step.done()
                step.then(dve.tensor_scalar(low[:, :, :], logs[:, 0:3, :], 1e-30, HUGE, ALU.max, ALU.mult))
                step(dve.tensor_scalar(low[:, :, :], low[:, :, :], 1.0, None, ALU.min))
                step(dve.tensor_scalar(logs[:, 0:3, :], logs[:, 0:3, :], 1.0 / HUGE, None, ALU.max))
                step.done()
                dve.sem_inc(split, 1)
                dve.wait_ge(q_raised, 1)
                step(dve.tensor_scalar(zg[:, 0:3, :], zg[:, 0:3, :], HD ** -0.5, None, ALU.mult))
                step(dve.tensor_scalar(zg[:, 9, :], zg[:, 9, :], 32 ** -0.5, None, ALU.mult))
                dve.wait_ge(u_logged, 2)
                step.then(dve.tensor_tensor(u[:, 2, :], u[:, 2, :], u[:, 1, :], ALU.subtract))
                step(dve.tensor_scalar(logs[:, 3, :], u[:, 2, :], 1.0 / 16.0, None, ALU.mult))
                dve.wait_ge(logged, 2)
                step(dve.tensor_tensor(logs[:, 0:3, :], logs[:, 0:3, :], low[:, :, :], ALU.add))
                step.done()


def stage_recurrence(core, turns, heads, source, values, gate, gain, mixed, base, scratch):
    nc, bank = core.nc, core.bank
    dk = P // heads
    NT = heads // 2
    NLV = len(LEVELS)
    with ExitStack() as st:
        halves = core.sb("halves", [P, NLV, P], U32, ctx=st)
        restart = core.sb("restart", [P, S], ctx=st)
        qs = core.sb("rec_q", [P, S], ctx=st)
        ks = core.sb("rec_k", [P, S], ctx=st)
        cum = core.sb("rec_cum", [P, S], ctx=st)
        q_end = core.sb("rec_q_end", [P, S], ctx=st)
        k_end = core.sb("rec_k_end", [P, S], ctx=st)
        total = core.sb("rec_total", [P, TT], ctx=st)
        far = core.sb("rec_far", [P, 2, P], ctx=st)
        dec = core.sb("rec_dec", [P, 2, S], ctx=st)
        qm = core.sb("rec_qm", [P, 2, S], ctx=st)
        km = core.sb("rec_km", [P, 2, S], ctx=st)
        vs = core.sb("rec_v", [P, TT, heads * HD], ctx=st)
        score = core.sb("rec_score", [P, heads, TT, S], ctx=st)
        tail = HeadTail(core, st, scratch)
        names = ("rec_tables", "staged", "q_staged", "k_staged", "summed", "total_ready", "ended", "raised", "far_ready", "halved", "dec_raised",
                 "q_ready", "k_ready", "scored", "merged", "far_scored", "far_copied")
        sems = core.sems(st, *names)
        (tables, staged, q_staged, k_staged, summed, total_ready, ended, raised, far_ready, halved, dec_raised, q_ready, k_ready, scored,
         merged, far_scored, far_copied) = sems
        o_full = tail.sems[0]
        with nc.Block() as block:
            @block.sync
            def _(sp):
                sp.dma_start(halves[:, :, :], core.dram["halves"]).then_inc(tables, 16)
                sp.dma_start(restart[:, :], core.dram["restart"]).then_inc(tables, 16)
                sp.wait_ge(tables, 32)
        tl = lambda ap, i: ap[:, i * P:i * P + P]

        def turn(i):
            q_in, k_in, log_in = [flat(s) for s in source(i)]
            with nc.Block() as block:
                @block.gpsimd
                def _(pool):
                    pool.tensor_copy(qs[:, :], q_in).then_inc(q_staged, 1)
                    pool.tensor_copy(ks[:, :], k_in).then_inc(k_staged, 1)
                    pool.tensor_copy(vs[:, :, :], values(i)).then_inc(staged, 1)
                    pool.wait_ge(k_staged, 1)
                    for l in range(NLV):
                        pool.wait_ge(dec_raised, l + 1)
                        if l >= 2:
                            pool.wait_ge(scored, heads * l)
                        pool.tensor_tensor(km[:, l % 2, :], ks[:, :], dec[:, l % 2, :], ALU.mult).then_inc(k_ready, 1)

                @block.scalar
                def _(act):
                    act.wait_ge(summed, 1)
                    act.activation(q_end[:, :], cum[:, :], ACT.Exp).then_inc(raised, 1)
                    act.wait_ge(ended, 1)
                    act.activation(k_end[:, :], k_end[:, :], ACT.Exp).then_inc(raised, 1)
                    act.wait_ge(total_ready, 1)
                    act.wait_ge(ended, 1)
                    act.activation(total[:, :], total[:, :], ACT.Exp).then_inc(raised, 1)
                    for l in range(NLV):
                        act.wait_ge(halved, 2 * l + 2)
                        act.activation(dec[:, l % 2, :], dec[:, l % 2, :], ACT.Exp).then_inc(dec_raised, 1)
                    for h in range(heads):
                        act.wait_ge(far_scored, 2 * h + 1)
                        act.activation(score[:, h, 0:3, P:2 * P], bank[4][:, 0:3 * P].rearrange("p (j t) -> p j t", t=P), ACT.Copy).then_inc(far_copied, 1)
                        act.wait_ge(far_scored, 2 * h + 2)
                        act.activation(score[:, h, 0:2, 2 * P:3 * P], bank[5][:, 0:2 * P].rearrange("p (j t) -> p j t", t=P), ACT.Copy).then_inc(far_copied, 1)
                        act.activation(score[:, h, 0, 3 * P:4 * P], bank[5][:, 2 * P:3 * P], ACT.Copy).then_inc(far_copied, 1)
                    for n in range(NT):
                        tail.on_scalar(act, n, bank[6:8], gate(i, n), core.col(gain, i + n))

                @block.tensor
                def _(pe):
                    unit = 0
                    for l in range(NLV + 1):
                        if l == 0:
                            pe.wait_ge(q_staged, 1)
                            pe.wait_ge(k_staged, 1)
                            a, b = ks, qs
                        else:
                            pe.wait_ge(q_ready, l)
                            pe.wait_ge(k_ready, l)
                            a, b = km[:, (l - 1) % 2, :], qm[:, (l - 1) % 2, :]
                        for h in range(heads):
                            if unit >= 4:
                                pe.wait_ge(merged, unit - 3)
                            r = slice(dk * h, dk * h + dk)
                            for t in range(TT):
                                mm = pe.matmul(bank[unit % 4][:, t * P:t * P + P], a[r, t * P:t * P + P], b[r, t * P:t * P + P], start=True, stop=True)
                            mm.then_inc(scored, 1)
                            unit += 1
                    pe.wait_ge(far_ready, 4)
                    for h in range(heads):
                        r = slice(dk * h, dk * h + dk)
                        if h >= 1:
                            pe.wait_ge(far_copied, 3 * h - 2)
                        for j in range(3):
                            mm = pe.matmul(bank[4][:, j * P:j * P + P], k_end[r, j * P:j * P + P], q_end[r, (j + 1) * P:(j + 2) * P], start=True, stop=True)
                        mm.then_inc(far_scored, 1)
                        if h >= 1:
                            pe.wait_ge(far_copied, 3 * h)
                        k0, k1, q2, q3 = far[r, 0, :], k_end[r, P:2 * P], q_end[r, 2 * P:3 * P], far[r, 1, :]
                        for j, (a, b) in enumerate(((k0, q2), (k1, q3), (k0, q3))):
                            mm = pe.matmul(bank[5][:, j * P:j * P + P], a, b, start=True, stop=True)
                        mm.then_inc(far_scored, 1)
                    pe.wait_ge(staged, 1)
                    for n in range(NT):
                        for hh in range(2):
                            h = 2 * n + hh
                            pe.wait_ge(far_copied, 3 * h + 3)
                            pe.wait_ge(merged, heads * NLV + h + 1)
                            if n >= 1:
                                pe.wait_ge(tail.sems[1], 2 * (n - 1) + hh + 1)
                            r = slice(HD * hh, HD * hh + HD)
                            for j in range(TT):
                                mm = pe.matmul(bank[6 + hh][r, j * P:S], vs[:, j, h * HD:h * HD + HD], score[:, h, j, 0:S - j * P], start=j == 0, stop=j == TT - 1)
                            mm.then_inc(o_full, 1)
                        tail.on_tensor(pe, n, lambda: pe.wait_ge(merged, heads * (NLV + 1)))

                @block.vector
                def _(dve):
                    dve.tensor_tensor_scan(cum[:, :], restart[:, :], log_in, 0.0, ALU.mult, ALU.add).then_inc(summed, 1)
                    dve.wait_ge(summed, 1)
                    dve.tensor_copy(total[:, :], cum[:, P - 1:S:P]).then_inc(total_ready, 1)
                    dve.wait_ge(total_ready, 1)
                    c3 = cum[:, :].rearrange("p (i t) -> p i t", t=P)
                    dve.tensor_tensor(k_end[:, :].rearrange("p (i t) -> p i t", t=P), repeat(total[:, :], P), c3, ALU.subtract).then_inc(ended, 1)

                    def halve(l):
                        m = LEVELS[l]
                        if l >= 2:
                            dve.wait_ge(k_ready, l - 1)
                            dve.wait_ge(q_ready, l - 1)
                        cm = cum[:, :].rearrange("p (b w) -> p b w", w=2 * m)
                        dm = dec[:, l % 2, :].rearrange("p (b w) -> p b w", w=2 * m)
                        mid = cm[:, :, m - 1:m].to_broadcast([P, S // (2 * m), m])
                        dve.tensor_tensor(dm[:, :, 0:m], mid, cm[:, :, 0:m], ALU.subtract).then_inc(halved, 1)
                        dve.tensor_tensor(dm[:, :, m:2 * m], cm[:, :, m:2 * m], mid, ALU.subtract).then_inc(halved, 1)

                    def query(l):
                        dve.wait_ge(dec_raised, l + 1)
                        if l >= 2:
                            dve.wait_ge(scored, heads * l)
                        dve.tensor_tensor(qm[:, l % 2, :], qs[:, :], dec[:, l % 2, :], ALU.mult).then_inc(q_ready, 1)

                    def merge(l):
                        for h in range(heads):
                            u = heads * l + h
                            dve.wait_ge(scored, u + 1)
                            src = bank[u % 4][:, :].rearrange("p (i t) -> p i t", t=P)
                            if l == 0:
                                dve.tensor_tensor(score[:, h, :, 0:P], src, tiled(core.ident[:, :], TT), ALU.mult).then_inc(merged, 1)
                            else:
                                dve.wait_ge(merged, heads * (l - 1) + h + 1)
                                dve.copy_predicated(score[:, h, :, 0:P], tiled(halves[:, l - 1, :], TT), src).then_inc(merged, 1)

                    halve(0)
                    halve(1)
                    dve.wait_ge(q_staged, 1)
                    merge(0)
                    for l in range(NLV):
                        query(l)
                        if l + 2 < NLV:
                            halve(l + 2)
                        merge(l + 1)
                    dve.wait_ge(raised, 3)
                    dve.tensor_tensor(q_end[:, :], q_end[:, :], qs[:, :], ALU.mult).then_inc(far_ready, 1)
                    dve.wait_ge(k_staged, 1)
                    dve.tensor_tensor(k_end[:, :], k_end[:, :], ks[:, :], ALU.mult).then_inc(far_ready, 1)
                    dve.wait_ge(far_ready, 2)
                    dve.tensor_scalar(far[:, 0, :], k_end[:, 0:P], total[:, 1:2], None, ALU.mult).then_inc(far_ready, 1)
                    dve.tensor_scalar(far[:, 1, :], q_end[:, 3 * P:S], total[:, 2:3], None, ALU.mult).then_inc(far_ready, 1)
                    for n in range(NT):
                        dest = mixed[:, bass.ds(i + base, 1), :] if turns > 1 else mixed[:, base + n:base + n + 1, :]
                        tail.on_vector(dve, n, dest)

        if turns > 1:
            with nc.Fori(0, turns) as i:
                core.clear(sems + tail.sems)
                turn(i)
        else:
            turn(0)


def stage_route(core, h, hN, place, weight, expert_row):
    nc, bank = core.nc, core.bank
    NR = N_GROUPS + N_EXPERTS
    with ExitStack() as st:
        w = core.sb("router_w", [P, KD, NR], ctx=st)
        b = core.sb("router_b", [P, NR], ctx=st)
        iota = core.sb("iota8", [P, TOPK], ctx=st)
        earlier = core.sb("earlier", [P, P], ctx=st)
        table = core.sb("dispatch", [P, 2 * MOE_TILES], ctx=st)
        lg = core.sb("logits", [P, TT, NR], ctx=st)
        top = core.sb("group_top", [P, TT], ctx=st)
        hot = core.sb("group_hot", [P, TT, N_GROUPS], ctx=st)
        free = core.sb("group_free", [P, TT], ctx=st)
        ex = core.sb("group_exp", [P, TT, N_GROUPS], ctx=st)
        gw = core.sb("group_w", [P, TT], ctx=st)
        within = core.sb("within", [P, TT, N_GROUPS, PER_GROUP], ctx=st)
        el = core.sb("expert_logit", [P, TT, PER_GROUP], ctx=st)
        best = core.sb("expert_best", [P, TT, 8], ctx=st)
        at = core.sb("expert_at", [P, TT, 8], U32, ctx=st)
        atf = core.sb("expert_atf", [P, TT, 8], ctx=st)
        pick = core.sb("expert_pick", [P, TT, PER_GROUP], ctx=st)
        chosen = core.sb("expert_chosen", [P, 2, TT, N_EXPERTS], ctx=st)
        either = core.sb("expert_either", [P, TT, N_EXPERTS], ctx=st)
        rank = core.sb("rank", [P, TT, N_EXPERTS], ctx=st)
        beyond = core.sb("rank_beyond", [P, TT, N_EXPERTS], ctx=st)
        count = core.sb("expert_count", [P, N_EXPERTS], ctx=st)
        extra = core.sb("extra_tiles", [P, N_EXPERTS], ctx=st)
        ends = core.sb("extra_ends", [P, N_EXPERTS], ctx=st)
        one = core.sb("expert_ones", [P, N_EXPERTS], ctx=st)
        jump = core.sb("extra_jump", [P, N_EXPERTS], ctx=st)
        whose = core.sb("extra_whose", [P, MOE_EXTRA, N_EXPERTS], ctx=st)
        spot = core.sb("spot", [P, TT], ctx=st)
        rowf = core.sb("expert_rowf", [P, MOE_TILES], ctx=st)
        loaded, scored, h_turned, h_copied, step_sem, g_shifted, g_raised, e_shifted, e_raised, chosen_done, ranked = core.sems(
            st, "router_loaded", "scored", "h_turned", "h_copied", "step", "g_shifted", "g_raised", "e_shifted", "e_raised",
            "chosen_done", "ranked")
        expert_no, extra_no, own_rows = table[:, 0:N_EXPERTS], table[:, N_EXPERTS:MOE_TILES], table[:, MOE_TILES:]
        with nc.Block() as block:
            @block.sync
            def _(sp):
                sp.dma_start(w[:, :, :], core.dram["router_w"].rearrange("(k p) n -> p k n", p=P)).then_inc(loaded, 16)
                sp.dma_start(b[:, :], core.dram["router_b"].rearrange("a n -> (a n)").partition_broadcast(P)).then_inc(loaded, 16)
                sp.dma_start(iota[:, :], core.dram["iota16"]).then_inc(loaded, 16)
                sp.dma_start(earlier[:, :], core.dram["earlier"]).then_inc(loaded, 16)
                sp.dma_start(table[:, :], core.dram["dispatch"]).then_inc(loaded, 16)
                sp.wait_ge(loaded, 80)

            @block.tensor
            def _(pe):
                pe.wait_ge(loaded, 80)
                for i in range(TT):
                    for k in range(KD):
                        mm = pe.matmul(bank[0][:, i * NR:i * NR + NR], h[:, k, i * P:i * P + P], w[:, k, :], start=k == 0, stop=k == KD - 1)
                mm.then_inc(scored, 1)
                for u in range(2 * TT):
                    i, half = divmod(u, 2)
                    if u >= 4:
                        pe.wait_ge(h_copied, u - 3)
                    for j in range(4):
                        mm = pe.transpose(bank[2 + u % 4][:, j * P:j * P + P], h[:, 4 * half + j, i * P:i * P + P], core.ident[:, :])
                    mm.then_inc(h_turned, 1)
                pe.wait_ge(chosen_done, 1)
                for i in range(TT):
                    for j in range(i + 1):
                        mm = pe.matmul(bank[1][:, i * N_EXPERTS:(i + 1) * N_EXPERTS], earlier[:, :] if j == i else core.ones[:, :],
                                       either[:, j, :], start=j == 0, stop=j == i)
                for j in range(TT):
                    mm = pe.matmul(bank[1][:, TT * N_EXPERTS:(TT + 1) * N_EXPERTS], core.ones[:, :], either[:, j, :],
                                   start=j == 0, stop=j == TT - 1)
                mm.then_inc(ranked, 1)

            @block.scalar
            def _(act):
                act.wait_ge(g_shifted, 1)
                act.activation(ex[:, :, :], ex[:, :, :], ACT.Exp).then_inc(g_raised, 1)
                act.wait_ge(e_shifted, 1)
                act.activation(weight[:, :, 1], weight[:, :, 1], ACT.Exp).then_inc(e_raised, 1)
                for u in range(2 * TT):
                    i, half = divmod(u, 2)
                    act.wait_ge(h_turned, u + 1)
                    act.activation(hN[:, i, half * S:half * S + S], bank[2 + u % 4][:, :], ACT.Copy).then_inc(h_copied, 1)

            @block.vector
            def _(dve):
                step = Steps(dve, step_sem)
                dve.wait_ge(scored, 1)
                dve.wait_ge(loaded, 80)
                step.then(dve.tensor_tensor(lg[:, :, :], bank[0][:, 0:TT * NR].rearrange("p (i n) -> p i n", n=NR), tiled(b[:, :], TT), ALU.add))
                gl = lg[:, :, 0:N_GROUPS]
                step.then(dve.tensor_reduce(top[:, :], gl, AX.X, ALU.max))
                dve.tensor_tensor(ex[:, :, :], gl, repeat(top[:, :], N_GROUPS), ALU.subtract).then_inc(g_shifted, 1)
                step.then(dve.tensor_tensor(hot[:, :, :], gl, repeat(top[:, :], N_GROUPS), ALU.is_equal))
                step.then(dve.tensor_scalar(free[:, :], hot[:, :, 0], -1.0, 1.0, ALU.mult, ALU.add))
                for g in range(1, N_GROUPS):
                    step.then(dve.tensor_tensor(hot[:, :, g], hot[:, :, g], free[:, :], ALU.mult))
                    step.then(dve.tensor_tensor(free[:, :], free[:, :], hot[:, :, g], ALU.subtract))
                el4 = lg[:, :, N_GROUPS:NR].rearrange("p i (g e) -> p i g e", g=N_GROUPS)
                four = [P, TT, N_GROUPS, PER_GROUP]
                hot4 = hot[:, :, :].unsqueeze(3).to_broadcast(four)
                step.then(dve.tensor_tensor(within[:, :, :, :], el4, hot4, ALU.mult))
                step.then(dve.tensor_reduce(el[:, :, :], within[:, :, :, :].rearrange("p i g e -> p i e g"), AX.X, ALU.add))
                for i in range(TT):
                    step(dve.max(best[:, i, :], el[:, i, :]))
                step.done()
                for i in range(TT):
                    step(dve.max_index(at[:, i, :], best[:, i, :], el[:, i, :]))
                dve.tensor_tensor(weight[:, :, 1], best[:, :, 1], best[:, :, 0], ALU.subtract).then_inc(e_shifted, 1)
                step.done()
                step.then(dve.tensor_copy(atf[:, :, :], at[:, :, :]))
                for j in range(2):
                    step.then(dve.tensor_tensor(pick[:, :, :], repeat(atf[:, :, j], PER_GROUP), tiled(iota[:, 0:PER_GROUP], TT), ALU.is_equal))
                    step.then(dve.tensor_tensor(chosen[:, j, :, :].rearrange("p i (g e) -> p i g e", g=N_GROUPS), hot4,
                                                pick[:, :, :].unsqueeze(2).to_broadcast(four), ALU.mult))
                dve.tensor_tensor(either[:, :, :], chosen[:, 0, :, :], chosen[:, 1, :, :], ALU.add).then_inc(chosen_done, 1)
                dve.wait_ge(g_raised, 1)
                step.then(dve.tensor_reduce(gw[:, :], ex[:, :, :], AX.X, ALU.add))
                dve.wait_ge(e_raised, 1)
                step.then(dve.tensor_scalar(weight[:, :, 0], weight[:, :, 1], 1.0, None, ALU.add))
                step.then(dve.tensor_tensor(gw[:, :], gw[:, :], weight[:, :, 0], ALU.mult))
                step.then(dve.reciprocal(weight[:, :, 0], gw[:, :]))
                step.then(dve.tensor_tensor(weight[:, :, 1], weight[:, :, 1], weight[:, :, 0], ALU.mult))
                step(dve.memset(one[:, :], 1.0))
                dve.wait_ge(ranked, 1)
                step(dve.tensor_copy(rank[:, :, :], bank[1][:, 0:TT * N_EXPERTS].rearrange("p (i e) -> p i e", e=N_EXPERTS)))
                step.then(dve.tensor_copy(count[:, :], bank[1][:, TT * N_EXPERTS:(TT + 1) * N_EXPERTS]))
                step.then(dve.tensor_scalar(extra[:, :], count[:, :], float(MOE_T), None, ALU.is_gt))
                for m in range(2, -(-S // MOE_T)):
                    step.then(dve.scalar_tensor_tensor(out=extra[:, :], in0=count[:, :], scalar=float(m * MOE_T), in1=extra[:, :],
                                                       op0=ALU.is_gt, op1=ALU.add))
                step.then(dve.tensor_tensor_scan(ends[:, :], one[:, :], extra[:, :], 0.0, ALU.mult, ALU.add))
                step.then(dve.tensor_tensor(jump[:, :], ends[:, :], extra[:, :], ALU.subtract))
                step.then(dve.scalar_tensor_tensor(out=jump[:, :], in0=jump[:, :], scalar=float(N_EXPERTS - 1), in1=expert_no,
                                                   op0=ALU.add, op1=ALU.subtract))
                step.then(dve.tensor_scalar(beyond[:, :, :], rank[:, :, :], float(MOE_T), None, ALU.is_ge))
                step.then(dve.tensor_tensor(beyond[:, :, :], beyond[:, :, :], tiled(jump[:, :], TT), ALU.mult))
                step.then(dve.tensor_tensor(beyond[:, :, :], beyond[:, :, :], tiled(expert_no, TT), ALU.add))
                step.then(dve.scalar_tensor_tensor(out=rank[:, :, :], in0=beyond[:, :, :], scalar=float(MOE_T), in1=rank[:, :, :],
                                                   op0=ALU.mult, op1=ALU.add))
                for j in range(2):
                    step.then(dve.tensor_tensor(chosen[:, j, :, :], chosen[:, j, :, :], rank[:, :, :], ALU.mult))
                    step.then(dve.tensor_reduce(spot[:, :], chosen[:, j, :, :], AX.X, ALU.add))
                    step.then(dve.tensor_copy(place[:, :, j], spot[:, :]))
                step.then(dve.tensor_tensor(whose[:, :, :], tiled(ends[:, :], MOE_EXTRA), repeat(extra_no, N_EXPERTS), ALU.is_le))
                step(dve.tensor_copy(rowf[:, 0:N_EXPERTS], own_rows[:, 0:N_EXPERTS]))
                step.then(dve.tensor_reduce(rowf[:, N_EXPERTS:], whose[:, :, :], AX.X, ALU.add))
                step.then(dve.tensor_scalar(rowf[:, N_EXPERTS:], rowf[:, N_EXPERTS:], float(N_EXPERTS - 1), float(P), ALU.min, ALU.mult))
                step.then(dve.tensor_tensor(rowf[:, N_EXPERTS:], rowf[:, N_EXPERTS:], own_rows[:, N_EXPERTS:], ALU.add))
                step.then(dve.tensor_copy(expert_row[:, :], rowf[:, :]))


def stage_moe(core, h):
    nc = core.nc
    with ExitStack() as st:
        place = core.sb("place", [P, TT, 2], U32, ctx=st)
        weight = core.sb("expert_weight", [P, TT, 2], ctx=st)
        expert_row = core.sb("expert_row", [P, MOE_TILES], U32, ctx=st)
        with ExitStack() as s2:
            hN = core.sb("h_rows", [P, TT, D], ctx=s2)
            stage_route(core, h, hN, place, weight, expert_row)
            spot = core.sb("spot_now", [P, TT, 2, 1], U32, ctx=s2)
            spotted, dispatched = core.sems(s2, "spotted", "rows_dispatched")
            with nc.Block() as block:
                @block.gpsimd
                def _(pool):
                    pool.tensor_copy(spot[:, :, :, 0], place[:, :, :]).then_inc(spotted, 1)
                    pool.wait_ge(spotted, 1)
                    for i in range(TT):
                        for j in range(2):
                            pool.indirect_dma_start(core.dispatched, bass.IndirectOffsetOnAxis(spot[:, i, j, :], 0),
                                                    hN[:, i, :], None).then_inc(dispatched, 16)
                    pool.wait_ge(dispatched, 2 * TT * 16)
        stage_experts(core, expert_row)
        stage_combine(core, place, weight)


def stage_experts(core, expert_row):
    nc, bank, T = core.nc, core.bank, MOE_T
    NF = D_EXPERT // P
    HALF = KD // 2
    TURNS = MOE_TILES // MOE_RING
    with ExitStack() as st:
        weights = core.sb("expert_w", [P, MOE_RING, 3 * KD * D_EXPERT], ctx=st)
        row = core.sb("expert_row_now", [P, MOE_RING], U32, ctx=st)
        tokens = core.sb("tile_tokens", [T, MOE_RING, D], ctx=st)
        tokT = core.sb("tile_turned", [P, MOE_RING, KD, T], ctx=st)
        hid = core.sb("hidden", [P, MOE_RING, NF, T], ctx=st)
        y = core.sb("tile_y", [T, MOE_RING, D], ctx=st)
        part = lambda s, i: weights[:, s, i * KD * D_EXPERT:(i + 1) * KD * D_EXPERT]
        gate_w = lambda s: part(s, 0).rearrange("p (k n) -> p k n", k=KD)
        up_w = lambda s: part(s, 1).rearrange("p (k n) -> p k n", k=KD)
        down_w = lambda s: part(s, 2).rearrange("p (f n) -> p f n", f=NF)
        turned_bank, hidden_bank, y_bank = bank[0:2], bank[2:5], bank[5:7]
        names = ["row_ready", "pool_gate", "tile_turned", "turned_copied", "gate_full", "silu_done", "hidden_ready", "y_full", "y_copied"]
        row_ready, pool_gate, tile_turned, turned_copied, gate_full, silu_done, hidden_ready, y_full, y_copied = core.sems(st, *names)
        w_arrived = [core.ctx.enter_context(nc.semaphore(f"expert_arrived{s}")) for s in range(MOE_RING)]
        t_arrived = [core.ctx.enter_context(nc.semaphore(f"tokens_arrived{s}")) for s in range(MOE_RING)]
        stored = [core.ctx.enter_context(nc.semaphore(f"tile_stored{s}")) for s in range(MOE_RING)]
        core.clear(w_arrived + t_arrived + stored)
        with nc.Block() as block:
            @block.vector
            def _(dve):
                dve.sem_inc(y_full, MOE_RING)
                dve.sem_inc(y_copied, 2)
                for s in range(MOE_RING):
                    dve.sem_inc(stored[s], 16)
        with nc.Block() as block:
            @block.gpsimd
            def _(pool):
                with pool.Fori(0, TURNS) as i:
                    for s in range(MOE_RING):
                        pool.wait_ge(y_full, i * MOE_RING + (s + 1))
                        pool.sem_inc(pool_gate, 1)
                        pool.tensor_copy(row[:, s:s + 1], expert_row[:, bass.ds(i * MOE_RING + s, 1)]).then_inc(row_ready, 1)
                        pool.wait_ge(row_ready, i * MOE_RING + (s + 1))
                        pool.sem_inc(pool_gate, 1)
                        pool.indirect_dma_start(weights[:, s, :], None, core.dram["experts"],
                                                bass.IndirectOffsetOnAxis(row[:, s:s + 1], 0)).then_inc(w_arrived[s], 16)
                pool.wait_ge(pool_gate, 2 * MOE_TILES)

            @block.sync
            def _(sp):
                for s in range(MOE_RING):
                    sp.dma_start(tokens[:, s, :], core.dispatched[s * T:(s + 1) * T, :]).then_inc(t_arrived[s], 16)
                with sp.Fori(0, TURNS) as i:
                    for s in range(MOE_RING):
                        sp.wait_ge(y_copied, i * (2 * MOE_RING) + (2 * s + 4))
                        sp.dma_start(core.answered[bass.ds((i * MOE_RING + s) * T, T), :], y[:, s, :]).then_inc(stored[s], 16)
                        sp.wait_ge(tile_turned, i * MOE_RING + (s + 1))
                        sp.dma_start(tokens[:, s, :], core.dispatched[bass.ds((i * MOE_RING + (s + MOE_RING)) * T, T), :]).then_inc(t_arrived[s], 16)
                for s in range(MOE_RING):
                    sp.wait_ge(stored[s], 16 * (TURNS + 1))
                    sp.wait_ge(t_arrived[s], 16 * (TURNS + 1))

            @block.tensor
            def _(pe):
                def turn(s):
                    for k in range(KD):
                        mm = pe.transpose(turned_bank[k // HALF][:, (k % HALF) * T:(k % HALF + 1) * T], tokens[:, s, k * P:(k + 1) * P],
                                          core.ident[0:T, 0:T])
                    mm.then_inc(tile_turned, 1)

                pe.wait_ge(t_arrived[0], 16)
                turn(0)
                with pe.Fori(0, TURNS) as i:
                    for s in range(MOE_RING):
                        pe.wait_ge(w_arrived[s], i * 16 + 16)
                        pe.wait_ge(turned_copied, i * (2 * MOE_RING) + (2 * s + 2))
                        for j, w in ((1, up_w(s)), (0, gate_w(s))):
                            for f in range(NF):
                                at = (NF * j + f) * T
                                for k in range(KD):
                                    mm = pe.matmul(hidden_bank[s][:, at:at + T], w[:, k, f * P:f * P + P], tokT[:, s, k, :],
                                                   start=k == 0, stop=k == KD - 1)
                        mm.then_inc(gate_full, 1)
                        after = (s + 1) % MOE_RING
                        pe.wait_ge(t_arrived[after], i * 16 + (32 if after == 0 else 16))
                        turn(after)
                        pe.wait_ge(hidden_ready, i * MOE_RING + (s + 1))
                        pe.wait_ge(y_copied, i * (2 * MOE_RING) + (2 * s + 2))
                        for half in range(2):
                            for f in range(NF):
                                mm = pe.matmul(y_bank[half][0:T, :], hid[:, s, f, :], down_w(s)[:, f, half * S:half * S + S],
                                               start=f == 0, stop=f == NF - 1)
                        mm.then_inc(y_full, 1)

            @block.scalar
            def _(act):
                def copy(s):
                    for half in range(2):
                        act.activation(tokT[:, s, half * HALF:(half + 1) * HALF, :],
                                       turned_bank[half][:, 0:HALF * T].rearrange("p (k t) -> p k t", t=T), ACT.Copy).then_inc(turned_copied, 1)

                act.wait_ge(tile_turned, 1)
                copy(0)
                with act.Fori(0, TURNS) as i:
                    for s in range(MOE_RING):
                        act.wait_ge(gate_full, i * MOE_RING + (s + 1))
                        act.activation(hid[:, s, :, :], hidden_bank[s][:, 0:NF * T].rearrange("p (f t) -> p f t", t=T), ACT.Silu).then_inc(silu_done, 1)
                        act.wait_ge(tile_turned, i * MOE_RING + (s + 2))
                        copy((s + 1) % MOE_RING)

            @block.vector
            def _(dve):
                with dve.Fori(0, TURNS) as i:
                    for s in range(MOE_RING):
                        dve.wait_ge(silu_done, i * MOE_RING + (s + 1))
                        dve.tensor_tensor(hid[:, s, :, :], hid[:, s, :, :],
                                          hidden_bank[s][:, NF * T:2 * NF * T].rearrange("p (f t) -> p f t", t=T), ALU.mult).then_inc(hidden_ready, 1)
                        dve.wait_ge(stored[s], i * 16 + 16)
                        dve.wait_ge(y_full, i * MOE_RING + (s + 1 + MOE_RING))
                        for half in range(2):
                            dve.tensor_copy(y[:, s, half * S:half * S + S], y_bank[half][0:T, :]).then_inc(y_copied, 1)


def stage_combine(core, place, weight):
    nc, bank, x = core.nc, core.bank, core.x
    gate = core.mod[:, 88:96]
    with ExitStack() as st:
        rows = core.sb("answers", [P, TT, 2, D], ctx=st)
        spot = core.sb("spot_then", [P, TT, 2, 1], U32, ctx=st)
        spotted, weighed, y_turned, x_added = core.sems(st, "spotted", "weighed", "y_turned", "x_added")
        arrived = [core.ctx.enter_context(nc.semaphore(f"answers_arrived{i}")) for i in range(TT)]
        core.clear(arrived)
        with nc.Block() as block:
            @block.gpsimd
            def _(pool):
                pool.tensor_copy(spot[:, :, :, 0], place[:, :, :]).then_inc(spotted, 1)
                pool.wait_ge(spotted, 1)
                for i in range(TT):
                    for j in range(2):
                        pool.indirect_dma_start(rows[:, i, j, :], None, core.answered,
                                                bass.IndirectOffsetOnAxis(spot[:, i, j, :], 0)).then_inc(arrived[i], 16)

            @block.vector
            def _(dve):
                for i in range(TT):
                    dve.wait_ge(arrived[i], 32)
                    dve.tensor_scalar(rows[:, i, 0, :], rows[:, i, 0, :], weight[:, i, 0:1], None, ALU.mult).then_inc(weighed, 1)
                    dve.wait_ge(weighed, 2 * i + 1)
                    dve.scalar_tensor_tensor(out=rows[:, i, 0, :], in0=rows[:, i, 1, :], scalar=weight[:, i, 1:2], in1=rows[:, i, 0, :],
                                             op0=ALU.mult, op1=ALU.add).then_inc(weighed, 1)
                    for k in range(KD):
                        if k % 4 == 0:
                            dve.wait_ge(y_turned, 2 * i + k // 4 + 1)
                        xk = x[:, k, i * P:i * P + P]
                        dve.scalar_tensor_tensor(out=xk, in0=bank[(2 * i + k // 4) % 4][:, (k % 4) * P:(k % 4) * P + P],
                                                 scalar=gate[:, k:k + 1], in1=xk, op0=ALU.mult, op1=ALU.add).then_inc(x_added, 1)

            @block.tensor
            def _(pe):
                for i in range(TT):
                    pe.wait_ge(weighed, 2 * i + 2)
                    for half in range(2):
                        if i >= 2:
                            pe.wait_ge(x_added, KD * (i - 2) + 4 * half + 4)
                        for k in range(4):
                            mm = pe.transpose(bank[(2 * i + half) % 4][:, k * P:k * P + P],
                                              rows[:, i, 0, (4 * half + k) * P:(4 * half + k + 1) * P], core.ident[:, :])
                        mm.then_inc(y_turned, 1)


def stage_output(core, buf, out):
    nc = core.nc
    stage_norm(core, buf, core.col("norm_final_2", 0, 8), None)
    stored = core.sems(core.ctx, "stored")
    with nc.Block() as block:
        @block.sync
        def _(sp):
            sp.dma_start(out.rearrange("(k p) t -> p k t", p=P), buf[:, :, :]).then_inc(stored, 16)
            sp.wait_ge(stored, 16)


def kernel(**inputs):
    import concourse.bacc as bacc
    from concourse.bass_utils import run_bass_kernel_spmd

    arrays = {f"in_{k}": a for k, a in inputs_to_dram(inputs).items()}
    nc = bacc.Bacc("TRN2", target_bir_lowering=False, num_devices=1)
    dram = {k[3:]: nc.dram_tensor(k, a.shape, mybir.dt.from_np(a.dtype), kind="ExternalInput").ap() for k, a in arrays.items()}
    out = nc.dram_tensor("outT", (D, S), F32, kind="ExternalOutput").ap()
    build(nc, dram, out)
    result = run_bass_kernel_spmd(nc, [arrays], core_ids=[0])
    return np.ascontiguousarray(result.results[0]["outT"].T)[None]
```

```python
from contextlib import ExitStack
import math

import numpy as np

import concourse.bass as bass
from concourse import mybir

ALU = mybir.AluOpType
ACT = mybir.ActivationFunctionType
AX = mybir.AxisListType
F32 = mybir.dt.float32
F32R = mybir.dt.float32r
I32 = mybir.dt.int32
U32 = mybir.dt.uint32

P = 128
S = 512
TT = S // P
D = 1024
KD = D // P
HD = 64
NEG_LOG_DECAY = math.exp(-0.5)
N_KEYS, PEER_HEADS, TOPK = 128, 8, 16
HK = PEER_HEADS * TOPK
N_EXPERTS, N_GROUPS, PER_GROUP, D_EXPERT = 32, 4, 8, 256
MOE_T = 94
MOE_EXTRA = 2 * S // MOE_T
MOE_TILES = N_EXPERTS + MOE_EXTRA
MOE_RING = 3

VEC_COLS = [("c", 8), ("c_2", 8), ("ada_b", 48), ("b_ada_2", 48), ("norm1_g", 8), ("norm2_g", 8),
            ("norm_mix_2", 8), ("norm_ffn_2", 8), ("norm_final_2", 8), ("mu_prev", 14), ("mu_next", 14),
            ("q_norm_g", 1), ("k_norm_g", 1), ("w_decay0", 8), ("a_gate0", 8), ("k_k", 4), ("k_a", 4),
            ("r_k", 4), ("lnx_g", 4), ("lnx_b", 4), ("ret_norm_2", 3), ("hgrn_norm_2", 3),
            ("hgrn_lb_logits_2", 3), ("gla_ba_2", 1), ("gla_norm_2", 2)]
VEC_AT, _n = {}, 0
for _name, _k in VEC_COLS:
    VEC_AT[_name] = (_n, _k)
    _n += _k
NVEC = _n

RET_HEADS = 6
LEVELS = [1, 2, 4, 8, 16, 32, 64]


def constant_tables():
    r = np.arange(P)[:, None]
    c = np.arange(P)[None, :]
    eye = (r == c).astype(np.float32)
    out = {"ident": eye, "ones": np.ones((P, P), np.float32),
           "headones": (r // HD == c // HD).astype(np.float32)}
    t = np.arange(S)[None, :]
    half = {m: ((r // (2 * m) == c // (2 * m)) & (r % (2 * m) < m) & (c % (2 * m) >= m)) for m in LEVELS}
    out["rw_fwd"] = np.stack([r < c, half[1].T, half[1] | (r == c)]
                             + [half[m].T | (r == c) for m in LEVELS[1:]] + [r <= c], 1).astype(np.float32)
    out["rw_rev"] = np.stack([r > c, half[1], half[1].T | (r == c)]
                             + [half[m] | (r == c) for m in LEVELS[1:]] + [r >= c], 1).astype(np.float32)
    out["halves"] = np.stack([half[m] for m in LEVELS], 1).astype(np.uint32)
    tq = np.arange(S)[:, None]
    dist = np.abs(tq - t)
    count = sum(((dist % d == 0) & (dist <= w // 2)).astype(np.float32) for w, d in ((128, 1), (512, 4), (2048, 16)))
    masked = np.where(count > 0, dist, 1e30).astype(np.float32)
    out["dist"] = np.ascontiguousarray(masked.reshape(TT, P, S).transpose(1, 0, 2))
    out["count"] = np.ascontiguousarray(count.reshape(TT, P, S).transpose(1, 0, 2)).astype(np.float32)
    out["slopes"] = np.broadcast_to(-np.exp2(-np.arange(1, 9, dtype=np.float32)), (P, 8)).copy()
    restart = np.ones((P, S), np.float32)
    restart[:, ::P] = 0.0
    out["restart"] = restart
    gamma = 1.0 - np.exp2(-5.0 - np.arange(RET_HEADS))
    rel = (t - np.arange(P)[:, None]).astype(np.float64)
    out["ret_decay"] = np.stack([np.where(rel >= 0, g ** np.maximum(rel, 0), 0.0) * HD ** -0.5 for g in gamma],
                                1).astype(np.float32)
    rot = np.zeros((P, P), np.float32)
    for h in range(P // HD):
        for i in range(HD // 2):
            rot[h * HD + HD // 2 + i, h * HD + i] = -1.0
            rot[h * HD + i, h * HD + HD // 2 + i] = 1.0
    out["rot"] = rot
    inv = np.float32(10000.0) ** (-np.arange(0, HD, 2, dtype=np.float32) / np.float32(HD))
    out["inv_freq"] = np.tile(inv.astype(np.float32), P // (HD // 2))[:, None].copy()
    out["iota16"] = np.broadcast_to(np.arange(16, dtype=np.float32), (P, 16)).copy()
    out["earlier"] = (r < c).astype(np.float32)
    n = np.concatenate([np.arange(N_EXPERTS), np.arange(MOE_EXTRA)])
    own = np.arange(N_EXPERTS)[None, :] * P + np.arange(P)[:, None]
    out["dispatch"] = np.concatenate([np.broadcast_to(n, (P, len(n))), own, np.broadcast_to(r, (P, MOE_EXTRA))],
                                     1).astype(np.float32)
    return out


class Core:

    def __init__(self, nc, dram, ctx):
        self.nc, self.dram, self.ctx = nc, dram, ctx
        self.names = {}
        self.bank = [ctx.enter_context(nc.psum_tensor(f"bank{i}", [P, S], F32)) for i in range(8)]

    def sb(self, name, shape, dt=F32, ctx=None):
        n = self.names[name] = self.names.get(name, 0) + 1
        name = name if n == 1 else f"{name}_{n}"
        return (ctx or self.ctx).enter_context(self.nc.sbuf_tensor(name, shape, dt))

    def sems(self, ctx, *names):
        found = [ctx.enter_context(self.nc.semaphore(n)) for n in names]
        self.clear(found)
        return found if len(found) > 1 else found[0]

    def clear(self, sems):
        with self.nc.Block() as block:
            @block.sync
            def _(sp):
                for s in sems:
                    sp.sem_clear(s)

    def col(self, name, i=0, n=1):
        at = VEC_AT[name][0]
        return self.vec[:, at + i:at + i + n] if isinstance(i, int) else self.vec[:, bass.ds(i + at, n)]


class Steps:

    def __init__(self, eng, sem):
        self.eng, self.sem, self.n = eng, sem, 0

    def __call__(self, ins):
        self.n += 1
        ins.then_inc(self.sem, 1)
        return ins

    def done(self):
        self.eng.wait_ge(self.sem, self.n)

    def then(self, ins):
        self(ins)
        self.done()


RING = 3


class WeightRing:

    def __init__(self, core, items):
        self.core, self.items, self.issued = core, items, 0
        self.slots = core.sb("weight_slots", [P, RING, KD * S])
        self.loaded = [core.ctx.enter_context(core.nc.semaphore(f"weight_loaded{i}")) for i in range(RING)]
        self.used = core.ctx.enter_context(core.nc.semaphore("weight_used"))

    def view(self, i):
        n = self.items[i].shape[1]
        return self.slots[:, i % RING, 0:KD * n].rearrange("p (k n) -> p k n", k=KD)

    def load(self, sp, upto):
        while self.issued < min(upto, len(self.items)):
            i = self.issued
            if i >= RING:
                sp.wait_ge(self.used, i - RING + 1)
            sp.dma_start(self.view(i), self.items[i].rearrange("(k p) n -> p k n", p=P)).then_inc(self.loaded[i % RING], 16)
            self.issued += 1

    def arrived(self, pe, i):
        pe.wait_ge(self.loaded[i % RING], 16 * (i // RING + 1))


def repeat(ap, n):
    return ap.unsqueeze(2).to_broadcast([ap.shape[0], ap.shape[1], n])


def tiled(ap, n):
    return ap.unsqueeze(1).to_broadcast([ap.shape[0], n, ap.shape[1]])


def allocate(core):
    nc = core.nc
    core.x = core.sb("x", [P, KD, S])
    core.vec = core.sb("vec", [P, NVEC])
    core.ident = core.sb("ident", [P, P])
    core.ones = core.sb("ones", [P, P])
    core.headones = core.sb("headones", [P, P])
    core.cond = core.sb("cond", [P, 2 * KD])
    core.mod = core.sb("mod", [P, 12 * KD])
    core.gain = core.sb("gain", [P, 4 * KD])
    n_rows = -(-(MOE_TILES + MOE_RING) * MOE_T // P) * P
    core.dispatched = nc.dram_tensor("dispatched", (n_rows, D), F32, kind="Internal").ap()
    core.answered = nc.dram_tensor("answered", (MOE_TILES * MOE_T, D), F32, kind="Internal").ap()


def stage_load(core, m):
    nc = core.nc
    with ExitStack() as st:
        in_loaded = core.sems(st, "in_loaded")
        with nc.Block() as block:
            @block.sync
            def _(sp):
                sp.dma_start(core.vec[:, :], core.dram["vec"]).then_inc(in_loaded, 16)
                m.load(sp, m.SLOTS)

            @block.scalar
            def _(act):
                act.dma_start(core.ident[:, :], core.dram["ident"]).then_inc(in_loaded, 16)
                act.dma_start(core.ones[:, :], core.dram["ones"]).then_inc(in_loaded, 16)
                act.dma_start(core.headones[:, :], core.dram["headones"]).then_inc(in_loaded, 16)
                act.wait_ge(in_loaded, 64)
                act.activation(core.cond[:, :], core.vec[:, 0:2 * KD], ACT.Silu)


class Modulation:
    SLOTS, SUMS, BANK = 3, 3, 5
    ITEMS, NEEDED = 24, 4

    def __init__(self, core, st):
        self.core, self.issued = core, 0
        self.w = core.sb("mod_w", [P, self.SLOTS, KD, S], ctx=st)
        self.acc = core.sb("mod_acc", [P, self.SUMS, 2, S], ctx=st)
        self.weighed, self.acc_ready, self.summed, self.added = core.sems(st, "mod_weighed", "mod_acc_ready", "mod_summed", "mod_added")
        self.loaded = [core.ctx.enter_context(core.nc.semaphore(f"mod_loaded{i}")) for i in range(self.SLOTS)]
        self.parts_added = 0

    def load(self, eng, upto):
        for n in range(self.issued, min(upto, self.ITEMS)):
            src = self.core.dram["ada_w" if n < 12 else "ada_w2"][:, n % 12 * S:(n % 12 + 1) * S]
            if n >= self.SLOTS:
                eng.wait_ge(self.acc_ready, n - self.SLOTS + 1)
            eng.dma_start(self.w[:, n % self.SLOTS, :, :], src.rearrange("(k p) n -> p k n", p=P)).then_inc(self.loaded[n % self.SLOTS], 16)
            self.issued = n + 1

    def on_vector(self, dve, n):
        dve.wait_ge(self.loaded[n % self.SLOTS], 16 * (n // self.SLOTS + 1))
        if n >= self.SUMS:
            dve.wait_ge(self.summed, n - self.SUMS + 1)
        acc = self.acc[:, n % self.SUMS, :, :]
        for k in range(KD):
            a, w = acc[:, k % 2, :], self.w[:, n % self.SLOTS, k, :]
            c = self.core.cond[:, n // 12 * KD + k:n // 12 * KD + k + 1]
            if k < 2:
                dve.tensor_scalar(a, w, c, None, ALU.mult).then_inc(self.weighed, 1)
            else:
                dve.wait_ge(self.weighed, KD * n + k - 1)
                dve.scalar_tensor_tensor(out=a, in0=w, scalar=c, in1=a, op0=ALU.mult, op1=ALU.add).then_inc(self.weighed, 1)
        dve.wait_ge(self.weighed, KD * (n + 1))
        dve.tensor_tensor(acc[:, 0, :], acc[:, 0, :], acc[:, 1, :], ALU.add).then_inc(self.acc_ready, 1)

    def on_tensor(self, pe, n):
        pe.wait_ge(self.acc_ready, n + 1)
        for f in range(4):
            mm = pe.matmul(self.core.bank[self.BANK][:, 4 * n + f:4 * n + f + 1], self.acc[:, n % self.SUMS, 0, f * P:f * P + P],
                           self.core.ones[:, 0:1], start=True, stop=True)
        mm.then_inc(self.summed, 1)

    def finish(self, dve, lo, hi, norms):
        core = self.core
        dve.wait_ge(self.summed, hi)
        at = VEC_AT["ada_b"][0]
        dve.tensor_tensor(core.mod[:, 4 * lo:4 * hi], core.bank[self.BANK][:, 4 * lo:4 * hi], core.vec[:, at + 4 * lo:at + 4 * hi],
                          ALU.add).then_inc(self.added, 1)
        self.parts_added += 1
        dve.wait_ge(self.added, self.parts_added)
        for j in norms:
            scale = 48 * (j // 2) + 24 * (j % 2) + 8
            g = ("norm1_g", "norm2_g", "norm_mix_2", "norm_ffn_2")[j]
            dve.scalar_tensor_tensor(out=core.gain[:, j * KD:(j + 1) * KD], in0=core.mod[:, scale:scale + KD], scalar=1.0,
                                     in1=core.col(g, 0, KD), op0=ALU.add, op1=ALU.mult)


def stage_modulation(core, m):
    nc = core.nc
    x_loaded = core.ctx.enter_context(nc.semaphore("x_loaded"))
    with nc.Block() as block:
        @block.sync
        def _(sp):
            m.load(sp, m.NEEDED)
            sp.dma_start(core.x[:, :, :], core.dram["xT"].rearrange("(k p) t -> p k t", p=P)).then_inc(x_loaded, 16)
            core.ring.load(sp, 1)
            m.load(sp, m.NEEDED + m.SLOTS)
            core.ring.load(sp, RING)
            sp.wait_ge(x_loaded, 16)

        @block.tensor
        def _(pe):
            for n in range(m.NEEDED):
                m.on_tensor(pe, n)

        @block.vector
        def _(dve):
            for n in range(m.NEEDED):
                m.on_vector(dve, n)
            m.finish(dve, 0, m.NEEDED, [0])


def stage_norm(core, out, gain, shift):
    nc, x, total = core.nc, core.x, core.bank[0]
    with ExitStack() as st:
        rms = core.sb("rms", [P, S], ctx=st)
        squared, summed, rooted, scaled, shifted = core.sems(
            st, "squared", "summed", "rooted", "scaled", "shifted")
        with nc.Block() as block:
            @block.scalar
            def _(act):
                for k in range(KD):
                    act.activation(out[:, k, :], x[:, k, :], ACT.Square).then_inc(squared, 1)
                act.wait_ge(summed, 1)
                act.activation(rms[:, :], total[:, :], ACT.Sqrt, scale=1.0 / D, bias=1e-6).then_inc(rooted, 1)
                if shift is not None:
                    for k in range(KD):
                        act.wait_ge(scaled, k + 2)
                        act.activation(out[:, k, :], out[:, k, :], ACT.Identity, bias=shift[:, k:k + 1]).then_inc(shifted, 1)

            @block.tensor
            def _(pe):
                for k in range(KD):
                    pe.wait_ge(squared, k + 1)
                    mm = pe.matmul(total[:, :], core.ones[:, :], out[:, k, :], start=k == 0, stop=k == KD - 1)
                mm.then_inc(summed, 1)

            @block.vector
            def _(dve):
                dve.wait_ge(rooted, 1)
                dve.reciprocal(rms[:, :], rms[:, :]).then_inc(scaled, 1)
                dve.wait_ge(scaled, 1)
                for k in range(KD):
                    dve.scalar_tensor_tensor(out=out[:, k, :], in0=x[:, k, :], scalar=gain[:, k:k + 1], in1=rms[:, :],
                                             op0=ALU.mult, op1=ALU.mult).then_inc(scaled, 1)


def tiles_of(core, first, plan):
    found = []
    for i, (kind, evac) in enumerate(plan):
        n = core.ring.items[first + i].shape[1]
        if kind == "T":
            found.append((kind, [(f, min(P, n - f * P), S, evac[f]) for f in range(-(-n // P))]))
        else:
            found.append((kind, [(t, P, n, evac) for t in range(TT)]))
    return found


def stage_project_first(core, first, plan, rhs, m):
    nc, ring = core.nc, core.ring
    units = [(i, kind) + tile for i, (kind, tiles) in enumerate(tiles_of(core, first, plan)) for tile in tiles]
    NB, LAG = 5, 2
    with ExitStack() as st:
        bank_full, emptied = core.sems(st, "bank_full", "act_emptied")
        with nc.Block() as block:
            @block.sync
            def _(sp):
                ring.load(sp, first + len(plan) + RING)

            @block.tensor
            def _(pe):
                for u, (i, kind, f, rows, width, _) in enumerate(units):
                    ring.arrived(pe, first + i)
                    if u >= NB:
                        pe.wait_ge(emptied, u - NB + 1)
                    w = ring.view(first + i)
                    for k in range(KD):
                        if kind == "T":
                            a, b = w[:, k, f * P:f * P + rows], rhs[:, k, :]
                        else:
                            a, b = rhs[:, k, f * P:f * P + P], w[:, k, :]
                        mm = pe.matmul(core.bank[u % NB][0:rows, 0:width], a, b, start=k == 0, stop=k == KD - 1)
                    mm.then_inc(bank_full, 1)
                    if u + 1 == len(units) or units[u + 1][0] != i:
                        pe.wait_ge(bank_full, u + 1)
                        pe.sem_inc(ring.used, 1)
                    if u >= LAG:
                        m.on_tensor(pe, m.NEEDED + u - LAG)
                for u in range(len(units) - LAG, len(units)):
                    m.on_tensor(pe, m.NEEDED + u)

            @block.scalar
            def _(act):
                for u, (_, kind, f, rows, width, evac) in enumerate(units):
                    act.wait_ge(bank_full, u + 1)
                    evac(act, core.bank[u % NB][0:rows, 0:width], f).then_inc(emptied, 1)
                    m.load(act, m.NEEDED + u + 1 + m.SLOTS)

            @block.vector
            def _(dve):
                for u in range(len(units)):
                    m.on_vector(dve, m.NEEDED + u)


def stage_project(core, first, plan, rhs, only_dve=False):
    nc, ring = core.nc, core.ring
    items = tiles_of(core, first, plan)
    CH = 4
    BANKS = 4
    on_act = lambda f: f % 2 == 0 and not only_dve
    n_act = [sum(on_act(t[0]) for t in tiles) for _, tiles in items]
    n_dve = [len(tiles) - n for (_, tiles), n in zip(items, n_act)]
    with ExitStack() as st:
        r_hi, r_lo = [core.sb(n, [P, KD, S], F32R, ctx=st) for n in ("rhs_hi", "rhs_lo")]
        w_hi, w_lo = [core.sb(n, [P, CH, S], F32R, ctx=st) for n in ("w_hi", "w_lo")]
        r_upper, r_split, w_upper, w_split, chunk_used, act_emptied, dve_emptied = core.sems(
            st, "r_upper", "r_split", "w_upper", "w_split", "chunk_used", "act_emptied", "dve_emptied")

        def evacuate(eng, i, mine, emptied):
            eng.wait_ge(chunk_used, (i + 1) * KD)
            for f, rows, width, evac in items[i][1]:
                if mine(f):
                    evac(eng, core.bank[i % 2 * BANKS + f][0:rows, 0:width], f).then_inc(emptied, 1)

        def by_chunk(eng, split, mine, emptied):
            for i in range(len(items)):
                for k in range(KD):
                    if k == CH and i >= 1:
                        evacuate(eng, i - 1, mine, emptied)
                    split(i, k)
            evacuate(eng, len(items) - 1, mine, emptied)

        with nc.Block() as block:
            @block.sync
            def _(sp):
                ring.load(sp, first + len(plan) + RING)

            @block.scalar
            def _(act):
                def upper(i, k):
                    c, w = i * KD + k, ring.view(first + i)
                    if i == 0:
                        act.activation(r_hi[:, k, :], rhs[:, k, :], ACT.Copy).then_inc(r_upper, 1)
                    if k == 0:
                        ring.arrived(act, first + i)
                    if c >= CH:
                        act.wait_ge(chunk_used, c - CH + 1)
                    act.activation(w_hi[:, c % CH, 0:w.shape[2]], w[:, k, :], ACT.Copy).then_inc(w_upper, 1)
                by_chunk(act, upper, on_act, act_emptied)

            @block.vector
            def _(dve):
                def lower(i, k):
                    c, w = i * KD + k, ring.view(first + i)
                    dve.wait_ge(w_upper, c + 1)
                    dve.tensor_tensor(w_lo[:, c % CH, 0:w.shape[2]], w[:, k, :], w_hi[:, c % CH, 0:w.shape[2]].bitcast(F32),
                                      ALU.subtract).then_inc(w_split, 1)
                by_chunk(dve, lower, lambda f: not on_act(f), dve_emptied)

            @block.gpsimd
            def _(pool):
                for k in range(KD):
                    pool.wait_ge(r_upper, k + 1)
                    pool.tensor_tensor(r_lo[:, k, :], rhs[:, k, :], r_hi[:, k, :].bitcast(F32), ALU.subtract).then_inc(r_split, 1)

            @block.tensor
            def _(pe):
                for i, (kind, tiles) in enumerate(items):
                    if i >= 2:
                        if n_act[i - 2]:
                            pe.wait_ge(act_emptied, sum(n_act[:i - 1]))
                        pe.wait_ge(dve_emptied, sum(n_dve[:i - 1]))
                    for k in range(KD):
                        c = i * KD + k
                        if i == 0:
                            pe.wait_ge(r_split, k + 1)
                        pe.wait_ge(w_split, c + 1)
                        if k == KD - 1:
                            pe.sem_inc(ring.used, 1)
                        for f, rows, width, _ in tiles:
                            out = core.bank[i % 2 * BANKS + f][0:rows, 0:width]
                            for j, (w, r) in enumerate(((w_lo, r_hi), (w_hi, r_lo), (w_hi, r_hi))):
                                if kind == "T":
                                    a, b = w[:, c % CH, f * P:f * P + rows], r[:, k, :]
                                else:
                                    a, b = r[:, k, f * P:f * P + P], w[:, c % CH, 0:width]
                                mm = pe.matmul(out, a, b, start=k == 0 and j == 0, stop=k == KD - 1 and j == 2)
                        mm.then_inc(chunk_used, 1)


def copy_to(dest):
    def evac(eng, psum, f):
        d = dest(f)
        if eng.engine == mybir.EngineType.Activation:
            return eng.activation(d, psum, ACT.Copy)
        return eng.tensor_copy(d, psum)
    return evac


def stage_attention(core, qk, v, att):
    nc = core.nc
    with ExitStack() as st:
        dist = core.sb("dist", [P, TT, S], ctx=st)
        count = core.sb("count", [P, TT, S], ctx=st)
        slopes = core.sb("slopes", [P, 8], ctx=st)
        qn = core.sb("q_heads", [P, 2, S], ctx=st)
        kn = core.sb("k_pair", [P, S], ctx=st)
        vs = core.sb("v_pair", [P, TT, P], ctx=st)
        score = core.sb("score", [P, 4, S], ctx=st)
        prob = core.sb("prob", [P, 2, S], ctx=st)
        diag = core.sb("diag", [P, 2, P], ctx=st)
        slope = core.sb("slope", [P, 2], ctx=st)
        top = core.sb("top", [P, 8], ctx=st)
        den = core.sb("den", [P, 8], ctx=st)
        probT = core.sb("probT", [P, 2, TT, S], ctx=st)
        tables, slots_filled = core.sems(st, "att_tables", "slots_filled")
        names = ("q_staged", "k_staged", "v_staged", "slope_staged", "scored", "biased", "topped",
                 "raised", "counted", "inverse", "scaled", "turned", "copied", "mixed", "stored")
        sems = core.sems(st, *names)
        (q_staged, k_staged, v_staged, slope_staged, scored, biased, topped, raised, counted, inverse,
         scaled, turned, copied, mixed, stored) = sems
        with nc.Block() as block:
            @block.sync
            def _(sp):
                sp.dma_start(dist[:, :, :], core.dram["dist"]).then_inc(tables, 16)
                sp.dma_start(count[:, :, :], core.dram["count"]).then_inc(tables, 16)
                sp.dma_start(slopes[:, :], core.dram["slopes"]).then_inc(tables, 16)
                rows = core.dispatched.rearrange("(n p) d -> p n d", p=P)
                for n in range(0, rows.shape[1], KD // 2):
                    m = min(KD // 2, rows.shape[1] - n)
                    sp.dma_start(rows[:, n:n + m, :], core.x[:, 0:2 * m, :].rearrange("p k t -> p (k t)").rearrange("p (n d) -> p n d", d=D)).then_inc(slots_filled, 16)
                sp.wait_ge(tables, 48)
        n_fills = -(-(core.dispatched.shape[0] // P) // (KD // 2))
        UNITS = [(h, i) for h in range(2) for i in range(TT)]
        with nc.Fori(0, 4) as pair:
            core.clear(sems)
            with nc.Block() as block:
                @block.gpsimd
                def _(pool):
                    pool.tensor_copy(kn[:, :], flat(qk[:, bass.ds(pair + 4, 1), :])).then_inc(k_staged, 1)
                    pool.tensor_copy(vs[:, :, :], v[:, :, bass.ds(pair * P, P)]).then_inc(v_staged, 1)

                @block.scalar
                def _(act):
                    def copy_turned(u):
                        h, i = UNITS[u]
                        act.wait_ge(turned, u + 1)
                        act.activation(probT[:, h, :, i * P:i * P + P],
                                       core.bank[4 + u % 2][:, :].rearrange("p (j t) -> p j t", j=TT), ACT.Copy).then_inc(copied, 1)

                    for h in range(2):
                        act.activation(qn[:, h, :], flat(qk[:, bass.ds(pair, 1), :]), ACT.Copy,
                                       scale=core.headones[:, HD * h:HD * h + 1]).then_inc(q_staged, 1)
                    for u, (h, i) in enumerate(UNITS):
                        act.wait_ge(topped, u + 1)
                        act.activation(score[:, u % 4, :], score[:, u % 4, :], ACT.Exp, bias=top[:, u:u + 1]).then_inc(raised, 1)
                        if u >= 2:
                            copy_turned(u - 2)
                    copy_turned(6)
                    copy_turned(7)
                    for h in range(2):
                        act.wait_ge(mixed, h + 1)
                        r = slice(HD * h, HD * h + HD)
                        act.activation(att[r, bass.ds(pair, 1), :], core.bank[6 + h][r, :], ACT.Copy).then_inc(stored, 1)

                @block.tensor
                def _(pe):
                    def scores(u):
                        h, i = UNITS[u]
                        if u >= 4:
                            pe.wait_ge(biased, u - 3)
                        pe.matmul(core.bank[u % 4][:, :], qn[:, h, i * P:i * P + P], kn[:, :],
                                  start=True, stop=True).then_inc(scored, 1)

                    def turn(u):
                        pe.wait_ge(scaled, u + 1)
                        if u >= 2:
                            pe.wait_ge(copied, u - 1)
                        for j in range(TT):
                            mm = pe.matmul(core.bank[4 + u % 2][:, j * P:j * P + P], prob[:, u % 2, j * P:j * P + P],
                                           diag[:, u % 2, :], start=True, stop=True)
                        mm.then_inc(turned, 1)

                    def mix(h):
                        pe.wait_ge(copied, 4 * h + 4)
                        pe.wait_ge(v_staged, 1)
                        r = slice(HD * h, HD * h + HD)
                        for j in range(TT):
                            mm = pe.matmul(core.bank[6 + h][r, :], vs[:, j, r], probT[:, h, j, :],
                                           start=j == 0, stop=j == TT - 1)
                        mm.then_inc(mixed, 1)

                    pe.wait_ge(q_staged, 2)
                    pe.wait_ge(k_staged, 1)
                    for u in range(3):
                        scores(u)
                    for u in range(8):
                        if u + 3 < 8:
                            scores(u + 3)
                        turn(u)
                        if u == 5:
                            mix(0)
                    mix(1)

                @block.vector
                def _(dve):
                    dve.tensor_copy(slope[:, :], slopes[:, bass.ds(pair * 2, 2)]).then_inc(slope_staged, 1)
                    dve.wait_ge(slope_staged, 1)

                    def bias_and_top(u):
                        h, i = UNITS[u]
                        dve.wait_ge(scored, u + 1)
                        if u >= 4:
                            dve.wait_ge(counted, u - 3)
                        dve.scalar_tensor_tensor(out=score[:, u % 4, :], in0=dist[:, i, :], scalar=slope[:, h:h + 1],
                                                 in1=core.bank[u % 4][:, :], op0=ALU.mult, op1=ALU.add).then_inc(biased, 1)
                        dve.wait_ge(biased, u + 1)
                        dve.tensor_reduce(top[:, u:u + 1], score[:, u % 4, :], AX.X, ALU.max, negate=True).then_inc(topped, 1)

                    def weigh(u):
                        h, i = UNITS[u]
                        dve.wait_ge(raised, u + 1)
                        if u >= 2:
                            dve.wait_ge(turned, u - 1)
                        dve.scalar_tensor_tensor(out=prob[:, u % 2, :], in0=score[:, u % 4, :], scalar=1.0, in1=count[:, i, :],
                                                 op0=ALU.mult, op1=ALU.mult, accum_out=den[:, u:u + 1]).then_inc(counted, 1)
                        dve.wait_ge(counted, u + 1)
                        dve.reciprocal(den[:, u:u + 1], den[:, u:u + 1]).then_inc(inverse, 1)
                        dve.wait_ge(inverse, u + 1)
                        dve.tensor_scalar(diag[:, u % 2, :], core.ident[:, :], den[:, u:u + 1], None, ALU.mult).then_inc(scaled, 1)

                    bias_and_top(0)
                    bias_and_top(1)
                    for u in range(8):
                        if u + 2 < 8:
                            bias_and_top(u + 2)
                        weigh(u)
        with nc.Block() as block:
            @block.sync
            def _(sp):
                sp.wait_ge(slots_filled, 16 * n_fills)


def inputs_to_dram(inputs):
    a = {k: np.asarray(v) for k, v in inputs.items()}
    cols = []
    for name, n in VEC_COLS:
        flat = a[name].reshape(-1)
        if name in ("q_norm_g", "k_norm_g"):
            flat = np.tile(flat, 2)
        cols.append(flat.reshape(n, P).T)
    rows = lambda name: a[name][0]
    dram = {"vec": np.concatenate(cols, 1), "xT": a["x"][0].T, "positions": a["positions_2"]}
    for name, src in (("ada_w", "ada_w"), ("ada_w2", "w_ada_2"), ("w_in", "w_in"), ("w_in2", "w_in_2"), ("w_out", "w_out"),
                      ("w_out2", "w_out_2"), ("w_query", "peer_w_query"), ("g_up", "g_up"), ("wa2", "gla_wa2_2")):
        dram[name] = rows(src)
    dram["experts"] = np.concatenate(
        [rows(n).reshape(N_EXPERTS, -1, P, w).transpose(0, 2, 1, 3).reshape(N_EXPERTS * P, -1)
         for n, w in (("expert_w_gate_2", D_EXPERT), ("expert_w_up_2", D_EXPERT), ("expert_w_down_2", D))], 1)
    dram["decay_up"] = np.concatenate(list(rows("w_decay_up")), 1)
    dram["a_up"] = np.concatenate(list(rows("a_gate_up")), 1)
    dram["keys"] = np.concatenate([rows("peer_sub_keys1").T, rows("peer_sub_keys2").T], 1)
    dram["uv"] = np.concatenate([rows("peer_u"), rows("peer_v")], 1)
    dram["router_w"] = np.concatenate([rows("router_group_w_2"), rows("router_expert_w_2")], 1)
    dram["router_b"] = np.concatenate([rows("router_group_b_2"), rows("router_expert_b_2")])[None]
    dram.update(constant_tables())
    return {k: np.ascontiguousarray(v) for k, v in dram.items()}


def build(nc, dram, out):
    with ExitStack() as ctx:
        core = Core(nc, dram, ctx)
        cuts = lambda w, widths: [w[:, sum(widths[:i]):sum(widths[:i + 1])] for i in range(len(widths))]
        IN1 = [512, 512, 512, 512, 512, 512, 256]
        IN2 = [384] * 8 + [256, 256, 272]
        core.ring = WeightRing(core, cuts(dram["w_in"], IN1) + cuts(dram["w_out"], [512] * 2)
                               + cuts(dram["w_query"], [512] * 4) + cuts(dram["w_in2"], IN2)
                               + cuts(dram["w_out2"], [512] * 2))
        allocate(core)
        mixed = core.sb("mixed", [P, KD, S])
        first_block(core, 0, mixed)
        second_block(core, 13, mixed)
        stage_output(core, mixed, out)
        ring = core.ring
        with nc.Block() as block:
            @block.sync
            def _(sp):
                for i in range(max(0, ring.issued - RING), ring.issued):
                    ring.arrived(sp, i)


def first_block(core, first, mixed):
    with ExitStack() as st:
        zr = core.sb("zr", [P, 14, S], ctx=st)
        with ExitStack() as s2:
            qk = core.sb("qk", [P, KD, S], ctx=s2)
            v = core.sb("v", [P, TT, S], ctx=s2)
            h = mixed
            with ExitStack() as s3:
                m = Modulation(core, s3)
                stage_load(core, m)
                stage_modulation(core, m)
                stage_norm(core, h, core.gain[:, 0:8], core.mod[:, 0:8])
                stage_project_first(core, first, [("T", [copy_to(lambda f: qk[:, f, :])] * 4), ("T", [copy_to(lambda f: qk[:, 4 + f, :])] * 4),
                                                  ("N", copy_to(lambda t: v[:, t, :]))], h, m)
                stage_shifted(core, first + 3, h, zr, qk, m)
            stage_attention(core, qk, v, mixed)
        stage_rwkv(core, zr, mixed)
    stage_residual(core, first + 7, mixed, core.mod[:, 16:24])
    stage_peer(core, first + 9, mixed)


def stage_shifted(core, first, h, zr, qk, m):
    nc, ring = core.nc, core.ring
    N = 14
    with ExitStack() as st:
        stay = core.sb("stay", [P, N], ctx=st)
        gains = core.sb("qk_gains", [P, 2], ctx=st)
        sq = core.sb("qk_sq", [P, 2, S], ctx=st)
        stay_ready, gains_ready, bank_full, stayed, left, emptied = core.sems(
            st, "stay_ready", "gains_ready", "bank_full", "stayed", "left", "emptied")
        squared, summed, rooted, inverted, normed = core.sems(st, "squared", "summed", "rooted", "inverted", "normed")
        NQ = 8
        NB = 5
        item = lambda u: m.ITEMS - N + u
        done = m.NEEDED + 12
        with nc.Block() as block:
            @block.sync
            def _(sp):
                ring.load(sp, first + 4 + RING)

            @block.tensor
            def _(pe):
                for u in range(N):
                    ring.arrived(pe, first + u // 4)
                    if u >= NB:
                        pe.wait_ge(emptied, u - NB + 1)
                    w = ring.view(first + u // 4)
                    for k in range(KD):
                        mm = pe.matmul(core.bank[u % NB][:, :], w[:, k, (u % 4) * P:(u % 4) * P + P], h[:, k, :],
                                       start=k == 0, stop=k == KD - 1)
                    mm.then_inc(bank_full, 1)
                    if u % 4 == 3 or u == N - 1:
                        pe.wait_ge(bank_full, u + 1)
                        pe.sem_inc(ring.used, 1)
                    if u < NQ:
                        pe.wait_ge(squared, u + 1)
                        if u >= 2:
                            pe.wait_ge(rooted, u - 1)
                        pe.matmul(core.bank[6 + u % 2][:, :], core.headones[:, :], sq[:, u % 2, :], start=True, stop=True).then_inc(summed, 1)
                    if item(u - 1) >= done:
                        m.on_tensor(pe, item(u - 1))
                m.on_tensor(pe, m.ITEMS - 1)

            @block.scalar
            def _(act):
                def square(j):
                    if j >= 2:
                        act.wait_ge(normed, j - 1)
                    act.activation(sq[:, j % 2, :], qk[:, j, :], ACT.Square).then_inc(squared, 1)

                def root(j):
                    act.wait_ge(summed, j + 1)
                    act.activation(sq[:, j % 2, :], core.bank[6 + j % 2][:, :], ACT.Sqrt, scale=1.0 / HD, bias=1e-6).then_inc(rooted, 1)

                act.wait_ge(stay_ready, 2)
                square(0)
                square(1)
                for u in range(N):
                    if 1 <= u <= NQ:
                        root(u - 1)
                    if 2 <= u + 1 < NQ:
                        square(u + 1)
                    act.wait_ge(bank_full, u + 1)
                    act.activation(zr[:, u, :], core.bank[u % NB][:, :], ACT.Copy, scale=stay[:, u:u + 1]).then_inc(stayed, 1)
                    if item(u) > done:
                        m.load(act, item(u) + m.SLOTS)

            @block.vector
            def _(dve):
                dve.tensor_tensor(stay[:, :], core.col("mu_prev", 0, N), core.col("mu_next", 0, N), ALU.add).then_inc(stay_ready, 1)
                dve.wait_ge(stay_ready, 1)
                dve.tensor_scalar(stay[:, :], stay[:, :], -1.0, 1.0, ALU.mult, ALU.add).then_inc(stay_ready, 1)
                dve.tensor_scalar(gains[:, 0:1], core.col("q_norm_g"), HD ** -0.5, None, ALU.mult).then_inc(gains_ready, 1)
                dve.tensor_copy(gains[:, 1:2], core.col("k_norm_g")).then_inc(gains_ready, 1)
                dve.wait_ge(gains_ready, 2)

                def normalise(j):
                    dve.wait_ge(rooted, j + 1)
                    dve.reciprocal(sq[:, j % 2, :], sq[:, j % 2, :]).then_inc(inverted, 1)
                    dve.wait_ge(inverted, j + 1)
                    dve.scalar_tensor_tensor(out=qk[:, j, :], in0=qk[:, j, :], scalar=gains[:, j // 4:j // 4 + 1], in1=sq[:, j % 2, :],
                                             op0=ALU.mult, op1=ALU.mult).then_inc(normed, 1)

                for u in range(N):
                    if 1 <= u <= NQ:
                        normalise(u - 1)
                    ps = core.bank[u % NB]
                    dve.wait_ge(stayed, u + 1)
                    dve.scalar_tensor_tensor(out=zr[:, u, 1:S], in0=ps[:, 0:S - 1], scalar=core.col("mu_prev", u),
                                             in1=zr[:, u, 1:S], op0=ALU.mult, op1=ALU.add).then_inc(left, 1)
                    dve.wait_ge(left, u + 1)
                    dve.scalar_tensor_tensor(out=zr[:, u, 0:S - 1], in0=ps[:, 1:S], scalar=core.col("mu_next", u),
                                             in1=zr[:, u, 0:S - 1], op0=ALU.mult, op1=ALU.add).then_inc(emptied, 1)
                    if item(u) >= done:
                        m.on_vector(dve, item(u))
                m.finish(dve, m.NEEDED, m.ITEMS, [1, 2, 3])


def stage_rwkv(core, zr, mixed):
    nc = core.nc
    R, K, V = 0, 4, 8
    with ExitStack() as st:
        sig = core.sb("decay_sig", [P, 8, S], ctx=st)
        a = core.sb("a", [P, 8, S], ctx=st)
        kk = core.sb("kk", [P, 4, S], ctx=st)
        sel = core.sb("rwkv_cols", [P, 4, 6], ctx=st)
        restart = core.sb("restart", [P, S], ctx=st)
        stage_rwkv_inputs(core, zr, sig, a, kk, sel, restart)
        for rev in range(2):
            stage_rwkv_scan(core, zr, sig, a, kk, sel, restart, mixed, rev)
        stage_rwkv_output(core, zr, a, sel, mixed)


def stage_rwkv_inputs(core, zr, sig, a, kk, sel, restart):
    nc = core.nc
    with ExitStack() as st:
        lora = core.sb("lora", [P, 2, 2 * S], ctx=st)
        low = core.sb("low", [P, S], ctx=st)
        sq = core.sb("kk_sq", [P, 2, S], ctx=st)
        lora_zeroed = core.sems(st, "lora_zeroed")
        loaded, squashed, bank_full, emptied, made, squared, kk_full, clamped, rooted, inverted = core.sems(
            st, "lora_loaded", "squashed", "bank_full", "emptied", "kk_made", "squared", "kk_full", "clamped", "rooted", "inverted")
        UNITS = [(d, f, which) for d in range(2) for f in range(4) for which in range(2)]
        with nc.Block() as block:
            @block.sync
            def _(sp):
                sp.dma_start(lora[0:HD, 0, :], core.dram["decay_up"]).then_inc(loaded, 16)
                sp.dma_start(lora[HD:P, 1, :], core.dram["a_up"]).then_inc(loaded, 16)
                sp.dma_start(restart[:, :], core.dram["restart"]).then_inc(loaded, 16)
                sp.wait_ge(loaded, 48)

            @block.scalar
            def _(act):
                act.activation(low[0:HD, :], zr[0:HD, 12, :], ACT.Tanh).then_inc(squashed, 1)
                act.activation(low[HD:P, :], zr[HD:P, 12, :], ACT.Copy).then_inc(squashed, 1)
                for u, (d, f, which) in enumerate(UNITS):
                    act.wait_ge(bank_full, u + 1)
                    dest, bias = (sig, "w_decay0") if which == 0 else (a, "a_gate0")
                    act.activation(dest[:, 4 * d + f, :], core.bank[u % 6][:, :], ACT.Sigmoid,
                                   bias=core.col(bias, 4 * d + f)).then_inc(emptied, 1)
                for f in range(4):
                    act.wait_ge(made, f + 1)
                    if f >= 2:
                        act.wait_ge(inverted, 2 * f - 2)
                    act.activation(sq[:, f % 2, :], kk[:, f, :], ACT.Square).then_inc(squared, 1)
                    act.wait_ge(clamped, f + 1)
                    act.activation(sq[:, f % 2, :], sq[:, f % 2, :], ACT.Sqrt).then_inc(rooted, 1)

            @block.tensor
            def _(pe):
                pe.wait_ge(loaded, 48)
                pe.wait_ge(squashed, 2)
                pe.wait_ge(lora_zeroed, 2)
                for u, (d, f, which) in enumerate(UNITS):
                    if u >= 6:
                        pe.wait_ge(emptied, u - 5)
                    pe.matmul(core.bank[u % 6][:, :], lora[:, which, d * S + f * P:d * S + f * P + P], low[:, :],
                              start=True, stop=True).then_inc(bank_full, 1)
                for f in range(4):
                    pe.wait_ge(squared, f + 1)
                    pe.matmul(core.bank[6 + f % 2][:, :], core.headones[:, :], sq[:, f % 2, :], start=True, stop=True).then_inc(kk_full, 1)

            @block.vector
            def _(dve):
                dve.memset(lora[HD:P, 0, :], 0.0).then_inc(lora_zeroed, 1)
                dve.memset(lora[0:HD, 1, :], 0.0).then_inc(lora_zeroed, 1)
                for f in range(4):
                    dve.tensor_scalar(kk[:, f, :], zr[:, 4 + f, :], core.col("k_k", f), None, ALU.mult).then_inc(made, 1)
                for i, name in ((0, "k_a"), (3, "r_k"), (4, "lnx_g"), (5, "lnx_b")):
                    dve.tensor_copy(sel[:, :, i], core.col(name, 0, 4))
                dve.tensor_scalar(sel[:, :, 1], core.col("k_a", 0, 4), -1.0, 1.0, ALU.mult, ALU.add)
                dve.tensor_scalar(sel[:, :, 2], core.col("k_a", 0, 4), 0.5, None, ALU.mult)
                for f in range(4):
                    dve.wait_ge(kk_full, f + 1)
                    dve.tensor_scalar(sq[:, f % 2, :], core.bank[6 + f % 2][:, :], 1e-12, None, ALU.max).then_inc(clamped, 1)
                    dve.wait_ge(rooted, f + 1)
                    dve.reciprocal(sq[:, f % 2, :], sq[:, f % 2, :]).then_inc(inverted, 1)
                    dve.wait_ge(inverted, 2 * f + 1)
                    dve.tensor_tensor(kk[:, f, :], kk[:, f, :], sq[:, f % 2, :], ALU.mult).then_inc(inverted, 1)


def stage_rwkv_scan(core, zr, sig, a, kk, sel, restart, mixed, rev):
    nc, bank = core.nc, core.bank
    R, K, V = 0, 4, 8
    NL = len(LEVELS) - 1
    order = list(range(TT))[::-1] if rev else list(range(TT))
    Q = 3 if rev else 0
    with ExitStack() as st:
        masks = core.sb("rwkv_masks", [P, 10, P], ctx=st)
        work = core.sb("rwkv_work", [P, 23, S], ctx=st)
        xs = core.sb("rwkv_x", [P, 2, TT, HD], ctx=st)
        u_sb = core.sb("rwkv_u", [P, 2, HD], ctx=st)
        state = core.sb("rwkv_state", [P, 2, HD], ctx=st)
        held = core.sb("rwkv_held", [P, HD], ctx=st)
        total = core.sb("rwkv_total", [P, TT], ctx=st)
        step = core.sb("rwkv_step", [P, TT], ctx=st)
        cols = core.sb("rwkv_col", [P, 6], ctx=st)
        slot = lambda i: work[:, i, :]
        e1, e2, p_at, p_inv, p_prev, alpha, beta, kappa, rho = [slot(i) for i in range(9)]
        alphaN, betaN, kappaN, vN = [work[:, 9 + i, :].rearrange("p (i d) -> p i d", i=TT) for i in range(4)]
        vT, ahat = slot(13), slot(14)
        tri = [slot(15), slot(16)]
        inv = [slot(17), slot(18)]
        invT = [slot(19), slot(20)]
        off = [slot(21), slot(22)]
        alpha_of, rho_of = [slot(14), slot(20)], [slot(19), slot(3)]
        m_rb = [slot(0), slot(1)]
        m_rk = [slot(2), slot(4)]
        mask = lambda i: tiled(masks[:, i, :], TT)
        four = lambda ap: ap.rearrange("p (i t) -> p i t", i=TT)
        t_of = lambda ap, i: ap[:, i * P:i * P + P]
        EARLIER, LATER = (1, 0) if rev else (0, 1)
        MS = LEVELS[1:]

        def columns(ap, m, half):
            return ap.rearrange("p (b w) -> p b w", w=2 * m)[:, :, half * m:half * m + m]

        def by_tile(ap):
            return ap.rearrange("p (i b) w -> p i b w", i=TT)

        def compact(ps, m):
            return ps[:, 0:S // 2].rearrange("p (b w) -> p b w", w=m)
        names = ("rwkv_tables", "summed", "raised", "v_staged", "ops_dve", "ops_pool", "turned", "turn_copied", "cols_staged", "padded", "eyed0", "eyed1",
                 "filled0", "filled1", "evac0", "evac1", "copied0", "copied1", "unit0", "unit1", "state0", "state1", "y_stored")
        sems = core.sems(st, *names)
        (tables, summed, raised, v_staged, ops_dve, ops_pool, turned, turn_copied, cols_staged, padded, eye0, eye1,
         f0, f1, d0, d1, a0, a1, u0, u1, s0, s1, y_stored) = sems
        filled, evac, copied, unit, stated, eyed = [f0, f1], [d0, d1], [a0, a1], [u0, u1], [s0, s1], [eye0, eye1]
        Z_FULL = [7 + 3 * l for l in range(NL)]
        W_LAST = Z_FULL[-1] + 1
        A_FULL = W_LAST + 1
        U_FULL = [A_FULL + 1 + 3 * n for n in range(TT)]
        Z_EVAC = [7 + l for l in range(NL)]
        U_EVAC = [7 + NL + n for n in range(TT)]
        W_COPY = [3 + 2 * l for l in range(NL - 1)] + [2 * NL]
        A_COPY = 2 * NL + 1
        with nc.Block() as block:
            @block.sync
            def _(sp):
                sp.dma_start(masks[:, :, :], core.dram["rw_rev" if rev else "rw_fwd"]).then_inc(tables, 16)
                sp.wait_ge(tables, 16)
        with nc.Fori(0, 4) as f:
            core.clear(sems)
            row = lambda t, first: t[:, bass.ds(f + first, 1), :].rearrange("p a t -> p (a t)")
            with nc.Block() as block:
                @block.vector
                def _(dve):
                    dve.tensor_copy(cols[:, :], row(sel, 0)).then_inc(cols_staged, 1)
                    dve.tensor_tensor_scan(e1, restart[:, :], row(sig, 4 * rev), 0.0, ALU.mult, ALU.add).then_inc(summed, 1)
                    dve.wait_ge(summed, 1)
                    dve.tensor_copy(total[:, :], e1[:, P - 1:S:P]).then_inc(summed, 1)
                    dve.wait_ge(summed, 2)
                    dve.scalar_tensor_tensor(out=four(e1), in0=repeat(total[:, :], P), scalar=-0.5, in1=four(e1),
                                             op0=ALU.mult, op1=ALU.add).then_inc(summed, 1)
                    dve.wait_ge(summed, 3)
                    dve.tensor_tensor(e2, e1, row(sig, 4 * rev), ALU.subtract).then_inc(summed, 1)
                    dve.tensor_tensor(step[:, 0:TT - 1], total[:, 0:TT - 1], total[:, 1:TT], ALU.add).then_inc(summed, 1)
                    dve.wait_ge(cols_staged, 1)
                    dve.tensor_scalar(kappa, row(a, 4 * rev), cols[:, 0:1], cols[:, 1:2], ALU.mult, ALU.add).then_inc(summed, 1)
                    dve.wait_ge(summed, 6)
                    dve.tensor_tensor(kappa, kappa, row(zr, K), ALU.mult).then_inc(summed, 1)
                    dve.wait_ge(raised, 2)
                    dve.scalar_tensor_tensor(out=alpha, in0=row(kk, 0), scalar=-1.0, in1=p_prev, op0=ALU.mult, op1=ALU.mult).then_inc(ops_dve, 1)
                    dve.wait_ge(ops_pool, 1)
                    dve.wait_ge(raised, 3)
                    dve.tensor_tensor(beta, beta, p_inv, ALU.mult).then_inc(ops_dve, 1)
                    dve.wait_ge(summed, 7)
                    dve.tensor_tensor(kappa, kappa, p_inv, ALU.mult).then_inc(ops_dve, 1)
                    for h in range(2):
                        dve.wait_ge(filled[h], 1)
                        dve.tensor_tensor(four(tri[h]), four(bank[4 * h][:, :]), mask(0), ALU.mult).then_inc(evac[h], 1)
                        dve.wait_ge(filled[h], 2)
                        dve.tensor_tensor(four(inv[h]), four(bank[4 * h + 1][:, :]), mask(1), ALU.mult).then_inc(evac[h], 1)
                        dve.wait_ge(filled[h], 3)
                        dve.tensor_tensor(four(off[h]), four(bank[4 * h + 2][:, :]), mask(0), ALU.mult).then_inc(evac[h], 1)
                        dve.wait_ge(filled[h], 4)
                        dve.wait_ge(ops_pool, 2)
                        dve.tensor_tensor(four(m_rb[h]), four(bank[4 * h + 3][:, :]), mask(9), ALU.mult).then_inc(evac[h], 1)
                    for h in range(2):
                        dve.wait_ge(filled[h], 5)
                        dve.tensor_tensor(four(m_rk[h]), four(bank[4 * h][:, :]), mask(9), ALU.mult).then_inc(evac[h], 1)
                        dve.wait_ge(unit[h], 1)
                        dve.tensor_tensor(four(invT[h]), four(tri[h]), mask(2), ALU.mult).then_inc(evac[h], 1)
                    for l in range(NL):
                        for h in range(2):
                            dve.wait_ge(filled[h], Z_FULL[l])
                            m = MS[l]
                            one = columns(masks[:, 3 + l, :], m, EARLIER).unsqueeze(1).to_broadcast([P, TT, P // (2 * m), m])
                            dve.tensor_tensor(by_tile(columns(off[h], m, EARLIER)), by_tile(compact(bank[4 * h + 2], m)), one,
                                              ALU.mult).then_inc(evac[h], 1)
                    held_n = 0
                    for n, i in enumerate(order):
                        for h in range(2):
                            dve.wait_ge(filled[h], U_FULL[n])
                            if n >= 1:
                                dve.wait_ge(filled[h], U_FULL[n - 1] + 2)
                            dve.tensor_copy(u_sb[:, h, :], bank[4 * h + 2][:, 0:HD]).then_inc(evac[h], 1)
                        if n == TT - 1:
                            break
                        for h in range(2):
                            r = slice(HD * h, HD * h + HD)
                            b = min(i, order[n + 1])
                            fac = step[r, b:b + 1]
                            if n == 0:
                                dve.wait_ge(raised, 4)
                                dve.wait_ge(filled[h], U_FULL[n] + 1)
                                dve.tensor_scalar(state[r, 0, :], bank[4 * h + 3][r, 0:HD], fac, None, ALU.mult).then_inc(stated[h], 1)
                                continue
                            dve.wait_ge(stated[h], 2 * n - 1)
                            dve.tensor_scalar(held[r, :], state[r, (n - 1) % 2, :], fac, None, ALU.mult).then_inc(stated[h], 1)
                            dve.wait_ge(stated[h], 2 * n)
                            dve.wait_ge(filled[h], U_FULL[n] + 1)
                            dve.scalar_tensor_tensor(out=state[r, n % 2, :], in0=bank[4 * h + 3][r, 0:HD], scalar=fac, in1=held[r, :],
                                                     op0=ALU.mult, op1=ALU.add).then_inc(stated[h], 1)
                    if rev:
                        for h in range(2):
                            r = slice(HD * h, HD * h + HD)
                            dve.wait_ge(filled[h], U_FULL[-1] + 1)
                            y = mixed[r, bass.ds(f + 4, 1), :].rearrange("p a t -> p (a t)")
                            dve.tensor_tensor(y, bank[4 * h][r, :], y, ALU.add).then_inc(y_stored, 1)

                @block.gpsimd
                def _(pool):
                    pool.tensor_copy(vT, row(zr, V)).then_inc(v_staged, 1)
                    pool.tensor_tensor(beta, row(a, 4 * rev), row(kk, 0), ALU.mult).then_inc(ops_pool, 1)
                    pool.wait_ge(raised, 1)
                    pool.tensor_tensor(rho, row(zr, R), p_at, ALU.mult).then_inc(ops_pool, 1)
                    for h in range(2):
                        pool.wait_ge(evac[h], 1)
                        pool.tensor_tensor(four(tri[h]), four(tri[h]), tiled(core.ident[:, :], TT), ALU.add).then_inc(unit[h], 1)
                        pool.wait_ge(evac[h], 2)
                        pool.tensor_tensor(four(inv[h]), four(inv[h]), tiled(core.ident[:, :], TT), ALU.add).then_inc(unit[h], 1)
                    for l, m in enumerate(MS):
                        for h in range(2):
                            pool.wait_ge(filled[h], Z_FULL[l] - 1)
                            one = columns(core.ident[:, :], m, LATER).unsqueeze(1).to_broadcast([P, TT, P // (2 * m), m])
                            pool.tensor_copy(by_tile(columns(off[h], m, LATER)), one).then_inc(eyed[h], 1)

                @block.scalar
                def _(act):
                    lam = NEG_LOG_DECAY
                    act.wait_ge(summed, 4)
                    at, prev, sign = (e2, e1, lam) if rev else (e1, e2, -lam)
                    act.activation(p_at, at, ACT.Exp, scale=sign).then_inc(raised, 1)
                    act.activation(p_prev, prev, ACT.Exp, scale=sign).then_inc(raised, 1)
                    act.activation(p_inv, at, ACT.Exp, scale=-sign).then_inc(raised, 1)
                    act.wait_ge(summed, 5)
                    act.activation(step[:, 0:TT - 1], step[:, 0:TT - 1], ACT.Exp, scale=-0.5 * lam).then_inc(raised, 1)
                    act.wait_ge(ops_dve, 1)
                    for h in range(2):
                        act.activation(alpha_of[h], alpha, ACT.Copy, scale=core.headones[:, HD * h:HD * h + 1]).then_inc(padded, 1)
                    act.wait_ge(ops_pool, 2)
                    act.wait_ge(ops_dve, 3)
                    for h in range(2):
                        act.activation(rho_of[h], rho, ACT.Copy, scale=core.headones[:, HD * h:HD * h + 1]).then_inc(padded, 1)
                    for j in range(4):
                        act.wait_ge(turned, j + 1)
                        act.activation(slot(9 + j), bank[(2, 3, 6, 7)[j]][:, :], ACT.Copy).then_inc(turn_copied, 1)
                    for h in range(2):
                        act.wait_ge(filled[h], 6)
                        act.activation(xs[:, h, :, :].rearrange("p i d -> p (i d)"), bank[4 * h + 1][:, 0:TT * HD], ACT.Copy).then_inc(copied[h], 1)
                    for l in range(NL):
                        for h in range(2):
                            if l < NL - 1:
                                act.wait_ge(filled[h], Z_FULL[l] + 2)
                                act.activation(columns(inv[h], MS[l], EARLIER), compact(bank[4 * h + 3], MS[l]), ACT.Copy).then_inc(copied[h], 1)
                            else:
                                act.wait_ge(filled[h], W_LAST)
                            act.activation(columns(invT[h], MS[l], LATER), compact(bank[4 * h], MS[l]), ACT.Copy).then_inc(copied[h], 1)
                    for h in range(2):
                        r = slice(HD * h, HD * h + HD)
                        act.wait_ge(filled[h], A_FULL)
                        act.activation(ahat[r, :], bank[4 * h + 1][r, :], ACT.Copy).then_inc(copied[h], 1)
                    if not rev:
                        for h in range(2):
                            r = slice(HD * h, HD * h + HD)
                            act.wait_ge(filled[h], U_FULL[-1] + 1)
                            act.activation(mixed[r, bass.ds(f + 4, 1), :].rearrange("p a t -> p (a t)"), bank[4 * h][r, :],
                                           ACT.Copy).then_inc(y_stored, 1)

                @block.tensor
                def _(pe):
                    for j, src in enumerate((alpha, beta, kappa, vT)):
                        if j < 3:
                            pe.wait_ge(ops_dve, j + 1)
                        else:
                            pe.wait_ge(v_staged, 1)
                        for i in range(TT):
                            mm = pe.transpose(bank[(2, 3, 6, 7)[j]][:, i * P:i * P + P], t_of(src, i), core.ident[:, :])
                        mm.then_inc(turned, 1)

                    def product(h, b, lhs, rhs):
                        for i in range(TT):
                            mm = pe.matmul(bank[4 * h + b][:, i * P:i * P + P], t_of(lhs, i), t_of(rhs, i), start=True, stop=True)
                        mm.then_inc(filled[h], 1)

                    def half_product(h, b, lhs, rhs, m, half):
                        n = P // (2 * m)
                        for i in range(TT):
                            mm = pe.matmul(compact(bank[4 * h + b], m)[:, i * n:i * n + n, :], t_of(lhs, i),
                                           columns(rhs, m, half)[:, i * n:i * n + n, :], start=True, stop=True)
                        mm.then_inc(filled[h], 1)

                    for h in range(2):
                        pe.wait_ge(padded, h + 1)
                        product(h, 0, beta, alpha_of[h])
                        product(h, 1, alpha_of[h], beta)
                    for h in range(2):
                        pe.wait_ge(turn_copied, 2 * h + 2)
                        pe.wait_ge(padded, h + 3)
                        product(h, 2, kappa, alpha_of[h])
                        product(h, 3, beta, rho_of[h])
                    for h in range(2):
                        pe.wait_ge(evac[h], 1)
                        product(h, 0, kappa, rho_of[h])
                    for h in range(2):
                        r = slice(HD * h, HD * h + HD)
                        pe.wait_ge(evac[h], 3)
                        pe.wait_ge(turn_copied, 4)
                        for i in range(TT):
                            mm = pe.matmul(bank[4 * h + 1][:, i * HD:i * HD + HD], t_of(off[h], i), vN[:, i, r], start=True, stop=True)
                        mm.then_inc(filled[h], 1)
                    for l in range(NL):
                        for h in range(2):
                            if l == 0:
                                pe.wait_ge(unit[h], 2)
                            else:
                                pe.wait_ge(copied[h], W_COPY[l - 1])
                            half_product(h, 2, tri[h], inv[h], MS[l], EARLIER)
                        for h in range(2):
                            pe.wait_ge(evac[h], Z_EVAC[l])
                            pe.wait_ge(eyed[h], l + 1)
                            if l < NL - 1:
                                half_product(h, 3, invT[h], off[h], MS[l], EARLIER)
                            half_product(h, 0, off[h], invT[h], MS[l], LATER)
                    for h in range(2):
                        r = slice(HD * h, HD * h + HD)
                        pe.wait_ge(copied[h], W_COPY[-1])
                        for i in range(TT):
                            mm = pe.matmul(bank[4 * h + 1][r, i * P:i * P + P], alphaN[:, i, r], t_of(invT[h], i), start=True, stop=True)
                        mm.then_inc(filled[h], 1)
                    for n, i in enumerate(order):
                        for h in range(2):
                            r = slice(HD * h, HD * h + HD)
                            u_ps = bank[4 * h + 2][:, 0:HD]
                            mm = pe.matmul(u_ps, t_of(invT[h], i), xs[:, h, i, :], start=True, stop=n == 0)
                            if n >= 1:
                                pe.wait_ge(copied[h], A_COPY)
                                pe.wait_ge(stated[h], 2 * n - 1)
                                mm = pe.matmul(u_ps, ahat[r, i * P:i * P + P], state[r, (n - 1) % 2, :], start=False, stop=True)
                            mm.then_inc(filled[h], 1)
                        for h in range(2):
                            r = slice(HD * h, HD * h + HD)
                            pe.wait_ge(evac[h], U_EVAC[n])
                            if n < TT - 1:
                                s_ps = bank[4 * h + 3][r, 0:HD]
                                pe.matmul(s_ps, betaN[:, i, r], u_sb[:, h, :], start=True, stop=False)
                                pe.matmul(s_ps, kappaN[:, i, r], vN[:, i, r], start=False, stop=True).then_inc(filled[h], 1)
                            y_ps = bank[4 * h][r, i * P:i * P + P]
                            pe.matmul(y_ps, u_sb[:, h, :], t_of(m_rb[h], i), start=True, stop=False)
                            mm = pe.matmul(y_ps, vN[:, i, r], t_of(m_rk[h], i), start=False, stop=n == 0)
                            if n >= 1:
                                mm = pe.matmul(y_ps, state[r, (n - 1) % 2, :], rho[r, i * P:i * P + P], start=False, stop=True)
                            mm.then_inc(filled[h], 1)


def stage_rwkv_output(core, zr, a, sel, mixed):
    nc, bank = core.nc, core.bank
    with ExitStack() as st:
        gate_in = core.sb("gate_in", [P, S], ctx=st)
        g_up = core.sb("g_up", [P, S], ctx=st)
        g_w = core.sb("g_w", [P, P], ctx=st)
        yc = core.sb("yc", [P, S], ctx=st)
        sq = core.sb("y_sq", [P, S], ctx=st)
        bonus = core.sb("bonus", [P, S], ctx=st)
        cols = core.sb("out_cols", [P, 6], ctx=st)
        sems = core.sems(st, "g_loaded", "cols_staged", "gate_staged", "y_summed", "centred", "squared", "sq_summed", "rooted",
                         "inverted", "normed", "rates", "weighed", "b_summed", "bonused", "added", "gated", "stored")
        (g_loaded, cols_staged, gate_staged, y_summed, centred, squared, sq_summed, rooted, inverted, normed, rates, weighed,
         b_summed, bonused, added, gated, stored) = sems
        with nc.Block() as block:
            @block.sync
            def _(sp):
                sp.dma_start(g_up[:, :], core.dram["g_up"]).then_inc(g_loaded, 16)
                sp.wait_ge(g_loaded, 16)

            @block.scalar
            def _(act):
                act.activation(gate_in[:, :], zr[:, 13, :], ACT.Sigmoid)
        with nc.Fori(0, 4) as f:
            core.clear(sems)
            row = lambda t, first: t[:, bass.ds(f + first, 1), :].rearrange("p a t -> p (a t)")
            with nc.Block() as block:
                @block.tensor
                def _(pe):
                    pe.matmul(bank[0][:, :], core.headones[:, :], row(mixed, 4), start=True, stop=True).then_inc(y_summed, 1)
                    pe.wait_ge(gate_staged, 1)
                    pe.matmul(bank[3][:, :], g_w[:, :], gate_in[:, :], start=True, stop=True).then_inc(gated, 1)
                    pe.wait_ge(squared, 1)
                    pe.matmul(bank[1][:, :], core.headones[:, :], sq[:, :], start=True, stop=True).then_inc(sq_summed, 1)
                    pe.wait_ge(weighed, 4)
                    pe.matmul(bank[2][:, :], core.headones[:, :], bonus[:, :], start=True, stop=True).then_inc(b_summed, 1)

                @block.gpsimd
                def _(pool):
                    pool.tensor_tensor(bonus[:, :], row(a, 0), row(a, 4), ALU.add).then_inc(rates, 1)
                    pool.tensor_copy(g_w[:, :], g_up[:, bass.ds(f * P, P)]).then_inc(gate_staged, 1)

                @block.scalar
                def _(act):
                    act.wait_ge(centred, 1)
                    act.activation(sq[:, :], yc[:, :], ACT.Square).then_inc(squared, 1)
                    act.wait_ge(sq_summed, 1)
                    act.activation(sq[:, :], bank[1][:, :], ACT.Sqrt, scale=1.0 / HD, bias=64e-5).then_inc(rooted, 1)

                @block.vector
                def _(dve):
                    dve.tensor_copy(cols[:, :], row(sel, 0)).then_inc(cols_staged, 1)
                    dve.wait_ge(y_summed, 1)
                    dve.scalar_tensor_tensor(out=yc[:, :], in0=bank[0][:, :], scalar=-1.0 / HD, in1=row(mixed, 4),
                                             op0=ALU.mult, op1=ALU.add).then_inc(centred, 1)
                    dve.wait_ge(cols_staged, 1)
                    dve.wait_ge(rates, 1)
                    dve.tensor_scalar(bonus[:, :], bonus[:, :], cols[:, 2:3], cols[:, 1:2], ALU.mult, ALU.add).then_inc(weighed, 1)
                    dve.wait_ge(weighed, 1)
                    dve.tensor_tensor(bonus[:, :], bonus[:, :], row(zr, 4), ALU.mult).then_inc(weighed, 1)
                    dve.wait_ge(weighed, 2)
                    dve.scalar_tensor_tensor(out=bonus[:, :], in0=bonus[:, :], scalar=cols[:, 3:4], in1=row(zr, 0),
                                             op0=ALU.mult, op1=ALU.mult).then_inc(weighed, 1)
                    dve.wait_ge(rooted, 1)
                    dve.wait_ge(weighed, 3)
                    dve.reciprocal(sq[:, :], sq[:, :]).then_inc(weighed, 1)
                    dve.wait_ge(weighed, 4)
                    dve.scalar_tensor_tensor(out=yc[:, :], in0=yc[:, :], scalar=cols[:, 4:5], in1=sq[:, :],
                                             op0=ALU.mult, op1=ALU.mult).then_inc(normed, 1)
                    dve.wait_ge(b_summed, 1)
                    dve.tensor_tensor(bonus[:, :], bank[2][:, :], row(zr, 8), ALU.mult).then_inc(bonused, 1)
                    dve.wait_ge(normed, 1)
                    dve.wait_ge(bonused, 1)
                    dve.scalar_tensor_tensor(out=yc[:, :], in0=yc[:, :], scalar=cols[:, 5:6], in1=bonus[:, :],
                                             op0=ALU.add, op1=ALU.add).then_inc(added, 1)
                    dve.wait_ge(added, 1)
                    dve.wait_ge(gated, 1)
                    dve.tensor_tensor(row(mixed, 4), bank[3][:, :], yc[:, :], ALU.mult).then_inc(stored, 1)


def stage_residual(core, first, src, gate):
    x = core.x

    def evac(half):
        def f(eng, psum, t):
            k = 4 * half + t
            return eng.scalar_tensor_tensor(out=x[:, k, :], in0=psum, scalar=gate[:, k:k + 1], in1=x[:, k, :],
                                            op0=ALU.mult, op1=ALU.add)
        return f
    stage_project(core, first, [("T", [evac(0)] * 4), ("T", [evac(1)] * 4)], src, only_dve=True)


def stage_peer(core, first, mixed):
    nc = core.nc
    h2 = mixed
    with ExitStack() as st:
        idx = core.sb("expert_idx", [P, TT, HK], U32, ctx=st)
        gates = core.sb("expert_gate", [P, TT, HK], ctx=st)
        q = core.sb("peer_q", [P, 2 * PEER_HEADS, S], ctx=st)
        stage_norm(core, h2, core.gain[:, 8:16], core.mod[:, 24:32])
        stage_project(core, first, [("T", [copy_to(lambda f, i=i: q[:, 4 * i + f, :])] * 4) for i in range(4)], h2)
        hN = core.sb("h_rows", [P, TT, D], ctx=st)
        sc = core.sb("peer_scores", [P, TT, 2 * PEER_HEADS, N_KEYS], ctx=st)
        stage_peer_scores(core, q, h2, sc, hN)
        stage_peer_experts(core, sc, idx, gates, hN, mixed, q)


def stage_peer_scores(core, q, h2, sc, hN):
    nc, bank = core.nc, core.bank
    with ExitStack() as st:
        keys = core.sb("peer_keys", [P, 2 * N_KEYS], ctx=st)
        keys_loaded, bank_full, act_emptied, dve_emptied = core.sems(st, "keys_loaded", "bank_full", "act_emptied", "dve_emptied")
        units = [("turn", i, g, 0) for i in range(TT) for g in range(2)]
        units += [("score", i, g, half) for i in range(TT) for half in range(2) for g in range(2)]

        def dest(unit):
            kind, i, g, half = unit
            if kind == "turn":
                return hN[:, i, g * S:g * S + S]
            at = half * PEER_HEADS + 4 * g
            return sc[:, i, at:at + 4, :].rearrange("p r n -> p (r n)")

        with nc.Block() as block:
            @block.sync
            def _(sp):
                sp.dma_start(keys[:, :], core.dram["keys"]).then_inc(keys_loaded, 16)
                sp.wait_ge(keys_loaded, 16)

            @block.tensor
            def _(pe):
                for u, (kind, i, g, half) in enumerate(units):
                    if u >= 6:
                        pe.wait_ge(dve_emptied if u % 2 else act_emptied, (u - 6) // 2 + 1)
                    if kind == "score":
                        pe.wait_ge(keys_loaded, 16)
                    for j in range(4):
                        out = bank[u % 6][:, j * P:j * P + P]
                        if kind == "turn":
                            mm = pe.transpose(out, h2[:, 4 * g + j, i * P:i * P + P], core.ident[:, :])
                        else:
                            mm = pe.matmul(out, q[:, 2 * (4 * g + j) + half, i * P:i * P + P],
                                           keys[:, half * N_KEYS:half * N_KEYS + N_KEYS], start=True, stop=True)
                    mm.then_inc(bank_full, 1)

            @block.scalar
            def _(act):
                for u in range(0, len(units), 2):
                    act.wait_ge(bank_full, u + 1)
                    act.activation(dest(units[u]), bank[u % 6][:, :], ACT.Copy).then_inc(act_emptied, 1)

            @block.vector
            def _(dve):
                for u in range(1, len(units), 2):
                    dve.wait_ge(bank_full, u + 1)
                    dve.tensor_copy(dest(units[u]), bank[u % 6][:, :]).then_inc(dve_emptied, 1)


class TopKeys:
    LOWEST = -3.0e38
    OPS = 27

    def __init__(self, core, st, sc, idx, gates, scratch, iota):
        self.sc, self.idx, self.gates, self.iota = sc, idx, gates, iota
        self.step, self.gate = core.sems(st, "topk_step", "topk_gate")
        self.row = scratch[:, 0, 0:2 * N_KEYS].rearrange("p (a n) -> p a n", a=2)
        self.rest = scratch[:, 0, 2 * N_KEYS:4 * N_KEYS].rearrange("p (a n) -> p a n", a=2)
        self.cand, self.cand_rest = scratch[:, 1, 0:TOPK * TOPK], scratch[:, 1, TOPK * TOPK:2 * TOPK * TOPK]
        self.pick = scratch[:, 2, :].rearrange("p (k a) -> p k a", a=TOPK)
        small = lambda i: scratch[:, 3, 2 * TOPK * i:2 * TOPK * (i + 1)].rearrange("p (a k) -> p a k", a=2)
        self.val, self.atf, self.partf, self.key = [small(i) for i in range(4)]
        self.best, self.expert, self.near = [scratch[:, 3, i * TOPK:(i + 1) * TOPK] for i in (8, 9, 10)]
        self.at = core.sb("topk_at", [P, 2, TOPK], U32, ctx=st)
        self.pos = core.sb("topk_pos", [P, TOPK], U32, ctx=st)
        self.part = core.sb("topk_part", [P, 2, TOPK], U32, ctx=st)

    @staticmethod
    def heads(ap, h):
        return ap.rearrange("p (h k) -> p h k", k=TOPK)[:, bass.ds(h, 1), :].rearrange("p h k -> p (h k)")

    def head(self, dve, t, h, calls):
        n = 0

        def do(ins):
            nonlocal n
            n += 1
            ins.then_inc(self.step, 1)

        def settled():
            dve.wait_ge(self.step, calls * self.OPS + n)

        def gated():
            settled()
            dve.sem_inc(self.gate, 1)

        def top16(v, where, values, others):
            rows = range(len(v))
            for r in rows:
                do(dve.max(v[r][:, 0:8], values[r]))
            gated()
            for r in rows:
                do(dve.match_replace(others[r], v[r][:, 0:8], values[r], self.LOWEST))
            for r in rows:
                do(dve.max_index(where[r][:, 0:8], v[r][:, 0:8], values[r]))
            gated()
            for r in rows:
                do(dve.max(v[r][:, 8:16], others[r]))
            gated()
            for r in rows:
                do(dve.max_index(where[r][:, 8:16], v[r][:, 8:16], others[r]))

        sc = self.sc[:, t, :, :].rearrange("p (a h) n -> p a h n", a=2)[:, :, bass.ds(h, 1), :]
        do(dve.tensor_copy(self.row, sc.rearrange("p a h n -> p a (h n)")))
        gated()
        two = lambda ap: [ap[:, 0, :], ap[:, 1, :]]
        top16(two(self.val), two(self.at), two(self.row), two(self.rest))
        square = [P, TOPK, TOPK]
        settled()
        do(dve.tensor_tensor(self.cand.rearrange("p (a b) -> p a b", a=TOPK), self.val[:, 0, :].unsqueeze(2).to_broadcast(square),
                             self.val[:, 1, :].unsqueeze(1).to_broadcast(square), ALU.add))
        settled()
        do(dve.tensor_copy(self.atf, self.at[:, :, :]))
        gated()
        top16([self.best], [self.pos[:, :]], [self.cand], [self.cand_rest])
        settled()
        do(dve.tensor_scalar(self.part[:, 0, :], self.pos[:, :], 4, None, ALU.logical_shift_right))
        do(dve.tensor_scalar(self.part[:, 1, :], self.pos[:, :], TOPK - 1, None, ALU.bitwise_and))
        do(dve.tensor_scalar(self.near if t == 0 else self.heads(self.gates[:, t, :], h), self.best, self.best[:, 0:1], None, ALU.subtract))
        settled()
        do(dve.tensor_copy(self.partf, self.part[:, :, :]))
        settled()
        flat_part = self.partf.rearrange("p a k -> p (a k)")
        do(dve.tensor_tensor(self.pick, repeat(flat_part, TOPK), tiled(self.iota[:, :], 2 * TOPK), ALU.is_equal))
        settled()
        p4 = self.pick.rearrange("p (a k) b -> p a k b", a=2)
        do(dve.tensor_tensor(p4, p4, self.atf.unsqueeze(2).to_broadcast([P, 2, TOPK, TOPK]), ALU.mult))
        settled()
        do(dve.tensor_reduce(self.key.rearrange("p a k -> p (a k)"), self.pick, AX.X, ALU.add))
        settled()
        do(dve.scalar_tensor_tensor(out=self.expert, in0=self.key[:, 0, :], scalar=float(N_KEYS), in1=self.key[:, 1, :],
                                    op0=ALU.mult, op1=ALU.add))
        settled()
        do(dve.tensor_copy(self.heads(self.idx[:, t, :], h), self.expert))
        settled()
        dve.sem_inc(self.gate, 1)
        assert n == self.OPS, n


def stage_peer_experts(core, sc, idx, gates, hN, scratch, queries):
    nc, bank, x = core.nc, core.bank, core.x
    SLOTS, PAIR = 8, 2
    TURNS = HK // SLOTS
    gate2 = core.mod[:, 40:48]
    with ExitStack() as st:
        in_q = queries.shape[1] * S // (2 * D)
        more_rows = core.sb("expert_rows", [P, SLOTS - in_q, 2 * D], ctx=st)
        rows = [queries[:, 4 * j:4 * j + 4, :].rearrange("p a t -> p (a t)") for j in range(in_q)]
        rows += [more_rows[:, j, :] for j in range(SLOTS - in_q)]
        place = core.sb("expert_place", [P, SLOTS], U32, ctx=st)
        dot = core.sb("expert_dot", [P, SLOTS], ctx=st)
        act_out = core.sb("expert_act", [P, SLOTS], ctx=st)
        y = scratch[:, 0:2, :].rearrange("p a t -> p (a t)")
        diag = scratch[:, 2:4, :].rearrange("p a t -> p (a t)").rearrange("p (s t) -> p s t", s=SLOTS)
        zeros = scratch[:, 7, S - P:S]
        iota = core.sb("iota16", [P, TOPK], ctx=st)
        den = core.sb("gate_den", [P, PEER_HEADS], ctx=st)
        topk = TopKeys(core, st, sc, idx, gates, scratch[:, 4:8, :], iota)
        names = ["slot_free", "pool_gate", "placed", "dotted", "gelued", "weighted", "zeroed", "y_full", "y_copied", "y_turned", "x_added",
                 "iota_loaded", "ranked", "raised", "normed", "near_ready", "near_raised", "near_summed", "near_inverted"]
        (slot_free, pool_gate, placed, dotted, gelued, weighted, zeroed, y_full, y_copied, y_turned, x_added,
         iota_loaded, ranked, raised, normed, near_ready, near_raised, near_summed, near_inverted) = core.sems(st, *names)
        RANKING = PEER_HEADS
        arrived = [core.ctx.enter_context(nc.semaphore(f"rows_arrived{j}")) for j in range(SLOTS)]
        core.clear(arrived)
        with nc.Block() as block:
            @block.sync
            def _(sp):
                sp.dma_start(iota[:, :], core.dram["iota16"]).then_inc(iota_loaded, 16)
                sp.wait_ge(iota_loaded, 16)

            @block.gpsimd
            def _(pool):
                def gather(t, j, n, column):
                    pool.wait_ge(slot_free, n + 1)
                    pool.sem_inc(pool_gate, 1)
                    pool.tensor_copy(place[:, j:j + 1], idx[:, t, bass.ds(column, 1)]).then_inc(placed, 1)
                    pool.wait_ge(placed, n + 1)
                    pool.sem_inc(pool_gate, 1)
                    pool.indirect_dma_start(rows[j], None, core.dram["uv"],
                                            bass.IndirectOffsetOnAxis(place[:, j:j + 1], 0)).then_inc(arrived[j], 16)

                with pool.Fori(0, PEER_HEADS) as h:
                    pool.wait_ge(near_ready, h + 1)
                    pool.sem_inc(pool_gate, 1)
                    for k in range(TOPK):
                        gather(0, k % SLOTS, h * TOPK + k, h * TOPK + k)
                for t in range(1, TT):
                    pool.wait_ge(ranked, t)
                    with pool.Fori(0, TURNS) as i:
                        for j in range(SLOTS):
                            gather(t, j, i * SLOTS + (t * HK + j), i * SLOTS + j)

            @block.vector
            def _(dve):
                def turn(t, i, per=1, at=0):
                    for g in range(SLOTS // PAIR):
                        for j in range(g * PAIR, g * PAIR + PAIR):
                            dve.wait_ge(arrived[j], i * (16 * per) + (t * TURNS + at + 1) * 16)
                            u = rows[j][:, 0:D]
                            dve.scalar_tensor_tensor(out=u, in0=u, scalar=1.0, in1=hN[:, t, :], op0=ALU.mult, op1=ALU.mult,
                                                     accum_out=dot[:, j:j + 1]).then_inc(dotted, 1)
                        dve.wait_ge(gelued, i * (SLOTS // PAIR * per) + ((t * TURNS + at) * (SLOTS // PAIR) + g + 1))
                        for j in range(g * PAIR, g * PAIR + PAIR):
                            dve.tensor_scalar(diag[:, j, :], core.ident[:, :], act_out[:, j:j + 1],
                                              gates[:, t, bass.ds(i * (SLOTS * per) + (at * SLOTS + j), 1)], ALU.mult, ALU.mult).then_inc(weighted, 1)

                def chosen(t):
                    dve.wait_ge(topk.step, (t + 1) * PEER_HEADS * topk.OPS)
                    dve.sem_inc(ranked, 1)

                def first_head(h, calls):
                    topk.head(dve, 0, h, calls)
                    dve.sem_inc(near_ready, 1)

                def first_gates(h):
                    dve.wait_ge(near_raised, h + 1)
                    dve.tensor_reduce(den[:, 0:1], topk.near, AX.X, ALU.add).then_inc(near_summed, 1)
                    dve.wait_ge(near_summed, h + 1)
                    dve.reciprocal(den[:, 0:1], den[:, 0:1]).then_inc(near_inverted, 1)
                    dve.wait_ge(near_inverted, h + 1)
                    dve.tensor_scalar(topk.heads(gates[:, 0, :], h), topk.near, den[:, 0:1], None, ALU.mult).then_inc(normed, 1)
                    dve.wait_ge(normed, h + 1)
                    dve.sem_inc(topk.gate, 1)

                dve.memset(zeros, 0.0).then_inc(zeroed, 1)
                dve.wait_ge(iota_loaded, 16)
                last = PEER_HEADS - 1
                first_head(0, 0)
                first_gates(0)
                for t in range(TT):
                    if t == 0:
                        with dve.Fori(0, last) as h:
                            turn(0, h, 2, 0)
                            first_head(h + 1, h * 2 + 1)
                            turn(0, h, 2, 1)
                            topk.head(dve, 1, h, h * 2 + 2)
                            first_gates(h + 1)
                        turn(0, last, 2, 0)
                        turn(0, last, 2, 1)
                        topk.head(dve, 1, last, 2 * PEER_HEADS - 1)
                        chosen(1)
                    else:
                        g = gates[:, t, :].rearrange("p (h k) -> p h k", h=PEER_HEADS)
                        so_far = PEER_HEADS + 3 * (t - 1)
                        dve.wait_ge(raised, t)
                        dve.tensor_reduce(den[:, :], g, AX.X, ALU.add).then_inc(normed, 1)
                        dve.wait_ge(normed, so_far + 1)
                        dve.reciprocal(den[:, :], den[:, :]).then_inc(normed, 1)
                        dve.wait_ge(normed, so_far + 2)
                        dve.tensor_tensor(g, g, repeat(den[:, :], TOPK), ALU.mult).then_inc(normed, 1)
                        dve.wait_ge(normed, so_far + 3)
                        with dve.Fori(0, RANKING) as i:
                            turn(t, i)
                            if t + 1 < TT:
                                topk.head(dve, t + 1, i, i + (t + 1) * PEER_HEADS)
                        if t + 1 < TT:
                            chosen(t + 1)
                        with dve.Fori(RANKING, TURNS) as i:
                            turn(t, i)
                    for k in range(KD):
                        if k % 4 == 0:
                            dve.wait_ge(y_turned, 2 * t + k // 4 + 1)
                        xk = x[:, k, t * P:t * P + P]
                        dve.scalar_tensor_tensor(out=xk, in0=bank[4 + k // 4][:, (k % 4) * P:(k % 4) * P + P],
                                                 scalar=gate2[:, k:k + 1], in1=xk, op0=ALU.mult, op1=ALU.add).then_inc(x_added, 1)

            @block.scalar
            def _(act):
                def turn(t, i, per=1, at=0):
                    for g in range(SLOTS // PAIR):
                        act.wait_ge(dotted, i * (SLOTS * per) + (t * HK + at * SLOTS + (g + 1) * PAIR))
                        act.activation(act_out[:, g * PAIR:(g + 1) * PAIR], dot[:, g * PAIR:(g + 1) * PAIR], ACT.Gelu).then_inc(gelued, 1)

                def first_exp(h):
                    act.wait_ge(near_ready, h + 1)
                    act.activation(topk.near, topk.near, ACT.Exp).then_inc(near_raised, 1)

                first_exp(0)
                for t in range(TT):
                    if t == 0:
                        with act.Fori(0, PEER_HEADS - 1) as h:
                            turn(0, h, 2, 0)
                            first_exp(h + 1)
                            turn(0, h, 2, 1)
                        turn(0, PEER_HEADS - 1, 2, 0)
                        turn(0, PEER_HEADS - 1, 2, 1)
                    else:
                        with act.Fori(0, RANKING) as i:
                            turn(t, i)
                    if t + 1 < TT:
                        act.wait_ge(ranked, t + 1)
                        act.activation(gates[:, t + 1, :], gates[:, t + 1, :], ACT.Exp).then_inc(raised, 1)
                    if t > 0:
                        with act.Fori(RANKING, TURNS) as i:
                            turn(t, i)
                    act.wait_ge(y_full, t + 1)
                    if t >= 1:
                        act.wait_ge(y_turned, 2 * t)
                    for half in range(2):
                        act.activation(y[:, half * S:half * S + S], bank[2 * (t % 2) + half][:, :], ACT.Copy).then_inc(y_copied, 1)

            @block.tensor
            def _(pe):
                pe.sem_inc(slot_free, SLOTS)
                pe.wait_ge(zeroed, 1)
                for t in range(TT):
                    yb = [bank[2 * (t % 2) + half] for half in range(2)]
                    if t >= 2:
                        pe.wait_ge(y_copied, 2 * t - 2)
                    for half in range(2):
                        pe.matmul(yb[half][:, :], zeros, hN[:, t, 0:S], start=True, stop=False)
                    with pe.Fori(0, TURNS) as i:
                        for j in range(SLOTS):
                            pe.wait_ge(weighted, i * SLOTS + (t * HK + j + 1))
                            for half in range(2):
                                mm = pe.matmul(yb[half][:, :], diag[:, j, :], rows[j][:, D + half * S:D + half * S + S],
                                               start=False, stop=False, skip_group_check=True)
                            mm.then_inc(slot_free, 1)
                    for half in range(2):
                        mm = pe.matmul(yb[half][:, :], zeros, hN[:, t, 0:S], start=False, stop=True)
                    mm.then_inc(y_full, 1)
                    pe.wait_ge(y_copied, 2 * t + 2)
                    for half in range(2):
                        if t >= 1:
                            pe.wait_ge(x_added, KD * (t - 1) + 4 * half + 4)
                        for k in range(4):
                            mm = pe.transpose(bank[4 + half][:, k * P:k * P + P], y[:, (4 * half + k) * P:(4 * half + k + 1) * P], core.ident[:, :])
                        mm.then_inc(y_turned, 1)


def second_block(core, first, mixed):
    nc = core.nc
    with ExitStack() as st:
        zg = core.sb("zg", [P, 14, S], ctx=st)
        v = core.sb("v2", [P, TT, D], ctx=st)
        with ExitStack() as s2:
            zt = core.sb("zt", [P, 9, S], ctx=s2)
            stage_norm(core, mixed, core.gain[:, 16:24], core.mod[:, 48:56])
            into = lambda z, at, n: ("T", [copy_to(lambda f: z[:, at + f, :])] * n)
            rows = lambda at, n: ("N", copy_to(lambda t: v[:, t, at:at + n]))
            plan = [into(zt, 0, 3), into(zt, 3, 3), rows(0, 384), into(zt, 6, 3), into(zg, 0, 3), into(zg, 3, 3), rows(384, 384),
                    into(zg, 6, 3), into(zg, 9, 2), rows(768, 256),
                    ("T", [copy_to(lambda f: zg[:, 11 + f, :])] * 2 + [copy_to(lambda f: zg[0:16, 13, :])])]
            stage_project(core, first, plan, mixed)
            stage_retention(core, zt, v, mixed)
        logs = core.sb("log_decay", [P, 4, S], ctx=st)
        keys = core.sb("hgrn_keys", [P, 3, S], ctx=st)
        stage_recurrence_inputs(core, zg, logs, keys)
        stage_recurrence(core, 3, 2, lambda i: (zg[:, bass.ds(i, 1), :], keys[:, bass.ds(i, 1), :], logs[:, bass.ds(i, 1), :]),
                         lambda i: v[:, :, bass.ds(i * P + 384, P)], lambda i, n: zg[:, bass.ds(i + 6, 1), :], "hgrn_norm_2", mixed, 3, zg[:, 3:6, :])
        stage_recurrence(core, 1, 4, lambda i: (zg[:, 9:10, :], zg[:, 10:11, :], logs[:, 3:4, :]),
                         lambda i: v[:, :, 768:1024], lambda i, n: zg[:, 11 + n:12 + n, :], "gla_norm_2", mixed, 6, zg[:, 3:6, :])
    stage_residual(core, first + 11, mixed, core.mod[:, 64:72])
    stage_norm(core, mixed, core.gain[:, 24:32], core.mod[:, 72:80])
    stage_moe(core, mixed)


def flat(ap):
    return ap.rearrange("p a t -> p (a t)")


class HeadTail:
    NAMES = ("o_full", "o_copied", "o_squared", "o_summed", "o_rooted", "o_inverted", "o_scaled", "gate_raised", "o_stored")

    def __init__(self, core, st, scratch=None):
        self.core = core
        if scratch is None:
            scratch = core.sb("head_scratch", [P, 3, S], ctx=st)
        self.o, self.sq, self.gate = [scratch[:, i, :] for i in range(3)]
        self.gain = core.sb("head_gain", [P, 1], ctx=st)
        self.sems = core.sems(st, *self.NAMES)

    def on_scalar(self, act, n, halves, gate, gain):
        (o_full, o_copied, o_squared, o_summed, o_rooted, o_inverted, o_scaled, gate_raised, o_stored) = self.sems
        if n >= 1:
            act.wait_ge(o_stored, n)
        act.activation(self.gain[:, :], gain, ACT.Copy).then_inc(gate_raised, 1)
        act.activation(self.gate[:, :], flat(gate), ACT.Silu).then_inc(gate_raised, 1)
        for h in range(2):
            act.wait_ge(o_full, 2 * n + h + 1)
            r = slice(HD * h, HD * h + HD)
            act.activation(self.o[r, :], halves[h][r, :], ACT.Copy).then_inc(o_copied, 1)
        act.wait_ge(o_copied, 2 * n + 2)
        act.activation(self.sq[:, :], self.o[:, :], ACT.Square).then_inc(o_squared, 1)
        act.wait_ge(o_summed, n + 1)
        act.activation(self.sq[:, :], self.core.bank[0][:, :], ACT.Sqrt, scale=1.0 / HD, bias=1e-6).then_inc(o_rooted, 1)

    def on_tensor(self, pe, n, bank_free):
        (o_full, o_copied, o_squared, o_summed, o_rooted, o_inverted, o_scaled, gate_raised, o_stored) = self.sems
        pe.wait_ge(o_squared, n + 1)
        bank_free()
        pe.matmul(self.core.bank[0][:, :], self.core.headones[:, :], self.sq[:, :], start=True, stop=True).then_inc(o_summed, 1)

    def on_vector(self, dve, n, dest):
        (o_full, o_copied, o_squared, o_summed, o_rooted, o_inverted, o_scaled, gate_raised, o_stored) = self.sems
        dve.wait_ge(o_rooted, n + 1)
        dve.reciprocal(self.sq[:, :], self.sq[:, :]).then_inc(o_inverted, 1)
        dve.wait_ge(gate_raised, 2 * n + 2)
        dve.wait_ge(o_inverted, n + 1)
        dve.scalar_tensor_tensor(out=self.o[:, :], in0=self.o[:, :], scalar=self.gain[:, 0:1], in1=self.sq[:, :],
                                 op0=ALU.mult, op1=ALU.mult).then_inc(o_scaled, 1)
        dve.wait_ge(o_scaled, n + 1)
        dve.tensor_tensor(flat(dest), self.o[:, :], self.gate[:, :], ALU.mult).then_inc(o_stored, 1)


def stage_retention(core, zt, v, mixed):
    nc, bank = core.nc, core.bank
    with ExitStack() as st:
        decay = core.sb("ret_decay", [P, RET_HEADS, S], ctx=st)
        rot = core.sb("rot", [P, P], ctx=st)
        cos = core.sb("cos", [P, S], ctx=st)
        sin = core.sb("sin", [P, S], ctx=st)
        qr = core.sb("qk_rot", [P, 2, S], ctx=st)
        part = core.sb("rot_part", [P, 2, S], ctx=st)
        vs = core.sb("v_pair2", [P, TT, P], ctx=st)
        score = core.sb("ret_score", [P, 2, TT, S], ctx=st)
        stage_rotary(core, cos, sin, decay, rot)
        tail = HeadTail(core, st)
        sems = core.sems(st, "turned", "cos_done", "sin_done", "rotated", "v_staged", "scored", "decayed")
        turned, cos_done, sin_done, rotated, v_staged, scored, decayed = sems
        o_full = tail.sems[0]
        UNITS = [(h, j) for h in range(2) for j in range(TT)]
        with nc.Fori(0, 3) as i:
            core.clear(sems + tail.sems)
            with nc.Block() as block:
                @block.gpsimd
                def _(pool):
                    for w in range(2):
                        pool.tensor_tensor(qr[:, w, :], flat(zt[:, bass.ds(i + 3 * w, 1), :]), cos[:, :], ALU.mult).then_inc(cos_done, 1)
                    pool.tensor_copy(vs[:, :, :], v[:, :, bass.ds(i * P, P)]).then_inc(v_staged, 1)

                @block.scalar
                def _(act):
                    tail.on_scalar(act, 0, bank[4:6], zt[:, bass.ds(i + 6, 1), :], core.col("ret_norm_2", i))

                @block.tensor
                def _(pe):
                    for w in range(2):
                        pe.matmul(bank[w][:, :], rot[:, :], flat(zt[:, bass.ds(i + 3 * w, 1), :]), start=True, stop=True).then_inc(turned, 1)
                    pe.wait_ge(rotated, 2)

                    def mix(h):
                        pe.wait_ge(decayed, 4 * h + 4)
                        pe.wait_ge(v_staged, 1)
                        r = slice(HD * h, HD * h + HD)
                        for j in range(TT):
                            mm = pe.matmul(bank[4 + h][r, j * P:S], vs[:, j, r], score[:, h, j, 0:S - j * P], start=j == 0, stop=j == TT - 1)
                        mm.then_inc(o_full, 1)

                    for u, (h, j) in enumerate(UNITS):
                        if u >= 2:
                            pe.wait_ge(decayed, u - 1)
                        r = slice(HD * h, HD * h + HD)
                        pe.matmul(bank[2 + u % 2][:, 0:S - j * P], qr[r, 1, j * P:j * P + P], qr[r, 0, j * P:S],
                                  start=True, stop=True).then_inc(scored, 1)
                        if u == 5:
                            mix(0)
                    mix(1)
                    tail.on_tensor(pe, 0, lambda: pe.wait_ge(sin_done, 1))

                @block.vector
                def _(dve):
                    for w in range(2):
                        dve.wait_ge(turned, w + 1)
                        dve.tensor_tensor(part[:, w, :], bank[w][:, :], sin[:, :], ALU.mult).then_inc(sin_done, 1)
                        dve.wait_ge(cos_done, w + 1)
                        dve.wait_ge(sin_done, w + 1)
                        dve.tensor_tensor(qr[:, w, :], qr[:, w, :], part[:, w, :], ALU.add).then_inc(rotated, 1)
                    for u, (h, j) in enumerate(UNITS):
                        dve.wait_ge(scored, u + 1)
                        dve.tensor_tensor(score[:, h, j, 0:S - j * P], bank[2 + u % 2][:, 0:S - j * P],
                                          flat(decay[:, bass.ds(i * 2 + h, 1), 0:S - j * P]), ALU.mult).then_inc(decayed, 1)
                    tail.on_vector(dve, 0, mixed[:, bass.ds(i, 1), :])


def stage_rotary(core, cos, sin, decay, rot):
    nc = core.nc
    TURN = 2.0 * math.pi
    C1 = 6.28125
    C2 = 0.0019350051879882812
    C3 = TURN - C1 - C2
    MAGIC = 12582912.0
    with ExitStack() as st:
        pos = core.sb("pos", [P, S], I32, ctx=st)
        turns = core.sb("turns", [P, S], ctx=st)
        freq = core.sb("inv_freq", [P, 1], ctx=st)
        loaded, step_sem, reduced, done = core.sems(st, "rot_loaded", "rot_step", "reduced", "rot_done")
        with nc.Block() as block:
            @block.sync
            def _(sp):
                sp.dma_start(pos[:, :], core.dram["positions"].rearrange("a t -> (a t)").partition_broadcast(P)).then_inc(loaded, 16)
                sp.dma_start(freq[:, :], core.dram["inv_freq"]).then_inc(loaded, 16)
                sp.dma_start(decay[:, :, :], core.dram["ret_decay"]).then_inc(loaded, 16)
                sp.dma_start(rot[:, :], core.dram["rot"]).then_inc(loaded, 16)
                sp.wait_ge(loaded, 64)

            @block.vector
            def _(dve):
                step = Steps(dve, step_sem)
                ang = sin[:, :]
                dve.wait_ge(loaded, 64)
                step.then(dve.tensor_copy(cos[:, :], pos[:, :]))
                step.then(dve.tensor_scalar(ang, cos[:, :], freq[:, 0:1], None, ALU.mult))
                step.then(dve.tensor_scalar(turns[:, :], ang, 1.0 / TURN, MAGIC, ALU.mult, ALU.add))
                step.then(dve.tensor_scalar(turns[:, :], turns[:, :], MAGIC, None, ALU.subtract))
                for c in (C1, C2, C3):
                    step.then(dve.scalar_tensor_tensor(out=ang, in0=turns[:, :], scalar=-c, in1=ang, op0=ALU.mult, op1=ALU.add))
                step.then(dve.tensor_scalar(ang, ang, math.pi, -math.pi, ALU.min, ALU.max))
                step.then(dve.scalar_tensor_tensor(out=cos[:, :], in0=ang, scalar=-1.0, in1=ang, op0=ALU.mult, op1=ALU.max))
                dve.tensor_scalar(cos[:, :], cos[:, :], -1.0, 0.5 * math.pi, ALU.mult, ALU.add).then_inc(reduced, 1)

            @block.scalar
            def _(act):
                act.wait_ge(reduced, 1)
                act.activation(cos[:, :], cos[:, :], ACT.Sin).then_inc(done, 1)
                act.activation(sin[:, :], sin[:, :], ACT.Sin).then_inc(done, 1)


def stage_recurrence_inputs(core, zg, logs, keys):
    nc, bank = core.nc, core.bank
    HUGE = 2.0 ** 60
    with ExitStack() as st:
        lb = core.sb("lower_bound", [P, 3, 3], ctx=st)
        low = core.sb("log_low", [P, 3, S], ctx=st)
        u = core.sb("gla_u", [P, 3, S], ctx=st)
        wa2 = core.sb("wa2", [16, P], ctx=st)
        (loaded, step_sem, lb_shift, lb_raised, sig_done, split, logged, u_full, u_biased, u_abs, u_logged, q_raised) = core.sems(
            st, "wa2_loaded", "step", "lb_shifted", "lb_raised", "sig_done", "split", "logged", "u_full", "u_biased", "u_abs",
            "u_logged", "q_raised")
        logits = core.col("hgrn_lb_logits_2", 0, 3)
        with nc.Block() as block:
            @block.sync
            def _(sp):
                sp.dma_start(wa2[:, :], core.dram["wa2"]).then_inc(loaded, 16)
                sp.wait_ge(loaded, 16)

            @block.tensor
            def _(pe):
                pe.wait_ge(loaded, 16)
                pe.matmul(bank[0][:, :], wa2[:, :], zg[0:16, 13, :], start=True, stop=True).then_inc(u_full, 1)

            @block.scalar
            def _(act):
                act.activation(logs[:, 0:3, :], zg[:, 3:6, :], ACT.Sigmoid).then_inc(sig_done, 1)
                act.activation(keys[:, :, :], zg[:, 3:6, :], ACT.Sigmoid, scale=-1.0).then_inc(sig_done, 1)
                act.activation(zg[:, 0:3, :], zg[:, 0:3, :], ACT.Silu).then_inc(q_raised, 1)
                act.wait_ge(u_full, 1)
                act.activation(u[:, 0, :], bank[0][:, :], ACT.Identity, bias=core.col("gla_ba_2")).then_inc(u_biased, 1)
                act.wait_ge(lb_shift, 1)
                act.activation(lb[:, 2, :], lb[:, 2, :], ACT.Exp).then_inc(lb_raised, 1)
                act.wait_ge(u_abs, 1)
                act.activation(u[:, 1, :], u[:, 1, :], ACT.Exp, scale=-1.0).then_inc(u_logged, 1)
                act.wait_ge(u_logged, 1)
                act.activation(u[:, 1, :], u[:, 1, :], ACT.Ln, bias=1.0).then_inc(u_logged, 1)
                act.wait_ge(split, 1)
                act.activation(logs[:, 0:3, :], logs[:, 0:3, :], ACT.Ln).then_inc(logged, 1)
                act.activation(low[:, :, :], low[:, :, :], ACT.Ln).then_inc(logged, 1)

            @block.vector
            def _(dve):
                step = Steps(dve, step_sem)
                dve.tensor_tensor(lb[:, 2, :], logits, logits, ALU.subtract).then_inc(lb_shift, 1)
                dve.wait_ge(lb_raised, 1)
                step.then(dve.reciprocal(lb[:, 0, :], lb[:, 2, :]))
                step.then(dve.tensor_tensor(lb[:, 2, :], lb[:, 2, :], lb[:, 0, :], ALU.mult))
                step.then(dve.tensor_tensor(lb[:, 0, :], lb[:, 2, :], lb[:, 2, :], ALU.subtract))
                step.then(dve.tensor_scalar(lb[:, 1, :], lb[:, 0, :], -1.0, 1.0, ALU.mult, ALU.add))
                dve.wait_ge(u_biased, 1)
                dve.scalar_tensor_tensor(out=u[:, 1, :], in0=u[:, 0, :], scalar=-1.0, in1=u[:, 0, :], op0=ALU.mult, op1=ALU.max).then_inc(u_abs, 1)
                step(dve.tensor_scalar(u[:, 2, :], u[:, 0, :], 0.0, None, ALU.min))
                dve.wait_ge(sig_done, 2)
                for f in range(3):
                    step(dve.tensor_scalar(logs[:, f, :], logs[:, f, :], lb[:, 1, f:f + 1], lb[:, 0, f:f + 1], ALU.mult, ALU.add))
                    step(dve.tensor_scalar(keys[:, f, :], keys[:, f, :], lb[:, 1, f:f + 1], None, ALU.mult))
                step.done()
                step.then(dve.tensor_scalar(low[:, :, :], logs[:, 0:3, :], 1e-30, HUGE, ALU.max, ALU.mult))
                step(dve.tensor_scalar(low[:, :, :], low[:, :, :], 1.0, None, ALU.min))
                step(dve.tensor_scalar(logs[:, 0:3, :], logs[:, 0:3, :], 1.0 / HUGE, None, ALU.max))
                step.done()
                dve.sem_inc(split, 1)
                dve.wait_ge(q_raised, 1)
                step(dve.tensor_scalar(zg[:, 0:3, :], zg[:, 0:3, :], HD ** -0.5, None, ALU.mult))
                step(dve.tensor_scalar(zg[:, 9, :], zg[:, 9, :], 32 ** -0.5, None, ALU.mult))
                dve.wait_ge(u_logged, 2)
                step.then(dve.tensor_tensor(u[:, 2, :], u[:, 2, :], u[:, 1, :], ALU.subtract))
                step(dve.tensor_scalar(logs[:, 3, :], u[:, 2, :], 1.0 / 16.0, None, ALU.mult))
                dve.wait_ge(logged, 2)
                step(dve.tensor_tensor(logs[:, 0:3, :], logs[:, 0:3, :], low[:, :, :], ALU.add))
                step.done()


def stage_recurrence(core, turns, heads, source, values, gate, gain, mixed, base, scratch):
    nc, bank = core.nc, core.bank
    dk = P // heads
    NT = heads // 2
    NLV = len(LEVELS)
    with ExitStack() as st:
        halves = core.sb("halves", [P, NLV, P], U32, ctx=st)
        restart = core.sb("restart", [P, S], ctx=st)
        qs = core.sb("rec_q", [P, S], ctx=st)
        ks = core.sb("rec_k", [P, S], ctx=st)
        cum = core.sb("rec_cum", [P, S], ctx=st)
        q_end = core.sb("rec_q_end", [P, S], ctx=st)
        k_end = core.sb("rec_k_end", [P, S], ctx=st)
        total = core.sb("rec_total", [P, TT], ctx=st)
        far = core.sb("rec_far", [P, 2, P], ctx=st)
        dec = core.sb("rec_dec", [P, 2, S], ctx=st)
        qm = core.sb("rec_qm", [P, 2, S], ctx=st)
        km = core.sb("rec_km", [P, 2, S], ctx=st)
        vs = core.sb("rec_v", [P, TT, heads * HD], ctx=st)
        score = core.sb("rec_score", [P, heads, TT, S], ctx=st)
        tail = HeadTail(core, st, scratch)
        names = ("rec_tables", "staged", "q_staged", "k_staged", "summed", "total_ready", "ended", "raised", "far_ready", "halved", "dec_raised",
                 "q_ready", "k_ready", "scored", "merged", "far_scored", "far_copied")
        sems = core.sems(st, *names)
        (tables, staged, q_staged, k_staged, summed, total_ready, ended, raised, far_ready, halved, dec_raised, q_ready, k_ready, scored,
         merged, far_scored, far_copied) = sems
        o_full = tail.sems[0]
        with nc.Block() as block:
            @block.sync
            def _(sp):
                sp.dma_start(halves[:, :, :], core.dram["halves"]).then_inc(tables, 16)
                sp.dma_start(restart[:, :], core.dram["restart"]).then_inc(tables, 16)
                sp.wait_ge(tables, 32)
        tl = lambda ap, i: ap[:, i * P:i * P + P]

        def turn(i):
            q_in, k_in, log_in = [flat(s) for s in source(i)]
            with nc.Block() as block:
                @block.gpsimd
                def _(pool):
                    pool.tensor_copy(qs[:, :], q_in).then_inc(q_staged, 1)
                    pool.tensor_copy(ks[:, :], k_in).then_inc(k_staged, 1)
                    pool.wait_ge(k_staged, 1)
                    for l in range(NLV):
                        pool.wait_ge(dec_raised, l + 1)
                        if l >= 2:
                            pool.wait_ge(scored, heads * l)
                        pool.tensor_tensor(km[:, l % 2, :], ks[:, :], dec[:, l % 2, :], ALU.mult).then_inc(k_ready, 1)
                    pool.tensor_copy(vs[:, :, :], values(i)).then_inc(staged, 1)

                @block.scalar
                def _(act):
                    act.wait_ge(summed, 1)
                    act.activation(q_end[:, :], cum[:, :], ACT.Exp).then_inc(raised, 1)
                    act.wait_ge(ended, 1)
                    act.activation(k_end[:, :], k_end[:, :], ACT.Exp).then_inc(raised, 1)
                    act.wait_ge(total_ready, 1)
                    act.wait_ge(ended, 1)
                    act.activation(total[:, :], total[:, :], ACT.Exp).then_inc(raised, 1)
                    for l in range(NLV):
                        act.wait_ge(halved, 2 * l + 2)
                        act.activation(dec[:, l % 2, :], dec[:, l % 2, :], ACT.Exp).then_inc(dec_raised, 1)
                    for h in range(heads):
                        act.wait_ge(far_scored, 2 * h + 1)
                        act.activation(score[:, h, 0:3, P:2 * P], bank[4][:, 0:3 * P].rearrange("p (j t) -> p j t", t=P), ACT.Copy).then_inc(far_copied, 1)
                        act.wait_ge(far_scored, 2 * h + 2)
                        act.activation(score[:, h, 0:2, 2 * P:3 * P], bank[5][:, 0:2 * P].rearrange("p (j t) -> p j t", t=P), ACT.Copy).then_inc(far_copied, 1)
                        act.activation(score[:, h, 0, 3 * P:4 * P], bank[5][:, 2 * P:3 * P], ACT.Copy).then_inc(far_copied, 1)
                    for n in range(NT):
                        tail.on_scalar(act, n, bank[6:8], gate(i, n), core.col(gain, i + n))

                @block.tensor
                def _(pe):
                    unit = 0
                    for l in range(NLV + 1):
                        if l == 0:
                            pe.wait_ge(q_staged, 1)
                            pe.wait_ge(k_staged, 1)
                            a, b = ks, qs
                        else:
                            pe.wait_ge(q_ready, l)
                            pe.wait_ge(k_ready, l)
                            a, b = km[:, (l - 1) % 2, :], qm[:, (l - 1) % 2, :]
                        for h in range(heads):
                            if unit >= 4:
                                pe.wait_ge(merged, unit - 3)
                            r = slice(dk * h, dk * h + dk)
                            for t in range(TT):
                                mm = pe.matmul(bank[unit % 4][:, t * P:t * P + P], a[r, t * P:t * P + P], b[r, t * P:t * P + P], start=True, stop=True)
                            mm.then_inc(scored, 1)
                            unit += 1
                    pe.wait_ge(far_ready, 4)
                    for h in range(heads):
                        r = slice(dk * h, dk * h + dk)
                        if h >= 1:
                            pe.wait_ge(far_copied, 3 * h - 2)
                        for j in range(3):
                            mm = pe.matmul(bank[4][:, j * P:j * P + P], k_end[r, j * P:j * P + P], q_end[r, (j + 1) * P:(j + 2) * P], start=True, stop=True)
                        mm.then_inc(far_scored, 1)
                        if h >= 1:
                            pe.wait_ge(far_copied, 3 * h)
                        k0, k1, q2, q3 = far[r, 0, :], k_end[r, P:2 * P], q_end[r, 2 * P:3 * P], far[r, 1, :]
                        for j, (a, b) in enumerate(((k0, q2), (k1, q3), (k0, q3))):
                            mm = pe.matmul(bank[5][:, j * P:j * P + P], a, b, start=True, stop=True)
                        mm.then_inc(far_scored, 1)
                    pe.wait_ge(staged, 1)
                    for n in range(NT):
                        for hh in range(2):
                            h = 2 * n + hh
                            pe.wait_ge(far_copied, 3 * h + 3)
                            pe.wait_ge(merged, heads * NLV + h + 1)
                            if n >= 1:
                                pe.wait_ge(tail.sems[1], 2 * (n - 1) + hh + 1)
                            r = slice(HD * hh, HD * hh + HD)
                            for j in range(TT):
                                mm = pe.matmul(bank[6 + hh][r, j * P:S], vs[:, j, h * HD:h * HD + HD], score[:, h, j, 0:S - j * P], start=j == 0, stop=j == TT - 1)
                            mm.then_inc(o_full, 1)
                        tail.on_tensor(pe, n, lambda: pe.wait_ge(merged, heads * (NLV + 1)))

                @block.vector
                def _(dve):
                    dve.tensor_tensor_scan(cum[:, :], restart[:, :], log_in, 0.0, ALU.mult, ALU.add).then_inc(summed, 1)
                    dve.wait_ge(summed, 1)
                    dve.tensor_copy(total[:, :], cum[:, P - 1:S:P]).then_inc(total_ready, 1)
                    dve.wait_ge(total_ready, 1)
                    c3 = cum[:, :].rearrange("p (i t) -> p i t", t=P)
                    dve.tensor_tensor(k_end[:, :].rearrange("p (i t) -> p i t", t=P), repeat(total[:, :], P), c3, ALU.subtract).then_inc(ended, 1)

                    def halve(l):
                        m = LEVELS[l]
                        if l >= 2:
                            dve.wait_ge(k_ready, l - 1)
                            dve.wait_ge(q_ready, l - 1)
                        cm = cum[:, :].rearrange("p (b w) -> p b w", w=2 * m)
                        dm = dec[:, l % 2, :].rearrange("p (b w) -> p b w", w=2 * m)
                        mid = cm[:, :, m - 1:m].to_broadcast([P, S // (2 * m), m])
                        dve.tensor_tensor(dm[:, :, 0:m], mid, cm[:, :, 0:m], ALU.subtract).then_inc(halved, 1)
                        dve.tensor_tensor(dm[:, :, m:2 * m], cm[:, :, m:2 * m], mid, ALU.subtract).then_inc(halved, 1)

                    def query(l):
                        dve.wait_ge(dec_raised, l + 1)
                        if l >= 2:
                            dve.wait_ge(scored, heads * l)
                        dve.tensor_tensor(qm[:, l % 2, :], qs[:, :], dec[:, l % 2, :], ALU.mult).then_inc(q_ready, 1)

                    def merge(l):
                        for h in range(heads):
                            u = heads * l + h
                            dve.wait_ge(scored, u + 1)
                            src = bank[u % 4][:, :].rearrange("p (i t) -> p i t", t=P)
                            if l == 0:
                                dve.tensor_tensor(score[:, h, :, 0:P], src, tiled(core.ident[:, :], TT), ALU.mult).then_inc(merged, 1)
                            else:
                                dve.wait_ge(merged, heads * (l - 1) + h + 1)
                                dve.copy_predicated(score[:, h, :, 0:P], tiled(halves[:, l - 1, :], TT), src).then_inc(merged, 1)

                    def far_pairs():
                        dve.wait_ge(raised, 3)
                        dve.tensor_tensor(q_end[:, :], q_end[:, :], qs[:, :], ALU.mult).then_inc(far_ready, 1)
                        dve.wait_ge(k_staged, 1)
                        dve.tensor_tensor(k_end[:, :], k_end[:, :], ks[:, :], ALU.mult).then_inc(far_ready, 1)
                        dve.wait_ge(far_ready, 2)
                        dve.tensor_scalar(far[:, 0, :], k_end[:, 0:P], total[:, 1:2], None, ALU.mult).then_inc(far_ready, 1)
                        dve.tensor_scalar(far[:, 1, :], q_end[:, 3 * P:S], total[:, 2:3], None, ALU.mult).then_inc(far_ready, 1)

                    halve(0)
                    halve(1)
                    dve.wait_ge(q_staged, 1)
                    query(0)
                    halve(2)
                    merge(0)
                    for l in range(NLV):
                        if l + 1 < NLV:
                            query(l + 1)
                        if l + 3 < NLV:
                            halve(l + 3)
                        if l == 1:
                            far_pairs()
                        merge(l + 1)
                    for n in range(NT):
                        dest = mixed[:, bass.ds(i + base, 1), :] if turns > 1 else mixed[:, base + n:base + n + 1, :]
                        tail.on_vector(dve, n, dest)

        if turns > 1:
            with nc.Fori(0, turns) as i:
                core.clear(sems + tail.sems)
                turn(i)
        else:
            turn(0)


def stage_route(core, h, hN, place, weight, expert_row, first_weights):
    nc, bank = core.nc, core.bank
    NR = N_GROUPS + N_EXPERTS
    with ExitStack() as st:
        w = core.sb("router_w", [P, KD, NR], ctx=st)
        b = core.sb("router_b", [P, NR], ctx=st)
        iota = core.sb("iota8", [P, TOPK], ctx=st)
        earlier = core.sb("earlier", [P, P], ctx=st)
        table = core.sb("dispatch", [P, 2 * MOE_TILES], ctx=st)
        lg = core.sb("logits", [P, TT, NR], ctx=st)
        top = core.sb("group_top", [P, TT], ctx=st)
        hot = core.sb("group_hot", [P, TT, N_GROUPS], ctx=st)
        free = core.sb("group_free", [P, TT], ctx=st)
        ex = core.sb("group_exp", [P, TT, N_GROUPS], ctx=st)
        gw = core.sb("group_w", [P, TT], ctx=st)
        within = core.sb("within", [P, TT, N_GROUPS, PER_GROUP], ctx=st)
        el = core.sb("expert_logit", [P, TT, PER_GROUP], ctx=st)
        best = core.sb("expert_best", [P, TT, 8], ctx=st)
        at = core.sb("expert_at", [P, TT, 8], U32, ctx=st)
        atf = core.sb("expert_atf", [P, TT, 8], ctx=st)
        pick = core.sb("expert_pick", [P, TT, PER_GROUP], ctx=st)
        chosen = core.sb("expert_chosen", [P, 2, TT, N_EXPERTS], ctx=st)
        either = core.sb("expert_either", [P, TT, N_EXPERTS], ctx=st)
        rank = core.sb("rank", [P, TT, N_EXPERTS], ctx=st)
        beyond = core.sb("rank_beyond", [P, TT, N_EXPERTS], ctx=st)
        count = core.sb("expert_count", [P, N_EXPERTS], ctx=st)
        extra = core.sb("extra_tiles", [P, N_EXPERTS], ctx=st)
        ends = core.sb("extra_ends", [P, N_EXPERTS], ctx=st)
        one = core.sb("expert_ones", [P, N_EXPERTS], ctx=st)
        jump = core.sb("extra_jump", [P, N_EXPERTS], ctx=st)
        whose = core.sb("extra_whose", [P, MOE_EXTRA, N_EXPERTS], ctx=st)
        spot = core.sb("spot", [P, TT], ctx=st)
        rowf = core.sb("expert_rowf", [P, MOE_TILES], ctx=st)
        loaded, scored, h_turned, h_copied, step_sem, g_shifted, g_raised, e_shifted, e_raised, chosen_done, ranked = core.sems(
            st, "router_loaded", "scored", "h_turned", "h_copied", "step", "g_shifted", "g_raised", "e_shifted", "e_raised",
            "chosen_done", "ranked")
        expert_no, extra_no, own_rows = table[:, 0:N_EXPERTS], table[:, N_EXPERTS:MOE_TILES], table[:, MOE_TILES:]
        with nc.Block() as block:
            @block.sync
            def _(sp):
                sp.dma_start(w[:, :, :], core.dram["router_w"].rearrange("(k p) n -> p k n", p=P)).then_inc(loaded, 16)
                sp.dma_start(b[:, :], core.dram["router_b"].rearrange("a n -> (a n)").partition_broadcast(P)).then_inc(loaded, 16)
                sp.dma_start(iota[:, :], core.dram["iota16"]).then_inc(loaded, 16)
                sp.dma_start(earlier[:, :], core.dram["earlier"]).then_inc(loaded, 16)
                sp.dma_start(table[:, :], core.dram["dispatch"]).then_inc(loaded, 16)
                sp.wait_ge(loaded, 80)
                first_weights(sp)

            @block.tensor
            def _(pe):
                pe.wait_ge(loaded, 80)
                for i in range(TT):
                    for k in range(KD):
                        mm = pe.matmul(bank[0][:, i * NR:i * NR + NR], h[:, k, i * P:i * P + P], w[:, k, :], start=k == 0, stop=k == KD - 1)
                mm.then_inc(scored, 1)
                for u in range(2 * TT):
                    i, half = divmod(u, 2)
                    if u >= 4:
                        pe.wait_ge(h_copied, u - 3)
                    for j in range(4):
                        mm = pe.transpose(bank[2 + u % 4][:, j * P:j * P + P], h[:, 4 * half + j, i * P:i * P + P], core.ident[:, :])
                    mm.then_inc(h_turned, 1)
                pe.wait_ge(chosen_done, 1)
                for i in range(TT):
                    for j in range(i + 1):
                        mm = pe.matmul(bank[1][:, i * N_EXPERTS:(i + 1) * N_EXPERTS], earlier[:, :] if j == i else core.ones[:, :],
                                       either[:, j, :], start=j == 0, stop=j == i)
                for j in range(TT):
                    mm = pe.matmul(bank[1][:, TT * N_EXPERTS:(TT + 1) * N_EXPERTS], core.ones[:, :], either[:, j, :],
                                   start=j == 0, stop=j == TT - 1)
                mm.then_inc(ranked, 1)

            @block.scalar
            def _(act):
                act.wait_ge(g_shifted, 1)
                act.activation(ex[:, :, :], ex[:, :, :], ACT.Exp).then_inc(g_raised, 1)
                act.wait_ge(e_shifted, 1)
                act.activation(weight[:, :, 1], weight[:, :, 1], ACT.Exp).then_inc(e_raised, 1)
                for u in range(2 * TT):
                    i, half = divmod(u, 2)
                    act.wait_ge(h_turned, u + 1)
                    act.activation(hN[:, i, half * S:half * S + S], bank[2 + u % 4][:, :], ACT.Copy).then_inc(h_copied, 1)

            @block.vector
            def _(dve):
                step = Steps(dve, step_sem)
                dve.wait_ge(scored, 1)
                dve.wait_ge(loaded, 80)
                step.then(dve.tensor_tensor(lg[:, :, :], bank[0][:, 0:TT * NR].rearrange("p (i n) -> p i n", n=NR), tiled(b[:, :], TT), ALU.add))
                gl = lg[:, :, 0:N_GROUPS]
                step.then(dve.tensor_reduce(top[:, :], gl, AX.X, ALU.max))
                dve.tensor_tensor(ex[:, :, :], gl, repeat(top[:, :], N_GROUPS), ALU.subtract).then_inc(g_shifted, 1)
                step.then(dve.tensor_tensor(hot[:, :, :], gl, repeat(top[:, :], N_GROUPS), ALU.is_equal))
                step.then(dve.tensor_scalar(free[:, :], hot[:, :, 0], -1.0, 1.0, ALU.mult, ALU.add))
                for g in range(1, N_GROUPS):
                    step.then(dve.tensor_tensor(hot[:, :, g], hot[:, :, g], free[:, :], ALU.mult))
                    step.then(dve.tensor_tensor(free[:, :], free[:, :], hot[:, :, g], ALU.subtract))
                el4 = lg[:, :, N_GROUPS:NR].rearrange("p i (g e) -> p i g e", g=N_GROUPS)
                four = [P, TT, N_GROUPS, PER_GROUP]
                hot4 = hot[:, :, :].unsqueeze(3).to_broadcast(four)
                step.then(dve.tensor_tensor(within[:, :, :, :], el4, hot4, ALU.mult))
                step.then(dve.tensor_reduce(el[:, :, :], within[:, :, :, :].rearrange("p i g e -> p i e g"), AX.X, ALU.add))
                for i in range(TT):
                    step(dve.max(best[:, i, :], el[:, i, :]))
                step.done()
                for i in range(TT):
                    step(dve.max_index(at[:, i, :], best[:, i, :], el[:, i, :]))
                dve.tensor_tensor(weight[:, :, 1], best[:, :, 1], best[:, :, 0], ALU.subtract).then_inc(e_shifted, 1)
                step.done()
                step.then(dve.tensor_copy(atf[:, :, :], at[:, :, :]))
                for j in range(2):
                    step.then(dve.tensor_tensor(pick[:, :, :], repeat(atf[:, :, j], PER_GROUP), tiled(iota[:, 0:PER_GROUP], TT), ALU.is_equal))
                    step.then(dve.tensor_tensor(chosen[:, j, :, :].rearrange("p i (g e) -> p i g e", g=N_GROUPS), hot4,
                                                pick[:, :, :].unsqueeze(2).to_broadcast(four), ALU.mult))
                dve.tensor_tensor(either[:, :, :], chosen[:, 0, :, :], chosen[:, 1, :, :], ALU.add).then_inc(chosen_done, 1)
                dve.wait_ge(g_raised, 1)
                step.then(dve.tensor_reduce(gw[:, :], ex[:, :, :], AX.X, ALU.add))
                dve.wait_ge(e_raised, 1)
                step.then(dve.tensor_scalar(weight[:, :, 0], weight[:, :, 1], 1.0, None, ALU.add))
                step.then(dve.tensor_tensor(gw[:, :], gw[:, :], weight[:, :, 0], ALU.mult))
                step.then(dve.reciprocal(weight[:, :, 0], gw[:, :]))
                step.then(dve.tensor_tensor(weight[:, :, 1], weight[:, :, 1], weight[:, :, 0], ALU.mult))
                step(dve.memset(one[:, :], 1.0))
                dve.wait_ge(ranked, 1)
                step(dve.tensor_copy(rank[:, :, :], bank[1][:, 0:TT * N_EXPERTS].rearrange("p (i e) -> p i e", e=N_EXPERTS)))
                step.then(dve.tensor_copy(count[:, :], bank[1][:, TT * N_EXPERTS:(TT + 1) * N_EXPERTS]))
                step.then(dve.tensor_scalar(extra[:, :], count[:, :], float(MOE_T), None, ALU.is_gt))
                for m in range(2, -(-S // MOE_T)):
                    step.then(dve.scalar_tensor_tensor(out=extra[:, :], in0=count[:, :], scalar=float(m * MOE_T), in1=extra[:, :],
                                                       op0=ALU.is_gt, op1=ALU.add))
                step.then(dve.tensor_tensor_scan(ends[:, :], one[:, :], extra[:, :], 0.0, ALU.mult, ALU.add))
                step.then(dve.tensor_tensor(jump[:, :], ends[:, :], extra[:, :], ALU.subtract))
                step.then(dve.scalar_tensor_tensor(out=jump[:, :], in0=jump[:, :], scalar=float(N_EXPERTS - 1), in1=expert_no,
                                                   op0=ALU.add, op1=ALU.subtract))
                step.then(dve.tensor_scalar(beyond[:, :, :], rank[:, :, :], float(MOE_T), None, ALU.is_ge))
                step.then(dve.tensor_tensor(beyond[:, :, :], beyond[:, :, :], tiled(jump[:, :], TT), ALU.mult))
                step.then(dve.tensor_tensor(beyond[:, :, :], beyond[:, :, :], tiled(expert_no, TT), ALU.add))
                step.then(dve.scalar_tensor_tensor(out=rank[:, :, :], in0=beyond[:, :, :], scalar=float(MOE_T), in1=rank[:, :, :],
                                                   op0=ALU.mult, op1=ALU.add))
                for j in range(2):
                    step.then(dve.tensor_tensor(chosen[:, j, :, :], chosen[:, j, :, :], rank[:, :, :], ALU.mult))
                    step.then(dve.tensor_reduce(spot[:, :], chosen[:, j, :, :], AX.X, ALU.add))
                    step.then(dve.tensor_copy(place[:, :, j], spot[:, :]))
                step.then(dve.tensor_tensor(whose[:, :, :], tiled(ends[:, :], MOE_EXTRA), repeat(extra_no, N_EXPERTS), ALU.is_le))
                step(dve.tensor_copy(rowf[:, 0:N_EXPERTS], own_rows[:, 0:N_EXPERTS]))
                step.then(dve.tensor_reduce(rowf[:, N_EXPERTS:], whose[:, :, :], AX.X, ALU.add))
                step.then(dve.tensor_scalar(rowf[:, N_EXPERTS:], rowf[:, N_EXPERTS:], float(N_EXPERTS - 1), float(P), ALU.min, ALU.mult))
                step.then(dve.tensor_tensor(rowf[:, N_EXPERTS:], rowf[:, N_EXPERTS:], own_rows[:, N_EXPERTS:], ALU.add))
                step.then(dve.tensor_copy(expert_row[:, :], rowf[:, :]))


def stage_moe(core, h):
    nc = core.nc
    with ExitStack() as st:
        place = core.sb("place", [P, TT, 2], U32, ctx=st)
        weight = core.sb("expert_weight", [P, TT, 2], ctx=st)
        expert_row = core.sb("expert_row", [P, MOE_TILES], U32, ctx=st)
        weights = core.sb("expert_w", [P, MOE_RING, 3 * KD * D_EXPERT], ctx=st)
        w_first = core.ctx.enter_context(nc.semaphore("first_experts_arrived"))
        core.clear([w_first])

        def first_weights(sp):
            for s in range(MOE_RING):
                sp.dma_start(weights[:, s, :], core.dram["experts"][s * P:(s + 1) * P, :]).then_inc(w_first, 16)

        with ExitStack() as s2:
            hN = core.sb("h_rows", [P, TT, D], ctx=s2)
            stage_route(core, h, hN, place, weight, expert_row, first_weights)
            spot = core.sb("spot_now", [P, TT, 2, 1], U32, ctx=s2)
            spotted, dispatched = core.sems(s2, "spotted", "rows_dispatched")
            with nc.Block() as block:
                @block.gpsimd
                def _(pool):
                    pool.tensor_copy(spot[:, :, :, 0], place[:, :, :]).then_inc(spotted, 1)
                    pool.wait_ge(spotted, 1)
                    for i in range(TT):
                        for j in range(2):
                            pool.indirect_dma_start(core.dispatched, bass.IndirectOffsetOnAxis(spot[:, i, j, :], 0),
                                                    hN[:, i, :], None).then_inc(dispatched, 16)
                    pool.wait_ge(dispatched, 2 * TT * 16)
        stage_experts(core, expert_row, weights, w_first)
        stage_combine(core, place, weight)


def stage_experts(core, expert_row, weights, w_first):
    nc, bank, T = core.nc, core.bank, MOE_T
    NF = D_EXPERT // P
    HALF = KD // 2
    TURNS = MOE_TILES // MOE_RING
    with ExitStack() as st:
        row = core.sb("expert_row_now", [P, MOE_RING], U32, ctx=st)
        tokens = core.sb("tile_tokens", [T, MOE_RING, D], ctx=st)
        tokT = core.sb("tile_turned", [P, MOE_RING, KD, T], ctx=st)
        hid = core.sb("hidden", [P, NF, T], ctx=st)
        hid_hi, hid_lo = [core.sb(n, [P, NF, T], F32R, ctx=st) for n in ("hidden_hi", "hidden_lo")]
        down_hi, down_lo = [core.sb(n, [P, NF, D], F32R, ctx=st) for n in ("down_hi", "down_lo")]
        y = core.sb("tile_y", [T, MOE_RING, D], ctx=st)
        part = lambda s, i: weights[:, s, i * KD * D_EXPERT:(i + 1) * KD * D_EXPERT]
        gate_w = lambda s: part(s, 0).rearrange("p (k n) -> p k n", k=KD)
        up_w = lambda s: part(s, 1).rearrange("p (k n) -> p k n", k=KD)
        down_w = lambda s: part(s, 2).rearrange("p (f n) -> p f n", f=NF)
        turned_bank, (up_bank, gate_bank), y_bank = bank[0:2], bank[2:4], bank[4:6]
        names = ["row_ready", "pool_gate", "tile_turned", "turned_copied", "gate_full", "up_full", "silu_done", "hidden_upper", "hidden_ready",
                 "hidden_split", "down_upper", "down_split", "y_full", "y_copied"]
        (row_ready, pool_gate, tile_turned, turned_copied, gate_full, up_full, silu_done, hidden_upper, hidden_ready, hidden_split, down_upper, down_split,
         y_full, y_copied) = core.sems(st, *names)
        w_arrived = [core.ctx.enter_context(nc.semaphore(f"expert_arrived{s}")) for s in range(MOE_RING)]
        t_arrived = [core.ctx.enter_context(nc.semaphore(f"tokens_arrived{s}")) for s in range(MOE_RING)]
        stored = [core.ctx.enter_context(nc.semaphore(f"tile_stored{s}")) for s in range(MOE_RING)]
        core.clear(w_arrived + t_arrived + stored)
        with nc.Block() as block:
            @block.vector
            def _(dve):
                dve.sem_inc(y_full, MOE_RING)
                dve.sem_inc(y_copied, 2)
                dve.sem_inc(row_ready, MOE_RING)
                for s in range(MOE_RING):
                    dve.sem_inc(stored[s], 16)
        with nc.Block() as block:
            @block.gpsimd
            def _(pool):
                with pool.Fori(1, TURNS) as i:
                    for s in range(MOE_RING):
                        pool.wait_ge(y_full, i * MOE_RING + (s + 1))
                        pool.sem_inc(pool_gate, 1)
                        pool.tensor_copy(row[:, s:s + 1], expert_row[:, bass.ds(i * MOE_RING + s, 1)]).then_inc(row_ready, 1)
                        pool.wait_ge(row_ready, i * MOE_RING + (s + 1))
                        pool.sem_inc(pool_gate, 1)
                        pool.indirect_dma_start(weights[:, s, :], None, core.dram["experts"],
                                                bass.IndirectOffsetOnAxis(row[:, s:s + 1], 0)).then_inc(w_arrived[s], 16)
                pool.wait_ge(pool_gate, 2 * (MOE_TILES - MOE_RING))

            @block.sync
            def _(sp):
                for s in range(MOE_RING):
                    sp.dma_start(tokens[:, s, :], core.dispatched[s * T:(s + 1) * T, :]).then_inc(t_arrived[s], 16)
                with sp.Fori(0, TURNS) as i:
                    for s in range(MOE_RING):
                        sp.wait_ge(y_copied, i * (2 * MOE_RING) + (2 * s + 4))
                        sp.dma_start(core.answered[bass.ds((i * MOE_RING + s) * T, T), :], y[:, s, :]).then_inc(stored[s], 16)
                        sp.wait_ge(tile_turned, i * MOE_RING + (s + 1))
                        sp.dma_start(tokens[:, s, :], core.dispatched[bass.ds((i * MOE_RING + (s + MOE_RING)) * T, T), :]).then_inc(t_arrived[s], 16)
                for s in range(MOE_RING):
                    sp.wait_ge(stored[s], 16 * (TURNS + 1))
                    sp.wait_ge(t_arrived[s], 16 * (TURNS + 1))

            @block.tensor
            def _(pe):
                def turn(s):
                    for k in range(KD):
                        mm = pe.transpose(turned_bank[k // HALF][:, (k % HALF) * T:(k % HALF + 1) * T], tokens[:, s, k * P:(k + 1) * P],
                                          core.ident[0:T, 0:T])
                    mm.then_inc(tile_turned, 1)

                pe.wait_ge(t_arrived[0], 16)
                turn(0)
                pe.wait_ge(w_first, 16 * MOE_RING)
                with pe.Fori(0, TURNS) as i:
                    for s in range(MOE_RING):
                        pe.wait_ge(w_arrived[s], i * 16)
                        pe.wait_ge(turned_copied, i * (2 * MOE_RING) + (2 * s + 2))
                        for to, w, full in ((gate_bank, gate_w(s), gate_full), (up_bank, up_w(s), up_full)):
                            for f in range(NF):
                                for k in range(KD):
                                    mm = pe.matmul(to[:, f * T:f * T + T], w[:, k, f * P:f * P + P], tokT[:, s, k, :],
                                                   start=k == 0, stop=k == KD - 1)
                            mm.then_inc(full, 1)
                        after = (s + 1) % MOE_RING
                        pe.wait_ge(t_arrived[after], i * 16 + (32 if after == 0 else 16))
                        turn(after)
                        pe.wait_ge(hidden_upper, i * MOE_RING + (s + 1))
                        pe.wait_ge(down_split, i * MOE_RING + (s + 1))
                        pe.wait_ge(y_copied, i * (2 * MOE_RING) + (2 * s + 2))
                        for j, (a, w) in enumerate(((hid_hi, down_lo), (hid_hi, down_hi), (hid_lo, down_hi))):
                            if j == 2:
                                pe.wait_ge(hidden_split, i * MOE_RING + (s + 1))
                            for f in range(NF):
                                for half in range(2):
                                    mm = pe.matmul(y_bank[half][0:T, :], a[:, f, :], w[:, f, half * S:half * S + S],
                                                   start=j == 0 and f == 0, stop=j == 2 and f == NF - 1)
                        mm.then_inc(y_full, 1)

            @block.scalar
            def _(act):
                def copy(s):
                    for half in range(2):
                        act.activation(tokT[:, s, half * HALF:(half + 1) * HALF, :],
                                       turned_bank[half][:, 0:HALF * T].rearrange("p (k t) -> p k t", t=T), ACT.Copy).then_inc(turned_copied, 1)

                act.wait_ge(tile_turned, 1)
                copy(0)
                act.wait_ge(w_first, 16 * MOE_RING)
                with act.Fori(0, TURNS) as i:
                    for s in range(MOE_RING):
                        act.wait_ge(w_arrived[s], i * 16)
                        act.wait_ge(y_full, i * MOE_RING + (s + MOE_RING))
                        act.activation(down_hi[:, :, :], down_w(s), ACT.Copy).then_inc(down_upper, 1)
                        act.wait_ge(gate_full, i * MOE_RING + (s + 1))
                        act.activation(hid[:, :, :], gate_bank[:, 0:NF * T].rearrange("p (f t) -> p f t", t=T), ACT.Silu).then_inc(silu_done, 1)
                        act.wait_ge(tile_turned, i * MOE_RING + (s + 2))
                        copy((s + 1) % MOE_RING)

            @block.vector
            def _(dve):
                with dve.Fori(0, TURNS) as i:
                    for s in range(MOE_RING):
                        dve.wait_ge(down_upper, i * MOE_RING + (s + 1))
                        dve.tensor_tensor(down_lo[:, :, :], down_w(s), down_hi[:, :, :].bitcast(F32), ALU.subtract).then_inc(down_split, 1)
                        up = up_bank[:, 0:NF * T].rearrange("p (f t) -> p f t", t=T)
                        dve.wait_ge(silu_done, i * MOE_RING + (s + 1))
                        dve.wait_ge(up_full, i * MOE_RING + (s + 1))
                        dve.tensor_tensor(hid_hi[:, :, :], hid[:, :, :], up, ALU.mult).then_inc(hidden_upper, 1)
                        dve.wait_ge(hidden_upper, i * MOE_RING + (s + 1))
                        dve.tensor_tensor(hid[:, :, :], hid[:, :, :], up, ALU.mult).then_inc(hidden_ready, 1)
                        dve.wait_ge(hidden_ready, i * MOE_RING + (s + 1))
                        dve.tensor_tensor(hid_lo[:, :, :], hid[:, :, :], hid_hi[:, :, :].bitcast(F32), ALU.subtract).then_inc(hidden_split, 1)
                        dve.wait_ge(stored[s], i * 16 + 16)
                        dve.wait_ge(y_full, i * MOE_RING + (s + 1 + MOE_RING))
                        for half in range(2):
                            dve.tensor_copy(y[:, s, half * S:half * S + S], y_bank[half][0:T, :]).then_inc(y_copied, 1)


def stage_combine(core, place, weight):
    nc, bank, x = core.nc, core.bank, core.x
    gate = core.mod[:, 88:96]
    with ExitStack() as st:
        rows = core.sb("answers", [P, TT, 2, D], ctx=st)
        spot = core.sb("spot_then", [P, TT, 2, 1], U32, ctx=st)
        spotted, weighed, y_turned, x_added = core.sems(st, "spotted", "weighed", "y_turned", "x_added")
        arrived = [core.ctx.enter_context(nc.semaphore(f"answers_arrived{i}")) for i in range(TT)]
        core.clear(arrived)
        with nc.Block() as block:
            @block.gpsimd
            def _(pool):
                pool.tensor_copy(spot[:, :, :, 0], place[:, :, :]).then_inc(spotted, 1)
                pool.wait_ge(spotted, 1)
                for i in range(TT):
                    for j in range(2):
                        pool.indirect_dma_start(rows[:, i, j, :], None, core.answered,
                                                bass.IndirectOffsetOnAxis(spot[:, i, j, :], 0)).then_inc(arrived[i], 16)

            @block.vector
            def _(dve):
                for i in range(TT):
                    dve.wait_ge(arrived[i], 32)
                    dve.tensor_scalar(rows[:, i, 0, :], rows[:, i, 0, :], weight[:, i, 0:1], None, ALU.mult).then_inc(weighed, 1)
                    dve.wait_ge(weighed, 2 * i + 1)
                    dve.scalar_tensor_tensor(out=rows[:, i, 0, :], in0=rows[:, i, 1, :], scalar=weight[:, i, 1:2], in1=rows[:, i, 0, :],
                                             op0=ALU.mult, op1=ALU.add).then_inc(weighed, 1)
                    for k in range(KD):
                        if k % 4 == 0:
                            dve.wait_ge(y_turned, 2 * i + k // 4 + 1)
                        xk = x[:, k, i * P:i * P + P]
                        dve.scalar_tensor_tensor(out=xk, in0=bank[(2 * i + k // 4) % 4][:, (k % 4) * P:(k % 4) * P + P],
                                                 scalar=gate[:, k:k + 1], in1=xk, op0=ALU.mult, op1=ALU.add).then_inc(x_added, 1)

            @block.tensor
            def _(pe):
                for i in range(TT):
                    pe.wait_ge(weighed, 2 * i + 2)
                    for half in range(2):
                        if i >= 2:
                            pe.wait_ge(x_added, KD * (i - 2) + 4 * half + 4)
                        for k in range(4):
                            mm = pe.transpose(bank[(2 * i + half) % 4][:, k * P:k * P + P],
                                              rows[:, i, 0, (4 * half + k) * P:(4 * half + k + 1) * P], core.ident[:, :])
                        mm.then_inc(y_turned, 1)


def stage_output(core, buf, out):
    nc = core.nc
    stage_norm(core, buf, core.col("norm_final_2", 0, 8), None)
    stored = core.sems(core.ctx, "stored")
    with nc.Block() as block:
        @block.sync
        def _(sp):
            sp.dma_start(out.rearrange("(k p) t -> p k t", p=P), buf[:, :, :]).then_inc(stored, 16)
            sp.wait_ge(stored, 16)


def kernel(**inputs):
    import concourse.bacc as bacc
    from concourse.bass_utils import run_bass_kernel_spmd

    arrays = {f"in_{k}": a for k, a in inputs_to_dram(inputs).items()}
    nc = bacc.Bacc("TRN2", target_bir_lowering=False, num_devices=1)
    dram = {k[3:]: nc.dram_tensor(k, a.shape, mybir.dt.from_np(a.dtype), kind="ExternalInput").ap() for k, a in arrays.items()}
    out = nc.dram_tensor("outT", (D, S), F32, kind="ExternalOutput").ap()
    build(nc, dram, out)
    result = run_bass_kernel_spmd(nc, [arrays], core_ids=[0])
    return np.ascontiguousarray(result.results[0]["outT"].T)[None]
```
